# Optimizing a Trainium2 kernel written in Bass

```python
import jax, jax.numpy as jnp
from jax import lax
import numpy as np
import math

D_MODEL = 1024
BATCH = 1
SEQ = 512
DEPTH = 1

D_MIX = D_MODEL
HEAD_DIM = 64
GDN_HEADS = (D_MIX // 2) // HEAD_DIM
GDN_WIDTH = GDN_HEADS * HEAD_DIM
CONV_K = 4
CHUNK = 64
SWA_Q_HEADS = (D_MIX // 2) // HEAD_DIM
SWA_KV_HEADS = 2
SWA_GROUP = SWA_Q_HEADS // SWA_KV_HEADS
SWA_Q_WIDTH = SWA_Q_HEADS * HEAD_DIM
SWA_KV_WIDTH = SWA_KV_HEADS * HEAD_DIM
WINDOW = 128
BLOCK = 128
ROPE_THETA = 10000.0
N_GROUPS = 4
EXPERTS_PER_GROUP = 8
N_EXPERTS = N_GROUPS * EXPERTS_PER_GROUP
TOP_K = 2
D_EXPERT = D_MODEL // 4
EPS = 1e-6
IN_WIDTHS = (GDN_WIDTH, GDN_WIDTH, GDN_WIDTH, GDN_WIDTH, GDN_HEADS, GDN_HEADS,
             SWA_Q_WIDTH, SWA_KV_WIDTH, SWA_KV_WIDTH)
IN_WIDTH = sum(IN_WIDTHS)
MIX_OUT_WIDTH = GDN_WIDTH + SWA_Q_WIDTH


def rms_norm(x, gain):
    xf = x.astype(jnp.float32)
    y = xf * lax.rsqrt(jnp.mean(xf * xf, axis=-1, keepdims=True) + EPS)
    return (y * gain.astype(jnp.float32)).astype(x.dtype)

def l2_norm(x):
    return x * lax.rsqrt(jnp.sum(x * x, axis=-1, keepdims=True) + EPS)

def modulate(x, shift, scale):
    return x * (1 + scale[:, None, :]) + shift[:, None, :]

def causal_conv_silu(x, w):
    seq = x.shape[1]
    xp = jnp.pad(x, ((0, 0), (CONV_K - 1, 0), (0, 0)))
    y = xp[:, 0:seq] * w[0]
    for j in range(1, CONV_K):
        y = y + xp[:, j:j + seq] * w[j]
    return jax.nn.silu(y)

def rope(x, positions):
    half = x.shape[-1] // 2
    inv_freq = jnp.power(jnp.float32(ROPE_THETA), -jnp.arange(half, dtype=jnp.float32) / half)
    ang = positions.astype(jnp.float32)[..., None] * inv_freq
    cos = jnp.cos(ang)[:, :, None, :]
    sin = jnp.sin(ang)[:, :, None, :]
    xf = x.astype(jnp.float32)
    x1, x2 = xf[..., :half], xf[..., half:]
    out = jnp.concatenate([x1 * cos - x2 * sin, x1 * sin + x2 * cos], axis=-1)
    return out.astype(x.dtype)

def chunked_gated_delta_rule(q, k, v, g, beta):
    bsz, seq, heads, dh = q.shape
    n_chunks = seq // CHUNK

    def to_chunks(t):
        return t.reshape(bsz, n_chunks, CHUNK, heads, -1).transpose(0, 3, 1, 2, 4)

    q, k, v = to_chunks(q), to_chunks(k), to_chunks(v)
    g = g.reshape(bsz, n_chunks, CHUNK, heads).transpose(0, 3, 1, 2)
    beta = beta.reshape(bsz, n_chunks, CHUNK, heads).transpose(0, 3, 1, 2)
    G = jnp.cumsum(g, axis=-1)

    idx = jnp.arange(CHUNK)
    lower_incl = idx[:, None] >= idx[None, :]
    strict = idx[:, None] > idx[None, :]
    diff = G[..., :, None] - G[..., None, :]
    decay = jnp.where(lower_incl, jnp.exp(jnp.where(lower_incl, diff, 0.0)), 0.0)

    kb = k * beta[..., None]
    vb = v * beta[..., None]
    m = jnp.where(strict, jnp.einsum('bhncd,bhnsd->bhncs', kb, k) * decay, 0.0)
    eye = jnp.eye(CHUNK, dtype=jnp.float32)
    a_mat = eye + m
    t_mat = lax.linalg.triangular_solve(a_mat, jnp.broadcast_to(eye, a_mat.shape),
                                        left_side=True, lower=True)
    u = jnp.einsum('bhncs,bhnse->bhnce', t_mat, vb)
    w = jnp.einsum('bhncs,bhnsd->bhncd', t_mat, kb * jnp.exp(G)[..., None])
    qg = q * jnp.exp(G)[..., None]
    attn = jnp.einsum('bhncd,bhnsd->bhncs', q, k) * decay
    g_last = G[..., -1]
    k_dec = k * jnp.exp(g_last[..., None] - G)[..., None]

    xs = tuple(jnp.moveaxis(t, 2, 0) for t in (u, w, qg, attn, k_dec, g_last))

    def step(state, inp):
        u_n, w_n, qg_n, attn_n, kdec_n, gl_n = inp
        v_new = u_n - jnp.einsum('bhcd,bhde->bhce', w_n, state)
        o_n = (jnp.einsum('bhcd,bhde->bhce', qg_n, state)
               + jnp.einsum('bhcs,bhse->bhce', attn_n, v_new))
        state = (state * jnp.exp(gl_n)[..., None, None]
                 + jnp.einsum('bhcd,bhce->bhde', kdec_n, v_new))
        return state, o_n

    s0 = jnp.zeros((bsz, heads, dh, v.shape[-1]), jnp.float32)
    _, o = lax.scan(step, s0, xs)
    return o.transpose(1, 0, 3, 2, 4).reshape(bsz, seq, heads, -1)

def gated_deltanet(q_in, k_in, v_in, z, a, b, conv_w, a_log, dt_bias, out_norm):
    bsz, seq, _ = q_in.shape
    qkv = causal_conv_silu(jnp.concatenate([q_in, k_in, v_in], axis=-1), conv_w)
    q, k, v = jnp.split(qkv.astype(jnp.float32), 3, axis=-1)
    q = l2_norm(q.reshape(bsz, seq, GDN_HEADS, HEAD_DIM)) * (HEAD_DIM ** -0.5)
    k = l2_norm(k.reshape(bsz, seq, GDN_HEADS, HEAD_DIM))
    v = v.reshape(bsz, seq, GDN_HEADS, HEAD_DIM)
    g = -jnp.exp(a_log.astype(jnp.float32)) * jax.nn.softplus(
        a.astype(jnp.float32) + dt_bias.astype(jnp.float32))
    beta = jax.nn.sigmoid(b.astype(jnp.float32))
    o = chunked_gated_delta_rule(q, k, v, g, beta)
    zf = z.astype(jnp.float32).reshape(bsz, seq, GDN_HEADS, HEAD_DIM)
    o = rms_norm(o, out_norm) * jax.nn.silu(zf)
    return o.reshape(bsz, seq, GDN_WIDTH).astype(q_in.dtype)

def sliding_window_attention(q, k, v, q_norm, k_norm, sinks, positions):
    bsz, seq, _ = q.shape
    n_blk = seq // BLOCK
    q = rope(rms_norm(q.reshape(bsz, seq, SWA_Q_HEADS, HEAD_DIM), q_norm), positions)
    k = rope(rms_norm(k.reshape(bsz, seq, SWA_KV_HEADS, HEAD_DIM), k_norm), positions)
    v = v.reshape(bsz, seq, SWA_KV_HEADS, HEAD_DIM)

    qb = q.reshape(bsz, n_blk, BLOCK, SWA_KV_HEADS, SWA_GROUP, HEAD_DIM)

    def band(t):
        tb = t.reshape(bsz, n_blk, BLOCK, SWA_KV_HEADS, HEAD_DIM)
        prev = jnp.pad(tb[:, :-1], ((0, 0), (1, 0), (0, 0), (0, 0), (0, 0)))
        return jnp.concatenate([prev, tb], axis=2)

    k_band, v_band = band(k), band(v)
    scores = jnp.einsum('bnqhgd,bnkhd->bnhgqk', qb, k_band).astype(jnp.float32) * (HEAD_DIM ** -0.5)

    qi = jnp.arange(BLOCK)[:, None]
    kj = jnp.arange(2 * BLOCK)[None, :]
    rel = qi + BLOCK - kj
    in_window = (rel >= 0) & (rel < WINDOW)
    has_prev = jnp.arange(n_blk)[:, None, None] > 0
    valid = in_window[None] & (has_prev | (kj >= BLOCK)[None])
    scores = jnp.where(valid[None, :, None, None], scores, -jnp.inf)

    sink = sinks.astype(jnp.float32).reshape(SWA_KV_HEADS, SWA_GROUP)[None, None, :, :, None]
    mx = jnp.maximum(scores.max(axis=-1), sink)
    p = jnp.exp(scores - mx[..., None])
    denom = p.sum(axis=-1) + jnp.exp(sink - mx)
    p = p / denom[..., None]
    out = jnp.einsum('bnhgqk,bnkhd->bnqhgd', p, v_band.astype(jnp.float32))
    return out.reshape(bsz, seq, SWA_Q_WIDTH).astype(q.dtype)

def hierarchical_moe(h, w_group, b_group, w_router, b_router, w_gate, w_up, w_down):
    bsz, seq, d = h.shape
    t = h.reshape(-1, d)
    group_prob = jax.nn.softmax((t @ w_group + b_group).astype(jnp.float32), axis=-1)
    p_group, g_idx = lax.top_k(group_prob, 1)
    expert_logits = (t @ w_router + b_router).astype(jnp.float32).reshape(
        -1, N_GROUPS, EXPERTS_PER_GROUP)
    g_onehot = jax.nn.one_hot(g_idx[:, 0], N_GROUPS, dtype=jnp.float32)
    in_group = jnp.einsum('tg,tge->te', g_onehot, expert_logits)
    p_exp = jax.nn.softmax(in_group, axis=-1)
    w_top, e_idx = lax.top_k(p_exp, TOP_K)
    w_top = w_top / jnp.sum(w_top, axis=-1, keepdims=True) * p_group
    expert_ids = g_idx * EXPERTS_PER_GROUP + e_idx
    combine = jnp.sum(jax.nn.one_hot(expert_ids, N_EXPERTS, dtype=jnp.float32)
                      * w_top[..., None], axis=1)
    out = jnp.zeros(t.shape, jnp.float32)
    for e in range(N_EXPERTS):
        hid = jax.nn.silu(t @ w_gate[e]) * (t @ w_up[e])
        out = out + combine[:, e:e + 1] * (hid @ w_down[e]).astype(jnp.float32)
    return out.astype(h.dtype).reshape(bsz, seq, d)

def first_inputs(seed: int = 0) -> dict:
    key = jax.random.key(seed)
    ks = jax.random.split(key, 24)
    f32 = jnp.float32
    nrm = lambda k, shape: jax.random.normal(k, shape, f32)
    dt = jnp.exp(jax.random.uniform(ks[6], (DEPTH, GDN_HEADS), f32,
                                    jnp.log(jnp.float32(1e-3)), jnp.log(jnp.float32(1e-1))))
    return {
        "x": nrm(ks[0], (BATCH, SEQ, D_MODEL)),
        "c": nrm(ks[1], (BATCH, D_MODEL)),
        "positions": jnp.broadcast_to(jnp.arange(SEQ, dtype=jnp.int32), (BATCH, SEQ)),
        "w_ada": nrm(ks[2], (DEPTH, D_MODEL, 6 * D_MODEL)) * (0.5 * D_MODEL ** -0.5),
        "b_ada": 0.01 * nrm(ks[3], (DEPTH, 6 * D_MODEL)),
        "norm_mix": 1.0 + 0.1 * nrm(ks[4], (DEPTH, D_MODEL)),
        "w_in": nrm(ks[5], (DEPTH, D_MODEL, IN_WIDTH)) * D_MODEL ** -0.5,
        "conv_w": nrm(ks[7], (DEPTH, CONV_K, 3 * GDN_WIDTH)) * CONV_K ** -0.5,
        "a_log": jnp.log(jax.random.uniform(ks[8], (DEPTH, GDN_HEADS), f32, 1.0, 16.0)),
        "dt_bias": jnp.log(jnp.expm1(dt)),
        "gdn_out_norm": 1.0 + 0.1 * nrm(ks[9], (DEPTH, HEAD_DIM)),
        "q_norm": 1.0 + 0.1 * nrm(ks[10], (DEPTH, HEAD_DIM)),
        "k_norm": 1.0 + 0.1 * nrm(ks[11], (DEPTH, HEAD_DIM)),
        "sinks": nrm(ks[12], (DEPTH, SWA_Q_HEADS)),
        "w_out": nrm(ks[13], (DEPTH, MIX_OUT_WIDTH, D_MODEL)) * MIX_OUT_WIDTH ** -0.5,
        "norm_ffn": 1.0 + 0.1 * nrm(ks[14], (DEPTH, D_MODEL)),
        "w_group": nrm(ks[15], (DEPTH, D_MODEL, N_GROUPS)) * D_MODEL ** -0.5,
        "b_group": 0.01 * nrm(ks[16], (DEPTH, N_GROUPS)),
        "w_router": nrm(ks[17], (DEPTH, D_MODEL, N_EXPERTS)) * D_MODEL ** -0.5,
        "b_router": 0.01 * nrm(ks[18], (DEPTH, N_EXPERTS)),
        "w_gate": nrm(ks[19], (DEPTH, N_EXPERTS, D_MODEL, D_EXPERT)) * D_MODEL ** -0.5,
        "w_up": nrm(ks[20], (DEPTH, N_EXPERTS, D_MODEL, D_EXPERT)) * D_MODEL ** -0.5,
        "w_down": nrm(ks[21], (DEPTH, N_EXPERTS, D_EXPERT, D_MODEL)) * D_EXPERT ** -0.5,
    }

def first_block(x, c, positions, w_ada, b_ada, norm_mix, w_in, conv_w, a_log, dt_bias,
              gdn_out_norm, q_norm, k_norm, sinks, w_out, norm_ffn, w_group, b_group,
              w_router, b_router, w_gate, w_up, w_down):
    split_points = tuple(int(s) for s in np.cumsum(IN_WIDTHS)[:-1])
    c_act = jax.nn.silu(c)
    for l in range(DEPTH):
        mod = c_act @ w_ada[l] + b_ada[l]
        shift1, scale1, gate1, shift2, scale2, gate2 = jnp.split(mod, 6, axis=-1)

        h = modulate(rms_norm(x, norm_mix[l]), shift1, scale1)
        proj = h @ w_in[l]
        (g_q, g_k, g_v, g_z, g_a, g_b, s_q, s_k, s_v) = jnp.split(proj, split_points, axis=-1)
        gdn_out = gated_deltanet(g_q, g_k, g_v, g_z, g_a, g_b, conv_w[l], a_log[l],
                                 dt_bias[l], gdn_out_norm[l])
        swa_out = sliding_window_attention(s_q, s_k, s_v, q_norm[l], k_norm[l],
                                           sinks[l], positions)
        mixed = jnp.concatenate([gdn_out, swa_out], axis=-1) @ w_out[l]
        x = x + gate1[:, None, :] * mixed

        h2 = modulate(rms_norm(x, norm_ffn[l]), shift2, scale2)
        ffn = hierarchical_moe(h2, w_group[l], b_group[l], w_router[l], b_router[l],
                               w_gate[l], w_up[l], w_down[l])
        x = x + gate2[:, None, :] * ffn
    return x


HEAD_DIM_2 = 128
HEADS_PER_GROUP = 4
DILATED_GROUPS = ((128, 1), (512, 4), (2048, 16))
N_GROUPS_2 = 3
N_ATTN_HEADS = N_GROUPS_2 * HEADS_PER_GROUP
ATTN_QKV_WIDTH = N_ATTN_HEADS * HEAD_DIM_2
ATTN_OUT_WIDTH = HEADS_PER_GROUP * HEAD_DIM_2
BAND_BLOCK = 128
LRU_WIDTH = D_MODEL
LRU_HEADS = 4
LRU_HEAD_DIM = LRU_WIDTH // LRU_HEADS
CONV_WIDTH = 4
LRU_C = 8.0
D_FF = 2816
REL_BUCKETS = 32
REL_MAX_DISTANCE = 2048
NORM_EPS = 1e-6
N_BRANCHES = 2
W_IN_COLS = 3 * ATTN_QKV_WIDTH + 2 * LRU_WIDTH + N_BRANCHES * D_MODEL


def rms_norm_2(x, g):
    xf = x.astype(jnp.float32)
    y = xf * lax.rsqrt(jnp.mean(xf * xf, axis=-1, keepdims=True) + NORM_EPS)
    return (y * g.astype(jnp.float32)).astype(x.dtype)

def swiglu(x, w_gate, w_up, w_down):
    return (jax.nn.silu(x @ w_gate) * (x @ w_up)) @ w_down

def t5_causal_bucket(distance):
    max_exact = REL_BUCKETS // 2
    nf = jnp.maximum(distance, 1).astype(jnp.float32)
    large = max_exact + (jnp.log(nf / max_exact) / math.log(REL_MAX_DISTANCE / max_exact)
                         * (REL_BUCKETS - max_exact)).astype(jnp.int32)
    large = jnp.minimum(large, REL_BUCKETS - 1)
    return jnp.where(distance < max_exact, distance, large)

def dilated_group_attention(q, k, v, bias_table_g, window, dilation):
    B, S, H, E = q.shape
    d = dilation
    L = S // d
    nb = -(-L // BAND_BLOCK)
    Lp = nb * BAND_BLOCK
    m_max = window // d

    def to_blocks(t):
        t = t.reshape(B, L, d, H, E)
        t = jnp.pad(t, ((0, 0), (0, Lp - L), (0, 0), (0, 0), (0, 0)))
        return t.reshape(B, nb, BAND_BLOCK, d, H, E)

    def band(t):
        tb = jnp.pad(to_blocks(t), ((0, 0), (1, 0), (0, 0), (0, 0), (0, 0), (0, 0)))
        return jnp.concatenate([tb[:, :-1], tb[:, 1:]], axis=2)

    qb = to_blocks(q)
    kb = band(k)
    vb = band(v)

    qi = jnp.arange(BAND_BLOCK)[:, None]
    kj = jnp.arange(2 * BAND_BLOCK)[None, :]
    steps = qi + BAND_BLOCK - kj
    key_idx = jnp.arange(nb)[:, None, None] * BAND_BLOCK - BAND_BLOCK + kj[None]
    valid = (steps >= 0) & (steps <= m_max) & (key_idx >= 0)
    bucket = t5_causal_bucket(jnp.maximum(steps, 0) * d)
    bias = jnp.transpose(bias_table_g[bucket], (2, 0, 1)).astype(jnp.float32)

    scale = 1.0 / math.sqrt(E)
    scores = jnp.einsum('bnqphe,bnkphe->bphnqk', qb, kb).astype(jnp.float32) * scale
    scores = scores + bias[None, None, :, None]
    scores = jnp.where(valid[None, None, None], scores, -jnp.inf)
    mx = jnp.max(scores, axis=-1, keepdims=True)
    e = jnp.exp(scores - mx)
    den = jnp.sum(e, axis=-1, keepdims=True)
    o = jnp.einsum('bphnqk,bnkphe->bnqphe', (e / den).astype(v.dtype), vb)
    lse = (mx + jnp.log(den))[..., 0]
    o = o.reshape(B, Lp, d, H, E)[:, :L].reshape(B, S, H, E)
    lse = jnp.transpose(lse, (0, 3, 4, 1, 2)).reshape(B, Lp, d, H)[:, :L].reshape(B, S, H)
    return o, lse

def rg_lru_branch(xr, conv_w, conv_b, w_x, b_x, w_a, b_a, a_param):
    B, S, C = xr.shape
    xc = lax.conv_general_dilated(
        xr, conv_w[:, None, :].astype(xr.dtype), window_strides=(1,),
        padding=((CONV_WIDTH - 1, 0),), dimension_numbers=('NWC', 'WIO', 'NWC'),
        feature_group_count=C) + conv_b
    xh = xc.reshape(B, S, LRU_HEADS, LRU_HEAD_DIM)
    gate_x = jax.nn.sigmoid(jnp.einsum('bshi,hij->bshj', xh, w_x) + b_x).reshape(B, S, C)
    gate_a = jax.nn.sigmoid(jnp.einsum('bshi,hij->bshj', xh, w_a) + b_a).reshape(B, S, C)
    log_a = -LRU_C * gate_a.astype(jnp.float32) * jax.nn.softplus(-a_param.astype(jnp.float32))
    a = jnp.exp(log_a)
    b = jnp.sqrt(-jnp.expm1(2.0 * log_a)) * (gate_x * xc).astype(jnp.float32)

    def combine(left, right):
        a_l, b_l = left
        a_r, b_r = right
        return a_l * a_r, a_r * b_l + b_r

    _, h = lax.associative_scan(combine, (a, b), axis=1)
    return h.astype(xr.dtype)

def second_inputs(seed: int = 0) -> dict:
    key = jax.random.key(seed)
    ks = jax.random.split(key, 32)
    f32 = jnp.float32

    def w(k, shape, fan_in):
        return jax.random.normal(k, shape, f32) * (fan_in ** -0.5)

    def gain(k):
        return 1.0 + 0.05 * jax.random.normal(k, (DEPTH, D_MODEL), f32)

    a0 = jax.random.uniform(ks[20], (DEPTH, LRU_WIDTH), f32, 0.9, 0.999)
    s = a0 ** (1.0 / LRU_C)
    a_param = jnp.log(s) - jnp.log1p(-s)

    return {
        "x": jax.random.normal(ks[0], (BATCH, SEQ, D_MODEL), f32),
        "ffn1_norm_pre": gain(ks[1]),
        "ffn1_norm_post": gain(ks[2]),
        "ffn1_w_gate": w(ks[3], (DEPTH, D_MODEL, D_FF), D_MODEL),
        "ffn1_w_up": w(ks[4], (DEPTH, D_MODEL, D_FF), D_MODEL),
        "ffn1_w_down": w(ks[5], (DEPTH, D_FF, D_MODEL), D_FF),
        "mix_norm_pre": gain(ks[6]),
        "mix_norm_post": gain(ks[7]),
        "w_in": w(ks[8], (DEPTH, D_MODEL, W_IN_COLS), D_MODEL),
        "rel_bias_table": 0.2 * jax.random.normal(ks[9], (REL_BUCKETS, N_ATTN_HEADS), f32),
        "conv_w": w(ks[10], (DEPTH, CONV_WIDTH, LRU_WIDTH), CONV_WIDTH),
        "conv_b": 0.02 * jax.random.normal(ks[11], (DEPTH, LRU_WIDTH), f32),
        "lru_w_x": w(ks[12], (DEPTH, LRU_HEADS, LRU_HEAD_DIM, LRU_HEAD_DIM), LRU_HEAD_DIM),
        "lru_b_x": 0.02 * jax.random.normal(ks[13], (DEPTH, LRU_HEADS, LRU_HEAD_DIM), f32),
        "lru_w_a": w(ks[14], (DEPTH, LRU_HEADS, LRU_HEAD_DIM, LRU_HEAD_DIM), LRU_HEAD_DIM),
        "lru_b_a": 0.02 * jax.random.normal(ks[15], (DEPTH, LRU_HEADS, LRU_HEAD_DIM), f32),
        "lru_a_param": a_param,
        "w_attn_branch": w(ks[16], (DEPTH, ATTN_OUT_WIDTH, D_MODEL), ATTN_OUT_WIDTH),
        "w_rec_branch": w(ks[17], (DEPTH, LRU_WIDTH, D_MODEL), LRU_WIDTH),
        "w_out": w(ks[18], (DEPTH, D_MODEL, D_MODEL), D_MODEL),
        "ffn2_norm_pre": gain(ks[21]),
        "ffn2_norm_post": gain(ks[22]),
        "ffn2_w_gate": w(ks[23], (DEPTH, D_MODEL, D_FF), D_MODEL),
        "ffn2_w_up": w(ks[24], (DEPTH, D_MODEL, D_FF), D_MODEL),
        "ffn2_w_down": w(ks[25], (DEPTH, D_FF, D_MODEL), D_FF),
    }

def second_block(x, ffn1_norm_pre, ffn1_norm_post, ffn1_w_gate, ffn1_w_up, ffn1_w_down,
              mix_norm_pre, mix_norm_post, w_in, rel_bias_table, conv_w, conv_b,
              lru_w_x, lru_b_x, lru_w_a, lru_b_a, lru_a_param,
              w_attn_branch, w_rec_branch, w_out,
              ffn2_norm_pre, ffn2_norm_post, ffn2_w_gate, ffn2_w_up, ffn2_w_down):
    B, S, _ = x.shape
    splits = [ATTN_QKV_WIDTH, 2 * ATTN_QKV_WIDTH, 3 * ATTN_QKV_WIDTH,
              3 * ATTN_QKV_WIDTH + LRU_WIDTH, 3 * ATTN_QKV_WIDTH + 2 * LRU_WIDTH]
    h = x
    for l in range(DEPTH):
        f = swiglu(rms_norm_2(h, ffn1_norm_pre[l]), ffn1_w_gate[l], ffn1_w_up[l], ffn1_w_down[l])
        h = h + 0.5 * rms_norm_2(f, ffn1_norm_post[l])

        u = rms_norm_2(h, mix_norm_pre[l])
        proj = u @ w_in[l]
        q, k, v, xr, yr, gl = jnp.split(proj, splits, axis=-1)
        q = q.reshape(B, S, N_GROUPS_2, HEADS_PER_GROUP, HEAD_DIM_2)
        k = k.reshape(B, S, N_GROUPS_2, HEADS_PER_GROUP, HEAD_DIM_2)
        v = v.reshape(B, S, N_GROUPS_2, HEADS_PER_GROUP, HEAD_DIM_2)

        outs, lses = [], []
        for g, (window, dilation) in enumerate(DILATED_GROUPS):
            o_g, lse_g = dilated_group_attention(
                q[:, :, g], k[:, :, g], v[:, :, g],
                rel_bias_table[:, g * HEADS_PER_GROUP:(g + 1) * HEADS_PER_GROUP],
                window, dilation)
            outs.append(o_g)
            lses.append(lse_g)
        alpha = jax.nn.softmax(jnp.stack(lses, axis=0), axis=0)
        attn = jnp.einsum('gbsh,gbshe->bshe', alpha, jnp.stack(outs, axis=0).astype(jnp.float32))
        attn_d = attn.astype(x.dtype).reshape(B, S, ATTN_OUT_WIDTH) @ w_attn_branch[l]

        rec = rg_lru_branch(xr, conv_w[l], conv_b[l], lru_w_x[l], lru_b_x[l],
                            lru_w_a[l], lru_b_a[l], lru_a_param[l]) * jax.nn.gelu(yr)
        rec_d = rec @ w_rec_branch[l]

        gates = jax.nn.sigmoid(gl).reshape(B, S, N_BRANCHES, D_MODEL)
        merged = gates[:, :, 0] * attn_d + gates[:, :, 1] * rec_d
        h = h + rms_norm_2(merged @ w_out[l], mix_norm_post[l])

        f = swiglu(rms_norm_2(h, ffn2_norm_pre[l]), ffn2_w_gate[l], ffn2_w_up[l], ffn2_w_down[l])
        h = h + 0.5 * rms_norm_2(f, ffn2_norm_post[l])
    return h


def setup_inputs(seed=0):
    out = dict(first_inputs(seed))
    for name, value in second_inputs(seed + 1).items():
        if name != "x":
            out[name + "_2"] = value
    return out


def reference(
    x, c, positions, w_ada, b_ada, norm_mix, w_in, conv_w, a_log, dt_bias, gdn_out_norm, q_norm,
    k_norm, sinks, w_out, norm_ffn, w_group, b_group, w_router, b_router, w_gate, w_up, w_down,
    ffn1_norm_pre_2, ffn1_norm_post_2, ffn1_w_gate_2, ffn1_w_up_2, ffn1_w_down_2,
    mix_norm_pre_2, mix_norm_post_2, w_in_2, rel_bias_table_2, conv_w_2, conv_b_2, lru_w_x_2,
    lru_b_x_2, lru_w_a_2, lru_b_a_2, lru_a_param_2, w_attn_branch_2, w_rec_branch_2, w_out_2,
    ffn2_norm_pre_2, ffn2_norm_post_2, ffn2_w_gate_2, ffn2_w_up_2, ffn2_w_down_2,
):
    x = first_block(
        x, c, positions, w_ada, b_ada, norm_mix, w_in, conv_w, a_log, dt_bias, gdn_out_norm,
        q_norm, k_norm, sinks, w_out, norm_ffn, w_group, b_group, w_router, b_router, w_gate,
        w_up, w_down,
    )
    return second_block(
        x, ffn1_norm_pre_2, ffn1_norm_post_2, ffn1_w_gate_2, ffn1_w_up_2, ffn1_w_down_2,
        mix_norm_pre_2, mix_norm_post_2, w_in_2, rel_bias_table_2, conv_w_2, conv_b_2,
        lru_w_x_2, lru_b_x_2, lru_w_a_2, lru_b_a_2, lru_a_param_2, w_attn_branch_2,
        w_rec_branch_2, w_out_2, ffn2_norm_pre_2, ffn2_norm_post_2, ffn2_w_gate_2, ffn2_w_up_2,
        ffn2_w_down_2,
    )


_drawn_inputs = setup_inputs


def setup_inputs(seed=0):
    import zlib

    import numpy as np

    out = dict(_drawn_inputs(seed))
    spreads = {}
    factors = {'q_norm': 5.17,
     'k_norm': 5.405,
     'sinks': 63.76,
     'b_group': 22.529,
     'b_router': 7.832,
     'lru_b_x_2': 8.0,
     'lru_b_a_2': 8.0,
     'ffn2_norm_post_2': 3.785}
    for name, (base, spread) in spreads.items():
        noise = np.random.default_rng([zlib.crc32(name.encode()), seed]).standard_normal(out[name].shape)
        drawn = base * np.exp(spread * noise) if base else spread * noise
        out[name] = __import__('jax').numpy.asarray(drawn.astype(out[name].dtype))
    for name, factor in factors.items():
        out[name] = (out[name] * factor).astype(out[name].dtype)
    return out
```

```python
from contextlib import ExitStack

import numpy as np

import concourse.bass as bass
from concourse import mybir

F32 = mybir.dt.float32
I32 = mybir.dt.int32
U32 = mybir.dt.uint32
BF16 = mybir.dt.bfloat16
ALU = mybir.AluOpType
ACT = mybir.ActivationFunctionType
AX_X = mybir.AxisListType.X

P = 128
T = 512
D = 1024
NT = T // P
KD = D // P
HD = 64
H = 8
NPAIR = H // 2
CHUNK = 64
WINW = 2832
QKV = 1536
N_EXP, N_GRP, EPG, F_EXP = 32, 4, 8, 256
CAP = P
FF = 2816
NFF = FF // P
WIN2 = 8704
HD2 = 128
EPS = 1e-6
BIG = 1.0e30
RING = 6
SLOT = 2048
DILATIONS = (1, 4, 16)


def bucket_of(distance):
    nf = np.maximum(distance, 1).astype(np.float32)
    large = 16 + (np.log(nf / np.float32(16)).astype(np.float32) / np.float32(np.log(2048 / 16))
                  * np.float32(16)).astype(np.int32)
    return np.where(distance < 16, distance, np.minimum(large, 31))


def constants():
    p = np.arange(P)[:, None]
    c = np.arange(P)[None, :]
    same = (p // CHUNK) == (c // CHUNK)
    parts = {
        "ident": (p == c),
        "ones": np.ones((P, P)),
        "cumsum": (p <= c) & same,
        "chunk_all": same,
        "chunk0": np.broadcast_to(p < CHUNK, (P, P)),
        "chunk1": np.broadcast_to(p >= CHUNK, (P, P)),
    }
    for b in (1, 2, 4, 8, 16, 32):
        parts[f"level{b}"] = ((c // b) % 2 == 1) & ((p // b) == (c // b) - 1)
    k = np.arange(2 * P)[None, :]
    rel = p + P - k
    parts["window"] = np.where((rel >= 0) & (rel < P), 0.0, -BIG)
    parts["iota"] = np.broadcast_to(c, (P, P))
    parts["before"] = (p < c)
    half = HD // 2
    parts["inv_freq"] = np.broadcast_to(
        np.power(np.float32(10000.0), -np.arange(half, dtype=np.float32) / np.float32(half)), (P, half))
    parts["tie4"] = np.broadcast_to(N_GRP - np.arange(N_GRP), (P, N_GRP))
    parts["tie8"] = np.broadcast_to(EPG - np.arange(EPG), (P, EPG))
    parts["partition"] = p
    parts["eps"] = np.full((P, 1), EPS)
    parts["zero"] = np.zeros((P, 1))
    for g, dil in enumerate(DILATIONS):
        steps = 2 * P - 1 - np.arange(4 * P)
        onehot = np.zeros((P, 4 * P))
        ok = (steps >= 0) & (steps <= P)
        b = bucket_of(np.maximum(steps, 0) * dil)
        onehot[b[ok], np.nonzero(ok)[0]] = 1.0
        onehot[32] = np.where(ok, 0.0, -BIG)
        parts[f"bucket{g}"] = onehot
    q = T // DILATIONS[2]
    parts["phase16"] = np.where((p // q) == (c // q), 0.0, -BIG)
    at, where = 0, {}
    for name, a in parts.items():
        a = np.asarray(a, np.float32)
        where[name] = (at, a.shape[1])
        at += a.shape[1]
    return np.ascontiguousarray(np.concatenate([np.asarray(a, np.float32) for a in parts.values()], 1)), where


NAMES = [
    "x", "c", "positions", "w_ada", "b_ada", "norm_mix", "w_in", "conv_w", "a_log", "dt_bias", "gdn_out_norm",
    "q_norm", "k_norm", "sinks", "w_out", "norm_ffn", "w_group", "b_group", "w_router", "b_router", "w_gate",
    "w_up", "w_down", "ffn1_norm_pre_2", "ffn1_norm_post_2", "ffn1_w_gate_2", "ffn1_w_up_2", "ffn1_w_down_2",
    "mix_norm_pre_2", "mix_norm_post_2", "w_in_2", "rel_bias_table_2", "conv_w_2", "conv_b_2", "lru_w_x_2",
    "lru_b_x_2", "lru_w_a_2", "lru_b_a_2", "lru_a_param_2", "w_attn_branch_2", "w_rec_branch_2", "w_out_2",
    "ffn2_norm_pre_2", "ffn2_norm_post_2", "ffn2_w_gate_2", "ffn2_w_up_2", "ffn2_w_down_2",
]
POSITION_CONSTANTS, WHERE = constants()


def build(nc, a, const_dram, out):
    ctx = ExitStack()
    with ctx:
        def sb(name, shape, dt=F32):
            return ctx.enter_context(nc.sbuf_tensor(name, shape, dt))

        sems = {}

        c, v = NT, 2 * NT
        SUCCESSOR = {
            "d_scores": ("w_scores", 16), "d_s_taken": ("w_s_taken", 16), "d_max": ("w_max", 16),
            "d_p": ("w_p", 16), "d_p_turned": ("w_p_turned", 16), "d_pT": ("w_pT_ready", 16),
            "d_values": ("w_values", 16), "d_o_taken": ("w_o_taken", NT), "d_ps0": ("g_turned", 4 * c),
            "d_taken0": ("g_T_even", v), "d_taken1": ("g_T_odd", v), "d_v_taken": ("g_T1", v),
            "x_final": ("mixed_ready", 1), "hT_phased": ("z_taken", 1),
            "l_abs": ("g_abs", 1), "l_exp": ("g_exp", 1), "l_c": ("g_ss", 1), "l_in": ("g_X", 10 * c),
            "l_conv": ("g_Xs", 10 * c), "l_ps": ("g_w", c), "l_gate_ps": ("g_nw", c), "l_gates": ("g_v", v),
            "l_tanh": ("g_vnew", v), "l_floor": ("g_out", v), "l_sqrt": ("g_o_taken", c), "l_y_ps": ("g_osq", 1),
            "l_gelu": ("g_oss", 1), "ffn1_free": ("g_Ml", 10 * c), "ffn1_gu": ("g_T", 12 * c),
            "ffn1_sg": ("g_Y", 10 * c), "ffn2_free": ("g_state", v), "ffn2_gu": ("g_kk", c), "ffn2_sg": ("g_kq", c),
            "f_squares": ("w_ss", 1), "f_ss": ("w_roots", 1), "f_root": ("angles", 1), "post_loaded": ("rotation", 1),
            "c_diff": ("g_U", c), "c_exp": ("g_Grow", c), "attn_ready": ("g_oroot", 1), "attn_turned": ("w_turned", 1),
            "attnT_ready": ("w_kT", 1), "rec_ready": ("w_qk", 1), "m_even_ps": ("w_qT", 1),
            "m_sigmoids": ("g_roots", 1), "m_merged": ("g_G", 1),
        }

        def before(name):
            return SUCCESSOR[name][1] if name in SUCCESSOR else 0

        def S(name):
            if name in SUCCESSOR:
                return S(SUCCESSOR[name][0])
            if name not in sems:
                sems[name] = ctx.enter_context(nc.semaphore(name))
            return sems[name]

        tally = {}

        def nxt(e, name, by=1):
            key = (str(e.engine), name)
            tally[key] = tally.get(key, before(name)) + by
            e.wait_ge(S(name), tally[key])

        def meet(e):
            e.drain().then_inc(S("meet"), 1)
            nxt(e, "meet", 4)

        n_const = POSITION_CONSTANTS.shape[1]
        n_keep = WHERE["bucket0"][0]
        K = sb("constants", [P, n_keep])

        def con(name):
            at, n = WHERE[name]
            return K[:, at:at + n]

        ident, ones, eps = con("ident"), con("ones"), con("eps")
        ring = sb("ring", [P, RING, SLOT])
        X = sb("residual", [P, NT, D])
        hT = sb("hT", [P, KD, T])
        cols1 = sb("cols1", [P, 120])
        cols2 = sb("cols2", [P, 88])
        mod = sb("mod", [P, 48])
        cact = sb("cact", [P, KD])
        rows = sb("rows", [P, 256])
        ss = sb("ss", [P, NT])
        rstd = sb("rstd", [P, NT])
        ARENA = 29900
        A = sb("arena", [P, ARENA])
        bank = [ctx.enter_context(nc.psum_tensor(f"bank{i}", [P, 512], F32)) for i in range(8)]

        def region(at, width, pattern=None, base=None, **kw):
            r = (A if base is None else base)[:, at:at + width]
            return r.rearrange(pattern, **kw) if pattern else r

        hflat = hT[:, :, :].rearrange("p k t -> p (k t)")

        ROWS = {}
        at = 0
        for name, n in (("a_log", H), ("dt_bias", H), ("gdn_out_norm", HD), ("q_norm", HD), ("k_norm", HD),
                        ("sinks", H), ("b_group", N_GRP), ("b_router", N_EXP)):
            ROWS[name] = (at, n)
            at += n

        def row(name):
            at, n = ROWS[name]
            return rows[:, at:at + n]

        SLOTS = []
        FIRST = {}

        def plan(name, sources):
            FIRST[name] = len(SLOTS)
            SLOTS.extend(sources)

        def t_slots(w, c0, c1):
            return [w[:, n:n + 256].rearrange("(k p) n -> p k n", p=P) for n in range(c0, c1, 256)]

        def n_slots(w, c0, c1):
            return [w[r:r + 512, n:n + 512].rearrange("(k p) n -> p k n", p=P)
                    for n in range(c0, c1, 512) for r in (0, 512)]

        def d_slots(w, r1):
            return [w[r:r + 256, :].rearrange("(k p) n -> p k n", p=P) for r in range(0, r1, 256)]

        w_ada, w_in, w_in2 = a["w_ada"][0], a["w_in"][0], a["w_in_2"][0]
        plan("ada1", t_slots(w_ada, 0, 2 * D))
        plan("qkv", t_slots(w_in, 0, QKV))
        plan("z", n_slots(w_in, QKV, QKV + 512))
        plan("sq", n_slots(w_in, 2064, 2064 + 512))
        plan("skv", t_slots(w_in, 2576, 2832))
        plan("ada2", t_slots(w_ada, 2 * D, 6 * D))
        plan("w_out", d_slots(a["w_out"][0], D))
        MOE_AT = len(SLOTS)

        def ffn_slots(tag):
            g, u = (t_slots(a[f"{tag}_w_{n}_2"][0], 0, FF) for n in ("gate", "up"))
            plan(tag, [s for pair in zip(g, u) for s in pair])
            plan(tag + "_down", d_slots(a[f"{tag}_w_down_2"][0], FF))

        ffn_slots("ffn1")
        for g in range(3):
            plan(f"q{g}", t_slots(w_in2, 512 * g, 512 * g + 512))
            plan(f"k{g}", t_slots(w_in2, 1536 + 512 * g, 1536 + 512 * g + 512))
            plan(f"v{g}", n_slots(w_in2, 3072 + 512 * g, 3072 + 512 * g + 512))
        plan("xr", t_slots(w_in2, 4608, 5632))
        plan("lru", [a[n][0].rearrange("h (i p) j -> p (h i) j", p=P) for n in ("lru_w_x_2", "lru_w_a_2")])
        plan("yr", t_slots(w_in2, 5632, 6656))
        for m in range(4):
            plan(f"gl{m}", t_slots(w_in2, 6656 + 256 * m, 6656 + 256 * m + 256)
                 + t_slots(w_in2, 7680 + 256 * m, 7680 + 256 * m + 256))
            plan(f"attn{m}", [a["w_attn_branch_2"][0][:, 256 * m:256 * m + 256].rearrange("(k p) n -> p k n", p=P)])
            plan(f"rec{m}", t_slots(a["w_rec_branch_2"][0], 256 * m, 256 * m + 256))
        plan("w_out2", d_slots(a["w_out_2"][0], D))
        ffn_slots("ffn2")

        loaded = [S(f"slot{i}_loaded") for i in range(RING)]

        def slot_view(i, n):
            return ring[:, i % RING, :].rearrange("p (k n) -> p k n", n=n)

        def load(sp, first, count):
            for i in range(first, first + count):
                if i >= RING:
                    if i < MOE_AT or i >= MOE_AT + RING:
                        sp.wait_ge(S("slots_used"), i - RING + 1)
                src = SLOTS[i]
                n = src.shape[-1]
                view = ring[:, i % RING, 0:src.shape[1] * n].rearrange("p (k n) -> p k n", n=n)
                sp.dma_start(view, src).then_inc(loaded[i % RING], 16)

        def need(pe, i):
            pe.wait_ge(loaded[i % RING], 16 * (i // RING + 1))

        vec1 = region(0, P)
        vec2 = region(P, P)
        VEC1 = [("b_ada", 48), ("norm_mix", 8), ("norm_ffn", 8), ("c", 8), ("conv_w", 48)]
        VEC2 = [("ffn1_norm_pre_2", 8), ("mix_norm_pre_2", 8), ("ffn2_norm_pre_2", 8), ("conv_w_2", 32),
                ("conv_b_2", 8), ("lru_b_x_2", 8), ("lru_b_a_2", 8), ("lru_a_param_2", 8)]
        wab = region(28752, KD * 16, "p (k n) -> p k n", n=16)

        def chunked(v, n):
            dims = " ".join("abcd"[:len(v.shape)])
            flat = v.rearrange(f"{dims} -> ({dims})")
            return flat.rearrange("(r p) -> r p", p=P)

        def col(c, table):
            at = 0
            for name, n in table:
                if name == c:
                    return at, n
                at += n

        def sp_small(sp):
            sp.dma_start(K[:, :], const_dram[:, 0:n_keep]).then_inc(S("const_loaded"), 16)
            for vec, table in ((vec1, VEC1), (vec2, VEC2)):
                at = 0
                for name, n in table:
                    sp.dma_start(vec[at:at + n, :], chunked(a[name], n)).then_inc(S("vectors_loaded"), 16)
                    at += n
            for t in range(NT):
                sp.dma_start(X[:, t, :], a["x"][0, t * P:(t + 1) * P, :]).then_inc(S("x_loaded"), 16)

        def act_small(act):
            for name, (at, n) in ROWS.items():
                src = a[name][0:1, :].broadcast_to([P, n])
                act.dma_start(rows[:, at:at + n], src).then_inc(S("rows_loaded"), 16)
            act.dma_start(wab, w_in[:, 2048:2064].rearrange("(k p) n -> p k n", p=P)).then_inc(S("wab_loaded"), 16)

        def pe_small(pe):
            nxt(pe, "const_loaded", 16)
            nxt(pe, "vectors_loaded", 16 * (len(VEC1) + len(VEC2)))
            pe.transpose(bank[0][:, 0:120], vec1[0:120, :], ident[0:120, 0:120])
            pe.transpose(bank[1][:, 0:88], vec2[0:88, :], ident[0:88, 0:88]).then_inc(S("vectors_turned"), 1)

        def dve_small(dve):
            nxt(dve, "vectors_turned")
            dve.tensor_copy(cols1[:, :], bank[0][:, 0:120])
            dve.tensor_copy(cols2[:, :], bank[1][:, 0:88]).then_inc(S("columns_ready"), 1)

        def act_c(act):
            nxt(act, "columns_ready")
            at, n = col("c", VEC1)
            act.activation(cact[:, :], cols1[:, at:at + n], ACT.Silu).then_inc(S("cact_ready"), 1)

        def pe_ada(pe, name, m0, m1, b):
            if m0 == 0:
                nxt(pe, "cact_ready")
            for i in range(m0 // 2, m1 // 2):
                s = FIRST[name] + i - m0 // 2
                need(pe, s)
                w = slot_view(s, 256)
                for j in range(2):
                    m = 2 * i + j
                    for k in range(KD):
                        mm = pe.matmul(bank[b][:, m:m + 1], w[:, k, j * P:(j + 1) * P], cact[:, k:k + 1],
                                       start=(k == 0), stop=(k == KD - 1))
                mm.then_inc(S("slots_used"), 1)

        def dve_ada(dve, m0, m1, b):
            last = FIRST["ada1"] + 8 if m0 == 0 else FIRST["ada2"] + 16
            dve.wait_ge(S("slots_used"), last)
            dve.tensor_tensor(mod[:, m0:m1], bank[b][:, m0:m1], cols1[:, m0:m1], ALU.add)
            dve.drain()
            s0, gain = (8, "norm_mix") if m0 == 0 else (32, "norm_ffn")
            at, n = col(gain, VEC1)
            dve.scalar_tensor_tensor(mod[:, s0:s0 + 8], mod[:, s0:s0 + 8], 1.0, cols1[:, at:at + n],
                                     ALU.add, ALU.mult)
            dve.drain().then_inc(S("mod_ready"), 1)

        def act_norm(act, junk, scale, shift):
            for t in range(NT):
                act.activation(junk, X[:, t, :], ACT.Square, accum_out=ss[:, t:t + 1])
                act.drain()
            act.activation(rstd[:, :], ss[:, :], ACT.Sqrt, bias=eps, scale=1.0 / D).then_inc(S("rms_ready"), 1)
            for k in range(0, KD, 2):
                nxt(act, "x_turned", 2 if k else 1)
                if shift is None:
                    i = act.activation(hT[:, k, :], bank[k][:, :], ACT.Copy, scale=scale[:, k:k + 1])
                else:
                    i = act.activation(hT[:, k, :], bank[k][:, :], ACT.Identity, bias=shift[:, k:k + 1],
                                       scale=scale[:, k:k + 1])
            tally[(str(act.engine), "x_turned")] += 1
            i.then_inc(S("hT_even"), 1)

        def dve_norm(dve, xn, scale, shift):
            nxt(dve, "rms_ready")
            dve.reciprocal(ss[:, :], rstd[:, :])
            dve.drain()
            for t in range(NT):
                i = dve.tensor_scalar(xn[:, t, :], X[:, t, :], ss[:, t:t + 1], None, ALU.mult)
            i.then_inc(S("xn_ready"), 1)
            for k in range(1, KD, 2):
                nxt(dve, "x_turned", 2)
                if shift is None:
                    i = dve.tensor_scalar(hT[:, k, :], bank[k][:, :], scale[:, k:k + 1], None, ALU.mult)
                else:
                    i = dve.tensor_scalar(hT[:, k, :], bank[k][:, :], scale[:, k:k + 1], shift[:, k:k + 1],
                                          ALU.mult, ALU.add)
            i.then_inc(S("hT_odd"), 1)

        def pe_turn(pe, src, ready):
            nxt(pe, *ready)
            for k in range(KD):
                for t in range(NT):
                    mm = pe.transpose(bank[k][:, t * P:(t + 1) * P], src[:, t, k * P:(k + 1) * P], ident)
                mm.then_inc(S("x_turned"), 1)

        def pe_hT(pe):
            nxt(pe, "hT_even")
            nxt(pe, "hT_odd")

        convT = region(0, QKV // P * T, "p (m t) -> p m t", t=T)
        qkv = region(6144, NT * QKV, "p (t n) -> p t n", n=QKV)
        kbG = region(12288, 2048, "p (t n) -> p t n", n=512)
        z = region(14336, 2048, "p (t n) -> p t n", n=512)
        mixed = region(16384, 4096, "p (t n) -> p t n", n=D)
        ab = region(20480, 64, "p (t n) -> p t n", n=16)
        sq = region(20544, 2048, "p (t n) -> p t n", n=512)
        skv = region(22592, 1024, "p (t n) -> p t n", n=256)
        convin = region(23616, 1040, "p (b t) -> p b t", b=2)
        xn1 = region(24656, 4096, "p (t n) -> p t n", n=D)
        junk1 = region(1024, D)
        convacc = region(24656, 1024, "p (b t) -> p b t", b=2)
        NM = QKV // P

        def pe_gemm_t(pe, s, nk, rhs, banks, ready, free=None):
            need(pe, s)
            n = SLOTS[s].shape[-1]
            w = ring[:, s % RING, 0:nk * n].rearrange("p (k n) -> p k n", n=n)
            for j in range(n // P):
                if free is not None:
                    free(j)
                for k in range(nk):
                    mm = pe.matmul(banks[j][:, :], w[:, k, j * P:(j + 1) * P], rhs[:, k, :],
                                   start=(k == 0), stop=(k == nk - 1))
                if j < n // P - 1:
                    mm.then_inc(S(ready), 1)
            return mm

        def pe_gemm_n(pe, s, lhs, banks):
            for half in range(2):
                need(pe, s + half)
                w = slot_view(s + half, 512)
                for t in range(NT):
                    for k in range(4):
                        mm = pe.matmul(banks[t][:, :], lhs(4 * half + k, t), w[:, k, :],
                                       start=(half == 0 and k == 0), stop=(half == 1 and k == 3))
                mm.then_inc(S("slots_used"), 1)

        def tokens(k, t):
            return hT[:, k, t * P:(t + 1) * P]

        def pe_proj1(pe):
            for i in range(NM // 2):
                s = FIRST["qkv"] + i
                need(pe, s)
                w = slot_view(s, 256)
                for j in range(2):
                    if i > 0:
                        nxt(pe, "conv_in")
                    for k in range(KD):
                        mm = pe.matmul(bank[j][:, :], w[:, k, j * P:(j + 1) * P], hT[:, k, :],
                                       start=(k == 0), stop=(k == KD - 1))
                    if j == 0:
                        mm.then_inc(S("qkvT_ps"), 1)
                mm.then_inc(S("slots_used"), 1)
            nxt(pe, "conv_in", 2)
            pe_gemm_n(pe, FIRST["z"], tokens, bank[2:6])
            nxt(pe, "wab_loaded", 16)
            for t in range(NT):
                for k in range(KD):
                    mm = pe.matmul(bank[6][:, 16 * t:16 * t + 16], tokens(k, t), wab[:, k, :],
                                   start=(k == 0), stop=(k == KD - 1))
            mm.then_inc(S("ab_ps"), 1)
            nxt(pe, "z_taken")
            pe_gemm_n(pe, FIRST["sq"], tokens, bank[2:6])
            nxt(pe, "sq_taken")
            need(pe, FIRST["skv"])
            w = slot_view(FIRST["skv"], 256)
            for t in range(NT):
                for k in range(KD):
                    mm = pe.matmul(bank[2 + t][:, 0:256], tokens(k, t), w[:, k, :],
                                   start=(k == 0), stop=(k == KD - 1))
            mm.then_inc(S("slots_used"), 1)

        def act_proj1(act):
            for m in range(NM):
                i, j = m // 2, m % 2
                if j == 0:
                    nxt(act, "qkvT_ps")
                else:
                    act.wait_ge(S("slots_used"), FIRST["qkv"] + i + 1)
                if m >= 2:
                    nxt(act, "conv_done")
                act.activation(convin[:, j, 3:3 + T], bank[j][:, :], ACT.Copy).then_inc(S("conv_in"), 1)
                if m >= 2:
                    act.activation(convT[:, m - 2, :], convacc[:, j, :], ACT.Silu).then_inc(S("silu_done"), 1)
            for m in (NM - 2, NM - 1):
                nxt(act, "conv_done")
                act.activation(convT[:, m, :], convacc[:, m % 2, :], ACT.Silu).then_inc(S("silu_done"), 1)

        def dve_proj1(dve):
            dve.memset(convin[:, :, 0:3], 0.0)
            at, _ = col("conv_w", VEC1)
            for m in range(NM):
                j = m % 2
                nxt(dve, "conv_in")
                if m >= 2:
                    nxt(dve, "silu_done")
                dve.drain()
                dve.tensor_scalar(convacc[:, j, :], convin[:, j, 3:3 + T], cols1[:, at + 36 + m:at + 37 + m],
                                  None, ALU.mult)
                for tap in range(3):
                    dve.drain()
                    w = cols1[:, at + 12 * tap + m:at + 12 * tap + m + 1]
                    i = dve.scalar_tensor_tensor(convacc[:, j, :], convin[:, j, tap:tap + T], w,
                                                 convacc[:, j, :], ALU.mult, ALU.add)
                i.then_inc(S("conv_done"), 1)
            dve.wait_ge(S("slots_used"), FIRST["z"] + 2)
            for t in range(NT):
                i = dve.tensor_copy(z[:, t, :], bank[2 + t][:, :])
            i.then_inc(S("z_taken"), 1)
            nxt(dve, "ab_ps")
            dve.tensor_copy(ab, bank[6][:, 0:64].rearrange("p (t n) -> p t n", n=16))
            dve.wait_ge(S("slots_used"), FIRST["sq"] + 2)
            for t in range(NT):
                i = dve.tensor_copy(sq[:, t, :], bank[2 + t][:, :])
            i.then_inc(S("sq_taken"), 1)
            dve.wait_ge(S("slots_used"), FIRST["skv"] + 1)
            for t in range(NT):
                dve.tensor_copy(skv[:, t, :], bank[2 + t][:, 0:256])
            dve.drain().then_inc(S("proj1_done"), 1)

        def pe_qkv(pe):
            nxt(pe, "silu_done", NM)
            for t in range(NT):
                for g in range(3):
                    b = bank[(3 * t + g) % 2]
                    if 3 * t + g >= 2:
                        nxt(pe, "qkv_taken")
                    for m in range(4):
                        mm = pe.transpose(b[:, m * P:(m + 1) * P], convT[:, 4 * g + m, t * P:(t + 1) * P], ident)
                    mm.then_inc(S("qkv_turned"), 1)

        def act_qkv(act):
            for t in range(NT):
                for g in range(3):
                    nxt(act, "qkv_turned")
                    act.activation(qkv[:, t, 512 * g:512 * g + 512], bank[(3 * t + g) % 2][:, :], ACT.Copy)\
                       .then_inc(S("qkv_taken"), 1)

        small = region(28880, 1020)
        NW = H + 2

        def sm(at, width, pattern=None, **kw):
            r = small[:, at:at + width]
            return r.rearrange(pattern, **kw) if pattern else r

        pos_i = sm(0, NT).bitcast(I32)
        pos_f = sm(4, NT)
        cos = region(26960, 128, "p (t f) -> p t f", t=NT)
        sin = region(27088, 128, "p (t f) -> p t f", t=NT)
        ang = region(27216, 128, "p (t f) -> p t f", t=NT)
        turns = region(27344, 128, "p (t f) -> p t f", t=NT)
        w_ss = sm(8, 40, "p (t h) -> p t h", t=NT)
        w_r = sm(48, 40, "p (t h) -> p t h", t=NT)
        w_mx, w_nmx, w_den, w_es = (sm(88 + 32 * i, 32) for i in range(4))
        sq4 = sq.rearrange("p t (h e) -> p t h e", e=HD)
        sk3 = skv[:, :, 0:128]
        squares_q = region(0, 2048, "p (t n) -> p t n", t=NT)
        squares_k = region(2048, 512, "p (t n) -> p t n", t=NT)
        kk = region(4096, 1024, "p (t g i e) -> p t g i e", t=NT, g=2, i=2)
        q_T = region(0, 2048, "p (j t) -> p j t", base=hflat, t=T)
        k_T = region(2048, 1024, "p (g t) -> p g t", base=hflat, t=T)
        Pw = region(23616, 1024, "p (b i k) -> p b i k", b=2, i=2)
        PwT = region(24656, 1024, "p (b i k) -> p b i k", b=2, i=2)
        TWO_PI = 2 * np.pi
        C1 = 6.28125
        C2 = float(np.float32(TWO_PI - C1))
        C3 = TWO_PI - C1 - C2
        ROUND = 12582912.0
        NEAR_PI = 3.1415925

        def sp_positions(sp):
            sp.dma_start(pos_i, a["positions"][0].rearrange("(t p) -> p t", p=P),
                         allow_slow_non_contiguous=True).then_inc(S("positions_loaded"), 16)

        def act_swa_prep(act):
            nxt(act, "rows_loaded", 16 * len(ROWS))
            act.activation(squares_q, sq, ACT.Square)
            act.activation(squares_k, sk3, ACT.Square).then_inc(S("w_squares"), 1)
            nxt(act, "w_ss")
            act.activation(w_r, w_ss, ACT.Sqrt, bias=eps, scale=1.0 / HD).then_inc(S("w_roots"), 1)
            nxt(act, "angles")
            act.activation(sin, ang, ACT.Sin)
            act.activation(cos, turns, ACT.Sin).then_inc(S("rotation"), 1)

        def dve_swa_prep(dve):
            nxt(dve, "w_squares")
            dve.tensor_reduce(w_ss[:, :, 0:H], squares_q.rearrange("p t (h e) -> p t h e", e=HD), AX_X, ALU.add)
            dve.tensor_reduce(w_ss[:, :, H:NW], squares_k.rearrange("p t (h e) -> p t h e", e=HD), AX_X, ALU.add)\
               .then_inc(S("w_ss"), 1)
            nxt(dve, "positions_loaded", 16)
            dve.tensor_copy(pos_f, pos_i)
            dve.drain()
            shape = [P, NT, HD // 2]
            dve.tensor_tensor(ang, pos_f.unsqueeze(2).broadcast_to(shape),
                              con("inv_freq").unsqueeze(1).broadcast_to(shape), ALU.mult)
            dve.drain()
            dve.tensor_scalar(turns, ang, 1.0 / TWO_PI, ROUND, ALU.mult, ALU.add)
            dve.drain()
            dve.tensor_scalar(turns, turns, ROUND, None, ALU.subtract)
            for c in (C1, C2, C3):
                dve.drain()
                dve.scalar_tensor_tensor(ang, turns, -c, ang, ALU.mult, ALU.add)
            dve.drain()
            dve.tensor_scalar(ang, ang, NEAR_PI, -NEAR_PI, ALU.min, ALU.max)
            dve.drain()
            dve.scalar_tensor_tensor(turns, ang, -1.0, ang, ALU.mult, ALU.min)
            dve.drain()
            dve.tensor_scalar(turns, turns, float(np.pi / 2), None, ALU.add).then_inc(S("angles"), 1)
            nxt(dve, "w_roots")
            dve.reciprocal(w_ss, w_r)
            dve.drain()
            for t in range(NT):
                shape = [P, H, HD]
                dve.tensor_tensor(sq4[:, t], sq4[:, t], w_ss[:, t, 0:H].unsqueeze(2).broadcast_to(shape), ALU.mult)
                k4 = sk3[:, t, :].rearrange("p (h e) -> p h e", e=HD)
                dve.tensor_tensor(k4, k4, w_ss[:, t, H:NW].unsqueeze(2).broadcast_to([P, 2, HD]), ALU.mult)
            dve.drain()
            for t in range(NT):
                dve.tensor_tensor(sq4[:, t], sq4[:, t], row("q_norm").unsqueeze(1).broadcast_to([P, H, HD]), ALU.mult)
                k4 = sk3[:, t, :].rearrange("p (h e) -> p h e", e=HD)
                dve.tensor_tensor(k4, k4, row("k_norm").unsqueeze(1).broadcast_to([P, 2, HD]), ALU.mult)
            nxt(dve, "rotation")
            dve.drain()
            half = HD // 2
            for t in range(NT):
                for heads, src in ((H, sq4[:, t]), (2, sk3[:, t, :].rearrange("p (h e) -> p h e", e=HD))):
                    shape = [P, heads, half]
                    c = cos[:, t, :].unsqueeze(1).broadcast_to(shape)
                    s = sin[:, t, :].unsqueeze(1).broadcast_to(shape)
                    x1, x2 = src[:, :, 0:half], src[:, :, half:HD]
                    base = 1024 * (t % 2) + (0 if heads == H else 2048)
                    u = [region(base + 256 * i, heads * half, "p (h f) -> p h f", f=half) for i in range(4)]
                    dve.tensor_tensor(u[0], x1, c, ALU.mult)
                    dve.tensor_tensor(u[1], x2, s, ALU.mult)
                    dve.tensor_tensor(u[2], x1, s, ALU.mult)
                    dve.tensor_tensor(u[3], x2, c, ALU.mult)
                    dve.drain()
                    if heads == H:
                        dve.tensor_tensor(x1, u[0], u[1], ALU.subtract)
                        dve.tensor_tensor(x2, u[2], u[3], ALU.add)
                    else:
                        for i in range(2):
                            dve.tensor_tensor(kk[:, t, :, i, 0:half], u[0], u[1], ALU.subtract)
                            dve.tensor_tensor(kk[:, t, :, i, half:HD], u[2], u[3], ALU.add)
                    if t >= 1:
                        dve.drain()
            dve.drain().then_inc(S("w_qk"), 1)

        def pe_swa_turn(pe):
            nxt(pe, "w_qk")
            for j in range(NPAIR):
                for t in range(NT):
                    pe.transpose(bank[j][:, t * P:(t + 1) * P], sq[:, t, j * P:(j + 1) * P], ident)
            for g in range(2):
                for t in range(NT):
                    mm = pe.transpose(bank[4 + g][:, t * P:(t + 1) * P],
                                      kk[:, t, g].rearrange("p i e -> p (i e)"), ident)
            mm.then_inc(S("w_turned"), 1)

        def dve_swa_turn(dve):
            nxt(dve, "w_turned")
            for j in range(NPAIR):
                dve.tensor_copy(q_T[:, j, :], bank[j][:, :])
            dve.drain().then_inc(S("w_qT"), 1)

        def act_swa_turn(act):
            nxt(act, "w_turned")
            for g in range(2):
                act.activation(k_T[:, g, :], bank[4 + g][:, :], ACT.Copy)
            act.drain().then_inc(S("w_kT"), 1)

        UNITS = [(n, j) for n in range(NT) for j in range(NPAIR)]

        def span(n):
            return (n - 1, 2 * P) if n else (0, P)

        def pe_swa(pe):
            def scores(u):
                n, j = UNITS[u]
                n0, w = span(n)
                if u >= 2:
                    nxt(pe, "w_s_taken")
                for i in range(2):
                    r = slice(64 * i, 64 * i + 64)
                    mm = pe.matmul(bank[2 * (u % 2) + i][:, 0:w], q_T[r, j, n * P:(n + 1) * P],
                                   k_T[r, j // 2, n0 * P:n0 * P + w], start=True, stop=True)
                mm.then_inc(S("w_scores"), 1)

            def turn(u):
                n, j = UNITS[u]
                nxt(pe, "w_p")
                for i in range(2):
                    for b in range(span(n)[1] // P):
                        mm = pe.transpose(bank[4 + u % 2][:, (2 * i + b) * P:(2 * i + b + 1) * P],
                                          Pw[:, u % 2, i, b * P:(b + 1) * P], ident)
                mm.then_inc(S("w_p_turned"), 1)

            def values(u):
                n, j = UNITS[u]
                n0, w = span(n)
                nxt(pe, "w_pT_ready")
                if j == 0 and n >= 2:
                    nxt(pe, "w_o_taken")
                for i in range(2):
                    h = 2 * j + i
                    for b in range(w // P):
                        mm = pe.matmul(bank[6 + n % 2][:, h * HD:(h + 1) * HD], PwT[:, u % 2, i, b * P:(b + 1) * P],
                                       skv[:, n0 + b, 128 + HD * (h // 4):128 + HD * (h // 4) + HD],
                                       start=(b == 0), stop=(b == w // P - 1))
                mm.then_inc(S("w_values"), 1)

            nxt(pe, "w_qT")
            nxt(pe, "w_kT")
            scores(0)
            for u in range(len(UNITS)):
                if u + 1 < len(UNITS):
                    scores(u + 1)
                turn(u)
                if u:
                    values(u - 1)
            values(len(UNITS) - 1)

        def dve_swa(dve):
            mask = con("window")
            for u, (n, j) in enumerate(UNITS):
                _, w = span(n)
                c = slice(2 * u, 2 * u + 2)
                nxt(dve, "w_scores")
                if u >= 2:
                    nxt(dve, "w_p_turned")
                for i in range(2):
                    s = dve.scalar_tensor_tensor(Pw[:, u % 2, i, 0:w], bank[2 * (u % 2) + i][:, 0:w], HD ** -0.5,
                                                 mask[:, 2 * P - w:2 * P], ALU.mult, ALU.add)
                s.then_inc(S("w_s_taken"), 1)
                dve.drain()
                dve.tensor_reduce(w_mx[:, c], Pw[:, u % 2, :, 0:w], AX_X, ALU.max)
                dve.drain()
                dve.tensor_tensor(w_mx[:, c], w_mx[:, c], row("sinks")[:, 2 * j:2 * j + 2], ALU.max)
                dve.drain()
                dve.tensor_scalar(w_nmx[:, c], w_mx[:, c], -1.0, None, ALU.mult).then_inc(S("w_max"), 1)
                if u >= 1 and u % NPAIR == 0:
                    outputs(dve, n - 1)
            outputs(dve, NT - 1)

        def outputs(dve, n):
            c = slice(8 * n, 8 * n + 8)
            dve.wait_ge(S("w_values"), 4 * (n + 1))
            dve.wait_ge(S("w_p"), 4 * (n + 1))
            dve.tensor_tensor(w_den[:, c], w_den[:, c], w_es[:, c], ALU.add)
            dve.drain()
            dve.reciprocal(w_es[:, c], w_den[:, c])
            dve.drain()
            dve.tensor_tensor(mixed[:, n, 512:1024].rearrange("p (h e) -> p h e", e=HD),
                              bank[6 + n % 2][:, :].rearrange("p (h e) -> p h e", e=HD),
                              w_es[:, c].unsqueeze(2).broadcast_to([P, H, HD]), ALU.mult)\
               .then_inc(S("w_o_taken"), 1)

        def act_swa(act):
            def exps(u):
                n, j = UNITS[u]
                w = span(n)[1]
                nxt(act, "w_max")
                for i in range(2):
                    c = slice(2 * u + i, 2 * u + i + 1)
                    act.activation(w_es[:, c], row("sinks")[:, 2 * j + i:2 * j + i + 1], ACT.Exp, bias=w_nmx[:, c])
                    act.activation(Pw[:, u % 2, i, 0:w], Pw[:, u % 2, i, 0:w], ACT.Exp, bias=w_nmx[:, c],
                                   accum_out=w_den[:, c])
                act.drain().then_inc(S("w_p"), 1)

            def copy(u):
                w = span(UNITS[u][0])[1]
                nxt(act, "w_p_turned")
                if u >= 2:
                    nxt(act, "w_values")
                act.activation(PwT[:, u % 2, :, 0:w],
                               bank[4 + u % 2][:, :].rearrange("p (i k) -> p i k", i=2)[:, :, 0:w], ACT.Copy)
                act.drain().then_inc(S("w_pT_ready"), 1)

            exps(0)
            for u in range(len(UNITS)):
                if u + 1 < len(UNITS):
                    exps(u + 1)
                copy(u)

        a_in, b_in = ab[:, :, 0:H], ab[:, :, H:2 * H]

        def th(at):
            return sm(at, 32, "p (t h) -> p t h", t=NT)

        g_u, g_e, g_s, g_z, g_q, g_g, g_beta, g_G, g_expG, g_kdec, g_ea = (th(216 + 32 * i) for i in range(11))
        g_dec = sm(568, 32, "p (t c j) -> p t c j", t=NT, c=2)
        g_ss = sm(600, 64, "p (t h) -> p t h", t=NT)
        g_r = sm(664, 64, "p (t h) -> p t h", t=NT)
        g_os = th(728)
        g_or = th(760)
        squares = region(0, 4096, "p (t n) -> p t n", t=NT)
        qg = region(0, 2048, "p (t n) -> p t n", t=NT)
        kb = region(2048, 2048, "p (t n) -> p t n", t=NT)
        kdec = region(4096, 2048, "p (t n) -> p t n", t=NT)
        qn, kn, vb = (qkv[:, :, 512 * i:512 * i + 512] for i in range(3))
        TT, Tm, Xs, MT = (region(1024 * i, 1024, "p (h c) -> p h c", base=hflat, c=P) for i in range(4))
        MTl, DT, attnT, gU = (region(20544 + 1024 * i, 1024, "p (h c) -> p h c", c=P) for i in range(4))
        kT, kbT, qT, qgT, nwT = (region(24640 + 512 * i, 512, "p (j c) -> p j c", c=P) for i in range(5))
        vnew = region(27200, 1024, "p (c n) -> p c n", c=2)
        state = region(28224, 512, "p (j e) -> p j e", e=P)
        LEVELS = (2, 4, 8, 16, 32)

        def dve_log1p(dve, e, z_, q_, shape_out):
            dve.tensor_scalar(q_, e, 2.0, None, ALU.add)
            dve.drain()
            dve.reciprocal(q_, q_)
            dve.drain()
            dve.tensor_tensor(z_, e, q_, ALU.mult)
            dve.drain()
            dve.tensor_tensor(e, z_, z_, ALU.mult)
            dve.drain()
            dve.tensor_scalar(q_, e, 1.0 / 13, None, ALU.mult)
            for n in (11, 9, 7, 5, 3):
                dve.drain()
                dve.scalar_tensor_tensor(q_, q_, 1.0 / n, e, ALU.add, ALU.mult)
            dve.drain()
            dve.scalar_tensor_tensor(shape_out, q_, 1.0, z_, ALU.add, ALU.mult)
            dve.drain()
            dve.tensor_scalar(shape_out, shape_out, 2.0, None, ALU.mult)
            dve.drain()

        def dve_gdn_prep(dve):
            wide = [P, NT, H]
            dve.tensor_tensor(g_u, a_in, row("dt_bias").unsqueeze(1).broadcast_to(wide), ALU.add)
            dve.drain()
            dve.scalar_tensor_tensor(g_s, g_u, -1.0, g_u, ALU.mult, ALU.max).then_inc(S("g_abs"), 1)
            nxt(dve, "g_exp")
            dve_log1p(dve, g_e, g_z, g_q, g_s)
            dve.scalar_tensor_tensor(g_s, g_u, 0.0, g_s, ALU.max, ALU.add)
            dve.drain()
            dve.scalar_tensor_tensor(g_g, g_s, -1.0, g_ea, ALU.mult, ALU.mult).then_inc(S("g_ready"), 1)
            nxt(dve, "g_squares")
            dve.tensor_reduce(g_ss, squares.rearrange("p t (h e) -> p t h e", e=HD), AX_X, ALU.add)\
               .then_inc(S("g_ss"), 1)
            nxt(dve, "g_sums")
            dve.tensor_copy(g_G, bank[0][:, 0:32].rearrange("p (t h) -> p t h", t=NT))
            dve.drain()
            dve.tensor_tensor(g_kdec, bank[0][:, 32:64].rearrange("p (t h) -> p t h", t=NT), g_G, ALU.subtract)\
               .then_inc(S("g_G"), 1)
            nxt(dve, "g_roots")
            dve.reciprocal(g_ss, g_r)
            dve.drain()
            dve.tensor_scalar(g_ss[:, :, 0:H], g_ss[:, :, 0:H], HD ** -0.5, None, ALU.mult)
            dve.drain()
            nxt(dve, "g_exps")

            def scaled(dst, src, by):
                for t in range(NT):
                    dve.tensor_tensor(dst[:, t, :].rearrange("p (h e) -> p h e", e=HD),
                                      src[:, t, :].rearrange("p (h e) -> p h e", e=HD),
                                      by[:, t, :].unsqueeze(2).broadcast_to([P, H, HD]), ALU.mult)

            scaled(qn, qn, g_ss[:, :, 0:H])
            scaled(kn, kn, g_ss[:, :, H:2 * H])
            scaled(vb, vb, g_beta)
            dve.drain()
            scaled(qg, qn, g_expG)
            scaled(kb, kn, g_beta)
            scaled(kdec, kn, g_kdec)
            dve.drain()
            scaled(kbG, kb, g_expG)
            dve.memset(state, 0.0)
            dve.memset(vnew, 0.0)
            dve.drain().then_inc(S("g_scaled"), 1)

        def act_gdn_prep(act):
            act.activation(squares, qkv[:, :, 0:1024], ACT.Square).then_inc(S("g_squares"), 1)
            nxt(act, "g_abs")
            act.activation(g_e, g_s, ACT.Exp, scale=-1.0)
            act.activation(g_ea, row("a_log").unsqueeze(1).broadcast_to([P, NT, H]), ACT.Exp)
            act.activation(g_beta, b_in, ACT.Sigmoid)
            act.drain().then_inc(S("g_exp"), 1)
            nxt(act, "g_ss")
            act.activation(g_r, g_ss, ACT.Sqrt, bias=eps).then_inc(S("g_roots"), 1)
            nxt(act, "g_G")
            act.activation(g_expG, g_G, ACT.Exp)
            act.activation(g_kdec, g_kdec, ACT.Exp)
            for c in range(2):
                for i in range(2):
                    r = slice(64 * i, 64 * i + 64)
                    src = bank[0][r, 64 + 32 * c:96 + 32 * c].rearrange("p (t j i) -> p t j i", t=NT, i=2)
                    act.activation(g_dec[r, :, c, :], src[:, :, :, i], ACT.Exp)
            act.drain().then_inc(S("g_exps"), 1)

        def pe_gdn_prep(pe):
            nxt(pe, "g_ready")
            g = g_g.rearrange("p t h -> p (t h)")
            for i, name in enumerate(("cumsum", "chunk_all", "chunk0", "chunk1")):
                mm = pe.matmul(bank[0][:, 32 * i:32 * i + 32], con(name), g, start=True, stop=True)
            mm.then_inc(S("g_sums"), 1)
            nxt(pe, "g_scaled")

        def place(h):
            return 4 * (h % 2) + h // 2

        def by_parity(x):
            return x.rearrange("p (j i) -> p i j", i=2)

        def heads(x, g):
            return x[:, 4 * g:4 * g + 4, :].rearrange("p h c -> p (h c)")

        def pe_gdn(pe, t):
            if t:
                nxt(pe, "g_state")
            for i, x in enumerate((kn, kb, qn, qg)):
                for j in range(NPAIR):
                    mm = pe.transpose(bank[i][:, j * P:(j + 1) * P], x[:, t, j * P:(j + 1) * P], ident)
                mm.then_inc(S("g_turned"), 1)
            nxt(pe, "g_U")
            for g in range(2):
                mm = pe.matmul(bank[4 + g][:, :], ones, heads(gU, g), start=True, stop=True)
            mm.then_inc(S("g_Grow"), 1)
            nxt(pe, "g_T_even", 2)
            nxt(pe, "g_T_odd", 2)
            for h in range(H):
                j, r = h // 2, slice(64 * (h % 2), 64 * (h % 2) + 64)
                mm = pe.matmul(bank[6 + h % 2][:, j * P:(j + 1) * P], kT[r, j, :], kbT[r, j, :],
                               start=True, stop=True)
            mm.then_inc(S("g_kk"), 1)
            for h in range(H):
                j, r = h // 2, slice(64 * (h % 2), 64 * (h % 2) + 64)
                mm = pe.matmul(bank[h % 2][:, j * P:(j + 1) * P], kT[r, j, :], qT[r, j, :],
                               start=True, stop=True)
            mm.then_inc(S("g_kq"), 1)
            for g in range(2):
                nxt(pe, "g_T1")
                for h in range(4 * g, 4 * g + 4):
                    mm = pe.matmul(bank[2 + g][:, (h % 4) * P:(h % 4 + 1) * P], MTl[:, h, :], ident,
                                   start=True, stop=True)
                mm.then_inc(S("g_X1"), 1)
            for lv in LEVELS:
                last = lv == LEVELS[-1]
                for g in range(2):
                    nxt(pe, "g_Ml")
                    nxt(pe, "g_T")
                    for h in range(4 * g, 4 * g + 4):
                        mm = pe.matmul(bank[g][:, (h % 4) * P:(h % 4 + 1) * P], MTl[:, h, :], Tm[:, h, :],
                                       start=True, stop=True)
                    mm.then_inc(S("g_X"), 1)
                for g in range(2):
                    nxt(pe, "g_Xs")
                    for h in range(4 * g, 4 * g + 4):
                        mm = pe.matmul(bank[4 + g][:, (h % 4) * P:(h % 4 + 1) * P], Xs[:, h, :], TT[:, h, :],
                                       start=True, stop=True)
                    if not last:
                        for h in range(4 * g, 4 * g + 4):
                            mm = pe.matmul(bank[2 + g][:, (h % 4) * P:(h % 4 + 1) * P], TT[:, h, :], Xs[:, h, :],
                                           start=True, stop=True)
                    mm.then_inc(S("g_Y"), 1)
            nxt(pe, "g_T", 2)
            for h in range(H):
                j, r = h // 2, slice(64 * (h % 2), 64 * (h % 2) + 64)
                mm = pe.matmul(bank[1][r, j * P:(j + 1) * P], kbG[:, t, h * HD:(h + 1) * HD], TT[:, place(h), :],
                               start=True, stop=True)
            mm.then_inc(S("g_w"), 1)
            nxt(pe, "g_nw")
            for c in range(2):
                rc = slice(64 * c, 64 * c + 64)
                if c:
                    nxt(pe, "g_state")
                for j in range(NPAIR):
                    dst = bank[6][rc, j * P:(j + 1) * P]
                    pe.matmul(dst, nwT[:, j, rc], state[:, j, :], start=True, stop=False)
                    for i in range(2):
                        h = 2 * j + i
                        mm = pe.matmul(bank[6][rc, h * HD:(h + 1) * HD], TT[:, place(h), rc],
                                       vb[:, t, h * HD:(h + 1) * HD], start=False, stop=(i == 1))
                mm.then_inc(S("g_v"), 1)
                nxt(pe, "g_vnew")
                for j in range(NPAIR):
                    pe.matmul(bank[7][rc, j * P:(j + 1) * P], qgT[:, j, rc], state[:, j, :], start=True, stop=False)
                    for i in range(2):
                        h = 2 * j + i
                        pe.matmul(bank[7][rc, h * HD:(h + 1) * HD], attnT[:, place(h), rc],
                                  vnew[:, c, h * HD:(h + 1) * HD], start=False, stop=(i == 1))
                for j in range(NPAIR):
                    mm = pe.matmul(bank[0][:, j * P:(j + 1) * P], kdec[:, t, j * P:(j + 1) * P],
                                   vnew[:, c, j * P:(j + 1) * P], start=True, stop=True)
                mm.then_inc(S("g_out"), 1)
            nxt(pe, "g_o_taken")

        def act_gdn(act, t):
            for i, dst in enumerate((kT, kbT, qT, qgT)):
                nxt(act, "g_turned")
                if i % 2 == 0:
                    act.activation(dst.rearrange("p j c -> p (j c)"), bank[i][:, :], ACT.Copy)\
                       .then_inc(S("g_T_even"), 1)
            nxt(act, "g_diff")
            act.activation(DT, DT, ACT.Exp).then_inc(S("g_decay"), 1)
            for lv in LEVELS:
                for g in range(2):
                    nxt(act, "g_X")
                    act.activation(heads(Xs, g), bank[g][:, :], ACT.Copy).then_inc(S("g_Xs"), 1)
            nxt(act, "g_w")
            act.activation(nwT.rearrange("p j c -> p (j c)"), bank[1][:, :], ACT.Copy, scale=-1.0)\
               .then_inc(S("g_nw"), 1)
            for c in range(2):
                rc = slice(64 * c, 64 * c + 64)
                nxt(act, "g_v")
                act.activation(vnew[rc, c, :], bank[6][rc, :], ACT.Copy).then_inc(S("g_vnew"), 1)
            nxt(act, "g_out", 2)
            act.activation(mixed[:, t, 0:512], bank[7][:, :], ACT.Copy).then_inc(S("g_o_taken"), 1)

        def pool_gdn(pool, t):
            if t:
                pool.wait_ge(S("g_out"), 2 * t)
            else:
                nxt(pool, "g_ready")
            for g in range(2):
                four = [P, NPAIR, P]
                i = pool.tensor_tensor(gU[:, 4 * g:4 * g + 4, :], con("cumsum").unsqueeze(1).broadcast_to(four),
                                       by_parity(g_g[:, t, :])[:, g, :].unsqueeze(2).broadcast_to(four), ALU.mult)
            i.then_inc(S("g_U"), 1)
            nxt(pool, "g_MT")
            nxt(pool, "g_X1", 2)
            for n, lv in enumerate(LEVELS):
                for g in range(2):
                    if n:
                        nxt(pool, "g_X")
                    pool.tensor_tensor(MTl[:, 4 * g:4 * g + 4, :], MT[:, 4 * g:4 * g + 4, :],
                                       con(f"level{lv}").unsqueeze(1).broadcast_to([P, 4, P]), ALU.mult)\
                        .then_inc(S("g_Ml"), 1)
            nxt(pool, "g_X", 2)

        def dve_gdn(dve, t):
            for i, dst in enumerate((kT, kbT, qT, qgT)):
                nxt(dve, "g_turned")
                if i % 2 == 1:
                    dve.tensor_copy(dst.rearrange("p j c -> p (j c)"), bank[i][:, :]).then_inc(S("g_T_odd"), 1)
            nxt(dve, "g_Grow")
            for g in range(2):
                dve.tensor_tensor(DT[:, 4 * g:4 * g + 4, :], bank[4 + g][:, :].rearrange("p (h c) -> p h c", c=P),
                                  by_parity(g_G[:, t, :])[:, g, :].unsqueeze(2).broadcast_to([P, 4, P]), ALU.subtract)
            dve.drain()
            dve.tensor_scalar(DT, DT, 0.0, None, ALU.min).then_inc(S("g_diff"), 1)
            nxt(dve, "g_decay")
            dve.tensor_tensor(DT, DT, con("cumsum").unsqueeze(1).broadcast_to([P, H, P]), ALU.mult)
            dve.drain()
            nxt(dve, "g_kk")
            for g in range(2):
                dve.tensor_tensor(heads(MT, g), bank[6 + g][:, :], heads(DT, g), ALU.mult)
            dve.drain().then_inc(S("g_MT"), 1)
            nxt(dve, "g_kq")
            for g in range(2):
                four = [P, 4, P]
                hs = slice(4 * g, 4 * g + 4)
                dve.tensor_tensor(MTl[:, hs, :], MT[:, hs, :], con("level1").unsqueeze(1).broadcast_to(four), ALU.mult)
                dve.drain()
                dve.tensor_tensor(TT[:, hs, :], ident.unsqueeze(1).broadcast_to(four), MTl[:, hs, :],
                                  ALU.subtract).then_inc(S("g_T1"), 1)
            for g in range(2):
                dve.tensor_tensor(heads(attnT, g), bank[g][:, :], heads(DT, g), ALU.mult)
            for g in range(2):
                nxt(dve, "g_X1")
                dve.drain()
                dve.tensor_tensor(Tm[:, 4 * g:4 * g + 4, :], ident.unsqueeze(1).broadcast_to([P, 4, P]),
                                  bank[2 + g][:, :].rearrange("p (h c) -> p h c", c=P), ALU.subtract)\
                   .then_inc(S("g_T"), 1)
            for lv in LEVELS:
                for g in range(2):
                    nxt(dve, "g_Y")
                    dve.drain()
                    i = dve.tensor_tensor(heads(TT, g), heads(TT, g), bank[4 + g][:, :], ALU.subtract)
                    if lv != LEVELS[-1]:
                        i = dve.tensor_tensor(heads(Tm, g), heads(Tm, g), bank[2 + g][:, :], ALU.subtract)
                    i.then_inc(S("g_T"), 1)
            for c in range(2):
                nxt(dve, "g_out")
                for i in range(2):
                    r = slice(64 * i, 64 * i + 64)
                    dve.tensor_tensor(state[r, :, r], state[r, :, r],
                                      g_dec[r, t, c, :].unsqueeze(2).broadcast_to([64, NPAIR, HD]), ALU.mult)
                dve.drain()
                for i in range(2):
                    r = slice(64 * i, 64 * i + 64)
                    dve.tensor_tensor(state[r, :, r], state[r, :, r],
                                      bank[0][r, :].rearrange("p (j e) -> p j e", e=P)[:, :, r], ALU.add)
                dve.drain().then_inc(S("g_state"), 1)

        def act_gdn_end(act):
            act.drain()
            act.activation(squares[:, :, 0:512], mixed[:, :, 0:512], ACT.Square).then_inc(S("g_osq"), 1)
            act.activation(z, z, ACT.Silu)
            nxt(act, "g_oss")
            act.activation(g_or, g_os, ACT.Sqrt, bias=eps, scale=1.0 / HD)
            act.drain().then_inc(S("g_oroot"), 1)

        def dve_gdn_end(dve):
            nxt(dve, "g_osq")
            dve.tensor_reduce(g_os, squares[:, :, 0:512].rearrange("p t (h e) -> p t h e", e=HD), AX_X, ALU.add)\
               .then_inc(S("g_oss"), 1)
            nxt(dve, "g_oroot")
            dve.reciprocal(g_os, g_or)
            dve.drain()
            for by in (0, 1):
                for t in range(NT):
                    o = mixed[:, t, 0:512].rearrange("p (h e) -> p h e", e=HD)
                    r = g_os[:, t, :].unsqueeze(2) if by == 0 else row("gdn_out_norm").unsqueeze(1)
                    dve.tensor_tensor(o, o, r.broadcast_to([P, H, HD]), ALU.mult)
                dve.drain()
            for t in range(NT):
                dve.tensor_tensor(mixed[:, t, 0:512], mixed[:, t, 0:512], z[:, t, :], ALU.mult)
            dve.drain().then_inc(S("mixed_ready"), 1)

        def dve_gate(dve, dg, m0):
            for k in range(KD):
                i = dve.tensor_scalar(dg[:, k * P:(k + 1) * P], ident, mod[:, m0 + k:m0 + k + 1], None, ALU.mult)
            i.then_inc(S("gate_diag"), 1)

        def pe_gate(pe, dg, b0):
            nxt(pe, "gate_diag")
            for half in range(2):
                mm = pe.matmul(bank[b0 + half][:, :], ones, dg[:, 512 * half:512 * half + 512], start=True, stop=True)
            mm.then_inc(S("gate_row"), 1)

        def dve_gate_row(dve, gate, b0):
            nxt(dve, "gate_row")
            dve.tensor_copy(gate[:, 0:512], bank[b0][:, :])
            dve.tensor_copy(gate[:, 512:D], bank[b0 + 1][:, :])
            dve.drain().then_inc(S("gate_taken"), 1)

        gate1 = region(24656, D)
        diag1 = region(25680, D)

        def act_turned(act):
            for k in range(0, KD, 2):
                nxt(act, "x_turned", 2 if k else 1)
                i = act.activation(hT[:, k, :], bank[k][:, :], ACT.Copy)
            tally[(str(act.engine), "x_turned")] += 1
            i.then_inc(S("hT_even"), 1)

        def dve_turned(dve):
            for k in range(1, KD, 2):
                nxt(dve, "x_turned", 2)
                i = dve.tensor_copy(hT[:, k, :], bank[k][:, :])
            i.then_inc(S("hT_odd"), 1)

        def pe_down(pe, name, n_slots_, lhs):
            for i in range(n_slots_):
                s = FIRST[name] + i
                need(pe, s)
                w = slot_view(s, D)
                for kk_ in range(2):
                    k = 2 * i + kk_
                    for t in range(NT):
                        for half in range(2):
                            mm = pe.matmul(bank[2 * t + half][:, :], lhs(k, t), w[:, kk_, 512 * half:512 * half + 512],
                                           start=(k == 0), stop=(k == 2 * n_slots_ - 1))
                mm.then_inc(S("slots_used"), 1)

        def dve_out1(dve):
            dve.wait_ge(S("slots_used"), FIRST["w_out"] + 4)
            tmp = region(26704, 1024, "p (b n) -> p b n", b=2)
            for t in range(NT):
                for half in range(2):
                    c = slice(512 * half, 512 * half + 512)
                    dve.tensor_tensor(tmp[:, half, :], bank[2 * t + half][:, :], gate1[:, c], ALU.mult)
                dve.drain()
                dve.tensor_tensor(X[:, t, :], X[:, t, :], tmp.rearrange("p b n -> p (b n)"), ALU.add)
                dve.drain()

        NR = N_GRP + N_EXP
        m_y = region(0, 8192, "p (c t n) -> p c t n", c=2, t=NT)
        h2tok = m_y[:, 0]
        xn2 = m_y[:, 1]
        m_x = region(8192, 2048, "p (b n) -> p b n", b=2)
        m_xT = region(10240, 2048, "p (b k s) -> p b k s", b=2, k=KD)
        m_sg = region(12288, 512, "p (b f) -> p b f", b=2)
        m_hid = region(12800, 512, "p (b f) -> p b f", b=2)
        m_hT = region(13312, 512, "p (b f s) -> p b f s", b=2, f=2)
        m_out = region(13824, 2048, "p (b n) -> p b n", b=2)
        m_P = region(15872, 1024).bitcast(BF16).rearrange("p (b t s) -> p b t s", b=4, t=NT)
        m_code = region(16896, 256).bitcast(BF16).rearrange("p (t e c) -> p t e c", t=NT, c=4)
        m_rw = region(17152, KD * NR, "p (k n) -> p k n", n=NR)
        junk2 = region(10240, D)

        def mr(at, width, pattern=None, **kw):
            r = region(17440 + at, width)
            return r.rearrange(pattern, **kw) if pattern else r

        r_lg = mr(0, NT * NR, "p (t n) -> p t n", t=NT)
        r_a = mr(144, 16, "p (t g) -> p t g", t=NT)
        r_b = mr(160, 16, "p (t g) -> p t g", t=NT)
        r_goh = mr(176, 16, "p (t g) -> p t g", t=NT)
        r_m = mr(192, 4)
        r_v = mr(196, 4)
        r_pg = mr(200, 4)
        r_m1 = mr(204, 4)
        r_m2 = mr(208, 4)
        r_w1 = mr(212, 4)
        r_w2 = mr(216, 4)
        r_ig = mr(224, 32, "p (t e) -> p t e", t=NT)
        r_o1 = mr(256, 32, "p (t e) -> p t e", t=NT)
        r_o2 = mr(288, 32, "p (t e) -> p t e", t=NT)
        r_c = mr(320, 32, "p (t e) -> p t e", t=NT)
        r_sel = mr(384, 128, "p (t e g) -> p t e g", t=NT, g=N_GRP)
        r_E = mr(512, 256, "p (c t e) -> p c t e", c=2, t=NT)
        r_M = mr(768, 128, "p (t e) -> p t e", t=NT)
        r_rank = mr(896, 128, "p (t e) -> p t e", t=NT)
        r_tab = mr(1024, 128, "p (e c) -> p e c", c=4)
        r_f = mr(1152, 64, "p (c e) -> p c e", c=2)
        r_idx = mr(1216, 64, "p (c e) -> p c e", c=2).bitcast(I32)
        r_cnt = mr(1280, 32)
        m_gi = mr(1314, 2).bitcast(I32)
        m_si = mr(1316, 2).bitcast(I32)
        o_iota = mr(1320, P)
        NONE = float(1 << 20)

        gate2 = region(22000, D)
        diag2 = region(23024, D)
        h2_dram = nc.dram_tensor("h2_rows", (T, D), F32, kind="Internal").ap()
        y_dram = nc.dram_tensor("expert_rows", (2 * T, D), F32, kind="Internal").ap()

        def act_router_weights(act):
            for n0, name in ((0, "w_group"), (N_GRP, "w_router")):
                act.dma_start(m_rw[:, :, n0:n0 + a[name].shape[-1]],
                              a[name][0].rearrange("(k p) n -> p k n", p=P)).then_inc(S("rw_loaded"), 16)

        def pe_route(pe):
            pe_hT(pe)
            nxt(pe, "rw_loaded", 32)
            for t in range(NT):
                for k in range(KD):
                    mm = pe.matmul(bank[0][:, NR * t:NR * t + NR], tokens(k, t), m_rw[:, k, :],
                                   start=(k == 0), stop=(k == KD - 1))
            mm.then_inc(S("r_logits"), 1)
            for t in range(1, NT):
                pe_h2(pe, t)
            pe.wait_ge(S("r_taken"), 1)
            pe_h2(pe, 0)
            nxt(pe, "h2_ready", NT)
            nxt(pe, "r_M")
            for t in range(NT):
                for s in range(t):
                    pe.matmul(bank[2][:, 32 * t:32 * t + 32], ones, r_M[:, s, :], start=(s == 0), stop=False)
                pe.matmul(bank[2][:, 32 * t:32 * t + 32], con("before"), r_M[:, t, :], start=(t == 0), stop=True)
            for t in range(NT):
                mm = pe.matmul(bank[2][:, 128:160], ones, r_M[:, t, :], start=(t == 0), stop=(t == NT - 1))
            mm.then_inc(S("r_ranks"), 1)
            for e in range(N_EXP):
                nxt(pe, "r_P")
                for t in range(NT):
                    mm = pe.matmul(bank[3][:, 4 * e:4 * e + 4], m_P[:, e % 4, t, :], m_code[:, t, e, :],
                                   start=(t == 0), stop=(t == NT - 1))
                mm.then_inc(S("r_coded"), 1)

        def pe_h2(pe, t):
            for k in range(KD):
                mm = pe.transpose(bank[2 * t + k // 4][:, (k % 4) * P:(k % 4 + 1) * P],
                                  hT[:, k, t * P:(t + 1) * P], ident)
            mm.then_inc(S("h2_turned"), 1)

        def act_h2(act):
            for t in (1, 2, 3, 0):
                nxt(act, "h2_turned")
                for half in range(2):
                    act.activation(h2tok[:, t, 512 * half:512 * half + 512], bank[2 * t + half][:, :], ACT.Copy)
                act.drain().then_inc(S("h2_ready"), 1)

        def sp_h2(sp):
            for t in (1, 2, 3, 0):
                nxt(sp, "h2_ready")
                sp.dma_start(h2_dram[t * P:(t + 1) * P, :], h2tok[:, t, :]).then_inc(S("h2_stored"), 16)

        def act_route(act):
            nxt(act, "r_gmax")
            act.activation(r_a, r_a, ACT.Exp)
            act.drain().then_inc(S("r_gexp"), 1)
            nxt(act, "r_diff")
            act.activation(r_w2, r_m2, ACT.Exp).then_inc(S("r_wexp"), 1)

        def dve_first_of(dve, dst, values, best, tie, n, tmp):
            shape = [P, NT, n]
            dve.tensor_tensor(tmp, values, best.unsqueeze(2).broadcast_to(shape), ALU.is_equal)
            dve.drain()
            dve.tensor_tensor(tmp, tmp, con(tie).unsqueeze(1).broadcast_to(shape), ALU.mult)
            dve.drain()
            dve.tensor_reduce(r_v, tmp, AX_X, ALU.max)
            dve.drain()
            dve.tensor_tensor(dst, tmp, r_v.unsqueeze(2).broadcast_to(shape), ALU.is_equal)
            dve.drain()

        def dve_route(dve):
            nxt(dve, "r_logits")
            at = ROWS["b_group"][0]
            dve.tensor_tensor(r_lg, bank[0][:, 0:NT * NR].rearrange("p (t n) -> p t n", t=NT),
                              rows[:, at:at + NR].unsqueeze(1).broadcast_to([P, NT, NR]), ALU.add)
            dve.drain().then_inc(S("r_taken"), 1)
            groups = r_lg[:, :, 0:N_GRP]
            dve.tensor_reduce(r_m, groups, AX_X, ALU.max)
            dve.drain()
            dve.tensor_tensor(r_a, groups, r_m.unsqueeze(2).broadcast_to([P, NT, N_GRP]), ALU.subtract)\
               .then_inc(S("r_gmax"), 1)
            dve_first_of(dve, r_goh, groups, r_m, "tie4", N_GRP, r_b)
            for t in range(NT):
                dve.tensor_tensor(r_sel[:, t], r_lg[:, t, N_GRP:NR].rearrange("p (g e) -> p e g", g=N_GRP),
                                  r_goh[:, t, :].unsqueeze(1).broadcast_to([P, EPG, N_GRP]), ALU.mult)
            dve.drain()
            dve.tensor_reduce(r_ig, r_sel, AX_X, ALU.add)
            dve.drain()
            dve.tensor_reduce(r_m1, r_ig, AX_X, ALU.max)
            dve.drain()
            dve_first_of(dve, r_o1, r_ig, r_m1, "tie8", EPG, r_c)
            dve.scalar_tensor_tensor(r_ig, r_o1, -BIG, r_ig, ALU.mult, ALU.add)
            dve.drain()
            dve.tensor_reduce(r_m2, r_ig, AX_X, ALU.max)
            dve.drain()
            dve_first_of(dve, r_o2, r_ig, r_m2, "tie8", EPG, r_c)
            dve.tensor_tensor(r_m2, r_m2, r_m1, ALU.subtract).then_inc(S("r_diff"), 1)
            nxt(dve, "r_gexp")
            dve.tensor_reduce(r_pg, r_a, AX_X, ALU.add)
            nxt(dve, "r_wexp")
            dve.drain()
            dve.tensor_scalar(r_w1, r_w2, 1.0, None, ALU.add)
            dve.drain()
            dve.tensor_tensor(r_w1, r_w1, r_pg, ALU.mult)
            dve.drain()
            dve.reciprocal(r_w1, r_w1)
            dve.drain()
            dve.tensor_tensor(r_w2, r_w2, r_w1, ALU.mult)
            for c, o in enumerate((r_o1, r_o2)):
                for t in range(NT):
                    shape = [P, N_GRP, EPG]
                    dve.tensor_tensor(r_E[:, c, t, :].rearrange("p (g e) -> p g e", g=N_GRP),
                                      r_goh[:, t, :].unsqueeze(2).broadcast_to(shape),
                                      o[:, t, :].unsqueeze(1).broadcast_to(shape), ALU.mult)
            dve.drain()
            dve.tensor_tensor(r_M, r_E[:, 0], r_E[:, 1], ALU.add)
            dve.drain().then_inc(S("r_M"), 1)
            dve.memset(m_code[:, :, :, 0:1], 1.0)
            for t in range(NT):
                dve.tensor_copy(m_code[:, t, :, 1:2], con("partition").unsqueeze(1).broadcast_to([P, N_EXP, 1]))
                dve.memset(m_code[:, t, :, 2:3], float(t))
                dve.tensor_copy(m_code[:, t, :, 3:4], r_E[:, 1, t, :].unsqueeze(2))
            nxt(dve, "r_ranks")
            dve.scalar_tensor_tensor(r_rank, bank[2][:, 0:128].rearrange("p (t e) -> p t e", t=NT), 1.0, r_M,
                                     ALU.add, ALU.mult)
            dve.tensor_copy(r_cnt, bank[2][:, 128:160])
            dve.drain()
            dve.tensor_scalar(r_rank, r_rank, 1.0, None, ALU.subtract)
            dve_more_list(dve)
            for e in range(N_EXP):
                if e >= 4:
                    nxt(dve, "r_coded")
                shape = [P, NT, P]
                dve.tensor_tensor(m_P[:, e % 4], con("iota").unsqueeze(1).broadcast_to(shape),
                                  r_rank[:, :, e].unsqueeze(2).broadcast_to(shape), ALU.is_equal)\
                   .then_inc(S("r_P"), 1)
            nxt(dve, "r_coded", 4)
            dve_indices(dve, bank[3][:, 0:128].rearrange("p (e c) -> p e c", c=4), r_tab, r_f, r_idx)
            dve.drain().then_inc(S("r_idx"), 1)

        def dve_indices(dve, ps, tab, f, idx):
            dve.tensor_copy(tab, ps)
            dve.drain()
            dve.scalar_tensor_tensor(f[:, 0, :], tab[:, :, 2], float(P), tab[:, :, 1], ALU.mult, ALU.add)
            dve.tensor_scalar(f[:, 1, :], tab[:, :, 0], -NONE, NONE, ALU.mult, ALU.add)
            dve.drain()
            dve.tensor_tensor(f[:, 0, :], f[:, 0, :], f[:, 1, :], ALU.add)
            dve.drain()
            dve.scalar_tensor_tensor(f[:, 1, :], tab[:, :, 3], float(T), f[:, 0, :], ALU.mult, ALU.add)
            dve.drain()
            dve.tensor_copy(idx, f)

        w_gate, w_up, w_down = a["w_gate"][0], a["w_up"][0], a["w_down"][0]
        gu = [ring[:, 2 * b:2 * b + 2, :].rearrange("p u (k n) -> p u k n", n=F_EXP) for b in range(2)]
        dn = [ring[:, 4 + b, :].rearrange("p (f n) -> p f n", n=D) for b in range(2)]

        def flat_rows(w, e, n):
            rows_ = w.shape[1]
            return w.rearrange("e k n -> (e k) n")[bass.ds(e * rows_, rows_), :].rearrange("(k p) n -> p k n", p=P)

        def sp_expert(sp, e, b, first=False):
            if not first:
                sp.wait_ge(S("gu_used"), e - 1)
            sp.dma_start(gu[b][:, 0], flat_rows(w_gate, e, F_EXP)).then_inc(S(f"gu_loaded{b}"), 16)
            sp.dma_start(gu[b][:, 1], flat_rows(w_up, e, F_EXP)).then_inc(S(f"gu_loaded{b}"), 16)
            if not first:
                sp.wait_ge(S("dn_used"), e - 1)
            sp.dma_start(dn[b], flat_rows(w_down, e, D)).then_inc(S(f"dn_loaded{b}"), 16)

        def sp_moe_first(sp):
            sp.wait_ge(S("slots_used"), MOE_AT)
            for e in range(2):
                sp_expert(sp, e, e, first=True)

        def sp_moe(sp):
            with sp.Fori(1, N_EXP // 2) as i:
                for b in range(2):
                    sp_expert(sp, 2 * i + b, b)

        def pool_gather(pool, i, b):
            pool.tensor_copy(m_gi[:, b:b + 1], r_idx[:, 0, bass.ds(2 * i + b, 1)])
            pool.drain()
            pool.indirect_dma_start(out=m_x[:, b, :], out_offset=None, in_=h2_dram,
                                    in_offset=bass.IndirectOffsetOnAxis(ap=m_gi[:, b:b + 1], axis=0),
                                    bounds_check=T - 1, oob_is_err=False).then_inc(S(f"m_gathered{b}"), 16)

        def pool_scatter(pool, i, b, rows_from=None):
            pool.tensor_copy(m_si[:, b:b + 1], r_idx[:, 1, bass.ds(2 * i + b, 1)])
            pool.drain()
            pool.indirect_dma_start(out=y_dram, in_=m_out[:, b, :], in_offset=None,
                                    out_offset=bass.IndirectOffsetOnAxis(ap=m_si[:, b:b + 1], axis=0),
                                    bounds_check=2 * T - 1, oob_is_err=False).then_inc(S(f"m_scattered{b}"), 16)

        def pool_moe(pool):
            pool.memset(m_x[:, :, :], 0.0)
            pool.drain()
            nxt(pool, "r_idx")
            nxt(pool, "h2_stored", 16 * NT)
            for b in range(2):
                pool_gather(pool, 0, b)

            def step(i, b, gather=True):
                if gather:
                    pool.wait_ge(S("m_x_turned"), 2 * i + b + 1)
                    pool.wait_ge(S(f"m_gathered{b}"), 16 * (i + 1))
                    pool_gather(pool, i + 1, b)
                pool.wait_ge(S("m_y_act"), 2 * i + b + 1)
                pool.wait_ge(S("m_y_dve"), 2 * i + b + 1)
                pool_scatter(pool, i, b)

            for b in range(2):
                step(0, b)
            with pool.Fori(1, N_EXP // 2 - 1) as i:
                for b in range(2):
                    pool.wait_ge(S(f"m_scattered{b}"), 16 * i)
                    step(i, b)
            for b in range(2):
                pool.wait_ge(S(f"m_scattered{b}"), 16 * (N_EXP // 2 - 1))
                step(N_EXP // 2 - 1, b, gather=False)
            for b in range(2):
                pool.wait_ge(S(f"m_scattered{b}"), 16 * (N_EXP // 2))

        def pe_moe(pe):
            def turn_x(i, b):
                e = 2 * i + b
                if not (isinstance(e, int) and e == 0):
                    pe.wait_ge(S("m_xT_act"), e)
                    pe.wait_ge(S("m_xT_dve"), e)
                pe.wait_ge(S(f"m_gathered{b}"), 16 * (i + 1))
                for k in range(KD):
                    mm = pe.transpose(bank[k // 4][:, (k % 4) * P:(k % 4 + 1) * P], m_x[:, b, k * P:(k + 1) * P], ident)
                mm.then_inc(S("m_x_turned"), 1)

            def gate_up(i, b):
                e = 2 * i + b
                pe.wait_ge(S(f"gu_loaded{b}"), 32 * (i + 1))
                pe.wait_ge(S("m_xT_act"), e + 1)
                pe.wait_ge(S("m_xT_dve"), e + 1)
                for k in range(KD):
                    mm = pe.matmul(bank[2 + b][:, :], m_xT[:, b, k, :], gu[b][:, :, k, :],
                                   start=(k == 0), stop=(k == KD - 1))
                mm.then_inc(S("gu_used"), 1)

            def turn_hidden(i, b):
                pe.wait_ge(S("m_hid"), 2 * i + b + 1)
                for f in range(2):
                    mm = pe.transpose(bank[4 + b][:, f * P:(f + 1) * P], m_hid[:, b, f * P:(f + 1) * P], ident)
                mm.then_inc(S("m_h_turned"), 1)

            def down(i, b):
                e = 2 * i + b
                pe.wait_ge(S(f"dn_loaded{b}"), 16 * (i + 1))
                pe.wait_ge(S("m_hT"), e + 1)
                if not (isinstance(e, int) and e == 0):
                    pe.wait_ge(S("m_y_act"), e)
                    pe.wait_ge(S("m_y_dve"), e)
                for f in range(2):
                    for half in range(2):
                        mm = pe.matmul(bank[6 + half][:, :], m_hT[:, b, f, :], dn[b][:, f, 512 * half:512 * half + 512],
                                       start=(f == 0), stop=(f == 1))
                mm.then_inc(S("dn_used"), 1)

            def pair(i, first=False, last=False):
                gate_up(i, 0)
                if not first:
                    down(i - 1, 1)
                if not last:
                    turn_x(i + 1, 0)
                turn_hidden(i, 0)
                gate_up(i, 1)
                down(i, 0)
                if not last:
                    turn_x(i + 1, 1)
                turn_hidden(i, 1)

            turn_x(0, 0)
            turn_x(0, 1)
            pair(0, first=True)
            with pe.Fori(1, N_EXP // 2 - 1) as i:
                pair(i)
            pair(N_EXP // 2 - 1, last=True)
            down(N_EXP // 2 - 1, 1)

        def act_moe(act):
            def x_half(i, b):
                act.wait_ge(S("m_x_turned"), 2 * i + b + 1)
                act.activation(m_xT[:, b, 0:4, :].rearrange("p k s -> p (k s)"), bank[0][:, :], ACT.Copy)
                act.drain().then_inc(S("m_xT_act"), 1)

            def silu(i, b):
                act.wait_ge(S("gu_used"), 2 * i + b + 1)
                if not (isinstance(i, int) and i == 0):
                    act.wait_ge(S("m_hid"), 2 * i + b - 1)
                act.activation(m_sg[:, b, :], bank[2 + b][:, 0:F_EXP], ACT.Silu).then_inc(S("m_sg"), 1)

            def y_half(i, b):
                act.wait_ge(S("dn_used"), 2 * i + b + 1)
                if not (isinstance(i, int) and i == 0):
                    act.wait_ge(S(f"m_scattered{b}"), 16 * i)
                act.activation(m_out[:, b, 0:512], bank[6][:, :], ACT.Copy)
                act.drain().then_inc(S("m_y_act"), 1)

            def pair(i, first=False, last=False):
                silu(i, 0)
                if not first:
                    y_half(i - 1, 1)
                if not last:
                    x_half(i + 1, 0)
                silu(i, 1)
                y_half(i, 0)
                if not last:
                    x_half(i + 1, 1)

            x_half(0, 0)
            x_half(0, 1)
            pair(0, first=True)
            pair(1)
            with act.Fori(2, N_EXP // 2 - 1) as i:
                pair(i)
            pair(N_EXP // 2 - 1, last=True)
            y_half(N_EXP // 2 - 1, 1)

        def dve_moe(dve):
            def x_half(i, b):
                dve.wait_ge(S("m_x_turned"), 2 * i + b + 1)
                dve.tensor_copy(m_xT[:, b, 4:8, :].rearrange("p k s -> p (k s)"), bank[1][:, :])
                dve.drain().then_inc(S("m_xT_dve"), 1)

            def hidden(i, b):
                dve.wait_ge(S("m_sg"), 2 * i + b + 1)
                dve.tensor_tensor(m_hid[:, b, :], m_sg[:, b, :], bank[2 + b][:, F_EXP:512], ALU.mult)
                dve.drain().then_inc(S("m_hid"), 1)

            def hidden_T(i, b):
                dve.wait_ge(S("m_h_turned"), 2 * i + b + 1)
                dve.tensor_copy(m_hT[:, b].rearrange("p f s -> p (f s)"), bank[4 + b][:, 0:256])
                dve.drain().then_inc(S("m_hT"), 1)

            def y_half(i, b):
                dve.wait_ge(S("dn_used"), 2 * i + b + 1)
                if not (isinstance(i, int) and i == 0):
                    dve.wait_ge(S(f"m_scattered{b}"), 16 * i)
                dve.tensor_copy(m_out[:, b, 512:D], bank[7][:, :])
                dve.drain().then_inc(S("m_y_dve"), 1)

            def pair(i, first=False, last=False):
                hidden(i, 0)
                if not first:
                    y_half(i - 1, 1)
                if not last:
                    x_half(i + 1, 0)
                hidden_T(i, 0)
                hidden(i, 1)
                y_half(i, 0)
                if not last:
                    x_half(i + 1, 1)
                hidden_T(i, 1)

            x_half(0, 0)
            x_half(0, 1)
            pair(0, first=True)
            pair(1)
            with dve.Fori(2, N_EXP // 2 - 1) as i:
                pair(i)
            pair(N_EXP // 2 - 1, last=True)
            y_half(N_EXP // 2 - 1, 1)

        MORE = T // CAP - 1
        ITEMS = (2 * T - 1) // CAP
        o_gu = region(0, 4096, "p (u k n) -> p u k n", u=2, n=F_EXP)
        o_dn = region(4096, 2048, "p (f n) -> p f n", n=D)
        o_tab = mr(1448, 4, "p (e c) -> p e c", c=4)
        o_f = mr(1452, 2, "p (c e) -> p c e", c=2)
        o_idx = mr(1454, 2, "p (c e) -> p c e", c=2).bitcast(I32)
        o_at = mr(1456, 2, "p (c e) -> p c e", c=2).bitcast(I32)
        o_expert = mr(1458, 8).bitcast(I32)
        o_place = mr(1466, 8)
        o_count = mr(1474, 2).bitcast(I32)

        def dve_more_list(dve):
            n = MORE * N_EXP
            flag, prefix, expert, place = (region(13824 + n * i, n, "p (q e) -> p q e", e=N_EXP) for i in range(4))
            sel, val = (region(14336 + 768 * i, ITEMS * n, "p (i j) -> p i j", j=n) for i in range(2))
            shape = [P, ITEMS, n]

            def flat(x):
                return x.rearrange("p q e -> p (q e)")

            for q in range(MORE):
                dve.tensor_scalar(flag[:, q, :], r_cnt, float(CAP * (q + 1)), None, ALU.is_gt)
                dve.memset(place[:, q, :], float(CAP * (q + 1)))
                dve.tensor_copy(expert[:, q, :], con("iota")[:, 0:N_EXP])
            dve.drain()
            dve.tensor_tensor_scan(flat(prefix), flat(flag), flat(flag), 0.0, ALU.add, ALU.bypass)
            dve.drain()
            dve.tensor_copy(o_count[:, 0:1], prefix[:, MORE - 1, N_EXP - 1:N_EXP])
            dve.tensor_tensor(sel, flat(prefix).unsqueeze(1).broadcast_to(shape),
                              con("iota")[:, 1:ITEMS + 1].unsqueeze(2).broadcast_to(shape), ALU.is_equal)
            dve.drain()
            dve.tensor_tensor(sel, sel, flat(flag).unsqueeze(1).broadcast_to(shape), ALU.mult)
            dve.drain()
            for table, dst in ((expert, o_expert), (place, o_place)):
                dve.tensor_tensor(val, sel, flat(table).unsqueeze(1).broadcast_to(shape), ALU.mult)
                dve.drain()
                dve.tensor_reduce(prefix[:, 0, 0:ITEMS], val, AX_X, ALU.add)
                dve.drain()
                dve.tensor_copy(dst[:, 0:ITEMS], prefix[:, 0, 0:ITEMS])
                dve.drain()
            dve.drain().then_inc(S("r_count"), 1)

        def more(e, body):
            e.wait_ge(S("r_count"), 1)
            count = e.value_load(o_count[0:1, 0:1], min_val=0, max_val=ITEMS)
            with e.Fori(0, ITEMS) as i:
                with e.If(count > i):
                    body(i)

        def expert_of(e, i):
            return e.value_load(o_expert[0:1, bass.ds(i, 1)], min_val=0, max_val=N_EXP - 1)

        def sp_more(sp):
            nxt(sp, "h2_stored", 16 * NT)
            def body(n):
                ex = expert_of(sp, n)
                sp.wait_ge(S("o_P"), n + 1)
                sp.dma_start(o_gu[:, 0], flat_rows(w_gate, ex, F_EXP)).then_inc(S("o_loaded"), 16)
                sp.dma_start(o_gu[:, 1], flat_rows(w_up, ex, F_EXP)).then_inc(S("o_loaded"), 16)
                sp.dma_start(o_dn, flat_rows(w_down, ex, D)).then_inc(S("o_loaded"), 16)
            more(sp, body)

        def dve_more(dve):
            def body(n):
                ex = expert_of(dve, n)
                dve.wait_ge(S("o_free"), n + 1)
                shape = [P, NT, P]
                dve.tensor_tensor(o_iota, con("iota"), o_place[:, bass.ds(n, 1)].broadcast_to([P, P]), ALU.add)
                dve.drain()
                dve.tensor_tensor(m_P[:, 0], o_iota.unsqueeze(1).broadcast_to(shape),
                                  r_rank[:, :, bass.ds(ex, 1)].broadcast_to(shape), ALU.is_equal)
                dve.tensor_copy(m_code[:, :, 0, 3:4], r_E[:, 1, :, bass.ds(ex, 1)])
                dve.drain().then_inc(S("o_P"), 1)
                dve.wait_ge(S("o_coded"), n + 1)
                dve_indices(dve, bank[3][:, 0:4].rearrange("p (e c) -> p e c", c=4), o_tab, o_f, o_idx)
                dve.drain().then_inc(S("o_idx"), 1)
                dve.wait_ge(S("o_x_turned"), n + 1)
                for half in range(2):
                    dve.tensor_copy(m_xT[:, 0, 4 * half:4 * half + 4, :].rearrange("p k s -> p (k s)"),
                                    bank[half][:, :])
                dve.drain().then_inc(S("o_xT"), 1)
                dve.wait_ge(S("o_sg"), n + 1)
                dve.tensor_tensor(m_hid[:, 0, :], m_sg[:, 0, :], bank[2][:, F_EXP:512], ALU.mult)
                dve.drain().then_inc(S("o_hid"), 1)
                dve.wait_ge(S("o_h_turned"), n + 1)
                dve.tensor_copy(m_hT[:, 0].rearrange("p f s -> p (f s)"), bank[4][:, 0:256])
                dve.drain().then_inc(S("o_hT"), 1)
                dve.wait_ge(S("o_y"), n + 1)
                for half in range(2):
                    dve.tensor_copy(m_out[:, 0, 512 * half:512 * half + 512], bank[6 + half][:, :])
                dve.drain().then_inc(S("o_out"), 1)

            more(dve, body)

        def act_more(act):
            def body(n):
                act.wait_ge(S("o_gate_up"), n + 1)
                act.activation(m_sg[:, 0, :], bank[2][:, 0:F_EXP], ACT.Silu).then_inc(S("o_sg"), 1)
            more(act, body)

        def pool_more(pool):
            nothing = con("zero").bitcast(I32)

            def body(n):
                pool.wait_ge(S("o_idx"), n + 1)
                pool.tensor_tensor(o_at[:, 0, :], o_idx[:, 0, :], nothing, ALU.add)
                pool.tensor_tensor(o_at[:, 1, :], o_idx[:, 1, :], nothing, ALU.add)
                pool.drain()
                pool.indirect_dma_start(out=m_x[:, 0, :], out_offset=None, in_=h2_dram,
                                        in_offset=bass.IndirectOffsetOnAxis(ap=o_at[:, 0, :], axis=0),
                                        bounds_check=T - 1, oob_is_err=False).then_inc(S("o_gathered"), 16)
                pool.wait_ge(S("o_out"), n + 1)
                pool.tensor_tensor(o_at[:, 1, :], o_idx[:, 1, :], nothing, ALU.add)
                pool.drain()
                pool.indirect_dma_start(out=y_dram, in_=m_out[:, 0, :], in_offset=None,
                                        out_offset=bass.IndirectOffsetOnAxis(ap=o_at[:, 1, :], axis=0),
                                        bounds_check=2 * T - 1, oob_is_err=False).then_inc(S("o_scattered"), 16)
                pool.wait_ge(S("o_scattered"), 16 * n + 16)
                pool.tensor_tensor(o_at[:, 0, :], o_idx[:, 0, :], nothing, ALU.add).then_inc(S("o_free"), 1)
            pool.drain().then_inc(S("o_free"), 1)
            more(pool, body)
            pool.drain().then_inc(S("rows_scattered"), 1)

        def pe_more(pe):
            def body(n):
                pe.wait_ge(S("o_P"), n + 1)
                for t in range(NT):
                    mm = pe.matmul(bank[3][:, 0:4], m_P[:, 0, t, :], m_code[:, t, 0, :],
                                   start=(t == 0), stop=(t == NT - 1))
                mm.then_inc(S("o_coded"), 1)
                pe.wait_ge(S("o_gathered"), 16 * n + 16)
                for k in range(KD):
                    mm = pe.transpose(bank[k // 4][:, (k % 4) * P:(k % 4 + 1) * P], m_x[:, 0, k * P:(k + 1) * P], ident)
                mm.then_inc(S("o_x_turned"), 1)
                pe.wait_ge(S("o_xT"), n + 1)
                pe.wait_ge(S("o_loaded"), 48 * n + 48)
                for k in range(KD):
                    mm = pe.matmul(bank[2][:, :], m_xT[:, 0, k, :], o_gu[:, :, k, :], start=(k == 0), stop=(k == KD - 1))
                mm.then_inc(S("o_gate_up"), 1)
                pe.wait_ge(S("o_hid"), n + 1)
                for f in range(2):
                    mm = pe.transpose(bank[4][:, f * P:(f + 1) * P], m_hid[:, 0, f * P:(f + 1) * P], ident)
                mm.then_inc(S("o_h_turned"), 1)
                pe.wait_ge(S("o_hT"), n + 1)
                for f in range(2):
                    for half in range(2):
                        mm = pe.matmul(bank[6 + half][:, :], m_hT[:, 0, f, :], o_dn[:, f, 512 * half:512 * half + 512],
                                       start=(f == 0), stop=(f == 1))
                mm.then_inc(S("o_y"), 1)
            more(pe, body)

        def act_moe_end(act):
            nxt(act, "rows_scattered")
            for c in range(2):
                for t in range(NT):
                    r = slice(c * T + t * P, c * T + (t + 1) * P)
                    act.dma_start(m_y[:, c, t, :], y_dram[r, :]).then_inc(S("y_loaded"), 16)

        def dve_moe_end(dve):
            nxt(dve, "y_loaded", 16 * 2 * NT)
            for t in range(NT):
                dve.tensor_scalar(m_y[:, 1, t, :], m_y[:, 1, t, :], r_w2[:, t:t + 1], None, ALU.mult)
            dve.drain()
            for t in range(NT):
                dve.scalar_tensor_tensor(m_y[:, 0, t, :], m_y[:, 0, t, :], r_w1[:, t:t + 1], m_y[:, 1, t, :],
                                         ALU.mult, ALU.add)
            dve.drain()
            for t in range(NT):
                dve.tensor_tensor(m_y[:, 0, t, :], m_y[:, 0, t, :], gate2, ALU.mult)
            dve.drain()
            for t in range(NT):
                dve.tensor_tensor(X[:, t, :], X[:, t, :], m_y[:, 0, t, :], ALU.add)
            dve.drain()

        hidT = region(0, NFF * T, "p (f t) -> p f t", t=T)
        f_sg = region(NFF * T, 1024, "p (b t) -> p b t", b=2)
        post = region(NFF * T + 1024, D)
        f_tmp = region(NFF * T + 2048, 2048, "p (b n) -> p b n", b=2)
        f_sq = region(NFF * T + 4096, 512)
        f_ss = region(NFF * T + 4608, 8, "p (t h) -> p t h", t=NT)
        f_r = region(NFF * T + 4616, 8, "p (c t) -> p c t", c=2)
        NPAIRS = NFF // 2
        ROUNDS = NPAIRS // 3
        xn3 = region(20480, 4096, "p (t n) -> p t n", n=D)
        junk3 = region(24576, D)

        def sp_ffn(sp, tag):
            f = FIRST[tag]
            load(sp, f, 6)
            wg, wu = a[f"{tag}_w_gate_2"][0], a[f"{tag}_w_up_2"][0]
            with sp.Fori(1, ROUNDS) as it:
                for jj in range(6):
                    sp.wait_ge(S("slots_used"), 6 * it + (f + jj - RING + 1))
                    src = (wg, wu)[jj % 2][:, bass.ds(768 * it + 256 * (jj // 2), 256)]
                    sp.dma_start(slot_view(f + jj, 256), src.rearrange("(k p) n -> p k n", p=P))\
                      .then_inc(loaded[(f + jj) % RING], 16)
            load(sp, f + 6 * ROUNDS, 2 * NPAIRS - 6 * ROUNDS)
            load(sp, FIRST[tag + "_down"], NPAIRS)

        def pe_ffn(pe, tag):
            f = FIRST[tag]
            def pair(pp, it):
                for j in range(2):
                    u = 2 * pp + j
                    pe.wait_ge(S(f"{tag}_free"), 6 * it + (u + 1) + before(f"{tag}_free"))
                    for which in range(2):
                        jj = 2 * pp + which
                        if j == 0:
                            pe.wait_ge(loaded[(f + jj) % RING], 16 * it + 16 * ((f + jj) // RING + 1))
                        w = slot_view(f + jj, 256)
                        for k in range(KD):
                            mm = pe.matmul(bank[2 * (u % 3) + which][:, :], w[:, k, j * P:(j + 1) * P], hT[:, k, :],
                                           start=(k == 0), stop=(k == KD - 1))
                        if j == 1:
                            mm.then_inc(S("slots_used"), 1)
                    if j == 0:
                        mm.then_inc(S(f"{tag}_gu"), 1)

            with pe.Fori(0, ROUNDS) as it:
                for pp in range(3):
                    pair(pp, it)
            for pp in range(NPAIRS - 3 * ROUNDS):
                pair(pp, ROUNDS)
            pe.wait_ge(S(f"{tag}_free"), NFF + 3 + before(f"{tag}_free"))
            pe_down(pe, tag + "_down", NPAIRS, lambda k, t: hidT[:, k, t * P:(t + 1) * P])

        def act_ffn(act, tag):
            f = FIRST[tag]

            def unit(u, it):
                if u % 2 == 0:
                    act.wait_ge(S(f"{tag}_gu"), 3 * it + (u // 2 + 1) + before(f"{tag}_gu"))
                else:
                    act.wait_ge(S("slots_used"), 6 * it + (f + u + 1))
                act.wait_ge(S(f"{tag}_free"), 6 * it + (u + 2) + before(f"{tag}_free"))
                act.activation(f_sg[:, u % 2, :], bank[2 * (u % 3)][:, :], ACT.Silu).then_inc(S(f"{tag}_sg"), 1)

            with act.Fori(0, ROUNDS) as it:
                for u in range(6):
                    unit(u, it)
            for u in range(NFF - 6 * ROUNDS):
                unit(u, ROUNDS)

        def dve_ffn(dve, tag):
            dve.drain().then_inc(S(f"{tag}_free"), 3)

            def unit(u, it):
                dve.wait_ge(S(f"{tag}_sg"), 6 * it + (u + 1) + before(f"{tag}_sg"))
                dve.tensor_tensor(hidT[:, bass.ds(6 * it + u, 1), :].rearrange("p f t -> p (f t)"),
                                  f_sg[:, u % 2, :], bank[2 * (u % 3) + 1][:, :], ALU.mult)\
                   .then_inc(S(f"{tag}_free"), 1)

            with dve.Fori(0, ROUNDS) as it:
                for u in range(6):
                    unit(u, it)
            for u in range(NFF - 6 * ROUNDS):
                unit(u, ROUNDS)

        def act_gain(act, name):
            act.dma_start(post, a[name][0:1, :].broadcast_to([P, D])).then_inc(S("post_loaded"), 16)

        def act_post(act, last):
            act.wait_ge(S("slots_used"), last)
            for t in range(NT):
                for half in range(2):
                    act.activation(f_sq, bank[2 * t + half][:, :], ACT.Square, accum_out=f_ss[:, t, half:half + 1])
                    act.drain()
            act.drain().then_inc(S("f_squares"), 1)
            nxt(act, "f_ss")
            act.activation(f_r[:, 1, :], f_r[:, 0, :], ACT.Sqrt, bias=eps, scale=1.0 / D).then_inc(S("f_root"), 1)

        def dve_post(dve, factor):
            nxt(dve, "f_squares")
            dve.tensor_tensor(f_r[:, 0, :], f_ss[:, :, 0], f_ss[:, :, 1], ALU.add).then_inc(S("f_ss"), 1)
            nxt(dve, "f_root")
            dve.reciprocal(f_r[:, 0, :], f_r[:, 1, :])
            dve.drain()
            if factor != 1.0:
                dve.tensor_scalar(f_r[:, 0, :], f_r[:, 0, :], factor, None, ALU.mult)
            nxt(dve, "post_loaded", 16)
            dve.drain()
            for t in range(NT):
                for half in range(2):
                    c = slice(512 * half, 512 * half + 512)
                    dve.scalar_tensor_tensor(f_tmp[:, t % 2, c], bank[2 * t + half][:, :], f_r[:, 0, t:t + 1],
                                             post[:, c], ALU.mult, ALU.mult)
                dve.drain()
                dve.tensor_tensor(X[:, t, :], X[:, t, :], f_tmp[:, t % 2, :], ALU.add)
                if t == NT - 1:
                    dve.drain()

        d_q, d_k, d_v = ([region(6144 * g + 2048 * i, 2048, "p (h t) -> p h t", t=512) for g in range(3)]
                         for i in range(3))
        REC = 4 * HD2 + 8
        comb = [region(18432 + 2080 * g, 2080, "p (t n) -> p t n", t=NT) for g in range(3)]
        tables = [region(24672, 1024, "p (h k) -> p h k", h=4), region(25696, 512, "p (h k) -> p h k", h=4),
                  region(26208, 512, "p (h k) -> p h k", h=4)]
        Pd = region(26720, 1024, "p (b n) -> p b n", b=2)
        PdT = region(27744, 1024, "p (b n) -> p b n", b=2)
        rec = region(28768, 2 * REC, "p (b n) -> p b n", b=2)
        d_nmx = region(29808, 64)
        phase16 = Pd[:, 0, 0:P]
        BIAS = ((2 * P, 0, 3 * P), (P, P, 2 * P), (P, P, 2 * P))
        brow_dram = [nc.dram_tensor(f"bias_rows{g}", (4, P, BIAS[g][2]), F32, kind="Internal").ap() for g in range(3)]
        rec_dram = nc.dram_tensor("attention_rows", (2, T, REC), F32, kind="Internal").ap()
        buckets = region(2048, 1536)
        btab = region(3584, 12)
        brow = region(4096, 1536, "p (g j) -> p g j", g=3)

        def sp_bias(sp):
            at, _ = WHERE["bucket0"]
            sp.dma_start(buckets[0:33, :], const_dram[0:33, at:at + 1536]).then_inc(S("buckets_loaded"), 16)
            sp.dma_start(btab[0:32, :], a["rel_bias_table_2"]).then_inc(S("buckets_loaded"), 16)

        def dve_bias(dve):
            dve.memset(btab[32:33, :], 1.0).then_inc(S("btab_ones"), 1)
            nxt(dve, "brow_ps")
            for g in range(3):
                dve.tensor_copy(brow[0:12, g, :], bank[2 + g][0:12, :])
            dve.drain().then_inc(S("brow_ready"), 1)

        def pe_bias(pe):
            nxt(pe, "buckets_loaded", 32)
            nxt(pe, "btab_ones")
            for g in range(3):
                mm = pe.matmul(bank[2 + g][0:12, :], btab[0:33, :], buckets[0:33, 512 * g:512 * g + 512],
                               start=True, stop=True)
            mm.then_inc(S("brow_ps"), 1)

        def sp_bias_store(sp):
            nxt(sp, "brow_ready")
            for g, (w, lo, n) in enumerate(BIAS):
                sp.dma_start(brow_dram[g], brow[4 * g:4 * g + 4, g, lo:lo + n].unsqueeze(1).broadcast_to([4, P, n]))\
                  .then_inc(S("brow_stored"), 16)

        def act_tables(act):
            nxt(act, "brow_stored", 48)
            for g, (w, lo, n) in enumerate(BIAS):
                src = bass.AP(brow_dram[g].tensor, P - 1, [[n - 1, P], [P * n, 4], [1, w]])
                act.dma_start(tables[g], src).then_inc(S("tables_loaded"), 16)
            at, n = WHERE["phase16"]
            act.dma_start(phase16, const_dram[:, at:at + n]).then_inc(S("tables_loaded"), 16)

        def dve_tables(dve):
            nxt(dve, "tables_loaded", 64)
            dve.tensor_tensor(tables[2], tables[2], phase16.unsqueeze(1).broadcast_to([P, 4, P]), ALU.add)
            dve.drain()

        def phased(x, dil):
            return x.rearrange("p (l d) -> p d l", d=dil)

        hT16 = region(18432, KD * T, "p (k t) -> p k t", t=T)

        def pool_proj2(pool):
            nxt(pool, "hT_even", 5)
            nxt(pool, "hT_odd", 5)
            for k in range(KD):
                pool.tensor_copy(hT16[:, k, :].rearrange("p (d l) -> p d l", d=DILATIONS[2]),
                                 phased(hT[:, k, :], DILATIONS[2]))
            pool.drain().then_inc(S("hT_phased"), 1)

        def pe_proj2(pe):
            pe_hT(pe)
            for g, dil in enumerate(DILATIONS):
                for name in ("q", "k"):
                    for i in range(2):
                        s = FIRST[f"{name}{g}"] + i
                        need(pe, s)
                        w = slot_view(s, 256)
                        for j in range(2):
                            if not (g == 0 and name == "q" and i == 0):
                                nxt(pe, f"d_taken{j}")
                            for k in range(KD):
                                mm = pe.matmul(bank[j][:, :], w[:, k, j * P:(j + 1) * P], hT[:, k, :],
                                               start=(k == 0), stop=(k == KD - 1))
                            if j == 0:
                                mm.then_inc(S("d_ps0"), 1)
                        mm.then_inc(S("slots_used"), 1)
                if g:
                    nxt(pe, "d_v_taken")
                if g == 2:
                    nxt(pe, "hT_phased")

                def places(k, i, dil=dil):
                    if dil == 1:
                        return tokens(k, i)
                    if dil == DILATIONS[1]:
                        return phased(hT[:, k, :], dil)[:, i, :]
                    return hT16[:, k, i * P:(i + 1) * P]

                pe_gemm_n(pe, FIRST[f"v{g}"], places, bank[2:6])

        def unphased(x, dil):
            return x.rearrange("p (d l) -> p l d", d=dil)

        def act_proj2(act):
            for g, dil in enumerate(DILATIONS):
                for dst in (d_q[g], d_k[g]):
                    for i in range(2):
                        nxt(act, "d_ps0")
                        act.activation(unphased(dst[:, 2 * i, :], dil),
                                       bank[0][:, :].rearrange("p (l d) -> p l d", d=dil), ACT.Copy)\
                           .then_inc(S("d_taken0"), 1)

        def dve_proj2(dve):
            for g, dil in enumerate(DILATIONS):
                for name, dst in (("q", d_q[g]), ("k", d_k[g])):
                    for i in range(2):
                        dve.wait_ge(S("slots_used"), FIRST[f"{name}{g}"] + i + 1)
                        dve.tensor_copy(unphased(dst[:, 2 * i + 1, :], dil),
                                        bank[1][:, :].rearrange("p (l d) -> p l d", d=dil))\
                           .then_inc(S("d_taken1"), 1)
                dve.wait_ge(S("slots_used"), FIRST[f"v{g}"] + 2)
                for t in range(NT):
                    i = dve.tensor_copy(d_v[g][:, t, :], bank[2 + t][:, :])
                i.then_inc(S("d_v_taken"), 1)

        DUNITS = [(0, n, hs, max(n - 1, 0), P if n == 0 else 2 * P) for n in range(NT) for hs in ((0, 1), (2, 3))]
        DUNITS += [(g, i, (0, 1, 2, 3), i, P) for g in (1, 2) for i in range(NT)]

        def record(u):
            g, i, hs, k0, w = DUNITS[u]
            return comb[0][:, i, :] if g == 0 else rec[:, u % 2, :]

        def pe_dil(pe):
            def scores(u):
                g, i, hs, k0, w = DUNITS[u]
                if u >= 2:
                    nxt(pe, "d_s_taken")
                for n, h in enumerate(hs):
                    mm = pe.matmul(bank[u % 2][:, n * w:(n + 1) * w], d_q[g][:, h, i * P:(i + 1) * P],
                                   d_k[g][:, h, k0 * P:k0 * P + w], start=True, stop=True)
                mm.then_inc(S("d_scores"), 1)

            def turn(u):
                g, i, hs, k0, w = DUNITS[u]
                nxt(pe, "d_p")
                for n in range(len(hs) * w // P):
                    mm = pe.transpose(bank[2 + u % 2][:, n * P:(n + 1) * P], Pd[:, u % 2, n * P:(n + 1) * P], ident)
                mm.then_inc(S("d_p_turned"), 1)

            def values(u):
                g, i, hs, k0, w = DUNITS[u]
                nxt(pe, "d_pT")
                if u >= 2:
                    nxt(pe, "d_o_taken")
                nb = w // P
                for n, h in enumerate(hs):
                    for b in range(nb):
                        c = (n * nb + b) * P
                        mm = pe.matmul(bank[4 + u % 2][:, n * HD2:(n + 1) * HD2], PdT[:, u % 2, c:c + P],
                                       d_v[g][:, k0 + b, h * HD2:(h + 1) * HD2], start=(b == 0), stop=(b == nb - 1))
                mm.then_inc(S("d_values"), 1)

            scores(0)
            for u in range(len(DUNITS)):
                if u + 1 < len(DUNITS):
                    scores(u + 1)
                turn(u)
                if u:
                    values(u - 1)
            values(len(DUNITS) - 1)

        def dve_dil(dve):
            def outputs(u):
                g, i, hs, k0, w = DUNITS[u]
                nxt(dve, "d_values")
                dve.tensor_copy(record(u)[:, hs[0] * HD2:(hs[-1] + 1) * HD2], bank[4 + u % 2][:, 0:len(hs) * HD2])
                dve.drain().then_inc(S("d_o_taken"), 1)

            for u, (g, i, hs, k0, w) in enumerate(DUNITS):
                nh = len(hs)
                nxt(dve, "d_scores")
                if u >= 2:
                    nxt(dve, "d_p_turned")
                p3 = Pd[:, u % 2, 0:nh * w].rearrange("p (h k) -> p h k", h=nh)
                tab = tables[g][:, hs[0]:hs[-1] + 1, :]
                tab = tab[:, :, 2 * P - w:2 * P] if g == 0 else tab
                dve.scalar_tensor_tensor(p3, bank[u % 2][:, 0:nh * w].rearrange("p (h k) -> p h k", h=nh),
                                         HD2 ** -0.5, tab, ALU.mult, ALU.add).then_inc(S("d_s_taken"), 1)
                dve.drain()
                if g and u >= 10:
                    n_st = 1 if DUNITS[u - 2][0] == 1 else 4
                    nxt(dve, f"rec_stored{u % 2}", 16 * n_st)
                mx = record(u)[:, 512 + hs[0]:512 + hs[-1] + 1]
                dve.tensor_reduce(mx, p3, AX_X, ALU.max)
                dve.drain()
                dve.tensor_scalar(d_nmx[:, 4 * u:4 * u + nh], mx, -1.0, None, ALU.mult).then_inc(S("d_max"), 1)
                if u:
                    outputs(u - 1)
            outputs(len(DUNITS) - 1)

        def act_dil(act):
            def exps(u):
                g, i, hs, k0, w = DUNITS[u]
                nxt(act, "d_max")
                for n, h in enumerate(hs):
                    p = Pd[:, u % 2, n * w:(n + 1) * w]
                    act.activation(p, p, ACT.Exp, bias=d_nmx[:, 4 * u + n:4 * u + n + 1],
                                   accum_out=record(u)[:, 516 + h:517 + h])
                act.drain().then_inc(S("d_p"), 1)

            def copy(u):
                g, i, hs, k0, w = DUNITS[u]
                n = len(hs) * w
                nxt(act, "d_p_turned")
                if u >= 2:
                    nxt(act, "d_values")
                act.activation(PdT[:, u % 2, 0:n], bank[2 + u % 2][:, 0:n], ACT.Copy)
                act.drain().then_inc(S("d_pT"), 1)

            exps(0)
            for u in range(len(DUNITS)):
                if u + 1 < len(DUNITS):
                    exps(u + 1)
                copy(u)

        def pool_dil(pool):
            for u, (g, i, hs, k0, w) in enumerate(DUNITS):
                if g == 0:
                    continue
                pool.wait_ge(S("d_o_taken"), u + 1 + before("d_o_taken"))
                pool.wait_ge(S("d_p"), u + 1 + before("d_p"))
                rows_ = rec_dram[g - 1].rearrange("(l d) c -> d l c", d=DILATIONS[g])
                if g == 1:
                    pool.dma_start(rows_[i], rec[:, u % 2, :]).then_inc(S(f"rec_stored{u % 2}"), 16)
                else:
                    for q in range(4):
                        pool.dma_start(rows_[4 * i + q], rec[32 * q:32 * q + 32, u % 2, :])\
                            .then_inc(S(f"rec_stored{u % 2}"), 16)
            for b in range(2):
                pool.wait_ge(S(f"rec_stored{b}"), 16 * (2 + 8) + before(f"rec_stored{b}"))
            for g in (1, 2):
                pool.dma_start(comb[g], rec_dram[g - 1].rearrange("(t p) c -> p t c", p=P))\
                    .then_inc(S("rec_loaded"), 16)

        c_m = region(4096, 16, "p (t h) -> p t h", t=NT)
        c_e = [region(4112 + 16 * g, 16, "p (t h) -> p t h", t=NT) for g in range(3)]
        c_x = [region(4160 + 16 * g, 16, "p (t h) -> p t h", t=NT) for g in range(3)]
        c_s = region(4208, 16, "p (t h) -> p t h", t=NT)
        attn = region(0, 2048, "p (t n) -> p t n", t=NT)
        attnT2 = region(2048, 2048, "p (k t) -> p k t", t=T)

        def dve_combine(dve):
            nxt(dve, "rec_loaded", 32)
            mx = [comb[g][:, :, 512:516] for g in range(3)]
            den = [comb[g][:, :, 516:520] for g in range(3)]
            dve.tensor_tensor(c_m, mx[0], mx[1], ALU.max)
            dve.drain()
            dve.tensor_tensor(c_m, c_m, mx[2], ALU.max)
            dve.drain()
            for g in range(3):
                dve.tensor_tensor(c_e[g], mx[g], c_m, ALU.subtract)
            dve.drain().then_inc(S("c_diff"), 1)
            nxt(dve, "c_exp")
            for g in range(3):
                dve.tensor_tensor(c_x[g], c_e[g], den[g], ALU.mult)
            dve.drain()
            dve.tensor_tensor(c_s, c_x[0], c_x[1], ALU.add)
            dve.drain()
            dve.tensor_tensor(c_s, c_s, c_x[2], ALU.add)
            dve.drain()
            dve.reciprocal(c_m, c_s)
            dve.drain()
            for g in range(3):
                dve.tensor_tensor(c_e[g], c_e[g], c_m, ALU.mult)
            dve.drain()
            for g in range(3):
                for t in range(NT):
                    o = comb[g][:, t, 0:512].rearrange("p (h e) -> p h e", h=4)
                    dve.tensor_tensor(o, o, c_e[g][:, t, :].unsqueeze(2).broadcast_to([P, 4, HD2]), ALU.mult)
            dve.drain()
            dve.tensor_tensor(attn, comb[0][:, :, 0:512], comb[1][:, :, 0:512], ALU.add)
            dve.drain()
            dve.tensor_tensor(attn, attn, comb[2][:, :, 0:512], ALU.add)
            dve.drain().then_inc(S("attn_ready"), 1)

        def act_combine(act):
            nxt(act, "c_diff")
            for g in range(3):
                act.activation(c_e[g], c_e[g], ACT.Exp)
            act.drain().then_inc(S("c_exp"), 1)
            nxt(act, "attn_turned")
            for k in range(4):
                act.activation(attnT2[:, k, :], bank[k][:, :], ACT.Copy)
            act.drain().then_inc(S("attnT_ready"), 1)

        def pe_combine(pe):
            nxt(pe, "attn_ready")
            for k in range(4):
                for t in range(NT):
                    mm = pe.transpose(bank[k][:, t * P:(t + 1) * P], attn[:, t, k * P:(k + 1) * P], ident)
            mm.then_inc(S("attn_turned"), 1)

        l_in = region(4096, 1040, "p (b t) -> p b t", b=2)
        l_xc, l_gx, l_t, l_q, l_r, l_gy = (region(5200 + 4100 * i, 4096, "p (m t) -> p m t", t=T) for i in range(6))
        l_c = region(29800, 8)
        l_e, l_z, l_p, l_s = (region(29808 + 8 * i, 8) for i in range(4))
        merged = l_q
        s_gate = l_xc[:, 0:4, :]
        s_val = l_xc[:, 4:8, :]

        def col2(name, i):
            at, _ = col(name, VEC2)
            return cols2[:, at + i:at + i + 1]

        def pe_lru(pe):
            for m in range(KD):
                i, j = m // 2, m % 2
                s = FIRST["xr"] + i
                if j == 0:
                    need(pe, s)
                if m >= 2:
                    nxt(pe, "l_in")
                for k in range(KD):
                    mm = pe.matmul(bank[j][:, :], slot_view(s, 256)[:, k, j * P:(j + 1) * P], hT[:, k, :],
                                   start=(k == 0), stop=(k == KD - 1))
                if j == 0:
                    mm.then_inc(S("l_ps"), 1)
                else:
                    mm.then_inc(S("slots_used"), 1)
            nxt(pe, "l_in", 2)
            need(pe, FIRST["lru"])
            need(pe, FIRST["lru"] + 1)
            for m in range(KD):
                h, j = m // 2, m % 2
                pe.wait_ge(S("l_conv"), 2 * h + 2 + before("l_conv"))
                if m >= 2:
                    nxt(pe, "l_gates")
                for which in range(2):
                    w = slot_view(FIRST["lru"] + which, 256)
                    for i in range(2):
                        mm = pe.matmul(bank[2 + 2 * j + which][:, :], w[:, 2 * h + i, j * P:(j + 1) * P],
                                       l_xc[:, 2 * h + i, :], start=(i == 0), stop=(i == 1))
                    if which == 0 and m == KD - 1:
                        mm.then_inc(S("slots_used"), 1)
                if m < KD - 1:
                    mm.then_inc(S("l_gate_ps"), 1)
                else:
                    mm.then_inc(S("slots_used"), 1)
            for m in range(KD):
                i, j = m // 2, m % 2
                s = FIRST["yr"] + i
                if j == 0:
                    need(pe, s)
                if m >= 2:
                    nxt(pe, "l_gelu")
                for k in range(KD):
                    mm = pe.matmul(bank[6 + j][:, :], slot_view(s, 256)[:, k, j * P:(j + 1) * P], hT[:, k, :],
                                   start=(k == 0), stop=(k == KD - 1))
                if j == 0:
                    mm.then_inc(S("l_y_ps"), 1)
                else:
                    mm.then_inc(S("slots_used"), 1)

        def act_lru(act):
            nxt(act, "l_abs")
            act.activation(l_e, l_z, ACT.Exp, scale=-1.0).then_inc(S("l_exp"), 1)
            for m in range(KD):
                j = m % 2
                if j == 0:
                    nxt(act, "l_ps")
                else:
                    act.wait_ge(S("slots_used"), FIRST["xr"] + m // 2 + 1)
                if m >= 2:
                    act.wait_ge(S("l_conv"), m - 1 + before("l_conv"))
                act.activation(l_in[:, j, 3:3 + T], bank[j][:, :], ACT.Copy).then_inc(S("l_in"), 1)
            nxt(act, "l_c")
            for m in range(KD):
                j = m % 2
                if m < KD - 1:
                    nxt(act, "l_gate_ps")
                else:
                    act.wait_ge(S("slots_used"), FIRST["lru"] + 2)
                act.activation(l_gx[:, m, :], bank[2 + 2 * j][:, :], ACT.Sigmoid, bias=col2("lru_b_x_2", m))
                act.activation(l_t[:, m, :], bank[3 + 2 * j][:, :], ACT.Sigmoid, bias=col2("lru_b_a_2", m))
                act.drain().then_inc(S("l_gates"), 1)
                act.activation(l_t[:, m, :], l_t[:, m, :], ACT.Tanh, scale=l_c[:, m:m + 1])
            act.drain().then_inc(S("l_tanh"), 1)
            nxt(act, "l_floor")
            for m in range(KD):
                act.activation(l_q[:, m, :], l_t[:, m, :], ACT.Sqrt).then_inc(S("l_sqrt"), 1)
            for m in range(KD):
                j = m % 2
                if j == 0:
                    nxt(act, "l_y_ps")
                else:
                    act.wait_ge(S("slots_used"), FIRST["yr"] + m // 2 + 1)
                act.activation(l_gy[:, m, :], bank[6 + j][:, :], ACT.Gelu_apprx_tanh).then_inc(S("l_gelu"), 1)

        def dve_lru(dve):
            at, _ = col("lru_a_param_2", VEC2)
            ap_ = cols2[:, at:at + 8]
            dve.memset(l_in[:, :, 0:3], 0.0)
            dve.scalar_tensor_tensor(l_z, ap_, -1.0, ap_, ALU.mult, ALU.max).then_inc(S("l_abs"), 1)
            nxt(dve, "l_exp")
            dve_log1p(dve, l_e, l_z, l_p, l_s)
            dve.tensor_scalar(l_z, ap_, -1.0, 0.0, ALU.mult, ALU.max)
            dve.drain()
            dve.tensor_tensor(l_s, l_z, l_s, ALU.add)
            dve.drain()
            dve.tensor_scalar(l_c, l_s, 4.0, None, ALU.mult)
            dve.drain().then_inc(S("l_c"), 1)
            for m in range(KD):
                j = m % 2
                dve.wait_ge(S("l_in"), m + 1 + before("l_in"))
                dve.tensor_scalar(l_xc[:, m, :], l_in[:, j, 3:3 + T], col2("conv_w_2", 24 + m),
                                  col2("conv_b_2", m), ALU.mult, ALU.add)
                for tap in range(3):
                    dve.drain()
                    dve.scalar_tensor_tensor(l_xc[:, m, :], l_in[:, j, tap:tap + T], col2("conv_w_2", 8 * tap + m),
                                             l_xc[:, m, :], ALU.mult, ALU.add)
                dve.drain().then_inc(S("l_conv"), 1)
            nxt(dve, "l_tanh")
            dve.tensor_scalar(l_t, l_t, 1.0e-30, None, ALU.max)
            dve.drain().then_inc(S("l_floor"), 1)
            dve.tensor_scalar(l_r, l_t, -1.0, -1.0, ALU.mult, ALU.add)
            dve.drain()
            for m in range(KD):
                dve.reciprocal(l_r[:, m, :], l_r[:, m, :])
                dve.tensor_tensor(l_gx[:, m, :], l_gx[:, m, :], l_xc[:, m, :], ALU.mult)
                dve.drain()
                nxt(dve, "l_sqrt")
                dve.scalar_tensor_tensor(l_t[:, m, :], l_t[:, m, :], -1.0, l_r[:, m, :], ALU.add, ALU.mult)
                dve.scalar_tensor_tensor(l_q[:, m, :], l_r[:, m, :], -2.0, l_q[:, m, :], ALU.mult, ALU.mult)
                dve.drain()
                dve.tensor_tensor(l_q[:, m, :], l_q[:, m, :], l_gx[:, m, :], ALU.mult)
                dve.drain()
                dve.tensor_tensor_scan(l_r[:, m, :], l_t[:, m, :], l_q[:, m, :], 0.0, ALU.mult, ALU.add)
                dve.drain()
            for m in range(KD):
                nxt(dve, "l_gelu")
                dve.tensor_tensor(l_r[:, m, :], l_r[:, m, :], l_gy[:, m, :], ALU.mult)
            dve.drain().then_inc(S("rec_ready"), 1)

        def pe_merge(pe):
            nxt(pe, "attnT_ready")
            nxt(pe, "rec_ready")
            for m in range(KD):
                q, j = m // 2, m % 2
                base = 4 * j
                if m >= 2:
                    nxt(pe, "m_merged")
                parts = [(FIRST[f"gl{q}"], hT, KD), (FIRST[f"gl{q}"] + 1, hT, KD), (FIRST[f"attn{q}"], attnT2, 4),
                         (FIRST[f"rec{q}"], l_r, KD)]
                for b, (s, rhs, nk) in enumerate(parts):
                    if j == 0:
                        need(pe, s)
                    w = ring[:, s % RING, 0:nk * 256].rearrange("p (k n) -> p k n", n=256)
                    for k in range(nk):
                        mm = pe.matmul(bank[base + b][:, :], w[:, k, j * P:(j + 1) * P], rhs[:, k, :],
                                       start=(k == 0), stop=(k == nk - 1))
                    if j == 1:
                        mm.then_inc(S("slots_used"), 1)
                    elif b in (1, 3):
                        mm.then_inc(S("m_even_ps"), 1)

        def act_merge(act):
            for m in range(KD):
                q, j = m // 2, m % 2
                if j == 0:
                    act.wait_ge(S("m_even_ps"), m + 1 + before("m_even_ps"))
                else:
                    act.wait_ge(S("slots_used"), FIRST[f"gl{q}"] + 2)
                if m >= 2:
                    act.wait_ge(S("m_merged"), m - 1 + before("m_merged"))
                for b in range(2):
                    act.activation(s_gate[:, 2 * j + b, :], bank[4 * j + b][:, :], ACT.Sigmoid)
                act.drain().then_inc(S("m_sigmoids"), 1)

        def dve_merge(dve):
            for m in range(KD):
                q, j = m // 2, m % 2
                nxt(dve, "m_sigmoids")
                if j == 0:
                    dve.wait_ge(S("m_even_ps"), m + 2 + before("m_even_ps"))
                else:
                    dve.wait_ge(S("slots_used"), FIRST[f"rec{q}"] + 1)
                for b in range(2):
                    dve.tensor_tensor(s_val[:, 2 * j + b, :], s_gate[:, 2 * j + b, :], bank[4 * j + 2 + b][:, :],
                                      ALU.mult)
                dve.drain()
                dve.tensor_tensor(merged[:, m, :], s_val[:, 2 * j, :], s_val[:, 2 * j + 1, :], ALU.add)
                dve.drain().then_inc(S("m_merged"), 1)

        def sp_out(sp):
            nxt(sp, "x_final")
            for t in range(NT):
                sp.dma_start(out[t * P:(t + 1) * P, :], X[:, t, :]).then_inc(S("out_stored"), 16)
            sp.wait_ge(S("out_stored"), 16 * NT)

        block = ctx.enter_context(nc.Block())

        def c1(i):
            return mod[:, i:i + 8]

        def gain2(name):
            at, n = col(name, VEC2)
            return cols2[:, at:at + n]

        @block.sync
        def _(sp):
            sp_small(sp)
            sp_bias(sp)
            load(sp, 0, 8)
            sp_bias_store(sp)
            load(sp, 8, FIRST["ada2"] - 8)
            sp_positions(sp)
            load(sp, FIRST["ada2"], MOE_AT - FIRST["ada2"])
            sp_moe_first(sp)
            sp_h2(sp)
            sp_moe(sp)
            sp_more(sp)
            sp.wait_ge(S("gu_used"), N_EXP)
            sp.wait_ge(S("dn_used"), N_EXP)
            sp_ffn(sp, "ffn1")
            load(sp, FIRST["q0"], FIRST["ffn2"] - FIRST["q0"])
            sp_ffn(sp, "ffn2")
            sp_out(sp)

        @block.scalar
        def _(act):
            act_small(act)
            act_c(act)
            nxt(act, "x_loaded", 16 * NT)
            nxt(act, "mod_ready")
            act_norm(act, junk1, c1(8), c1(0))
            act_proj1(act)
            act_qkv(act)
            meet(act)
            act_swa_prep(act)
            act_swa_turn(act)
            act_swa(act)
            meet(act)
            act_gdn_prep(act)
            for t in range(NT):
                act_gdn(act, t)
            act_gdn_end(act)
            act_turned(act)
            meet(act)
            act_router_weights(act)
            nxt(act, "mod_ready")
            act_norm(act, junk2, c1(32), c1(24))
            act_h2(act)
            act_route(act)
            act_moe(act)
            act_more(act)
            act_moe_end(act)
            meet(act)
            act_gain(act, "ffn1_norm_post_2")
            act_norm(act, junk3, gain2("ffn1_norm_pre_2"), None)
            act_ffn(act, "ffn1")
            act_post(act, FIRST["ffn1_down"] + NPAIRS)
            meet(act)
            act_tables(act)
            act_norm(act, region(0, D), gain2("mix_norm_pre_2"), None)
            act_proj2(act)
            meet(act)
            act_dil(act)
            meet(act)
            act_combine(act)
            meet(act)
            act_lru(act)
            act_merge(act)
            meet(act)
            act_gain(act, "mix_norm_post_2")
            act_post(act, FIRST["w_out2"] + 4)
            meet(act)
            act_gain(act, "ffn2_norm_post_2")
            act_norm(act, junk3, gain2("ffn2_norm_pre_2"), None)
            act_ffn(act, "ffn2")
            act_post(act, FIRST["ffn2_down"] + NPAIRS)

        @block.tensor
        def _(pe):
            pe_small(pe)
            pe_bias(pe)
            pe_ada(pe, "ada1", 0, 16, 7)
            pe_turn(pe, xn1, ("xn_ready",))
            pe_hT(pe)
            pe_proj1(pe)
            pe_qkv(pe)
            pe_ada(pe, "ada2", 16, 48, 7)
            meet(pe)
            pe_swa_turn(pe)
            pe_swa(pe)
            meet(pe)
            pe_gdn_prep(pe)
            for t in range(NT):
                pe_gdn(pe, t)
            pe_gate(pe, diag1, 0)
            nxt(pe, "gate_taken")
            pe_turn(pe, mixed, ("mixed_ready",))
            pe_hT(pe)
            pe_down(pe, "w_out", 4, tokens)
            meet(pe)
            pe_turn(pe, xn2, ("xn_ready",))
            pe_route(pe)
            pe_moe(pe)
            pe_more(pe)
            pe_gate(pe, diag2, 0)
            meet(pe)
            pe_turn(pe, xn3, ("xn_ready",))
            pe_hT(pe)
            pe_ffn(pe, "ffn1")
            meet(pe)
            pe_turn(pe, xn3, ("xn_ready",))
            pe_proj2(pe)
            meet(pe)
            pe_dil(pe)
            meet(pe)
            pe_combine(pe)
            meet(pe)
            pe_lru(pe)
            pe_merge(pe)
            nxt(pe, "m_merged", 2)
            meet(pe)
            pe_down(pe, "w_out2", 4, lambda k, t: merged[:, k, t * P:(t + 1) * P])
            meet(pe)
            pe_turn(pe, xn3, ("xn_ready",))
            pe_hT(pe)
            pe_ffn(pe, "ffn2")

        @block.vector
        def _(dve):
            dve_small(dve)
            dve_bias(dve)
            nxt(dve, "x_loaded", 16 * NT)
            dve_ada(dve, 0, 16, 7)
            dve_norm(dve, xn1, c1(8), c1(0))
            dve_proj1(dve)
            meet(dve)
            dve_ada(dve, 16, 48, 7)
            dve_swa_prep(dve)
            dve_swa_turn(dve)
            dve_swa(dve)
            meet(dve)
            dve_gdn_prep(dve)
            for t in range(NT):
                dve_gdn(dve, t)
            dve_gate(dve, diag1, 16)
            dve_gate_row(dve, gate1, 0)
            dve_gdn_end(dve)
            dve_turned(dve)
            dve_out1(dve)
            meet(dve)
            dve_norm(dve, xn2, c1(32), c1(24))
            dve_route(dve)
            dve_moe(dve)
            dve_more(dve)
            dve_gate(dve, diag2, 40)
            dve_gate_row(dve, gate2, 0)
            dve_moe_end(dve)
            meet(dve)
            dve_norm(dve, xn3, gain2("ffn1_norm_pre_2"), None)
            dve_ffn(dve, "ffn1")
            dve_post(dve, 0.5)
            meet(dve)
            dve_norm(dve, xn3, gain2("mix_norm_pre_2"), None)
            dve_proj2(dve)
            dve_tables(dve)
            meet(dve)
            dve_dil(dve)
            meet(dve)
            dve_combine(dve)
            meet(dve)
            dve_lru(dve)
            dve_merge(dve)
            meet(dve)
            dve_post(dve, 1.0)
            meet(dve)
            dve_norm(dve, xn3, gain2("ffn2_norm_pre_2"), None)
            dve_ffn(dve, "ffn2")
            dve_post(dve, 0.5)
            dve.drain().then_inc(S("x_final"), 1)

        @block.gpsimd
        def _(pool):
            meet(pool)
            meet(pool)
            for t in range(NT):
                pool_gdn(pool, t)
            meet(pool)
            pool_moe(pool)
            pool_more(pool)
            meet(pool)
            meet(pool)
            pool_proj2(pool)
            meet(pool)
            pool_dil(pool)
            meet(pool)
            meet(pool)
            meet(pool)
            meet(pool)


def kernel(**inputs):
    import concourse.bacc as bacc
    from concourse.bass_utils import run_bass_kernel_spmd

    nc = bacc.Bacc("TRN2", target_bir_lowering=False, num_devices=1)
    arrays, args = {}, {}
    for name in NAMES:
        v = np.ascontiguousarray(inputs[name])
        arrays[f"in_{name}"] = v
        args[name] = nc.dram_tensor(f"in_{name}", v.shape, mybir.dt.from_np(v.dtype), kind="ExternalInput").ap()
    arrays["constants_dram"] = POSITION_CONSTANTS
    const_dram = nc.dram_tensor("constants_dram", POSITION_CONSTANTS.shape, F32, kind="ExternalInput").ap()
    out = nc.dram_tensor("out", (T, D), F32, kind="ExternalOutput").ap()
    build(nc, args, const_dram, out)
    r = run_bass_kernel_spmd(nc, [arrays], core_ids=[0])
    return r.results[0]["out"].reshape(1, T, D)
```

```python
from contextlib import ExitStack

import numpy as np

import concourse.bass as bass
from concourse import mybir

F32 = mybir.dt.float32
F32R = mybir.dt.float32r
I32 = mybir.dt.int32
U32 = mybir.dt.uint32
BF16 = mybir.dt.bfloat16
ALU = mybir.AluOpType
ACT = mybir.ActivationFunctionType
AX_X = mybir.AxisListType.X

P = 128
T = 512
D = 1024
NT = T // P
KD = D // P
HD = 64
H = 8
NPAIR = H // 2
CHUNK = 64
WINW = 2832
QKV = 1536
N_EXP, N_GRP, EPG, F_EXP = 32, 4, 8, 256
CAP = P
FF = 2816
NFF = FF // P
WIN2 = 8704
HD2 = 128
EPS = 1e-6
BIG = 1.0e30
RING = 6
SLOT = 2048
DILATIONS = (1, 4, 16)


def bucket_of(distance):
    nf = np.maximum(distance, 1).astype(np.float32)
    large = 16 + (np.log(nf / np.float32(16)).astype(np.float32) / np.float32(np.log(2048 / 16))
                  * np.float32(16)).astype(np.int32)
    return np.where(distance < 16, distance, np.minimum(large, 31))


def constants():
    p = np.arange(P)[:, None]
    c = np.arange(P)[None, :]
    same = (p // CHUNK) == (c // CHUNK)
    parts = {
        "ident": (p == c),
        "ones": np.ones((P, P)),
        "cumsum": (p <= c) & same,
        "chunk_all": same,
        "chunk0": np.broadcast_to(p < CHUNK, (P, P)),
        "chunk1": np.broadcast_to(p >= CHUNK, (P, P)),
    }
    for b in (1, 2, 4, 8, 16, 32):
        parts[f"level{b}"] = ((c // b) % 2 == 1) & ((p // b) == (c // b) - 1)
    k = np.arange(2 * P)[None, :]
    rel = p + P - k
    parts["window"] = np.where((rel >= 0) & (rel < P), 0.0, -BIG)
    parts["iota"] = np.broadcast_to(c, (P, P))
    parts["before"] = (p < c)
    half = HD // 2
    parts["inv_freq"] = np.broadcast_to(
        np.power(np.float32(10000.0), -np.arange(half, dtype=np.float32) / np.float32(half)), (P, half))
    parts["tie4"] = np.broadcast_to(N_GRP - np.arange(N_GRP), (P, N_GRP))
    parts["tie8"] = np.broadcast_to(EPG - np.arange(EPG), (P, EPG))
    parts["partition"] = p
    parts["eps"] = np.full((P, 1), EPS)
    parts["zero"] = np.zeros((P, 1))
    for g, dil in enumerate(DILATIONS):
        steps = 2 * P - 1 - np.arange(4 * P)
        onehot = np.zeros((P, 4 * P))
        ok = (steps >= 0) & (steps <= P)
        b = bucket_of(np.maximum(steps, 0) * dil)
        onehot[b[ok], np.nonzero(ok)[0]] = 1.0
        onehot[32] = np.where(ok, 0.0, -BIG)
        parts[f"bucket{g}"] = onehot
    q = T // DILATIONS[2]
    parts["phase16"] = np.where((p // q) == (c // q), 0.0, -BIG)
    at, where = 0, {}
    for name, a in parts.items():
        a = np.asarray(a, np.float32)
        where[name] = (at, a.shape[1])
        at += a.shape[1]
    return np.ascontiguousarray(np.concatenate([np.asarray(a, np.float32) for a in parts.values()], 1)), where


NAMES = [
    "x", "c", "positions", "w_ada", "b_ada", "norm_mix", "w_in", "conv_w", "a_log", "dt_bias", "gdn_out_norm",
    "q_norm", "k_norm", "sinks", "w_out", "norm_ffn", "w_group", "b_group", "w_router", "b_router", "w_gate",
    "w_up", "w_down", "ffn1_norm_pre_2", "ffn1_norm_post_2", "ffn1_w_gate_2", "ffn1_w_up_2", "ffn1_w_down_2",
    "mix_norm_pre_2", "mix_norm_post_2", "w_in_2", "rel_bias_table_2", "conv_w_2", "conv_b_2", "lru_w_x_2",
    "lru_b_x_2", "lru_w_a_2", "lru_b_a_2", "lru_a_param_2", "w_attn_branch_2", "w_rec_branch_2", "w_out_2",
    "ffn2_norm_pre_2", "ffn2_norm_post_2", "ffn2_w_gate_2", "ffn2_w_up_2", "ffn2_w_down_2",
]
POSITION_CONSTANTS, WHERE = constants()


def build(nc, a, const_dram, out):
    ctx = ExitStack()
    with ctx:
        memory = ctx.enter_context(ExitStack())

        def sb(name, shape, dt=F32):
            tensors.append((name, shape))
            return memory.enter_context(nc.sbuf_tensor(name, shape, dt))

        tensors = []

        sems = {}

        c, v = NT, 2 * NT
        SUCCESSOR = {
            "d_scores": ("w_scores", 16), "d_s_taken": ("w_s_taken", 16), "d_max": ("w_max", 16),
            "d_p": ("w_p", 16), "d_p_turned": ("w_p_turned", 16), "d_pT": ("w_pT_ready", 16),
            "d_values": ("w_values", 16), "d_o_taken": ("w_o_taken", NT), "d_ps0": ("g_turned", 4 * c),
            "d_taken0": ("g_T_even", v), "d_taken1": ("g_T_odd", v), "d_v_taken": ("g_T1", v),
            "x_final": ("mixed_ready", 1), "hT_phased": ("z_taken", 1),
            "l_abs": ("g_abs", 1), "l_exp": ("g_exp", 1), "l_c": ("g_ss", 1), "l_in": ("g_X", 10 * c),
            "l_conv": ("g_Xs", 10 * c), "l_ps": ("g_w", c), "l_gate_ps": ("g_nw", c), "l_gates": ("g_v", v),
            "l_tanh": ("g_vnew", v), "l_floor": ("g_out", v), "l_sqrt": ("g_o_taken", c), "l_y_ps": ("g_osq", 1),
            "l_gelu": ("g_oss", 1), "ffn1_free": ("g_Ml", 10 * c), "ffn1_gu": ("g_T", 12 * c),
            "ffn1_sg": ("g_Y", 10 * c), "ffn2_free": ("g_state", v), "ffn2_gu": ("g_kk", c), "ffn2_sg": ("g_kq", c),
            "f_squares": ("w_ss", 1), "f_ss": ("w_roots", 1), "f_root": ("angles", 1), "post_loaded": ("rotation", 1),
            "c_diff": ("g_U", c), "c_exp": ("g_Grow", c), "attn_ready": ("g_oroot", 1), "attn_turned": ("w_turned", 1),
            "attnT_ready": ("w_kT", 1), "rec_ready": ("w_qk", 1), "m_even_ps": ("w_qT", 1),
            "m_sigmoids": ("g_roots", 1), "m_merged": ("g_G", 1),
        }

        def before(name):
            return SUCCESSOR[name][1] if name in SUCCESSOR else 0

        def S(name):
            if name in SUCCESSOR:
                return S(SUCCESSOR[name][0])
            if name not in sems:
                sems[name] = ctx.enter_context(nc.semaphore(name))
            return sems[name]

        tally = {}

        def nxt(e, name, by=1):
            key = (str(e.engine), name)
            tally[key] = tally.get(key, before(name)) + by
            e.wait_ge(S(name), tally[key])

        def meet(e):
            e.drain().then_inc(S("meet"), 1)
            nxt(e, "meet", 4)

        n_const = POSITION_CONSTANTS.shape[1]
        n_keep = WHERE["bucket0"][0]
        K = sb("constants", [P, n_keep])

        def con(name):
            at, n = WHERE[name]
            return K[:, at:at + n]

        ident, ones, eps = con("ident"), con("ones"), con("eps")
        ring = sb("ring", [P, RING, SLOT])
        X = sb("residual", [P, NT, D])
        hT = sb("hT", [P, KD, T])
        cols1 = sb("cols1", [P, 120])
        cols2 = sb("cols2", [P, 88])
        mod = sb("mod", [P, 48])
        cact = sb("cact", [P, KD])
        rows = sb("rows", [P, 256])
        ss = sb("ss", [P, NT])
        rstd = sb("rstd", [P, NT])
        ARENA = 29900
        A = sb("arena", [P, ARENA])
        memory.close()
        HID = NFF * T
        split = {}
        for name, shape in tensors[:-1] + [("hid_high", [P, HID]), ("hid_low", [P, HID]), ("between", [P, 1024]),
                                           ("hT_high", [P, KD * T])]:
            split[name] = ctx.enter_context(nc.sbuf_tensor(name + "_split", shape, F32R))
        bank = [ctx.enter_context(nc.psum_tensor(f"bank{i}", [P, 512], F32)) for i in range(8)]

        def region(at, width, pattern=None, base=None, **kw):
            r = (A if base is None else base)[:, at:at + width]
            return r.rearrange(pattern, **kw) if pattern else r

        hflat = hT[:, :, :].rearrange("p k t -> p (k t)")

        ROWS = {}
        at = 0
        for name, n in (("a_log", H), ("dt_bias", H), ("gdn_out_norm", HD), ("q_norm", HD), ("k_norm", HD),
                        ("sinks", H), ("b_group", N_GRP), ("b_router", N_EXP)):
            ROWS[name] = (at, n)
            at += n

        def row(name):
            at, n = ROWS[name]
            return rows[:, at:at + n]

        SLOTS = []
        FIRST = {}

        def plan(name, sources):
            FIRST[name] = len(SLOTS)
            SLOTS.extend(sources)

        def t_slots(w, c0, c1):
            return [w[:, n:n + 256].rearrange("(k p) n -> p k n", p=P) for n in range(c0, c1, 256)]

        def n_slots(w, c0, c1):
            return [w[r:r + 512, n:n + 512].rearrange("(k p) n -> p k n", p=P)
                    for n in range(c0, c1, 512) for r in (0, 512)]

        def d_slots(w, r1):
            return [w[r:r + 256, :].rearrange("(k p) n -> p k n", p=P) for r in range(0, r1, 256)]

        w_ada, w_in, w_in2 = a["w_ada"][0], a["w_in"][0], a["w_in_2"][0]
        plan("ada1", t_slots(w_ada, 0, 2 * D))
        plan("qkv", t_slots(w_in, 0, QKV))
        plan("z", n_slots(w_in, QKV, QKV + 512))
        plan("sq", n_slots(w_in, 2064, 2064 + 512))
        plan("skv", t_slots(w_in, 2576, 2832))
        plan("ada2", t_slots(w_ada, 2 * D, 6 * D))
        plan("w_out", d_slots(a["w_out"][0], D))
        MOE_AT = len(SLOTS)

        def ffn_slots(tag):
            g, u = (t_slots(a[f"{tag}_w_{n}_2"][0], 0, FF) for n in ("gate", "up"))
            plan(tag, [s for pair in zip(g, u) for s in pair])
            plan(tag + "_down", d_slots(a[f"{tag}_w_down_2"][0], FF))

        ffn_slots("ffn1")
        for g in range(3):
            plan(f"q{g}", t_slots(w_in2, 512 * g, 512 * g + 512))
            plan(f"k{g}", t_slots(w_in2, 1536 + 512 * g, 1536 + 512 * g + 512))
            plan(f"v{g}", n_slots(w_in2, 3072 + 512 * g, 3072 + 512 * g + 512))
        plan("xr", t_slots(w_in2, 4608, 5632))
        plan("lru", [a[n][0].rearrange("h (i p) j -> p (h i) j", p=P) for n in ("lru_w_x_2", "lru_w_a_2")])
        plan("yr", t_slots(w_in2, 5632, 6656))
        for m in range(4):
            plan(f"gl{m}", t_slots(w_in2, 6656 + 256 * m, 6656 + 256 * m + 256)
                 + t_slots(w_in2, 7680 + 256 * m, 7680 + 256 * m + 256))
            plan(f"attn{m}", [a["w_attn_branch_2"][0][:, 256 * m:256 * m + 256].rearrange("(k p) n -> p k n", p=P)])
            plan(f"rec{m}", t_slots(a["w_rec_branch_2"][0], 256 * m, 256 * m + 256))
        plan("w_out2", d_slots(a["w_out_2"][0], D))
        ffn_slots("ffn2")

        loaded = [S(f"slot{i}_loaded") for i in range(RING)]

        def turn_of(i):
            return i - sum(3 * (NFF // 2) for tag in ("ffn1", "ffn2") if i >= FIRST[tag] + 3 * (NFF // 2))

        def slot_view(i, n):
            return ring[:, turn_of(i) % RING, :].rearrange("p (k n) -> p k n", n=n)

        def load(sp, first, count):
            for i in range(first, first + count):
                start = FIRST["q0"] if i >= FIRST["q0"] else 0
                if i - RING >= start:
                    sp.wait_ge(S("slots_used"), i - RING + 1)
                elif start:
                    sp.wait_ge(S("slots_used"), start)
                src = SLOTS[i]
                n = src.shape[-1]
                view = ring[:, turn_of(i) % RING, 0:src.shape[1] * n].rearrange("p (k n) -> p k n", n=n)
                sp.dma_start(view, src).then_inc(loaded[turn_of(i) % RING], 16)

        def need(pe, i):
            pe.wait_ge(loaded[turn_of(i) % RING], 16 * (turn_of(i) // RING + 1))

        vec1 = region(0, P)
        vec2 = region(P, P)
        VEC1 = [("b_ada", 48), ("norm_mix", 8), ("norm_ffn", 8), ("c", 8), ("conv_w", 48)]
        VEC2 = [("ffn1_norm_pre_2", 8), ("mix_norm_pre_2", 8), ("ffn2_norm_pre_2", 8), ("conv_w_2", 32),
                ("conv_b_2", 8), ("lru_b_x_2", 8), ("lru_b_a_2", 8), ("lru_a_param_2", 8)]
        wab = region(28752, KD * 16, "p (k n) -> p k n", n=16)

        def chunked(v, n):
            dims = " ".join("abcd"[:len(v.shape)])
            flat = v.rearrange(f"{dims} -> ({dims})")
            return flat.rearrange("(r p) -> r p", p=P)

        def col(c, table):
            at = 0
            for name, n in table:
                if name == c:
                    return at, n
                at += n

        def sp_small(sp):
            sp.dma_start(K[:, :], const_dram[:, 0:n_keep]).then_inc(S("const_loaded"), 16)
            for vec, table in ((vec1, VEC1), (vec2, VEC2)):
                at = 0
                for name, n in table:
                    sp.dma_start(vec[at:at + n, :], chunked(a[name], n)).then_inc(S("vectors_loaded"), 16)
                    at += n
            for t in range(NT):
                sp.dma_start(X[:, t, :], a["x"][0, t * P:(t + 1) * P, :]).then_inc(S("x_loaded"), 16)

        def act_small(act):
            for name, (at, n) in ROWS.items():
                src = a[name][0:1, :].broadcast_to([P, n])
                act.dma_start(rows[:, at:at + n], src).then_inc(S("rows_loaded"), 16)
            act.dma_start(wab, w_in[:, 2048:2064].rearrange("(k p) n -> p k n", p=P)).then_inc(S("wab_loaded"), 16)

        def pe_small(pe):
            nxt(pe, "const_loaded", 16)
            nxt(pe, "vectors_loaded", 16 * (len(VEC1) + len(VEC2)))
            pe.transpose(bank[0][:, 0:120], vec1[0:120, :], ident[0:120, 0:120])
            pe.transpose(bank[1][:, 0:88], vec2[0:88, :], ident[0:88, 0:88]).then_inc(S("vectors_turned"), 1)

        def dve_small(dve):
            nxt(dve, "vectors_turned")
            dve.tensor_copy(cols1[:, :], bank[0][:, 0:120])
            dve.tensor_copy(cols2[:, :], bank[1][:, 0:88]).then_inc(S("columns_ready"), 1)

        def act_c(act):
            nxt(act, "columns_ready")
            at, n = col("c", VEC1)
            act.activation(cact[:, :], cols1[:, at:at + n], ACT.Silu).then_inc(S("cact_ready"), 1)

        def pe_ada(pe, name, m0, m1, b):
            if m0 == 0:
                nxt(pe, "cact_ready")
            for i in range(m0 // 2, m1 // 2):
                s = FIRST[name] + i - m0 // 2
                need(pe, s)
                w = slot_view(s, 256)
                for j in range(2):
                    m = 2 * i + j
                    for k in range(KD):
                        mm = pe.matmul(bank[b][:, m:m + 1], w[:, k, j * P:(j + 1) * P], cact[:, k:k + 1],
                                       start=(k == 0), stop=(k == KD - 1))
                mm.then_inc(S("slots_used"), 1)

        def dve_ada(dve, m0, m1, b):
            last = FIRST["ada1"] + 8 if m0 == 0 else FIRST["ada2"] + 16
            dve.wait_ge(S("slots_used"), last)
            dve.tensor_tensor(mod[:, m0:m1], bank[b][:, m0:m1], cols1[:, m0:m1], ALU.add)
            dve.drain()
            s0, gain = (8, "norm_mix") if m0 == 0 else (32, "norm_ffn")
            at, n = col(gain, VEC1)
            dve.scalar_tensor_tensor(mod[:, s0:s0 + 8], mod[:, s0:s0 + 8], 1.0, cols1[:, at:at + n],
                                     ALU.add, ALU.mult)
            dve.drain().then_inc(S("mod_ready"), 1)

        def act_norm(act, junk, scale, shift, high=None):
            for t in range(NT):
                act.activation(junk, X[:, t, :], ACT.Square, accum_out=ss[:, t:t + 1])
                act.drain()
            act.activation(rstd[:, :], ss[:, :], ACT.Sqrt, bias=eps, scale=1.0 / D).then_inc(S("rms_ready"), 1)
            for k in range(0, KD, 2):
                nxt(act, "x_turned", 2 if k else 1)
                if shift is None:
                    i = act.activation(hT[:, k, :], bank[k][:, :], ACT.Copy, scale=scale[:, k:k + 1])
                else:
                    i = act.activation(hT[:, k, :], bank[k][:, :], ACT.Identity, bias=shift[:, k:k + 1],
                                       scale=scale[:, k:k + 1])
                if high is not None:
                    act.drain()
                    i = act.activation(high[:, k, :], hT[:, k, :], ACT.Copy)
            tally[(str(act.engine), "x_turned")] += 1
            i.then_inc(S("hT_even"), 1)

        def dve_norm(dve, xn, scale, shift, high=None, high_number=0):
            nxt(dve, "rms_ready")
            dve.reciprocal(ss[:, :], rstd[:, :])
            dve.drain()
            for t in range(NT):
                i = dve.tensor_scalar(xn[:, t, :], X[:, t, :], ss[:, t:t + 1], None, ALU.mult)
            i.then_inc(S("xn_ready"), 1)
            for k in range(1, KD, 2):
                nxt(dve, "x_turned", 2)
                if shift is None:
                    i = dve.tensor_scalar(hT[:, k, :], bank[k][:, :], scale[:, k:k + 1], None, ALU.mult)
                else:
                    i = dve.tensor_scalar(hT[:, k, :], bank[k][:, :], scale[:, k:k + 1], shift[:, k:k + 1],
                                          ALU.mult, ALU.add)
                if high is not None:
                    dve.drain()
                    i = dve_split(dve, high[:, k, :], hT[:, k, :], hT_lo[:, k, :])
            if high is not None:
                dve.wait_ge(S("hT_even"), high_number)
                for k in range(0, KD, 2):
                    i = dve.tensor_tensor(hT_lo[:, k, :], hT[:, k, :], high[:, k, :].bitcast(F32), ALU.subtract)
            i.then_inc(S("hT_odd"), 1)

        def pe_turn(pe, src, ready):
            nxt(pe, *ready)
            for k in range(KD):
                for t in range(NT):
                    mm = pe.transpose(bank[k][:, t * P:(t + 1) * P], src[:, t, k * P:(k + 1) * P], ident)
                mm.then_inc(S("x_turned"), 1)

        def pe_hT(pe):
            nxt(pe, "hT_even")
            nxt(pe, "hT_odd")

        convT = region(0, QKV // P * T, "p (m t) -> p m t", t=T)
        qkv = region(6144, NT * QKV, "p (t n) -> p t n", n=QKV)
        kbG = region(12288, 2048, "p (t n) -> p t n", n=512)
        z = region(14336, 2048, "p (t n) -> p t n", n=512)
        mixed = region(16384, 4096, "p (t n) -> p t n", n=D)
        ab = region(20480, 64, "p (t n) -> p t n", n=16)
        sq = region(20544, 2048, "p (t n) -> p t n", n=512)
        skv = region(22592, 1024, "p (t n) -> p t n", n=256)
        convin = region(23616, 1040, "p (b t) -> p b t", b=2)
        xn1 = region(24656, 4096, "p (t n) -> p t n", n=D)
        junk1 = region(1024, D)
        convacc = region(24656, 1024, "p (b t) -> p b t", b=2)
        NM = QKV // P

        def pe_gemm_t(pe, s, nk, rhs, banks, ready, free=None):
            need(pe, s)
            n = SLOTS[s].shape[-1]
            w = ring[:, turn_of(s) % RING, 0:nk * n].rearrange("p (k n) -> p k n", n=n)
            for j in range(n // P):
                if free is not None:
                    free(j)
                for k in range(nk):
                    mm = pe.matmul(banks[j][:, :], w[:, k, j * P:(j + 1) * P], rhs[:, k, :],
                                   start=(k == 0), stop=(k == nk - 1))
                if j < n // P - 1:
                    mm.then_inc(S(ready), 1)
            return mm

        def pe_gemm_n(pe, s, lhs, banks):
            for half in range(2):
                need(pe, s + half)
                w = slot_view(s + half, 512)
                for t in range(NT):
                    for k in range(4):
                        mm = pe.matmul(banks[t][:, :], lhs(4 * half + k, t), w[:, k, :],
                                       start=(half == 0 and k == 0), stop=(half == 1 and k == 3))
                mm.then_inc(S("slots_used"), 1)

        def tokens(k, t):
            return hT[:, k, t * P:(t + 1) * P]

        def pe_proj1(pe):
            for i in range(NM // 2):
                s = FIRST["qkv"] + i
                need(pe, s)
                w = slot_view(s, 256)
                for j in range(2):
                    if i > 0:
                        nxt(pe, "conv_in")
                    for k in range(KD):
                        mm = pe.matmul(bank[j][:, :], w[:, k, j * P:(j + 1) * P], hT[:, k, :],
                                       start=(k == 0), stop=(k == KD - 1))
                    if j == 0:
                        mm.then_inc(S("qkvT_ps"), 1)
                mm.then_inc(S("slots_used"), 1)
            nxt(pe, "conv_in", 2)
            pe_gemm_n(pe, FIRST["z"], tokens, bank[2:6])
            nxt(pe, "wab_loaded", 16)
            for t in range(NT):
                for k in range(KD):
                    mm = pe.matmul(bank[6][:, 16 * t:16 * t + 16], tokens(k, t), wab[:, k, :],
                                   start=(k == 0), stop=(k == KD - 1))
            mm.then_inc(S("ab_ps"), 1)
            nxt(pe, "z_taken")
            pe_gemm_n(pe, FIRST["sq"], tokens, bank[2:6])
            nxt(pe, "sq_taken")
            need(pe, FIRST["skv"])
            w = slot_view(FIRST["skv"], 256)
            for t in range(NT):
                for k in range(KD):
                    mm = pe.matmul(bank[2 + t][:, 0:256], tokens(k, t), w[:, k, :],
                                   start=(k == 0), stop=(k == KD - 1))
            mm.then_inc(S("slots_used"), 1)

        def act_proj1(act):
            for m in range(NM):
                i, j = m // 2, m % 2
                if j == 0:
                    nxt(act, "qkvT_ps")
                else:
                    act.wait_ge(S("slots_used"), FIRST["qkv"] + i + 1)
                if m >= 2:
                    nxt(act, "conv_done")
                act.activation(convin[:, j, 3:3 + T], bank[j][:, :], ACT.Copy).then_inc(S("conv_in"), 1)
                if m >= 2:
                    act.activation(convT[:, m - 2, :], convacc[:, j, :], ACT.Silu).then_inc(S("silu_done"), 1)
            for m in (NM - 2, NM - 1):
                nxt(act, "conv_done")
                act.activation(convT[:, m, :], convacc[:, m % 2, :], ACT.Silu).then_inc(S("silu_done"), 1)

        def dve_proj1(dve):
            dve.memset(convin[:, :, 0:3], 0.0)
            at, _ = col("conv_w", VEC1)
            for m in range(NM):
                j = m % 2
                nxt(dve, "conv_in")
                if m >= 2:
                    nxt(dve, "silu_done")
                dve.drain()
                dve.tensor_scalar(convacc[:, j, :], convin[:, j, 3:3 + T], cols1[:, at + 36 + m:at + 37 + m],
                                  None, ALU.mult)
                for tap in range(3):
                    dve.drain()
                    w = cols1[:, at + 12 * tap + m:at + 12 * tap + m + 1]
                    i = dve.scalar_tensor_tensor(convacc[:, j, :], convin[:, j, tap:tap + T], w,
                                                 convacc[:, j, :], ALU.mult, ALU.add)
                i.then_inc(S("conv_done"), 1)
            dve.wait_ge(S("slots_used"), FIRST["z"] + 2)
            for t in range(NT):
                i = dve.tensor_copy(z[:, t, :], bank[2 + t][:, :])
            i.then_inc(S("z_taken"), 1)
            nxt(dve, "ab_ps")
            dve.tensor_copy(ab, bank[6][:, 0:64].rearrange("p (t n) -> p t n", n=16))
            dve.wait_ge(S("slots_used"), FIRST["sq"] + 2)
            for t in range(NT):
                i = dve.tensor_copy(sq[:, t, :], bank[2 + t][:, :])
            i.then_inc(S("sq_taken"), 1)
            dve.wait_ge(S("slots_used"), FIRST["skv"] + 1)
            for t in range(NT):
                dve.tensor_copy(skv[:, t, :], bank[2 + t][:, 0:256])
            dve.drain().then_inc(S("proj1_done"), 1)

        def pe_qkv(pe):
            nxt(pe, "silu_done", NM)
            for t in range(NT):
                for g in range(3):
                    b = bank[(3 * t + g) % 2]
                    if 3 * t + g >= 2:
                        nxt(pe, "qkv_taken")
                    for m in range(4):
                        mm = pe.transpose(b[:, m * P:(m + 1) * P], convT[:, 4 * g + m, t * P:(t + 1) * P], ident)
                    mm.then_inc(S("qkv_turned"), 1)

        def act_qkv(act):
            for t in range(NT):
                for g in range(3):
                    nxt(act, "qkv_turned")
                    act.activation(qkv[:, t, 512 * g:512 * g + 512], bank[(3 * t + g) % 2][:, :], ACT.Copy)\
                       .then_inc(S("qkv_taken"), 1)

        small = region(28880, 1020)
        NW = H + 2

        def sm(at, width, pattern=None, **kw):
            r = small[:, at:at + width]
            return r.rearrange(pattern, **kw) if pattern else r

        pos_i = sm(0, NT).bitcast(I32)
        pos_f = sm(4, NT)
        cos = region(26960, 128, "p (t f) -> p t f", t=NT)
        sin = region(27088, 128, "p (t f) -> p t f", t=NT)
        ang = region(27216, 128, "p (t f) -> p t f", t=NT)
        turns = region(27344, 128, "p (t f) -> p t f", t=NT)
        w_ss = sm(8, 40, "p (t h) -> p t h", t=NT)
        w_r = sm(48, 40, "p (t h) -> p t h", t=NT)
        w_mx, w_nmx, w_den, w_es = (sm(88 + 32 * i, 32) for i in range(4))
        sq4 = sq.rearrange("p t (h e) -> p t h e", e=HD)
        sk3 = skv[:, :, 0:128]
        squares_q = region(0, 2048, "p (t n) -> p t n", t=NT)
        squares_k = region(2048, 512, "p (t n) -> p t n", t=NT)
        kk = region(4096, 1024, "p (t g i e) -> p t g i e", t=NT, g=2, i=2)
        q_T = region(0, 2048, "p (j t) -> p j t", base=hflat, t=T)
        k_T = region(2048, 1024, "p (g t) -> p g t", base=hflat, t=T)
        Pw = region(23616, 1024, "p (b i k) -> p b i k", b=2, i=2)
        PwT = region(24656, 1024, "p (b i k) -> p b i k", b=2, i=2)
        TWO_PI = 2 * np.pi
        C1 = 6.28125
        C2 = float(np.float32(TWO_PI - C1))
        C3 = TWO_PI - C1 - C2
        ROUND = 12582912.0
        NEAR_PI = 3.1415925

        def sp_positions(sp):
            sp.dma_start(pos_i, a["positions"][0].rearrange("(t p) -> p t", p=P),
                         allow_slow_non_contiguous=True).then_inc(S("positions_loaded"), 16)

        def act_swa_prep(act):
            nxt(act, "rows_loaded", 16 * len(ROWS))
            act.activation(squares_q, sq, ACT.Square)
            act.activation(squares_k, sk3, ACT.Square).then_inc(S("w_squares"), 1)
            nxt(act, "w_ss")
            act.activation(w_r, w_ss, ACT.Sqrt, bias=eps, scale=1.0 / HD).then_inc(S("w_roots"), 1)
            nxt(act, "angles")
            act.activation(sin, ang, ACT.Sin)
            act.activation(cos, turns, ACT.Sin).then_inc(S("rotation"), 1)

        def dve_swa_prep(dve):
            nxt(dve, "w_squares")
            dve.tensor_reduce(w_ss[:, :, 0:H], squares_q.rearrange("p t (h e) -> p t h e", e=HD), AX_X, ALU.add)
            dve.tensor_reduce(w_ss[:, :, H:NW], squares_k.rearrange("p t (h e) -> p t h e", e=HD), AX_X, ALU.add)\
               .then_inc(S("w_ss"), 1)
            nxt(dve, "positions_loaded", 16)
            dve.tensor_copy(pos_f, pos_i)
            dve.drain()
            shape = [P, NT, HD // 2]
            dve.tensor_tensor(ang, pos_f.unsqueeze(2).broadcast_to(shape),
                              con("inv_freq").unsqueeze(1).broadcast_to(shape), ALU.mult)
            dve.drain()
            dve.tensor_scalar(turns, ang, 1.0 / TWO_PI, ROUND, ALU.mult, ALU.add)
            dve.drain()
            dve.tensor_scalar(turns, turns, ROUND, None, ALU.subtract)
            for c in (C1, C2, C3):
                dve.drain()
                dve.scalar_tensor_tensor(ang, turns, -c, ang, ALU.mult, ALU.add)
            dve.drain()
            dve.tensor_scalar(ang, ang, NEAR_PI, -NEAR_PI, ALU.min, ALU.max)
            dve.drain()
            dve.scalar_tensor_tensor(turns, ang, -1.0, ang, ALU.mult, ALU.min)
            dve.drain()
            dve.tensor_scalar(turns, turns, float(np.pi / 2), None, ALU.add).then_inc(S("angles"), 1)
            nxt(dve, "w_roots")
            dve.reciprocal(w_ss, w_r)
            dve.drain()
            for t in range(NT):
                shape = [P, H, HD]
                dve.tensor_tensor(sq4[:, t], sq4[:, t], w_ss[:, t, 0:H].unsqueeze(2).broadcast_to(shape), ALU.mult)
                k4 = sk3[:, t, :].rearrange("p (h e) -> p h e", e=HD)
                dve.tensor_tensor(k4, k4, w_ss[:, t, H:NW].unsqueeze(2).broadcast_to([P, 2, HD]), ALU.mult)
            dve.drain()
            for t in range(NT):
                dve.tensor_tensor(sq4[:, t], sq4[:, t], row("q_norm").unsqueeze(1).broadcast_to([P, H, HD]), ALU.mult)
                k4 = sk3[:, t, :].rearrange("p (h e) -> p h e", e=HD)
                dve.tensor_tensor(k4, k4, row("k_norm").unsqueeze(1).broadcast_to([P, 2, HD]), ALU.mult)
            nxt(dve, "rotation")
            dve.drain()
            half = HD // 2
            for t in range(NT):
                for heads, src in ((H, sq4[:, t]), (2, sk3[:, t, :].rearrange("p (h e) -> p h e", e=HD))):
                    shape = [P, heads, half]
                    c = cos[:, t, :].unsqueeze(1).broadcast_to(shape)
                    s = sin[:, t, :].unsqueeze(1).broadcast_to(shape)
                    x1, x2 = src[:, :, 0:half], src[:, :, half:HD]
                    base = 1024 * (t % 2) + (0 if heads == H else 2048)
                    u = [region(base + 256 * i, heads * half, "p (h f) -> p h f", f=half) for i in range(4)]
                    dve.tensor_tensor(u[0], x1, c, ALU.mult)
                    dve.tensor_tensor(u[1], x2, s, ALU.mult)
                    dve.tensor_tensor(u[2], x1, s, ALU.mult)
                    dve.tensor_tensor(u[3], x2, c, ALU.mult)
                    dve.drain()
                    if heads == H:
                        dve.tensor_tensor(x1, u[0], u[1], ALU.subtract)
                        dve.tensor_tensor(x2, u[2], u[3], ALU.add)
                    else:
                        for i in range(2):
                            dve.tensor_tensor(kk[:, t, :, i, 0:half], u[0], u[1], ALU.subtract)
                            dve.tensor_tensor(kk[:, t, :, i, half:HD], u[2], u[3], ALU.add)
                    if t >= 1:
                        dve.drain()
            dve.drain().then_inc(S("w_qk"), 1)

        def pe_swa_turn(pe):
            nxt(pe, "w_qk")
            for j in range(NPAIR):
                for t in range(NT):
                    pe.transpose(bank[j][:, t * P:(t + 1) * P], sq[:, t, j * P:(j + 1) * P], ident)
            for g in range(2):
                for t in range(NT):
                    mm = pe.transpose(bank[4 + g][:, t * P:(t + 1) * P],
                                      kk[:, t, g].rearrange("p i e -> p (i e)"), ident)
            mm.then_inc(S("w_turned"), 1)

        def dve_swa_turn(dve):
            nxt(dve, "w_turned")
            for j in range(NPAIR):
                dve.tensor_copy(q_T[:, j, :], bank[j][:, :])
            dve.drain().then_inc(S("w_qT"), 1)

        def act_swa_turn(act):
            nxt(act, "w_turned")
            for g in range(2):
                act.activation(k_T[:, g, :], bank[4 + g][:, :], ACT.Copy)
            act.drain().then_inc(S("w_kT"), 1)

        UNITS = [(n, j) for n in range(NT) for j in range(NPAIR)]

        def span(n):
            return (n - 1, 2 * P) if n else (0, P)

        def pe_swa(pe):
            def scores(u):
                n, j = UNITS[u]
                n0, w = span(n)
                if u >= 2:
                    nxt(pe, "w_s_taken")
                for i in range(2):
                    r = slice(64 * i, 64 * i + 64)
                    mm = pe.matmul(bank[2 * (u % 2) + i][:, 0:w], q_T[r, j, n * P:(n + 1) * P],
                                   k_T[r, j // 2, n0 * P:n0 * P + w], start=True, stop=True)
                mm.then_inc(S("w_scores"), 1)

            def turn(u):
                n, j = UNITS[u]
                nxt(pe, "w_p")
                for i in range(2):
                    for b in range(span(n)[1] // P):
                        mm = pe.transpose(bank[4 + u % 2][:, (2 * i + b) * P:(2 * i + b + 1) * P],
                                          Pw[:, u % 2, i, b * P:(b + 1) * P], ident)
                mm.then_inc(S("w_p_turned"), 1)

            def values(u):
                n, j = UNITS[u]
                n0, w = span(n)
                nxt(pe, "w_pT_ready")
                if j == 0 and n >= 2:
                    nxt(pe, "w_o_taken")
                for i in range(2):
                    h = 2 * j + i
                    for b in range(w // P):
                        mm = pe.matmul(bank[6 + n % 2][:, h * HD:(h + 1) * HD], PwT[:, u % 2, i, b * P:(b + 1) * P],
                                       skv[:, n0 + b, 128 + HD * (h // 4):128 + HD * (h // 4) + HD],
                                       start=(b == 0), stop=(b == w // P - 1))
                mm.then_inc(S("w_values"), 1)

            nxt(pe, "w_qT")
            nxt(pe, "w_kT")
            scores(0)
            for u in range(len(UNITS)):
                if u + 1 < len(UNITS):
                    scores(u + 1)
                turn(u)
                if u:
                    values(u - 1)
            values(len(UNITS) - 1)

        def dve_swa(dve):
            mask = con("window")
            for u, (n, j) in enumerate(UNITS):
                _, w = span(n)
                c = slice(2 * u, 2 * u + 2)
                nxt(dve, "w_scores")
                if u >= 2:
                    nxt(dve, "w_p_turned")
                for i in range(2):
                    s = dve.scalar_tensor_tensor(Pw[:, u % 2, i, 0:w], bank[2 * (u % 2) + i][:, 0:w], HD ** -0.5,
                                                 mask[:, 2 * P - w:2 * P], ALU.mult, ALU.add)
                s.then_inc(S("w_s_taken"), 1)
                dve.drain()
                dve.tensor_reduce(w_mx[:, c], Pw[:, u % 2, :, 0:w], AX_X, ALU.max)
                dve.drain()
                dve.tensor_tensor(w_mx[:, c], w_mx[:, c], row("sinks")[:, 2 * j:2 * j + 2], ALU.max)
                dve.drain()
                dve.tensor_scalar(w_nmx[:, c], w_mx[:, c], -1.0, None, ALU.mult).then_inc(S("w_max"), 1)
                if u >= 1 and u % NPAIR == 0:
                    outputs(dve, n - 1)
            outputs(dve, NT - 1)

        def outputs(dve, n):
            c = slice(8 * n, 8 * n + 8)
            dve.wait_ge(S("w_values"), 4 * (n + 1))
            dve.wait_ge(S("w_p"), 4 * (n + 1))
            dve.tensor_tensor(w_den[:, c], w_den[:, c], w_es[:, c], ALU.add)
            dve.drain()
            dve.reciprocal(w_es[:, c], w_den[:, c])
            dve.drain()
            dve.tensor_tensor(mixed[:, n, 512:1024].rearrange("p (h e) -> p h e", e=HD),
                              bank[6 + n % 2][:, :].rearrange("p (h e) -> p h e", e=HD),
                              w_es[:, c].unsqueeze(2).broadcast_to([P, H, HD]), ALU.mult)\
               .then_inc(S("w_o_taken"), 1)

        def act_swa(act):
            def exps(u):
                n, j = UNITS[u]
                w = span(n)[1]
                nxt(act, "w_max")
                for i in range(2):
                    c = slice(2 * u + i, 2 * u + i + 1)
                    act.activation(w_es[:, c], row("sinks")[:, 2 * j + i:2 * j + i + 1], ACT.Exp, bias=w_nmx[:, c])
                    act.activation(Pw[:, u % 2, i, 0:w], Pw[:, u % 2, i, 0:w], ACT.Exp, bias=w_nmx[:, c],
                                   accum_out=w_den[:, c])
                act.drain().then_inc(S("w_p"), 1)

            def copy(u):
                w = span(UNITS[u][0])[1]
                nxt(act, "w_p_turned")
                if u >= 2:
                    nxt(act, "w_values")
                act.activation(PwT[:, u % 2, :, 0:w],
                               bank[4 + u % 2][:, :].rearrange("p (i k) -> p i k", i=2)[:, :, 0:w], ACT.Copy)
                act.drain().then_inc(S("w_pT_ready"), 1)

            exps(0)
            for u in range(len(UNITS)):
                if u + 1 < len(UNITS):
                    exps(u + 1)
                copy(u)

        a_in, b_in = ab[:, :, 0:H], ab[:, :, H:2 * H]

        def th(at):
            return sm(at, 32, "p (t h) -> p t h", t=NT)

        g_u, g_e, g_s, g_z, g_q, g_g, g_beta, g_G, g_expG, g_kdec, g_ea = (th(216 + 32 * i) for i in range(11))
        g_dec = sm(568, 32, "p (t c j) -> p t c j", t=NT, c=2)
        g_ss = sm(600, 64, "p (t h) -> p t h", t=NT)
        g_r = sm(664, 64, "p (t h) -> p t h", t=NT)
        g_os = th(728)
        g_or = th(760)
        squares = region(0, 4096, "p (t n) -> p t n", t=NT)
        qg = region(0, 2048, "p (t n) -> p t n", t=NT)
        kb = region(2048, 2048, "p (t n) -> p t n", t=NT)
        kdec = region(4096, 2048, "p (t n) -> p t n", t=NT)
        qn, kn, vb = (qkv[:, :, 512 * i:512 * i + 512] for i in range(3))
        TT, Tm, Xs, MT = (region(1024 * i, 1024, "p (h c) -> p h c", base=hflat, c=P) for i in range(4))
        MTl, DT, attnT, gU = (region(20544 + 1024 * i, 1024, "p (h c) -> p h c", c=P) for i in range(4))
        kT, kbT, qT, qgT, nwT = (region(24640 + 512 * i, 512, "p (j c) -> p j c", c=P) for i in range(5))
        vnew = region(27200, 1024, "p (c n) -> p c n", c=2)
        state = region(28224, 512, "p (j e) -> p j e", e=P)
        LEVELS = (2, 4, 8, 16, 32)

        def dve_log1p(dve, e, z_, q_, shape_out):
            dve.tensor_scalar(q_, e, 2.0, None, ALU.add)
            dve.drain()
            dve.reciprocal(q_, q_)
            dve.drain()
            dve.tensor_tensor(z_, e, q_, ALU.mult)
            dve.drain()
            dve.tensor_tensor(e, z_, z_, ALU.mult)
            dve.drain()
            dve.tensor_scalar(q_, e, 1.0 / 13, None, ALU.mult)
            for n in (11, 9, 7, 5, 3):
                dve.drain()
                dve.scalar_tensor_tensor(q_, q_, 1.0 / n, e, ALU.add, ALU.mult)
            dve.drain()
            dve.scalar_tensor_tensor(shape_out, q_, 1.0, z_, ALU.add, ALU.mult)
            dve.drain()
            dve.tensor_scalar(shape_out, shape_out, 2.0, None, ALU.mult)
            dve.drain()

        def dve_gdn_prep(dve):
            wide = [P, NT, H]
            dve.tensor_tensor(g_u, a_in, row("dt_bias").unsqueeze(1).broadcast_to(wide), ALU.add)
            dve.drain()
            dve.scalar_tensor_tensor(g_s, g_u, -1.0, g_u, ALU.mult, ALU.max).then_inc(S("g_abs"), 1)
            nxt(dve, "g_exp")
            dve_log1p(dve, g_e, g_z, g_q, g_s)
            dve.scalar_tensor_tensor(g_s, g_u, 0.0, g_s, ALU.max, ALU.add)
            dve.drain()
            dve.scalar_tensor_tensor(g_g, g_s, -1.0, g_ea, ALU.mult, ALU.mult).then_inc(S("g_ready"), 1)
            nxt(dve, "g_squares")
            dve.tensor_reduce(g_ss, squares.rearrange("p t (h e) -> p t h e", e=HD), AX_X, ALU.add)\
               .then_inc(S("g_ss"), 1)
            nxt(dve, "g_sums")
            dve.tensor_copy(g_G, bank[0][:, 0:32].rearrange("p (t h) -> p t h", t=NT))
            dve.drain()
            dve.tensor_tensor(g_kdec, bank[0][:, 32:64].rearrange("p (t h) -> p t h", t=NT), g_G, ALU.subtract)\
               .then_inc(S("g_G"), 1)
            nxt(dve, "g_roots")
            dve.reciprocal(g_ss, g_r)
            dve.drain()
            dve.tensor_scalar(g_ss[:, :, 0:H], g_ss[:, :, 0:H], HD ** -0.5, None, ALU.mult)
            dve.drain()
            nxt(dve, "g_exps")

            def scaled(dst, src, by):
                for t in range(NT):
                    dve.tensor_tensor(dst[:, t, :].rearrange("p (h e) -> p h e", e=HD),
                                      src[:, t, :].rearrange("p (h e) -> p h e", e=HD),
                                      by[:, t, :].unsqueeze(2).broadcast_to([P, H, HD]), ALU.mult)

            scaled(qn, qn, g_ss[:, :, 0:H])
            scaled(kn, kn, g_ss[:, :, H:2 * H])
            scaled(vb, vb, g_beta)
            dve.drain()
            scaled(qg, qn, g_expG)
            scaled(kb, kn, g_beta)
            scaled(kdec, kn, g_kdec)
            dve.drain()
            scaled(kbG, kb, g_expG)
            dve.memset(state, 0.0)
            dve.memset(vnew, 0.0)
            dve.drain().then_inc(S("g_scaled"), 1)

        def act_gdn_prep(act):
            act.activation(squares, qkv[:, :, 0:1024], ACT.Square).then_inc(S("g_squares"), 1)
            nxt(act, "g_abs")
            act.activation(g_e, g_s, ACT.Exp, scale=-1.0)
            act.activation(g_ea, row("a_log").unsqueeze(1).broadcast_to([P, NT, H]), ACT.Exp)
            act.activation(g_beta, b_in, ACT.Sigmoid)
            act.drain().then_inc(S("g_exp"), 1)
            nxt(act, "g_ss")
            act.activation(g_r, g_ss, ACT.Sqrt, bias=eps).then_inc(S("g_roots"), 1)
            nxt(act, "g_G")
            act.activation(g_expG, g_G, ACT.Exp)
            act.activation(g_kdec, g_kdec, ACT.Exp)
            for c in range(2):
                for i in range(2):
                    r = slice(64 * i, 64 * i + 64)
                    src = bank[0][r, 64 + 32 * c:96 + 32 * c].rearrange("p (t j i) -> p t j i", t=NT, i=2)
                    act.activation(g_dec[r, :, c, :], src[:, :, :, i], ACT.Exp)
            act.drain().then_inc(S("g_exps"), 1)

        def pe_gdn_prep(pe):
            nxt(pe, "g_ready")
            g = g_g.rearrange("p t h -> p (t h)")
            for i, name in enumerate(("cumsum", "chunk_all", "chunk0", "chunk1")):
                mm = pe.matmul(bank[0][:, 32 * i:32 * i + 32], con(name), g, start=True, stop=True)
            mm.then_inc(S("g_sums"), 1)
            nxt(pe, "g_scaled")

        def place(h):
            return 4 * (h % 2) + h // 2

        def by_parity(x):
            return x.rearrange("p (j i) -> p i j", i=2)

        def heads(x, g):
            return x[:, 4 * g:4 * g + 4, :].rearrange("p h c -> p (h c)")

        def pe_gdn(pe, t):
            if t:
                nxt(pe, "g_state")
            for i, x in enumerate((kn, kb, qn, qg)):
                for j in range(NPAIR):
                    mm = pe.transpose(bank[i][:, j * P:(j + 1) * P], x[:, t, j * P:(j + 1) * P], ident)
                mm.then_inc(S("g_turned"), 1)
            nxt(pe, "g_U")
            for g in range(2):
                mm = pe.matmul(bank[4 + g][:, :], ones, heads(gU, g), start=True, stop=True)
            mm.then_inc(S("g_Grow"), 1)
            nxt(pe, "g_T_even", 2)
            nxt(pe, "g_T_odd", 2)
            for h in range(H):
                j, r = h // 2, slice(64 * (h % 2), 64 * (h % 2) + 64)
                mm = pe.matmul(bank[6 + h % 2][:, j * P:(j + 1) * P], kT[r, j, :], kbT[r, j, :],
                               start=True, stop=True)
            mm.then_inc(S("g_kk"), 1)
            for h in range(H):
                j, r = h // 2, slice(64 * (h % 2), 64 * (h % 2) + 64)
                mm = pe.matmul(bank[h % 2][:, j * P:(j + 1) * P], kT[r, j, :], qT[r, j, :],
                               start=True, stop=True)
            mm.then_inc(S("g_kq"), 1)
            for g in range(2):
                nxt(pe, "g_T1")
                for h in range(4 * g, 4 * g + 4):
                    mm = pe.matmul(bank[2 + g][:, (h % 4) * P:(h % 4 + 1) * P], MTl[:, h, :], ident,
                                   start=True, stop=True)
                mm.then_inc(S("g_X1"), 1)
            for lv in LEVELS:
                last = lv == LEVELS[-1]
                for g in range(2):
                    nxt(pe, "g_Ml")
                    nxt(pe, "g_T")
                    for h in range(4 * g, 4 * g + 4):
                        mm = pe.matmul(bank[g][:, (h % 4) * P:(h % 4 + 1) * P], MTl[:, h, :], Tm[:, h, :],
                                       start=True, stop=True)
                    mm.then_inc(S("g_X"), 1)
                for g in range(2):
                    nxt(pe, "g_Xs")
                    for h in range(4 * g, 4 * g + 4):
                        mm = pe.matmul(bank[4 + g][:, (h % 4) * P:(h % 4 + 1) * P], Xs[:, h, :], TT[:, h, :],
                                       start=True, stop=True)
                    if not last:
                        for h in range(4 * g, 4 * g + 4):
                            mm = pe.matmul(bank[2 + g][:, (h % 4) * P:(h % 4 + 1) * P], TT[:, h, :], Xs[:, h, :],
                                           start=True, stop=True)
                    mm.then_inc(S("g_Y"), 1)
            nxt(pe, "g_T", 2)
            for h in range(H):
                j, r = h // 2, slice(64 * (h % 2), 64 * (h % 2) + 64)
                mm = pe.matmul(bank[1][r, j * P:(j + 1) * P], kbG[:, t, h * HD:(h + 1) * HD], TT[:, place(h), :],
                               start=True, stop=True)
            mm.then_inc(S("g_w"), 1)
            nxt(pe, "g_nw")
            for c in range(2):
                rc = slice(64 * c, 64 * c + 64)
                if c:
                    nxt(pe, "g_state")
                for j in range(NPAIR):
                    dst = bank[6][rc, j * P:(j + 1) * P]
                    pe.matmul(dst, nwT[:, j, rc], state[:, j, :], start=True, stop=False)
                    for i in range(2):
                        h = 2 * j + i
                        mm = pe.matmul(bank[6][rc, h * HD:(h + 1) * HD], TT[:, place(h), rc],
                                       vb[:, t, h * HD:(h + 1) * HD], start=False, stop=(i == 1))
                mm.then_inc(S("g_v"), 1)
                nxt(pe, "g_vnew")
                for j in range(NPAIR):
                    pe.matmul(bank[7][rc, j * P:(j + 1) * P], qgT[:, j, rc], state[:, j, :], start=True, stop=False)
                    for i in range(2):
                        h = 2 * j + i
                        pe.matmul(bank[7][rc, h * HD:(h + 1) * HD], attnT[:, place(h), rc],
                                  vnew[:, c, h * HD:(h + 1) * HD], start=False, stop=(i == 1))
                for j in range(NPAIR):
                    mm = pe.matmul(bank[0][:, j * P:(j + 1) * P], kdec[:, t, j * P:(j + 1) * P],
                                   vnew[:, c, j * P:(j + 1) * P], start=True, stop=True)
                mm.then_inc(S("g_out"), 1)
            nxt(pe, "g_o_taken")

        def act_gdn(act, t):
            for i, dst in enumerate((kT, kbT, qT, qgT)):
                nxt(act, "g_turned")
                if i % 2 == 0:
                    act.activation(dst.rearrange("p j c -> p (j c)"), bank[i][:, :], ACT.Copy)\
                       .then_inc(S("g_T_even"), 1)
            nxt(act, "g_diff")
            act.activation(DT, DT, ACT.Exp).then_inc(S("g_decay"), 1)
            for lv in LEVELS:
                for g in range(2):
                    nxt(act, "g_X")
                    act.activation(heads(Xs, g), bank[g][:, :], ACT.Copy).then_inc(S("g_Xs"), 1)
            nxt(act, "g_w")
            act.activation(nwT.rearrange("p j c -> p (j c)"), bank[1][:, :], ACT.Copy, scale=-1.0)\
               .then_inc(S("g_nw"), 1)
            for c in range(2):
                rc = slice(64 * c, 64 * c + 64)
                nxt(act, "g_v")
                act.activation(vnew[rc, c, :], bank[6][rc, :], ACT.Copy).then_inc(S("g_vnew"), 1)
            nxt(act, "g_out", 2)
            act.activation(mixed[:, t, 0:512], bank[7][:, :], ACT.Copy).then_inc(S("g_o_taken"), 1)

        def pool_gdn(pool, t):
            if t:
                pool.wait_ge(S("g_out"), 2 * t)
            else:
                nxt(pool, "g_ready")
            for g in range(2):
                four = [P, NPAIR, P]
                i = pool.tensor_tensor(gU[:, 4 * g:4 * g + 4, :], con("cumsum").unsqueeze(1).broadcast_to(four),
                                       by_parity(g_g[:, t, :])[:, g, :].unsqueeze(2).broadcast_to(four), ALU.mult)
            i.then_inc(S("g_U"), 1)
            nxt(pool, "g_MT")
            nxt(pool, "g_X1", 2)
            for n, lv in enumerate(LEVELS):
                for g in range(2):
                    if n:
                        nxt(pool, "g_X")
                    pool.tensor_tensor(MTl[:, 4 * g:4 * g + 4, :], MT[:, 4 * g:4 * g + 4, :],
                                       con(f"level{lv}").unsqueeze(1).broadcast_to([P, 4, P]), ALU.mult)\
                        .then_inc(S("g_Ml"), 1)
            nxt(pool, "g_X", 2)

        def dve_gdn(dve, t):
            for i, dst in enumerate((kT, kbT, qT, qgT)):
                nxt(dve, "g_turned")
                if i % 2 == 1:
                    dve.tensor_copy(dst.rearrange("p j c -> p (j c)"), bank[i][:, :]).then_inc(S("g_T_odd"), 1)
            nxt(dve, "g_Grow")
            for g in range(2):
                dve.tensor_tensor(DT[:, 4 * g:4 * g + 4, :], bank[4 + g][:, :].rearrange("p (h c) -> p h c", c=P),
                                  by_parity(g_G[:, t, :])[:, g, :].unsqueeze(2).broadcast_to([P, 4, P]), ALU.subtract)
            dve.drain()
            dve.tensor_scalar(DT, DT, 0.0, None, ALU.min).then_inc(S("g_diff"), 1)
            nxt(dve, "g_decay")
            dve.tensor_tensor(DT, DT, con("cumsum").unsqueeze(1).broadcast_to([P, H, P]), ALU.mult)
            dve.drain()
            nxt(dve, "g_kk")
            for g in range(2):
                dve.tensor_tensor(heads(MT, g), bank[6 + g][:, :], heads(DT, g), ALU.mult)
            dve.drain().then_inc(S("g_MT"), 1)
            nxt(dve, "g_kq")
            for g in range(2):
                four = [P, 4, P]
                hs = slice(4 * g, 4 * g + 4)
                dve.tensor_tensor(MTl[:, hs, :], MT[:, hs, :], con("level1").unsqueeze(1).broadcast_to(four), ALU.mult)
                dve.drain()
                dve.tensor_tensor(TT[:, hs, :], ident.unsqueeze(1).broadcast_to(four), MTl[:, hs, :],
                                  ALU.subtract).then_inc(S("g_T1"), 1)
            for g in range(2):
                dve.tensor_tensor(heads(attnT, g), bank[g][:, :], heads(DT, g), ALU.mult)
            for g in range(2):
                nxt(dve, "g_X1")
                dve.drain()
                dve.tensor_tensor(Tm[:, 4 * g:4 * g + 4, :], ident.unsqueeze(1).broadcast_to([P, 4, P]),
                                  bank[2 + g][:, :].rearrange("p (h c) -> p h c", c=P), ALU.subtract)\
                   .then_inc(S("g_T"), 1)
            for lv in LEVELS:
                for g in range(2):
                    nxt(dve, "g_Y")
                    dve.drain()
                    i = dve.tensor_tensor(heads(TT, g), heads(TT, g), bank[4 + g][:, :], ALU.subtract)
                    if lv != LEVELS[-1]:
                        i = dve.tensor_tensor(heads(Tm, g), heads(Tm, g), bank[2 + g][:, :], ALU.subtract)
                    i.then_inc(S("g_T"), 1)
            for c in range(2):
                nxt(dve, "g_out")
                for i in range(2):
                    r = slice(64 * i, 64 * i + 64)
                    dve.tensor_tensor(state[r, :, r], state[r, :, r],
                                      g_dec[r, t, c, :].unsqueeze(2).broadcast_to([64, NPAIR, HD]), ALU.mult)
                dve.drain()
                for i in range(2):
                    r = slice(64 * i, 64 * i + 64)
                    dve.tensor_tensor(state[r, :, r], state[r, :, r],
                                      bank[0][r, :].rearrange("p (j e) -> p j e", e=P)[:, :, r], ALU.add)
                dve.drain().then_inc(S("g_state"), 1)

        def act_gdn_end(act):
            act.drain()
            act.activation(squares[:, :, 0:512], mixed[:, :, 0:512], ACT.Square).then_inc(S("g_osq"), 1)
            act.activation(z, z, ACT.Silu)
            nxt(act, "g_oss")
            act.activation(g_or, g_os, ACT.Sqrt, bias=eps, scale=1.0 / HD)
            act.drain().then_inc(S("g_oroot"), 1)

        def dve_gdn_end(dve):
            nxt(dve, "g_osq")
            dve.tensor_reduce(g_os, squares[:, :, 0:512].rearrange("p t (h e) -> p t h e", e=HD), AX_X, ALU.add)\
               .then_inc(S("g_oss"), 1)
            nxt(dve, "g_oroot")
            dve.reciprocal(g_os, g_or)
            dve.drain()
            for by in (0, 1):
                for t in range(NT):
                    o = mixed[:, t, 0:512].rearrange("p (h e) -> p h e", e=HD)
                    r = g_os[:, t, :].unsqueeze(2) if by == 0 else row("gdn_out_norm").unsqueeze(1)
                    dve.tensor_tensor(o, o, r.broadcast_to([P, H, HD]), ALU.mult)
                dve.drain()
            for t in range(NT):
                dve.tensor_tensor(mixed[:, t, 0:512], mixed[:, t, 0:512], z[:, t, :], ALU.mult)
            dve.drain().then_inc(S("mixed_ready"), 1)

        def dve_gate(dve, dg, m0):
            for k in range(KD):
                i = dve.tensor_scalar(dg[:, k * P:(k + 1) * P], ident, mod[:, m0 + k:m0 + k + 1], None, ALU.mult)
            i.then_inc(S("gate_diag"), 1)

        def pe_gate(pe, dg, b0):
            nxt(pe, "gate_diag")
            for half in range(2):
                mm = pe.matmul(bank[b0 + half][:, :], ones, dg[:, 512 * half:512 * half + 512], start=True, stop=True)
            mm.then_inc(S("gate_row"), 1)

        def dve_gate_row(dve, gate, b0):
            nxt(dve, "gate_row")
            dve.tensor_copy(gate[:, 0:512], bank[b0][:, :])
            dve.tensor_copy(gate[:, 512:D], bank[b0 + 1][:, :])
            dve.drain().then_inc(S("gate_taken"), 1)

        gate1 = region(24656, D)
        diag1 = region(25680, D)

        def act_turned(act):
            for k in range(0, KD, 2):
                nxt(act, "x_turned", 2 if k else 1)
                i = act.activation(hT[:, k, :], bank[k][:, :], ACT.Copy)
            tally[(str(act.engine), "x_turned")] += 1
            i.then_inc(S("hT_even"), 1)

        def dve_turned(dve):
            for k in range(1, KD, 2):
                nxt(dve, "x_turned", 2)
                i = dve.tensor_copy(hT[:, k, :], bank[k][:, :])
            i.then_inc(S("hT_odd"), 1)

        def pe_down(pe, name, n_slots_, lhs):
            for i in range(n_slots_):
                s = FIRST[name] + i
                need(pe, s)
                w = slot_view(s, D)
                for kk_ in range(2):
                    k = 2 * i + kk_
                    for t in range(NT):
                        for half in range(2):
                            mm = pe.matmul(bank[2 * t + half][:, :], lhs(k, t), w[:, kk_, 512 * half:512 * half + 512],
                                           start=(k == 0), stop=(k == 2 * n_slots_ - 1))
                mm.then_inc(S("slots_used"), 1)

        def dve_out1(dve):
            dve.wait_ge(S("slots_used"), FIRST["w_out"] + 4)
            tmp = region(26704, 1024, "p (b n) -> p b n", b=2)
            for t in range(NT):
                for half in range(2):
                    c = slice(512 * half, 512 * half + 512)
                    dve.tensor_tensor(tmp[:, half, :], bank[2 * t + half][:, :], gate1[:, c], ALU.mult)
                dve.drain()
                dve.tensor_tensor(X[:, t, :], X[:, t, :], tmp.rearrange("p b n -> p (b n)"), ALU.add)
                dve.drain()

        NR = N_GRP + N_EXP
        SLOTS_ = 2 * T
        xn2 = region(4096, 4096, "p (t n) -> p t n", t=NT)
        h2tok = region(0, 4096, "p (t n) -> p t n", t=NT)
        m_G = region(4096, 4096, "p (t s) -> p t s", t=NT)
        m_xT = region(8192, KD * (SLOTS_ + CAP), "p (k s) -> p k s", k=KD)
        m_yT = region(19000, KD * (SLOTS_ + CAP), "p (k s) -> p k s", k=KD)
        m_C = region(19000, 4096, "p (t s) -> p t s", t=NT)
        m_eq = region(23096, 4096, "p (b c s) -> p b c s", b=2, c=2)
        m_CT = region(0, 4096, "p (s t) -> p s t", t=T)
        m_sg = region(28216, 512, "p (b f) -> p b f", b=2)
        m_hid = region(28728, 512, "p (b f s) -> p b f s", b=2, f=2)
        m_y = region(8192, 8192, "p (s n) -> p s n", n=D)
        m_rw = region(17152, KD * NR, "p (k n) -> p k n", n=NR)
        junk2 = region(10240, D)

        def mr(at, width, pattern=None, **kw):
            r = region(17440 + at, width)
            return r.rearrange(pattern, **kw) if pattern else r

        r_lg = mr(0, NT * NR, "p (t n) -> p t n", t=NT)
        r_a = mr(144, 16, "p (t g) -> p t g", t=NT)
        r_b = mr(160, 16, "p (t g) -> p t g", t=NT)
        r_goh = mr(176, 16, "p (t g) -> p t g", t=NT)
        r_m = mr(192, 4)
        r_v = mr(196, 4)
        r_pg = mr(200, 4)
        r_m1 = mr(204, 4)
        r_m2 = mr(208, 4)
        r_w1 = mr(212, 4)
        r_w2 = mr(216, 4)
        r_ig = mr(224, 32, "p (t e) -> p t e", t=NT)
        r_o1 = mr(256, 32, "p (t e) -> p t e", t=NT)
        r_o2 = mr(288, 32, "p (t e) -> p t e", t=NT)
        r_c = mr(320, 32, "p (t e) -> p t e", t=NT)
        r_sel = mr(384, 128, "p (t e g) -> p t e g", t=NT, g=N_GRP)
        r_E = mr(512, 256, "p (c t e) -> p c t e", c=2, t=NT)
        r_M = mr(768, 128, "p (t e) -> p t e", t=NT)
        r_rank = mr(896, 128, "p (t e) -> p t e", t=NT)
        r_prod = mr(1024, 256, "p (c t e) -> p c t e", c=2, t=NT)
        r_place = mr(1280, 8, "p (c t) -> p c t", c=2)
        r_cnt = mr(1288, 32)
        r_ends = mr(1320, 32)
        r_off = mr(1352, 32)
        r_pm = mr(1384, 64, "p (c t s) -> p c t s", c=2, t=NT)
        r_offi = mr(1448, 32).bitcast(I32)
        o_expert = mr(1480, 8).bitcast(I32)
        o_place = mr(1488, 8).bitcast(I32)
        o_count = mr(1496, 2).bitcast(I32)

        gate2 = region(7168, D)
        diag2 = region(6144, D)

        def act_router_weights(act):
            for n0, name in ((0, "w_group"), (N_GRP, "w_router")):
                act.dma_start(m_rw[:, :, n0:n0 + a[name].shape[-1]],
                              a[name][0].rearrange("(k p) n -> p k n", p=P)).then_inc(S("rw_loaded"), 16)

        def pe_route(pe):
            pe_hT(pe)
            nxt(pe, "rw_loaded", 32)
            for t in range(NT):
                for k in range(KD):
                    mm = pe.matmul(bank[0][:, NR * t:NR * t + NR], tokens(k, t), m_rw[:, k, :],
                                   start=(k == 0), stop=(k == KD - 1))
            mm.then_inc(S("r_logits"), 1)
            for t in range(1, NT):
                pe_h2(pe, t)
            pe.wait_ge(S("r_taken"), 1)
            pe_h2(pe, 0)
            nxt(pe, "h2_ready", NT)
            nxt(pe, "r_M")
            for t in range(NT):
                for s in range(t):
                    pe.matmul(bank[2][:, 32 * t:32 * t + 32], ones, r_M[:, s, :], start=(s == 0), stop=False)
                pe.matmul(bank[2][:, 32 * t:32 * t + 32], con("before"), r_M[:, t, :], start=(t == 0), stop=True)
            for t in range(NT):
                mm = pe.matmul(bank[2][:, 128:160], ones, r_M[:, t, :], start=(t == 0), stop=(t == NT - 1))
            mm.then_inc(S("r_ranks"), 1)
            nxt(pe, "r_G", NT)
            for k in range(KD):
                for half in range(2):
                    n = 2 * k + half
                    if n >= 8:
                        nxt(pe, ("m_x_even", "m_x_odd")[half])
                    for t in range(NT):
                        mm = pe.matmul(bank[n % 8][:, :], h2tok[:, t, k * P:(k + 1) * P],
                                       m_G[:, t, 512 * half:512 * half + 512], start=(t == 0), stop=(t == NT - 1))
                    mm.then_inc(S("m_x_ps"), 1)
            nxt(pe, "m_x_even", 4)
            nxt(pe, "m_x_odd", 4)
            nxt(pe, "r_C", NT)
            for s in range(8):
                for t in range(NT):
                    mm = pe.transpose(bank[s][:, t * P:(t + 1) * P], m_C[:, t, s * P:(s + 1) * P], ident)
                mm.then_inc(S("r_C_turned"), 1)
            nxt(pe, "r_CT_even", 4)
            nxt(pe, "r_CT_odd", 4)

        def pe_h2(pe, t):
            for k in range(KD):
                mm = pe.transpose(bank[2 * t + k // 4][:, (k % 4) * P:(k % 4 + 1) * P],
                                  hT[:, k, t * P:(t + 1) * P], ident)
            mm.then_inc(S("h2_turned"), 1)

        def act_h2(act):
            for t in (1, 2, 3, 0):
                nxt(act, "h2_turned")
                for half in range(2):
                    act.activation(h2tok[:, t, 512 * half:512 * half + 512], bank[2 * t + half][:, :], ACT.Copy)
                act.drain().then_inc(S("h2_ready"), 1)

        def act_route(act):
            nxt(act, "r_gmax")
            act.activation(r_a, r_a, ACT.Exp)
            act.drain().then_inc(S("r_gexp"), 1)
            nxt(act, "r_diff")
            act.activation(r_w2, r_m2, ACT.Exp).then_inc(S("r_wexp"), 1)
            for k in range(KD):
                nxt(act, "m_x_ps", 2 if k else 1)
                act.activation(m_xT[:, k, 0:512], bank[2 * k % 8][:, :], ACT.Copy).then_inc(S("m_x_even"), 1)
            nxt(act, "m_x_ps")
            for s in range(0, 8, 2):
                nxt(act, "r_C_turned", 2 if s else 1)
                act.activation(m_CT[:, s, :], bank[s][:, :], ACT.Copy).then_inc(S("r_CT_even"), 1)

        def dve_first_of(dve, dst, values, best, tie, n, tmp):
            shape = [P, NT, n]
            dve.tensor_tensor(tmp, values, best.unsqueeze(2).broadcast_to(shape), ALU.is_equal)
            dve.drain()
            dve.tensor_tensor(tmp, tmp, con(tie).unsqueeze(1).broadcast_to(shape), ALU.mult)
            dve.drain()
            dve.tensor_reduce(r_v, tmp, AX_X, ALU.max)
            dve.drain()
            dve.tensor_tensor(dst, tmp, r_v.unsqueeze(2).broadcast_to(shape), ALU.is_equal)
            dve.drain()

        def dve_route(dve):
            nxt(dve, "r_logits")
            at = ROWS["b_group"][0]
            dve.tensor_tensor(r_lg, bank[0][:, 0:NT * NR].rearrange("p (t n) -> p t n", t=NT),
                              rows[:, at:at + NR].unsqueeze(1).broadcast_to([P, NT, NR]), ALU.add)
            dve.drain().then_inc(S("r_taken"), 1)
            groups = r_lg[:, :, 0:N_GRP]
            dve.tensor_reduce(r_m, groups, AX_X, ALU.max)
            dve.drain()
            dve.tensor_tensor(r_a, groups, r_m.unsqueeze(2).broadcast_to([P, NT, N_GRP]), ALU.subtract)\
               .then_inc(S("r_gmax"), 1)
            dve_first_of(dve, r_goh, groups, r_m, "tie4", N_GRP, r_b)
            for t in range(NT):
                dve.tensor_tensor(r_sel[:, t], r_lg[:, t, N_GRP:NR].rearrange("p (g e) -> p e g", g=N_GRP),
                                  r_goh[:, t, :].unsqueeze(1).broadcast_to([P, EPG, N_GRP]), ALU.mult)
            dve.drain()
            dve.tensor_reduce(r_ig, r_sel, AX_X, ALU.add)
            dve.drain()
            dve.tensor_reduce(r_m1, r_ig, AX_X, ALU.max)
            dve.drain()
            dve_first_of(dve, r_o1, r_ig, r_m1, "tie8", EPG, r_c)
            dve.scalar_tensor_tensor(r_ig, r_o1, -BIG, r_ig, ALU.mult, ALU.add)
            dve.drain()
            dve.tensor_reduce(r_m2, r_ig, AX_X, ALU.max)
            dve.drain()
            dve_first_of(dve, r_o2, r_ig, r_m2, "tie8", EPG, r_c)
            dve.tensor_tensor(r_m2, r_m2, r_m1, ALU.subtract).then_inc(S("r_diff"), 1)
            nxt(dve, "r_gexp")
            dve.tensor_reduce(r_pg, r_a, AX_X, ALU.add)
            nxt(dve, "r_wexp")
            dve.drain()
            dve.tensor_scalar(r_w1, r_w2, 1.0, None, ALU.add)
            dve.drain()
            dve.tensor_tensor(r_w1, r_w1, r_pg, ALU.mult)
            dve.drain()
            dve.reciprocal(r_w1, r_w1)
            dve.drain()
            dve.tensor_tensor(r_w2, r_w2, r_w1, ALU.mult)
            for c, o in enumerate((r_o1, r_o2)):
                for t in range(NT):
                    shape = [P, N_GRP, EPG]
                    dve.tensor_tensor(r_E[:, c, t, :].rearrange("p (g e) -> p g e", g=N_GRP),
                                      r_goh[:, t, :].unsqueeze(2).broadcast_to(shape),
                                      o[:, t, :].unsqueeze(1).broadcast_to(shape), ALU.mult)
            dve.drain()
            dve.tensor_tensor(r_M, r_E[:, 0], r_E[:, 1], ALU.add)
            dve.drain().then_inc(S("r_M"), 1)
            nxt(dve, "r_ranks")
            dve.tensor_copy(r_cnt, bank[2][:, 128:160])
            dve.drain()
            dve.tensor_tensor_scan(r_ends, r_cnt, r_cnt, 0.0, ALU.add, ALU.bypass)
            dve.drain()
            dve.tensor_tensor(r_off, r_ends, r_cnt, ALU.subtract)
            dve.drain()
            dve.tensor_copy(r_offi, r_off)
            dve.tensor_tensor(r_rank, bank[2][:, 0:128].rearrange("p (t e) -> p t e", t=NT),
                              r_off.unsqueeze(1).broadcast_to([P, NT, N_EXP]), ALU.add)
            dve.drain()
            for c in range(2):
                dve.tensor_tensor(r_prod[:, c], r_E[:, c], r_rank, ALU.mult)
            dve.drain()
            dve.tensor_reduce(r_place, r_prod, AX_X, ALU.add)
            dve.drain()
            for s in range(8):
                dve.tensor_scalar(r_pm[:, :, :, s], r_place, float(P * s), None, ALU.subtract)
            dve.drain()
            dve_more_list(dve)
            for t in range(NT):
                first, second = m_eq[:, t % 2, 0], m_eq[:, t % 2, 1]
                if t >= 2:
                    nxt(dve, "r_G")
                for c, eq in enumerate((first, second)):
                    shape = [P, 8, P]
                    dve.tensor_tensor(eq.rearrange("p (s i) -> p s i", i=P), con("iota").unsqueeze(1).broadcast_to(shape),
                                      r_pm[:, c, t, :].unsqueeze(2).broadcast_to(shape), ALU.is_equal)
                dve.drain().then_inc(S("m_eq"), 1)
                dve.tensor_scalar(m_C[:, t, :], first, r_w1[:, t:t + 1], None, ALU.mult)
                dve.drain()
                dve.scalar_tensor_tensor(m_C[:, t, :], second, r_w2[:, t:t + 1], m_C[:, t, :], ALU.mult, ALU.add)\
                   .then_inc(S("r_C"), 1)
                if t >= 1:
                    dve.drain()
            for k in range(KD):
                nxt(dve, "m_x_ps", 2)
                dve.tensor_copy(m_xT[:, k, 512:1024], bank[(2 * k + 1) % 8][:, :]).then_inc(S("m_x_odd"), 1)
            for s in range(1, 8, 2):
                nxt(dve, "r_C_turned", 2)
                dve.tensor_copy(m_CT[:, s, :], bank[s][:, :]).then_inc(S("r_CT_odd"), 1)

        def pool_route(pool):
            for t in range(NT):
                nxt(pool, "m_eq")
                pool.tensor_tensor(m_G[:, t, :], m_eq[:, t % 2, 0], m_eq[:, t % 2, 1], ALU.add).then_inc(S("r_G"), 1)

        w_gate, w_up, w_down = a["w_gate"][0], a["w_up"][0], a["w_down"][0]
        gu = [ring[:, 2 * b:2 * b + 2, :].rearrange("p u (k n) -> p u k n", n=F_EXP) for b in range(2)]
        dn = [ring[:, 4 + b, :].rearrange("p (f n) -> p f n", n=D) for b in range(2)]

        def flat_rows(w, e, n):
            rows_ = w.shape[1]
            return w.rearrange("e k n -> (e k) n")[bass.ds(e * rows_, rows_), :].rearrange("(k p) n -> p k n", p=P)

        def sp_expert(sp, e, b, first=False):
            if not first:
                sp.wait_ge(S("gu_used"), e - 1)
            sp.dma_start(gu[b][:, 0], flat_rows(w_gate, e, F_EXP)).then_inc(S(f"gu_loaded{b}"), 16)
            sp.dma_start(gu[b][:, 1], flat_rows(w_up, e, F_EXP)).then_inc(S(f"gu_loaded{b}"), 16)
            if not first:
                sp.wait_ge(S("dn_used"), e - 1)
            sp.dma_start(dn[b], flat_rows(w_down, e, D)).then_inc(S(f"dn_loaded{b}"), 16)

        def sp_moe_first(sp):
            sp.wait_ge(S("slots_used"), MOE_AT)
            for e in range(2):
                sp_expert(sp, e, e, first=True)

        def sp_moe(sp):
            with sp.Fori(1, N_EXP // 2) as i:
                for b in range(2):
                    sp_expert(sp, 2 * i + b, b)

        def first_place(e, expert):
            return e.value_load(r_offi[0:1, bass.ds(expert, 1)], min_val=0, max_val=SLOTS_)

        def places(x, at):
            return x[:, :, bass.ds(at, CAP)]

        def pe_gate_up(pe, dst, w, at):
            for u in range(2):
                for f in range(2):
                    c = (2 * u + f) * P
                    for k in range(KD):
                        mm = pe.matmul(dst[:, c:c + P], w[:, u, k, f * P:(f + 1) * P], m_xT[:, k, bass.ds(at, CAP)],
                                       start=(k == 0), stop=(k == KD - 1))
            return mm

        def pe_down_t(pe, dst, w, hid):
            for k in range(KD):
                for f in range(2):
                    mm = pe.matmul(dst[k // 4][:, (k % 4) * P:(k % 4 + 1) * P], w[:, f, k * P:(k + 1) * P], hid[:, f, :],
                                   start=(f == 0), stop=(f == 1))
            return mm

        def chunks(b):
            return b[:, :].rearrange("p (k s) -> p k s", s=CAP)

        def pe_moe(pe):
            def gate_up(i, b):
                at = first_place(pe, 2 * i + b)
                pe.wait_ge(S(f"gu_loaded{b}"), 32 * (i + 1))
                pe_gate_up(pe, bank[b], gu[b], at).then_inc(S("gu_used"), 1)

            def down(i, b):
                pe.wait_ge(S(f"dn_loaded{b}"), 16 * (i + 1))
                pe.wait_ge(S("m_hid"), 2 * i + b + 1)
                if not (isinstance(i, int) and i <= 0):
                    pe.wait_ge(S("m_y_act"), 2 * i + b - 1)
                    pe.wait_ge(S("m_y_dve"), 2 * i + b - 1)
                pe_down_t(pe, bank[2 + 2 * b:4 + 2 * b], dn[b], m_hid[:, b]).then_inc(S("dn_used"), 1)

            gate_up(0, 0)
            gate_up(0, 1)
            down(0, 0)
            gate_up(1, 0)
            down(0, 1)
            gate_up(1, 1)
            down(1, 0)
            with pe.Fori(2, N_EXP // 2) as i:
                gate_up(i, 0)
                down(i - 1, 1)
                gate_up(i, 1)
                down(i, 0)
            down(N_EXP // 2 - 1, 1)

        def act_moe(act):
            def silu(i, b):
                act.wait_ge(S("gu_used"), 2 * i + b + 1)
                if not (isinstance(i, int) and i == 0):
                    act.wait_ge(S("m_hid"), 2 * i + b - 1)
                act.activation(m_sg[:, b, :], bank[b][:, 0:F_EXP], ACT.Silu).then_inc(S("m_sg"), 1)

            def results(i, b):
                at = first_place(act, 2 * i + b)
                act.wait_ge(S("dn_used"), 2 * i + b + 1)
                act.activation(places(m_yT[:, 0:4, :], at), chunks(bank[2 + 2 * b]), ACT.Copy)
                act.drain().then_inc(S("m_y_act"), 1)

            silu(0, 0)
            silu(0, 1)
            results(0, 0)
            with act.Fori(1, N_EXP // 2) as i:
                silu(i, 0)
                results(i - 1, 1)
                silu(i, 1)
                results(i, 0)
            results(N_EXP // 2 - 1, 1)

        def dve_moe(dve):
            def hidden(i, b):
                dve.wait_ge(S("m_sg"), 2 * i + b + 1)
                dve.tensor_tensor(m_hid[:, b].rearrange("p f s -> p (f s)"), m_sg[:, b, :], bank[b][:, F_EXP:512],
                                  ALU.mult)
                dve.drain().then_inc(S("m_hid"), 1)

            def results(i, b):
                at = first_place(dve, 2 * i + b)
                dve.wait_ge(S("dn_used"), 2 * i + b + 1)
                dve.tensor_copy(places(m_yT[:, 4:8, :], at), chunks(bank[3 + 2 * b]))
                dve.drain().then_inc(S("m_y_dve"), 1)

            hidden(0, 0)
            hidden(0, 1)
            results(0, 0)
            with dve.Fori(1, N_EXP // 2) as i:
                hidden(i, 0)
                results(i - 1, 1)
                hidden(i, 1)
                results(i, 0)
            results(N_EXP // 2 - 1, 1)

        MORE = T // CAP - 1
        ITEMS = (2 * T - 1) // CAP
        o_gu = region(0, 4096, "p (u k n) -> p u k n", base=hflat, u=2, n=F_EXP)
        o_dn = region(4096, 2048, "p (f n) -> p f n", n=D)

        def dve_more_list(dve):
            n = MORE * N_EXP
            flag, prefix, expert, place = (region(8192 + n * i, n, "p (e q) -> p e q", q=MORE) for i in range(4))
            sel, val = (region(8704 + 768 * i, ITEMS * n, "p (i j) -> p i j", j=n) for i in range(2))
            shape = [P, ITEMS, n]

            def flat(x):
                return x.rearrange("p e q -> p (e q)")

            for q in range(MORE):
                dve.tensor_scalar(flag[:, :, q], r_cnt, float(CAP * (q + 1)), None, ALU.is_gt)
                dve.tensor_scalar(place[:, :, q], r_off, float(CAP * (q + 1)), None, ALU.add)
                dve.tensor_copy(expert[:, :, q], con("iota")[:, 0:N_EXP])
            dve.drain()
            dve.tensor_tensor_scan(flat(prefix), flat(flag), flat(flag), 0.0, ALU.add, ALU.bypass)
            dve.drain()
            dve.tensor_copy(o_count[:, 0:1], prefix[:, N_EXP - 1, MORE - 1:MORE])
            dve.tensor_tensor(sel, flat(prefix).unsqueeze(1).broadcast_to(shape),
                              con("iota")[:, 1:ITEMS + 1].unsqueeze(2).broadcast_to(shape), ALU.is_equal)
            dve.drain()
            dve.tensor_tensor(sel, sel, flat(flag).unsqueeze(1).broadcast_to(shape), ALU.mult)
            dve.drain()
            for table, dst in ((expert, o_expert), (place, o_place)):
                dve.tensor_tensor(val, sel, flat(table).unsqueeze(1).broadcast_to(shape), ALU.mult)
                dve.drain()
                dve.tensor_reduce(flat(prefix)[:, 0:ITEMS], val, AX_X, ALU.add)
                dve.drain()
                dve.tensor_copy(dst[:, 0:ITEMS], flat(prefix)[:, 0:ITEMS])
                dve.drain()
            dve.memset(m_xT[:, :, SLOTS_:SLOTS_ + CAP], 0.0)
            dve.drain().then_inc(S("r_count"), 1)

        def more(e, body):
            e.wait_ge(S("r_count"), 1)
            count = e.value_load(o_count[0:1, 0:1], min_val=0, max_val=ITEMS)
            with e.Fori(0, ITEMS) as i:
                with e.If(count > i):
                    body(i)

        def further_place(e, i):
            return e.value_load(o_place[0:1, bass.ds(i, 1)], min_val=0, max_val=SLOTS_)

        def sp_more(sp):
            nxt(sp, "h2_ready", NT)
            nxt(sp, "m_x_ps", 2 * KD)

            def body(n):
                ex = sp.value_load(o_expert[0:1, bass.ds(n, 1)], min_val=0, max_val=N_EXP - 1)
                sp.wait_ge(S("o_free"), n + 1)
                sp.dma_start(o_gu[:, 0], flat_rows(w_gate, ex, F_EXP)).then_inc(S("o_loaded"), 16)
                sp.dma_start(o_gu[:, 1], flat_rows(w_up, ex, F_EXP)).then_inc(S("o_loaded"), 16)
                sp.dma_start(o_dn, flat_rows(w_down, ex, D)).then_inc(S("o_loaded"), 16)
            more(sp, body)

        def pe_more(pe):
            pe.drain().then_inc(S("o_free"), 1)

            def body(n):
                at = further_place(pe, n)
                pe.wait_ge(S("o_loaded"), 48 * n + 48)
                pe_gate_up(pe, bank[0], o_gu, at).then_inc(S("o_gate_up"), 1)
                pe.wait_ge(S("o_hid"), n + 1)
                pe_down_t(pe, bank[2:4], o_dn, m_hid[:, 0]).then_inc(S("o_y"), 1)
                pe.wait_ge(S("o_out"), n + 1)
                pe.transpose(bank[1][:, 0:P], ident, ident).then_inc(S("o_free"), 1)
            more(pe, body)

        def act_more(act):
            def body(n):
                act.wait_ge(S("o_gate_up"), n + 1)
                act.activation(m_sg[:, 0, :], bank[0][:, 0:F_EXP], ACT.Silu).then_inc(S("o_sg"), 1)
            more(act, body)

        def dve_more(dve):
            def body(n):
                at = further_place(dve, n)
                dve.wait_ge(S("o_sg"), n + 1)
                dve.tensor_tensor(m_hid[:, 0].rearrange("p f s -> p (f s)"), m_sg[:, 0, :], bank[0][:, F_EXP:512],
                                  ALU.mult)
                dve.drain().then_inc(S("o_hid"), 1)
                dve.wait_ge(S("o_y"), n + 1)
                for half in range(2):
                    dve.tensor_copy(places(m_yT[:, 4 * half:4 * half + 4, :], at), chunks(bank[2 + half]))
                dve.drain().then_inc(S("o_out"), 1)
            more(dve, body)

        def pe_moe_end(pe):
            nxt(pe, "m_y_act", N_EXP)
            nxt(pe, "m_y_dve", N_EXP)
            for s in range(8):
                for half in range(2):
                    b = (2 * s + half) % 6
                    if 2 * s + half >= 6:
                        nxt(pe, f"m_rows{b % 2}")
                    for k in range(4):
                        mm = pe.transpose(bank[b][:, k * P:(k + 1) * P], m_yT[:, 4 * half + k, s * P:(s + 1) * P], ident)
                    mm.then_inc(S("m_y_turned"), 1)
            nxt(pe, "m_rows0", 3)
            nxt(pe, "m_rows1", 3)
            nxt(pe, "gate_taken")
            for t in range(NT):
                for half in range(2):
                    for s in range(8):
                        mm = pe.matmul(bank[2 * t + half][:, :], m_CT[:, s, t * P:(t + 1) * P],
                                       m_y[:, s, 512 * half:512 * half + 512], start=(s == 0), stop=(s == 7))
                mm.then_inc(S("m_sum_ps"), 1)

        def act_moe_end(act):
            for s in range(8):
                nxt(act, "m_y_turned", 2 if s else 1)
                act.activation(m_y[:, s, 0:512], bank[2 * s % 6][:, :], ACT.Copy).then_inc(S("m_rows0"), 1)

        def dve_moe_end(dve):
            for s in range(8):
                nxt(dve, "m_y_turned", 2)
                dve.tensor_copy(m_y[:, s, 512:D], bank[(2 * s + 1) % 6][:, :]).then_inc(S("m_rows1"), 1)
            tmp = region(19000, 2048, "p (b n) -> p b n", b=2)
            for t in range(NT):
                nxt(dve, "m_sum_ps")
                for half in range(2):
                    c = slice(512 * half, 512 * half + 512)
                    dve.tensor_tensor(tmp[:, t % 2, c], bank[2 * t + half][:, :], gate2[:, c], ALU.mult)
                dve.drain()
                dve.tensor_tensor(X[:, t, :], X[:, t, :], tmp[:, t % 2, :], ALU.add)
            dve.drain()

        NPAIRS = NFF // 2
        ROUNDS = NPAIRS // 3
        F_SLOTS = 3 * NPAIRS
        hid_hi = region(0, HID, "p (f t) -> p f t", base=split["hid_high"], t=T)
        hid_lo = region(0, HID, "p (f t) -> p f t", base=split["hid_low"], t=T)
        f_sg = region(2 * HID, 1024, "p (b t) -> p b t", b=2)
        hT_hi = region(0, KD * T, "p (k t) -> p k t", base=split["hT_high"], t=T)
        hT_lo = split["hT"]
        f_hid = region(27648, 1024, "p (b t) -> p b t", b=2)
        post = region(23552, D)
        f_tmp = region(24576, 2048, "p (b n) -> p b n", b=2)
        f_sq = region(26624, 512)
        f_ss = region(27136, 8, "p (t h) -> p t h", t=NT)
        f_r = region(27144, 8, "p (c t) -> p c t", c=2)
        xnf = region(0, 4096, "p (t n) -> p t n", n=D)
        junkf = region(4096, D)
        xn3 = region(20480, 4096, "p (t n) -> p t n", n=D)

        def raw(n):
            return ring[:, n % 3, :]

        def high(n):
            return split["ring"][:, 3 + n % 3, :]

        def low(n):
            return split["ring"][:, n % 3, :]

        def dve_split(dve, hi, x, lo):
            dve.tensor_copy(hi, x)
            dve.drain()
            return dve.tensor_tensor(lo, x, hi.bitcast(F32), ALU.subtract)

        def sp_ffn(sp, tag):
            f = FIRST[tag]
            wg, wu = a[f"{tag}_w_gate_2"][0], a[f"{tag}_w_up_2"][0]

            def load_slot(n, it, src):
                sp.dma_start(raw(n).rearrange("p (k n) -> p k n", n=src.shape[-1]),
                             src.rearrange("(k p) n -> p k n", p=P)).then_inc(S(f"{tag}_raw{n % 3}"), 16)

            sp.wait_ge(S("slots_used"), f)
            for jj in range(3):
                load_slot(jj, 0, (wg, wu)[jj % 2][:, 256 * (jj // 2):256 * (jj // 2) + 256])
            for jj in range(3, 6):
                sp.wait_ge(S("slots_used"), f + jj - 2)
                load_slot(jj, 0, (wg, wu)[jj % 2][:, 256 * (jj // 2):256 * (jj // 2) + 256])
            with sp.Fori(1, ROUNDS) as it:
                for jj in range(6):
                    sp.wait_ge(S("slots_used"), 6 * it + (f + jj - 2))
                    load_slot(jj, it, (wg, wu)[jj % 2][:, bass.ds(768 * it + 256 * (jj // 2), 256)])
            for n in range(6 * ROUNDS, F_SLOTS):
                sp.wait_ge(S("slots_used"), f + n - 2)
                if n < 2 * NPAIRS:
                    load_slot(n, 0, (wg, wu)[n % 2][:, 256 * (n // 2):256 * (n // 2) + 256])
                else:
                    r = 256 * (n - 2 * NPAIRS)
                    load_slot(n, 0, a[f"{tag}_w_down_2"][0][r:r + 256, :])

        def act_high(act, tag, n, it=0):
            act.wait_ge(S(f"{tag}_raw{n % 3}"), 32 * it + 16 * (n // 3 + 1))
            act.activation(high(n), raw(n), ACT.Copy).then_inc(S(f"{tag}_high"), 1)

        def pool_ffn(pool, tag):
            def one(n, it=0):
                pool.wait_ge(S(f"{tag}_high"), 6 * it + n + 1)
                pool.tensor_tensor(low(n), raw(n), high(n).bitcast(F32), ALU.subtract)\
                    .then_inc(S(f"{tag}_low"), 1)

            with pool.Fori(0, ROUNDS) as it:
                for n in range(6):
                    one(n, it)
            for n in range(6 * ROUNDS, F_SLOTS):
                one(n)

        def three(pe, dst, left, right, start, stop):
            for n, (l, r) in enumerate(((0, 0), (0, 1), (1, 0))):
                mm = pe.matmul(dst, left[l], right[r], start=start and n == 0, stop=stop and n == 2)
            return mm

        def pe_ffn(pe, tag):
            f = FIRST[tag]

            def parts(n, cols):
                return [x.rearrange("p (k n) -> p k n", n=cols) for x in (high(n), low(n))]

            def pair(pp, it):
                for which in range(2):
                    n = 2 * pp + which
                    pe.wait_ge(S(f"{tag}_low"), 6 * it + (n + 1))
                    w = parts(n, 256)
                    for j in range(2):
                        if which == 0:
                            pe.wait_ge(S(f"{tag}_free"), 6 * it + (2 * pp + j + 1) + before(f"{tag}_free"))
                        b = bank[2 * ((2 * pp + j) % 3) + which]
                        for k in range(KD):
                            mm = three(pe, b[:, :], [x[:, k, j * P:(j + 1) * P] for x in w],
                                       (hT_hi[:, k, :], hT_lo[:, k, :]), k == 0, k == KD - 1)
                        if j == 1:
                            mm.then_inc(S("slots_used"), 1)
                        elif which == 1:
                            mm.then_inc(S(f"{tag}_gu"), 1)

            with pe.Fori(0, ROUNDS) as it:
                for pp in range(3):
                    pair(pp, it)
            for pp in range(NPAIRS - 3 * ROUNDS):
                pair(pp, ROUNDS)
            pe.wait_ge(S(f"{tag}_free"), NFF + 3 + before(f"{tag}_free"))
            for i in range(NPAIRS):
                n = 2 * NPAIRS + i
                pe.wait_ge(S(f"{tag}_low"), n + 1)
                w = parts(n, D)
                for kk_ in range(2):
                    k = 2 * i + kk_
                    for t in range(NT):
                        for half in range(2):
                            c, r = slice(t * P, (t + 1) * P), slice(512 * half, 512 * half + 512)
                            mm = three(pe, bank[2 * t + half][:, :], (hid_hi[:, k, c], hid_lo[:, k, c]),
                                       [x[:, kk_, r] for x in w], k == 0, k == NFF - 1)
                mm.then_inc(S("slots_used"), 1)

        def act_ffn(act, tag):
            f = FIRST[tag]

            def unit(u, it):
                if u % 2 == 0:
                    act.wait_ge(S(f"{tag}_gu"), 3 * it + (u // 2 + 1) + before(f"{tag}_gu"))
                else:
                    act.wait_ge(S("slots_used"), 6 * it + (f + u + 1))
                act.wait_ge(S(f"{tag}_free"), 6 * it + (u + 2) + before(f"{tag}_free"))
                act.activation(f_sg[:, u % 2, :], bank[2 * (u % 3)][:, :], ACT.Silu).then_inc(S(f"{tag}_sg"), 1)

            def pair(pp, it):
                for n in (2 * pp + 2, 2 * pp + 3):
                    act_high(act, tag, n, it)
                for u in (2 * pp, 2 * pp + 1):
                    unit(u, it)

            act_high(act, tag, 0)
            act_high(act, tag, 1)
            with act.Fori(0, ROUNDS) as it:
                for pp in range(3):
                    pair(pp, it)
            for pp in range(NPAIRS - 3 * ROUNDS):
                pair(pp, ROUNDS)
            for n in range(2 * NPAIRS + 2, F_SLOTS):
                act_high(act, tag, n)

        def dve_ffn(dve, tag):
            dve.drain().then_inc(S(f"{tag}_free"), 3)

            def unit(u, it):
                dve.wait_ge(S(f"{tag}_sg"), 6 * it + (u + 1) + before(f"{tag}_sg"))
                hid = f_hid[:, u % 2, :]
                dve.tensor_tensor(hid, f_sg[:, u % 2, :], bank[2 * (u % 3) + 1][:, :], ALU.mult)
                dve.drain()
                at = [x[:, bass.ds(6 * it + u, 1), :].rearrange("p f t -> p (f t)") for x in (hid_hi, hid_lo)]
                dve.tensor_copy(at[0], hid)
                dve.drain()
                dve.tensor_tensor(at[1], hid, at[0].bitcast(F32), ALU.subtract).then_inc(S(f"{tag}_free"), 1)
                dve.drain()

            with dve.Fori(0, ROUNDS) as it:
                for u in range(6):
                    unit(u, it)
            for u in range(NFF - 6 * ROUNDS):
                unit(u, ROUNDS)

        def act_gain(act, name, after=None):
            if after is not None:
                act.wait_ge(S("slots_used"), after)
            act.dma_start(post, a[name][0:1, :].broadcast_to([P, D])).then_inc(S("post_loaded"), 16)

        def act_post(act, last):
            act.wait_ge(S("slots_used"), last)
            for t in range(NT):
                for half in range(2):
                    act.activation(f_sq, bank[2 * t + half][:, :], ACT.Square, accum_out=f_ss[:, t, half:half + 1])
                    act.drain()
            act.drain().then_inc(S("f_squares"), 1)
            nxt(act, "f_ss")
            act.activation(f_r[:, 1, :], f_r[:, 0, :], ACT.Sqrt, bias=eps, scale=1.0 / D).then_inc(S("f_root"), 1)

        def dve_post(dve, factor):
            nxt(dve, "f_squares")
            dve.tensor_tensor(f_r[:, 0, :], f_ss[:, :, 0], f_ss[:, :, 1], ALU.add).then_inc(S("f_ss"), 1)
            nxt(dve, "f_root")
            dve.reciprocal(f_r[:, 0, :], f_r[:, 1, :])
            dve.drain()
            if factor != 1.0:
                dve.tensor_scalar(f_r[:, 0, :], f_r[:, 0, :], factor, None, ALU.mult)
            nxt(dve, "post_loaded", 16)
            dve.drain()
            for t in range(NT):
                for half in range(2):
                    c = slice(512 * half, 512 * half + 512)
                    dve.scalar_tensor_tensor(f_tmp[:, t % 2, c], bank[2 * t + half][:, :], f_r[:, 0, t:t + 1],
                                             post[:, c], ALU.mult, ALU.mult)
                dve.drain()
                dve.tensor_tensor(X[:, t, :], X[:, t, :], f_tmp[:, t % 2, :], ALU.add)
                if t == NT - 1:
                    dve.drain()

        d_q, d_k, d_v = ([region(6144 * g + 2048 * i, 2048, "p (h t) -> p h t", t=512) for g in range(3)]
                         for i in range(3))
        REC = 4 * HD2 + 8
        comb = [region(18432 + 2080 * g, 2080, "p (t n) -> p t n", t=NT) for g in range(3)]
        tables = [region(24672, 1024, "p (h k) -> p h k", h=4), region(25696, 512, "p (h k) -> p h k", h=4),
                  region(26208, 512, "p (h k) -> p h k", h=4)]
        Pd = region(26720, 1024, "p (b n) -> p b n", b=2)
        PdT = region(27744, 1024, "p (b n) -> p b n", b=2)
        rec = region(28768, 2 * REC, "p (b n) -> p b n", b=2)
        d_nmx = region(29808, 64)
        phase16 = Pd[:, 0, 0:P]
        BIAS = ((2 * P, 0, 3 * P), (P, P, 2 * P), (P, P, 2 * P))
        brow_dram = [nc.dram_tensor(f"bias_rows{g}", (4, P, BIAS[g][2]), F32, kind="Internal").ap() for g in range(3)]
        rec_dram = nc.dram_tensor("attention_rows", (2, T, REC), F32, kind="Internal").ap()
        buckets = region(2048, 1536)
        btab = region(3584, 12)
        brow = region(4096, 1536, "p (g j) -> p g j", g=3)

        def sp_bias(sp):
            at, _ = WHERE["bucket0"]
            sp.dma_start(buckets[0:33, :], const_dram[0:33, at:at + 1536]).then_inc(S("buckets_loaded"), 16)
            sp.dma_start(btab[0:32, :], a["rel_bias_table_2"]).then_inc(S("buckets_loaded"), 16)

        def dve_bias(dve):
            dve.memset(btab[32:33, :], 1.0).then_inc(S("btab_ones"), 1)
            nxt(dve, "brow_ps")
            for g in range(3):
                dve.tensor_copy(brow[0:12, g, :], bank[2 + g][0:12, :])
            dve.drain().then_inc(S("brow_ready"), 1)

        def pe_bias(pe):
            nxt(pe, "buckets_loaded", 32)
            nxt(pe, "btab_ones")
            for g in range(3):
                mm = pe.matmul(bank[2 + g][0:12, :], btab[0:33, :], buckets[0:33, 512 * g:512 * g + 512],
                               start=True, stop=True)
            mm.then_inc(S("brow_ps"), 1)

        def sp_bias_store(sp):
            nxt(sp, "brow_ready")
            for g, (w, lo, n) in enumerate(BIAS):
                sp.dma_start(brow_dram[g], brow[4 * g:4 * g + 4, g, lo:lo + n].unsqueeze(1).broadcast_to([4, P, n]))\
                  .then_inc(S("brow_stored"), 16)

        def act_tables(act):
            nxt(act, "brow_stored", 48)
            for g, (w, lo, n) in enumerate(BIAS):
                src = bass.AP(brow_dram[g].tensor, P - 1, [[n - 1, P], [P * n, 4], [1, w]])
                act.dma_start(tables[g], src).then_inc(S("tables_loaded"), 16)
            at, n = WHERE["phase16"]
            act.dma_start(phase16, const_dram[:, at:at + n]).then_inc(S("tables_loaded"), 16)

        def dve_tables(dve):
            nxt(dve, "tables_loaded", 64)
            dve.tensor_tensor(tables[2], tables[2], phase16.unsqueeze(1).broadcast_to([P, 4, P]), ALU.add)
            dve.drain()

        def phased(x, dil):
            return x.rearrange("p (l d) -> p d l", d=dil)

        hT16 = region(18432, KD * T, "p (k t) -> p k t", t=T)

        def pool_proj2(pool):
            nxt(pool, "hT_even", 5)
            nxt(pool, "hT_odd", 5)
            for k in range(KD):
                pool.tensor_copy(hT16[:, k, :].rearrange("p (d l) -> p d l", d=DILATIONS[2]),
                                 phased(hT[:, k, :], DILATIONS[2]))
            pool.drain().then_inc(S("hT_phased"), 1)

        def pe_proj2(pe):
            pe_hT(pe)
            for g, dil in enumerate(DILATIONS):
                for name in ("q", "k"):
                    for i in range(2):
                        s = FIRST[f"{name}{g}"] + i
                        need(pe, s)
                        w = slot_view(s, 256)
                        for j in range(2):
                            if not (g == 0 and name == "q" and i == 0):
                                nxt(pe, f"d_taken{j}")
                            for k in range(KD):
                                mm = pe.matmul(bank[j][:, :], w[:, k, j * P:(j + 1) * P], hT[:, k, :],
                                               start=(k == 0), stop=(k == KD - 1))
                            if j == 0:
                                mm.then_inc(S("d_ps0"), 1)
                        mm.then_inc(S("slots_used"), 1)
                if g:
                    nxt(pe, "d_v_taken")
                if g == 2:
                    nxt(pe, "hT_phased")

                def places(k, i, dil=dil):
                    if dil == 1:
                        return tokens(k, i)
                    if dil == DILATIONS[1]:
                        return phased(hT[:, k, :], dil)[:, i, :]
                    return hT16[:, k, i * P:(i + 1) * P]

                pe_gemm_n(pe, FIRST[f"v{g}"], places, bank[2:6])

        def unphased(x, dil):
            return x.rearrange("p (d l) -> p l d", d=dil)

        def act_proj2(act):
            for g, dil in enumerate(DILATIONS):
                for dst in (d_q[g], d_k[g]):
                    for i in range(2):
                        nxt(act, "d_ps0")
                        act.activation(unphased(dst[:, 2 * i, :], dil),
                                       bank[0][:, :].rearrange("p (l d) -> p l d", d=dil), ACT.Copy)\
                           .then_inc(S("d_taken0"), 1)

        def dve_proj2(dve):
            for g, dil in enumerate(DILATIONS):
                for name, dst in (("q", d_q[g]), ("k", d_k[g])):
                    for i in range(2):
                        dve.wait_ge(S("slots_used"), FIRST[f"{name}{g}"] + i + 1)
                        dve.tensor_copy(unphased(dst[:, 2 * i + 1, :], dil),
                                        bank[1][:, :].rearrange("p (l d) -> p l d", d=dil))\
                           .then_inc(S("d_taken1"), 1)
                dve.wait_ge(S("slots_used"), FIRST[f"v{g}"] + 2)
                for t in range(NT):
                    i = dve.tensor_copy(d_v[g][:, t, :], bank[2 + t][:, :])
                i.then_inc(S("d_v_taken"), 1)

        DUNITS = [(0, n, hs, max(n - 1, 0), P if n == 0 else 2 * P) for n in range(NT) for hs in ((0, 1), (2, 3))]
        DUNITS += [(g, i, (0, 1, 2, 3), i, P) for g in (1, 2) for i in range(NT)]

        def record(u):
            g, i, hs, k0, w = DUNITS[u]
            return comb[0][:, i, :] if g == 0 else rec[:, u % 2, :]

        def pe_dil(pe):
            def scores(u):
                g, i, hs, k0, w = DUNITS[u]
                if u >= 2:
                    nxt(pe, "d_s_taken")
                for n, h in enumerate(hs):
                    mm = pe.matmul(bank[u % 2][:, n * w:(n + 1) * w], d_q[g][:, h, i * P:(i + 1) * P],
                                   d_k[g][:, h, k0 * P:k0 * P + w], start=True, stop=True)
                mm.then_inc(S("d_scores"), 1)

            def turn(u):
                g, i, hs, k0, w = DUNITS[u]
                nxt(pe, "d_p")
                for n in range(len(hs) * w // P):
                    mm = pe.transpose(bank[2 + u % 2][:, n * P:(n + 1) * P], Pd[:, u % 2, n * P:(n + 1) * P], ident)
                mm.then_inc(S("d_p_turned"), 1)

            def values(u):
                g, i, hs, k0, w = DUNITS[u]
                nxt(pe, "d_pT")
                if u >= 2:
                    nxt(pe, "d_o_taken")
                nb = w // P
                for n, h in enumerate(hs):
                    for b in range(nb):
                        c = (n * nb + b) * P
                        mm = pe.matmul(bank[4 + u % 2][:, n * HD2:(n + 1) * HD2], PdT[:, u % 2, c:c + P],
                                       d_v[g][:, k0 + b, h * HD2:(h + 1) * HD2], start=(b == 0), stop=(b == nb - 1))
                mm.then_inc(S("d_values"), 1)

            scores(0)
            for u in range(len(DUNITS)):
                if u + 1 < len(DUNITS):
                    scores(u + 1)
                turn(u)
                if u:
                    values(u - 1)
            values(len(DUNITS) - 1)

        def dve_dil(dve):
            def outputs(u):
                g, i, hs, k0, w = DUNITS[u]
                nxt(dve, "d_values")
                dve.tensor_copy(record(u)[:, hs[0] * HD2:(hs[-1] + 1) * HD2], bank[4 + u % 2][:, 0:len(hs) * HD2])
                dve.drain().then_inc(S("d_o_taken"), 1)

            for u, (g, i, hs, k0, w) in enumerate(DUNITS):
                nh = len(hs)
                nxt(dve, "d_scores")
                if u >= 2:
                    nxt(dve, "d_p_turned")
                p3 = Pd[:, u % 2, 0:nh * w].rearrange("p (h k) -> p h k", h=nh)
                tab = tables[g][:, hs[0]:hs[-1] + 1, :]
                tab = tab[:, :, 2 * P - w:2 * P] if g == 0 else tab
                dve.scalar_tensor_tensor(p3, bank[u % 2][:, 0:nh * w].rearrange("p (h k) -> p h k", h=nh),
                                         HD2 ** -0.5, tab, ALU.mult, ALU.add).then_inc(S("d_s_taken"), 1)
                dve.drain()
                if g and u >= 10:
                    n_st = 1 if DUNITS[u - 2][0] == 1 else 4
                    nxt(dve, f"rec_stored{u % 2}", 16 * n_st)
                mx = record(u)[:, 512 + hs[0]:512 + hs[-1] + 1]
                dve.tensor_reduce(mx, p3, AX_X, ALU.max)
                dve.drain()
                dve.tensor_scalar(d_nmx[:, 4 * u:4 * u + nh], mx, -1.0, None, ALU.mult).then_inc(S("d_max"), 1)
                if u:
                    outputs(u - 1)
            outputs(len(DUNITS) - 1)

        def act_dil(act):
            def exps(u):
                g, i, hs, k0, w = DUNITS[u]
                nxt(act, "d_max")
                for n, h in enumerate(hs):
                    p = Pd[:, u % 2, n * w:(n + 1) * w]
                    act.activation(p, p, ACT.Exp, bias=d_nmx[:, 4 * u + n:4 * u + n + 1],
                                   accum_out=record(u)[:, 516 + h:517 + h])
                act.drain().then_inc(S("d_p"), 1)

            def copy(u):
                g, i, hs, k0, w = DUNITS[u]
                n = len(hs) * w
                nxt(act, "d_p_turned")
                if u >= 2:
                    nxt(act, "d_values")
                act.activation(PdT[:, u % 2, 0:n], bank[2 + u % 2][:, 0:n], ACT.Copy)
                act.drain().then_inc(S("d_pT"), 1)

            exps(0)
            for u in range(len(DUNITS)):
                if u + 1 < len(DUNITS):
                    exps(u + 1)
                copy(u)

        def pool_dil(pool):
            for u, (g, i, hs, k0, w) in enumerate(DUNITS):
                if g == 0:
                    continue
                pool.wait_ge(S("d_o_taken"), u + 1 + before("d_o_taken"))
                pool.wait_ge(S("d_p"), u + 1 + before("d_p"))
                rows_ = rec_dram[g - 1].rearrange("(l d) c -> d l c", d=DILATIONS[g])
                if g == 1:
                    pool.dma_start(rows_[i], rec[:, u % 2, :]).then_inc(S(f"rec_stored{u % 2}"), 16)
                else:
                    for q in range(4):
                        pool.dma_start(rows_[4 * i + q], rec[32 * q:32 * q + 32, u % 2, :])\
                            .then_inc(S(f"rec_stored{u % 2}"), 16)
            for b in range(2):
                pool.wait_ge(S(f"rec_stored{b}"), 16 * (2 + 8) + before(f"rec_stored{b}"))
            for g in (1, 2):
                pool.dma_start(comb[g], rec_dram[g - 1].rearrange("(t p) c -> p t c", p=P))\
                    .then_inc(S("rec_loaded"), 16)

        c_m = region(4096, 16, "p (t h) -> p t h", t=NT)
        c_e = [region(4112 + 16 * g, 16, "p (t h) -> p t h", t=NT) for g in range(3)]
        c_x = [region(4160 + 16 * g, 16, "p (t h) -> p t h", t=NT) for g in range(3)]
        c_s = region(4208, 16, "p (t h) -> p t h", t=NT)
        attn = region(0, 2048, "p (t n) -> p t n", t=NT)
        attnT2 = region(2048, 2048, "p (k t) -> p k t", t=T)

        def dve_combine(dve):
            nxt(dve, "rec_loaded", 32)
            mx = [comb[g][:, :, 512:516] for g in range(3)]
            den = [comb[g][:, :, 516:520] for g in range(3)]
            dve.tensor_tensor(c_m, mx[0], mx[1], ALU.max)
            dve.drain()
            dve.tensor_tensor(c_m, c_m, mx[2], ALU.max)
            dve.drain()
            for g in range(3):
                dve.tensor_tensor(c_e[g], mx[g], c_m, ALU.subtract)
            dve.drain().then_inc(S("c_diff"), 1)
            nxt(dve, "c_exp")
            for g in range(3):
                dve.tensor_tensor(c_x[g], c_e[g], den[g], ALU.mult)
            dve.drain()
            dve.tensor_tensor(c_s, c_x[0], c_x[1], ALU.add)
            dve.drain()
            dve.tensor_tensor(c_s, c_s, c_x[2], ALU.add)
            dve.drain()
            dve.reciprocal(c_m, c_s)
            dve.drain()
            for g in range(3):
                dve.tensor_tensor(c_e[g], c_e[g], c_m, ALU.mult)
            dve.drain()
            for g in range(3):
                for t in range(NT):
                    o = comb[g][:, t, 0:512].rearrange("p (h e) -> p h e", h=4)
                    dve.tensor_tensor(o, o, c_e[g][:, t, :].unsqueeze(2).broadcast_to([P, 4, HD2]), ALU.mult)
            dve.drain()
            dve.tensor_tensor(attn, comb[0][:, :, 0:512], comb[1][:, :, 0:512], ALU.add)
            dve.drain()
            dve.tensor_tensor(attn, attn, comb[2][:, :, 0:512], ALU.add)
            dve.drain().then_inc(S("attn_ready"), 1)

        def act_combine(act):
            nxt(act, "c_diff")
            for g in range(3):
                act.activation(c_e[g], c_e[g], ACT.Exp)
            act.drain().then_inc(S("c_exp"), 1)
            nxt(act, "attn_turned")
            for k in range(4):
                act.activation(attnT2[:, k, :], bank[k][:, :], ACT.Copy)
            act.drain().then_inc(S("attnT_ready"), 1)

        def pe_combine(pe):
            nxt(pe, "attn_ready")
            for k in range(4):
                for t in range(NT):
                    mm = pe.transpose(bank[k][:, t * P:(t + 1) * P], attn[:, t, k * P:(k + 1) * P], ident)
            mm.then_inc(S("attn_turned"), 1)

        l_in = region(4096, 1040, "p (b t) -> p b t", b=2)
        l_xc, l_gx, l_t, l_q, l_r, l_gy = (region(5200 + 4100 * i, 4096, "p (m t) -> p m t", t=T) for i in range(6))
        l_c = region(29800, 8)
        l_e, l_z, l_p, l_s = (region(29808 + 8 * i, 8) for i in range(4))
        merged = l_q
        s_gate = l_xc[:, 0:4, :]
        s_val = l_xc[:, 4:8, :]

        def col2(name, i):
            at, _ = col(name, VEC2)
            return cols2[:, at + i:at + i + 1]

        def pe_lru(pe):
            for m in range(KD):
                i, j = m // 2, m % 2
                s = FIRST["xr"] + i
                if j == 0:
                    need(pe, s)
                if m >= 2:
                    nxt(pe, "l_in")
                for k in range(KD):
                    mm = pe.matmul(bank[j][:, :], slot_view(s, 256)[:, k, j * P:(j + 1) * P], hT[:, k, :],
                                   start=(k == 0), stop=(k == KD - 1))
                if j == 0:
                    mm.then_inc(S("l_ps"), 1)
                else:
                    mm.then_inc(S("slots_used"), 1)
            nxt(pe, "l_in", 2)
            need(pe, FIRST["lru"])
            need(pe, FIRST["lru"] + 1)
            for m in range(KD):
                h, j = m // 2, m % 2
                pe.wait_ge(S("l_conv"), 2 * h + 2 + before("l_conv"))
                if m >= 2:
                    nxt(pe, "l_gates")
                for which in range(2):
                    w = slot_view(FIRST["lru"] + which, 256)
                    for i in range(2):
                        mm = pe.matmul(bank[2 + 2 * j + which][:, :], w[:, 2 * h + i, j * P:(j + 1) * P],
                                       l_xc[:, 2 * h + i, :], start=(i == 0), stop=(i == 1))
                    if which == 0 and m == KD - 1:
                        mm.then_inc(S("slots_used"), 1)
                if m < KD - 1:
                    mm.then_inc(S("l_gate_ps"), 1)
                else:
                    mm.then_inc(S("slots_used"), 1)
            for m in range(KD):
                i, j = m // 2, m % 2
                s = FIRST["yr"] + i
                if j == 0:
                    need(pe, s)
                if m >= 2:
                    nxt(pe, "l_gelu")
                for k in range(KD):
                    mm = pe.matmul(bank[6 + j][:, :], slot_view(s, 256)[:, k, j * P:(j + 1) * P], hT[:, k, :],
                                   start=(k == 0), stop=(k == KD - 1))
                if j == 0:
                    mm.then_inc(S("l_y_ps"), 1)
                else:
                    mm.then_inc(S("slots_used"), 1)

        def act_lru(act):
            nxt(act, "l_abs")
            act.activation(l_e, l_z, ACT.Exp, scale=-1.0).then_inc(S("l_exp"), 1)
            for m in range(KD):
                j = m % 2
                if j == 0:
                    nxt(act, "l_ps")
                else:
                    act.wait_ge(S("slots_used"), FIRST["xr"] + m // 2 + 1)
                if m >= 2:
                    act.wait_ge(S("l_conv"), m - 1 + before("l_conv"))
                act.activation(l_in[:, j, 3:3 + T], bank[j][:, :], ACT.Copy).then_inc(S("l_in"), 1)
            nxt(act, "l_c")
            for m in range(KD):
                j = m % 2
                if m < KD - 1:
                    nxt(act, "l_gate_ps")
                else:
                    act.wait_ge(S("slots_used"), FIRST["lru"] + 2)
                act.activation(l_gx[:, m, :], bank[2 + 2 * j][:, :], ACT.Sigmoid, bias=col2("lru_b_x_2", m))
                act.activation(l_t[:, m, :], bank[3 + 2 * j][:, :], ACT.Sigmoid, bias=col2("lru_b_a_2", m))
                act.drain().then_inc(S("l_gates"), 1)
                act.activation(l_t[:, m, :], l_t[:, m, :], ACT.Tanh, scale=l_c[:, m:m + 1])
            act.drain().then_inc(S("l_tanh"), 1)
            nxt(act, "l_floor")
            for m in range(KD):
                act.activation(l_q[:, m, :], l_t[:, m, :], ACT.Sqrt).then_inc(S("l_sqrt"), 1)
            for m in range(KD):
                j = m % 2
                if j == 0:
                    nxt(act, "l_y_ps")
                else:
                    act.wait_ge(S("slots_used"), FIRST["yr"] + m // 2 + 1)
                act.activation(l_gy[:, m, :], bank[6 + j][:, :], ACT.Gelu_apprx_tanh).then_inc(S("l_gelu"), 1)

        def dve_lru(dve):
            at, _ = col("lru_a_param_2", VEC2)
            ap_ = cols2[:, at:at + 8]
            dve.memset(l_in[:, :, 0:3], 0.0)
            dve.scalar_tensor_tensor(l_z, ap_, -1.0, ap_, ALU.mult, ALU.max).then_inc(S("l_abs"), 1)
            nxt(dve, "l_exp")
            dve_log1p(dve, l_e, l_z, l_p, l_s)
            dve.tensor_scalar(l_z, ap_, -1.0, 0.0, ALU.mult, ALU.max)
            dve.drain()
            dve.tensor_tensor(l_s, l_z, l_s, ALU.add)
            dve.drain()
            dve.tensor_scalar(l_c, l_s, 4.0, None, ALU.mult)
            dve.drain().then_inc(S("l_c"), 1)
            for m in range(KD):
                j = m % 2
                dve.wait_ge(S("l_in"), m + 1 + before("l_in"))
                dve.tensor_scalar(l_xc[:, m, :], l_in[:, j, 3:3 + T], col2("conv_w_2", 24 + m),
                                  col2("conv_b_2", m), ALU.mult, ALU.add)
                for tap in range(3):
                    dve.drain()
                    dve.scalar_tensor_tensor(l_xc[:, m, :], l_in[:, j, tap:tap + T], col2("conv_w_2", 8 * tap + m),
                                             l_xc[:, m, :], ALU.mult, ALU.add)
                dve.drain().then_inc(S("l_conv"), 1)
            nxt(dve, "l_tanh")
            dve.tensor_scalar(l_t, l_t, 1.0e-30, None, ALU.max)
            dve.drain().then_inc(S("l_floor"), 1)
            dve.tensor_scalar(l_r, l_t, -1.0, -1.0, ALU.mult, ALU.add)
            dve.drain()
            for m in range(KD):
                dve.reciprocal(l_r[:, m, :], l_r[:, m, :])
                dve.tensor_tensor(l_gx[:, m, :], l_gx[:, m, :], l_xc[:, m, :], ALU.mult)
                dve.drain()
                nxt(dve, "l_sqrt")
                dve.scalar_tensor_tensor(l_t[:, m, :], l_t[:, m, :], -1.0, l_r[:, m, :], ALU.add, ALU.mult)
                dve.scalar_tensor_tensor(l_q[:, m, :], l_r[:, m, :], -2.0, l_q[:, m, :], ALU.mult, ALU.mult)
                dve.drain()
                dve.tensor_tensor(l_q[:, m, :], l_q[:, m, :], l_gx[:, m, :], ALU.mult)
                dve.drain()
                dve.tensor_tensor_scan(l_r[:, m, :], l_t[:, m, :], l_q[:, m, :], 0.0, ALU.mult, ALU.add)
                dve.drain()
            for m in range(KD):
                nxt(dve, "l_gelu")
                dve.tensor_tensor(l_r[:, m, :], l_r[:, m, :], l_gy[:, m, :], ALU.mult)
            dve.drain().then_inc(S("rec_ready"), 1)

        def pe_merge(pe):
            nxt(pe, "attnT_ready")
            nxt(pe, "rec_ready")
            for m in range(KD):
                q, j = m // 2, m % 2
                base = 4 * j
                if m >= 2:
                    nxt(pe, "m_merged")
                parts = [(FIRST[f"gl{q}"], hT, KD), (FIRST[f"gl{q}"] + 1, hT, KD), (FIRST[f"attn{q}"], attnT2, 4),
                         (FIRST[f"rec{q}"], l_r, KD)]
                for b, (s, rhs, nk) in enumerate(parts):
                    if j == 0:
                        need(pe, s)
                    w = ring[:, turn_of(s) % RING, 0:nk * 256].rearrange("p (k n) -> p k n", n=256)
                    for k in range(nk):
                        mm = pe.matmul(bank[base + b][:, :], w[:, k, j * P:(j + 1) * P], rhs[:, k, :],
                                       start=(k == 0), stop=(k == nk - 1))
                    if j == 1:
                        mm.then_inc(S("slots_used"), 1)
                    elif b in (1, 3):
                        mm.then_inc(S("m_even_ps"), 1)

        def act_merge(act):
            for m in range(KD):
                q, j = m // 2, m % 2
                if j == 0:
                    act.wait_ge(S("m_even_ps"), m + 1 + before("m_even_ps"))
                else:
                    act.wait_ge(S("slots_used"), FIRST[f"gl{q}"] + 2)
                if m >= 2:
                    act.wait_ge(S("m_merged"), m - 1 + before("m_merged"))
                for b in range(2):
                    act.activation(s_gate[:, 2 * j + b, :], bank[4 * j + b][:, :], ACT.Sigmoid)
                act.drain().then_inc(S("m_sigmoids"), 1)

        def dve_merge(dve):
            for m in range(KD):
                q, j = m // 2, m % 2
                nxt(dve, "m_sigmoids")
                if j == 0:
                    dve.wait_ge(S("m_even_ps"), m + 2 + before("m_even_ps"))
                else:
                    dve.wait_ge(S("slots_used"), FIRST[f"rec{q}"] + 1)
                for b in range(2):
                    dve.tensor_tensor(s_val[:, 2 * j + b, :], s_gate[:, 2 * j + b, :], bank[4 * j + 2 + b][:, :],
                                      ALU.mult)
                dve.drain()
                dve.tensor_tensor(merged[:, m, :], s_val[:, 2 * j, :], s_val[:, 2 * j + 1, :], ALU.add)
                dve.drain().then_inc(S("m_merged"), 1)

        def sp_out(sp):
            nxt(sp, "x_final")
            for t in range(NT):
                sp.dma_start(out[t * P:(t + 1) * P, :], X[:, t, :]).then_inc(S("out_stored"), 16)
            sp.wait_ge(S("out_stored"), 16 * NT)

        block = ctx.enter_context(nc.Block())

        def c1(i):
            return mod[:, i:i + 8]

        def gain2(name):
            at, n = col(name, VEC2)
            return cols2[:, at:at + n]

        @block.sync
        def _(sp):
            sp_small(sp)
            sp_bias(sp)
            load(sp, 0, 8)
            sp_bias_store(sp)
            load(sp, 8, FIRST["ada2"] - 8)
            sp_positions(sp)
            load(sp, FIRST["ada2"], MOE_AT - FIRST["ada2"])
            sp_moe_first(sp)
            sp_more(sp)
            sp_moe(sp)
            sp.wait_ge(S("gu_used"), N_EXP)
            sp.wait_ge(S("dn_used"), N_EXP)
            sp_ffn(sp, "ffn1")
            load(sp, FIRST["q0"], FIRST["ffn2"] - FIRST["q0"])
            sp_ffn(sp, "ffn2")
            sp_out(sp)

        @block.scalar
        def _(act):
            act_small(act)
            act_c(act)
            nxt(act, "x_loaded", 16 * NT)
            nxt(act, "mod_ready")
            act_norm(act, junk1, c1(8), c1(0))
            act_proj1(act)
            act_qkv(act)
            meet(act)
            act_swa_prep(act)
            act_swa_turn(act)
            act_swa(act)
            meet(act)
            act_gdn_prep(act)
            for t in range(NT):
                act_gdn(act, t)
            act_gdn_end(act)
            act_turned(act)
            meet(act)
            act_router_weights(act)
            nxt(act, "mod_ready")
            act_norm(act, junk2, c1(32), c1(24))
            act_h2(act)
            act_route(act)
            act_more(act)
            act_moe(act)
            act_moe_end(act)
            meet(act)
            act_norm(act, junkf, gain2("ffn1_norm_pre_2"), None, hT_hi)
            act_ffn(act, "ffn1")
            act_gain(act, "ffn1_norm_post_2", FIRST["ffn1"] + 2 * NPAIRS)
            act_post(act, FIRST["ffn1_down"] + NPAIRS)
            meet(act)
            act_tables(act)
            act_norm(act, region(0, D), gain2("mix_norm_pre_2"), None)
            act_proj2(act)
            meet(act)
            act_dil(act)
            meet(act)
            act_combine(act)
            meet(act)
            act_lru(act)
            act_merge(act)
            meet(act)
            act_gain(act, "mix_norm_post_2")
            act_post(act, FIRST["w_out2"] + 4)
            meet(act)
            act_norm(act, junkf, gain2("ffn2_norm_pre_2"), None, hT_hi)
            act_ffn(act, "ffn2")
            act_gain(act, "ffn2_norm_post_2", FIRST["ffn2"] + 2 * NPAIRS)
            act_post(act, FIRST["ffn2_down"] + NPAIRS)

        @block.tensor
        def _(pe):
            pe_small(pe)
            pe_bias(pe)
            pe_ada(pe, "ada1", 0, 16, 7)
            pe_turn(pe, xn1, ("xn_ready",))
            pe_hT(pe)
            pe_proj1(pe)
            pe_qkv(pe)
            pe_ada(pe, "ada2", 16, 48, 7)
            meet(pe)
            pe_swa_turn(pe)
            pe_swa(pe)
            meet(pe)
            pe_gdn_prep(pe)
            for t in range(NT):
                pe_gdn(pe, t)
            pe_gate(pe, diag1, 0)
            nxt(pe, "gate_taken")
            pe_turn(pe, mixed, ("mixed_ready",))
            pe_hT(pe)
            pe_down(pe, "w_out", 4, tokens)
            meet(pe)
            pe_turn(pe, xn2, ("xn_ready",))
            pe_route(pe)
            pe_gate(pe, diag2, 6)
            pe_more(pe)
            pe_moe(pe)
            pe_moe_end(pe)
            meet(pe)
            pe_turn(pe, xnf, ("xn_ready",))
            pe_hT(pe)
            pe_ffn(pe, "ffn1")
            meet(pe)
            pe_turn(pe, xn3, ("xn_ready",))
            pe_proj2(pe)
            meet(pe)
            pe_dil(pe)
            meet(pe)
            pe_combine(pe)
            meet(pe)
            pe_lru(pe)
            pe_merge(pe)
            nxt(pe, "m_merged", 2)
            meet(pe)
            pe_down(pe, "w_out2", 4, lambda k, t: merged[:, k, t * P:(t + 1) * P])
            meet(pe)
            pe_turn(pe, xnf, ("xn_ready",))
            pe_hT(pe)
            pe_ffn(pe, "ffn2")

        @block.vector
        def _(dve):
            dve_small(dve)
            dve_bias(dve)
            nxt(dve, "x_loaded", 16 * NT)
            dve_ada(dve, 0, 16, 7)
            dve_norm(dve, xn1, c1(8), c1(0))
            dve_proj1(dve)
            meet(dve)
            dve_ada(dve, 16, 48, 7)
            dve_swa_prep(dve)
            dve_swa_turn(dve)
            dve_swa(dve)
            meet(dve)
            dve_gdn_prep(dve)
            for t in range(NT):
                dve_gdn(dve, t)
            dve_gate(dve, diag1, 16)
            dve_gate_row(dve, gate1, 0)
            dve_gdn_end(dve)
            dve_turned(dve)
            dve_out1(dve)
            meet(dve)
            dve_norm(dve, xn2, c1(32), c1(24))
            dve_route(dve)
            dve_gate(dve, diag2, 40)
            dve_gate_row(dve, gate2, 6)
            dve_more(dve)
            dve_moe(dve)
            dve_moe_end(dve)
            meet(dve)
            dve_norm(dve, xnf, gain2("ffn1_norm_pre_2"), None, hT_hi, 4)
            dve_ffn(dve, "ffn1")
            dve_post(dve, 0.5)
            meet(dve)
            dve_norm(dve, xn3, gain2("mix_norm_pre_2"), None)
            dve_proj2(dve)
            dve_tables(dve)
            meet(dve)
            dve_dil(dve)
            meet(dve)
            dve_combine(dve)
            meet(dve)
            dve_lru(dve)
            dve_merge(dve)
            meet(dve)
            dve_post(dve, 1.0)
            meet(dve)
            dve_norm(dve, xnf, gain2("ffn2_norm_pre_2"), None, hT_hi, 6)
            dve_ffn(dve, "ffn2")
            dve_post(dve, 0.5)
            dve.drain().then_inc(S("x_final"), 1)

        @block.gpsimd
        def _(pool):
            meet(pool)
            meet(pool)
            for t in range(NT):
                pool_gdn(pool, t)
            meet(pool)
            pool_route(pool)
            meet(pool)
            pool_ffn(pool, "ffn1")
            meet(pool)
            pool_proj2(pool)
            meet(pool)
            pool_dil(pool)
            meet(pool)
            meet(pool)
            meet(pool)
            meet(pool)
            pool_ffn(pool, "ffn2")


def kernel(**inputs):
    import concourse.bacc as bacc
    from concourse.bass_utils import run_bass_kernel_spmd

    nc = bacc.Bacc("TRN2", target_bir_lowering=False, num_devices=1)
    arrays, args = {}, {}
    for name in NAMES:
        v = np.ascontiguousarray(inputs[name])
        arrays[f"in_{name}"] = v
        args[name] = nc.dram_tensor(f"in_{name}", v.shape, mybir.dt.from_np(v.dtype), kind="ExternalInput").ap()
    arrays["constants_dram"] = POSITION_CONSTANTS
    const_dram = nc.dram_tensor("constants_dram", POSITION_CONSTANTS.shape, F32, kind="ExternalInput").ap()
    out = nc.dram_tensor("out", (T, D), F32, kind="ExternalOutput").ap()
    build(nc, args, const_dram, out)
    r = run_bass_kernel_spmd(nc, [arrays], core_ids=[0])
    return r.results[0]["out"].reshape(1, T, D)
```

```python
from contextlib import ExitStack

import numpy as np

import concourse.bass as bass
from concourse import mybir

F32 = mybir.dt.float32
F32R = mybir.dt.float32r
I32 = mybir.dt.int32
U32 = mybir.dt.uint32
BF16 = mybir.dt.bfloat16
ALU = mybir.AluOpType
ACT = mybir.ActivationFunctionType
AX_X = mybir.AxisListType.X

P = 128
T = 512
D = 1024
NT = T // P
KD = D // P
HD = 64
H = 8
NPAIR = H // 2
CHUNK = 64
WINW = 2832
QKV = 1536
N_EXP, N_GRP, EPG, F_EXP = 32, 4, 8, 256
CAP = P
FF = 2816
NFF = FF // P
WIN2 = 8704
HD2 = 128
EPS = 1e-6
BIG = 1.0e30
RING = 6
SLOT = 2048
DILATIONS = (1, 4, 16)


def bucket_of(distance):
    nf = np.maximum(distance, 1).astype(np.float32)
    large = 16 + (np.log(nf / np.float32(16)).astype(np.float32) / np.float32(np.log(2048 / 16))
                  * np.float32(16)).astype(np.int32)
    return np.where(distance < 16, distance, np.minimum(large, 31))


def constants():
    p = np.arange(P)[:, None]
    c = np.arange(P)[None, :]
    same = (p // CHUNK) == (c // CHUNK)
    parts = {
        "ident": (p == c),
        "ones": np.ones((P, P)),
        "cumsum": (p <= c) & same,
        "chunk_all": same,
        "chunk0": np.broadcast_to(p < CHUNK, (P, P)),
        "chunk1": np.broadcast_to(p >= CHUNK, (P, P)),
    }
    for b in (1, 2, 4, 8, 16, 32):
        parts[f"level{b}"] = ((c // b) % 2 == 1) & ((p // b) == (c // b) - 1)
    k = np.arange(2 * P)[None, :]
    rel = p + P - k
    parts["window"] = np.where((rel >= 0) & (rel < P), 0.0, -BIG)
    parts["iota"] = np.broadcast_to(c, (P, P))
    parts["before"] = (p < c)
    half = HD // 2
    parts["inv_freq"] = np.broadcast_to(
        np.power(np.float32(10000.0), -np.arange(half, dtype=np.float32) / np.float32(half)), (P, half))
    parts["tie4"] = np.broadcast_to(N_GRP - np.arange(N_GRP), (P, N_GRP))
    parts["tie8"] = np.broadcast_to(EPG - np.arange(EPG), (P, EPG))
    parts["partition"] = p
    parts["eps"] = np.full((P, 1), EPS)
    parts["zero"] = np.zeros((P, 1))
    for g, dil in enumerate(DILATIONS):
        steps = 2 * P - 1 - np.arange(4 * P)
        onehot = np.zeros((P, 4 * P))
        ok = (steps >= 0) & (steps <= P)
        b = bucket_of(np.maximum(steps, 0) * dil)
        onehot[b[ok], np.nonzero(ok)[0]] = 1.0
        onehot[32] = np.where(ok, 0.0, -BIG)
        parts[f"bucket{g}"] = onehot
    q = T // DILATIONS[2]
    parts["phase16"] = np.where((p // q) == (c // q), 0.0, -BIG)
    at, where = 0, {}
    for name, a in parts.items():
        a = np.asarray(a, np.float32)
        where[name] = (at, a.shape[1])
        at += a.shape[1]
    return np.ascontiguousarray(np.concatenate([np.asarray(a, np.float32) for a in parts.values()], 1)), where


NAMES = [
    "x", "c", "positions", "w_ada", "b_ada", "norm_mix", "w_in", "conv_w", "a_log", "dt_bias", "gdn_out_norm",
    "q_norm", "k_norm", "sinks", "w_out", "norm_ffn", "w_group", "b_group", "w_router", "b_router", "w_gate",
    "w_up", "w_down", "ffn1_norm_pre_2", "ffn1_norm_post_2", "ffn1_w_gate_2", "ffn1_w_up_2", "ffn1_w_down_2",
    "mix_norm_pre_2", "mix_norm_post_2", "w_in_2", "rel_bias_table_2", "conv_w_2", "conv_b_2", "lru_w_x_2",
    "lru_b_x_2", "lru_w_a_2", "lru_b_a_2", "lru_a_param_2", "w_attn_branch_2", "w_rec_branch_2", "w_out_2",
    "ffn2_norm_pre_2", "ffn2_norm_post_2", "ffn2_w_gate_2", "ffn2_w_up_2", "ffn2_w_down_2",
]
POSITION_CONSTANTS, WHERE = constants()


def build(nc, a, const_dram, out):
    ctx = ExitStack()
    with ctx:
        memory = ctx.enter_context(ExitStack())

        def sb(name, shape, dt=F32):
            tensors.append((name, shape))
            return memory.enter_context(nc.sbuf_tensor(name, shape, dt))

        tensors = []

        sems = {}

        c, v = NT, 2 * NT
        SUCCESSOR = {
            "d_scores": ("w_scores", 16), "d_s_taken": ("w_s_taken", 16), "d_max": ("w_max", 16),
            "d_p": ("w_p", 16), "d_p_turned": ("w_p_turned", 16), "d_pT": ("w_pT_ready", 16),
            "d_values": ("w_values", 16), "d_o_taken": ("w_o_taken", NT), "d_ps0": ("g_turned", 4 * c),
            "d_taken0": ("g_T_even", v), "d_taken1": ("g_T_odd", v), "d_v_taken": ("g_T1", v),
            "d_vT_turned": ("z_taken", 1),
            "mix_high": ("r_gmax", 1), "mix_low": ("r_gexp", 1), "mix_raw0": ("r_M", 1), "mix_raw1": ("r_ranks", 1),
            "mix_raw2": ("r_diff", 1), "x_new": ("mixed_ready", 1),
            "l_abs": ("g_abs", 1), "l_exp": ("g_exp", 1), "l_c": ("g_ss", 1), "l_in": ("g_X", 10 * c),
            "l_conv": ("g_Xs", 10 * c), "l_ps": ("g_w", c), "l_gate_ps": ("g_nw", c), "l_gates": ("g_v", v),
            "l_tanh": ("g_vnew", v), "l_floor": ("g_out", v), "l_sqrt": ("g_o_taken", c), "l_y_ps": ("g_osq", 1),
            "l_gelu": ("g_oss", 1), "ffn1_free": ("g_Ml", 10 * c), "ffn1_gu": ("g_T", 12 * c),
            "ffn1_sg": ("g_Y", 10 * c), "ffn2_free": ("g_state", v), "ffn2_gu": ("g_kk", c), "ffn2_sg": ("g_kq", c),
            "f_squares": ("w_ss", 1), "f_ss": ("w_roots", 1), "f_root": ("angles", 1), "post_loaded": ("rotation", 1),
            "c_diff": ("g_U", c), "c_exp": ("g_Grow", c), "attn_ready": ("g_oroot", 1), "attn_turned": ("w_turned", 1),
            "attnT_ready": ("w_kT", 1), "rec_ready": ("w_qk", 1),
            "m_sigmoids": ("g_roots", 1), "l_mixed": ("g_diff", c), "l_rec": ("g_decay", c),
            "rec_high": ("w_squares", 1), "l_hT_high": ("r_wexp", 1), "l_hT_low": ("r_taken", 1),
            "rest_high": ("vectors_turned", 1), "rest_low": ("btab_ones", 1), "rest_raw0": ("ab_ps", 1),
            "rest_raw1": ("sq_taken", 1), "rest_raw2": ("proj1_done", 1), "m_merged": ("g_G", 1),
        }

        def before(name):
            return SUCCESSOR[name][1] if name in SUCCESSOR else 0

        def S(name):
            if name in SUCCESSOR:
                return S(SUCCESSOR[name][0])
            if name not in sems:
                sems[name] = ctx.enter_context(nc.semaphore(name))
            return sems[name]

        tally = {}

        def nxt(e, name, by=1):
            key = (str(e.engine), name)
            tally[key] = tally.get(key, before(name)) + by
            e.wait_ge(S(name), tally[key])

        def meet(e):
            e.drain().then_inc(S("meet"), 1)
            nxt(e, "meet", 4)

        n_const = POSITION_CONSTANTS.shape[1]
        n_keep = WHERE["bucket0"][0]
        K = sb("constants", [P, n_keep])

        def con(name):
            at, n = WHERE[name]
            return K[:, at:at + n]

        ident, ones, eps = con("ident"), con("ones"), con("eps")
        ring = sb("ring", [P, RING, SLOT])
        X = sb("residual", [P, NT, D])
        hT = sb("hT", [P, KD, T])
        cols1 = sb("cols1", [P, 120])
        cols2 = sb("cols2", [P, 88])
        mod = sb("mod", [P, 48])
        cact = sb("cact", [P, KD])
        rows = sb("rows", [P, 256])
        ss = sb("ss", [P, NT])
        rstd = sb("rstd", [P, NT])
        ARENA = 29900
        A = sb("arena", [P, ARENA])
        memory.close()
        HID = NFF * T
        HI_AT = 24672
        split = {}
        for name, shape in tensors[:-1] + [("hid_high", [P, HID]), ("hid_low", [P, HID]), ("between", [P, HI_AT - 2 * HID]),
                                           ("hT_high", [P, KD * T])]:
            split[name] = ctx.enter_context(nc.sbuf_tensor(name + "_split", shape, F32R))
        bank = [ctx.enter_context(nc.psum_tensor(f"bank{i}", [P, 512], F32)) for i in range(8)]

        def region(at, width, pattern=None, base=None, **kw):
            r = (A if base is None else base)[:, at:at + width]
            return r.rearrange(pattern, **kw) if pattern else r

        hflat = hT[:, :, :].rearrange("p k t -> p (k t)")

        ROWS = {}
        at = 0
        for name, n in (("a_log", H), ("dt_bias", H), ("gdn_out_norm", HD), ("q_norm", HD), ("k_norm", HD),
                        ("sinks", H), ("b_group", N_GRP), ("b_router", N_EXP)):
            ROWS[name] = (at, n)
            at += n

        def row(name):
            at, n = ROWS[name]
            return rows[:, at:at + n]

        SLOTS = []
        FIRST = {}

        def plan(name, sources):
            FIRST[name] = len(SLOTS)
            SLOTS.extend(sources)

        def t_slots(w, c0, c1):
            return [w[:, n:n + 256].rearrange("(k p) n -> p k n", p=P) for n in range(c0, c1, 256)]

        def n_slots(w, c0, c1):
            return [w[r:r + 512, n:n + 512].rearrange("(k p) n -> p k n", p=P)
                    for n in range(c0, c1, 512) for r in (0, 512)]

        def d_slots(w, r1):
            return [w[r:r + 256, :].rearrange("(k p) n -> p k n", p=P) for r in range(0, r1, 256)]

        w_ada, w_in, w_in2 = a["w_ada"][0], a["w_in"][0], a["w_in_2"][0]
        plan("ada1", t_slots(w_ada, 0, 2 * D))
        plan("qkv", t_slots(w_in, 0, QKV))
        plan("z", n_slots(w_in, QKV, QKV + 512))
        plan("sq", n_slots(w_in, 2064, 2064 + 512))
        plan("skv", t_slots(w_in, 2576, 2832))
        plan("ada2", t_slots(w_ada, 2 * D, 6 * D))
        plan("w_out", d_slots(a["w_out"][0], D))
        MOE_AT = len(SLOTS)

        def ffn_slots(tag):
            g, u = (t_slots(a[f"{tag}_w_{n}_2"][0], 0, FF) for n in ("gate", "up"))
            plan(tag, [s for pair in zip(g, u) for s in pair])
            plan(tag + "_down", d_slots(a[f"{tag}_w_down_2"][0], FF))

        ffn_slots("ffn1")
        for g in range(3):
            plan(f"q{g}", t_slots(w_in2, 512 * g, 512 * g + 512))
            plan(f"k{g}", t_slots(w_in2, 1536 + 512 * g, 1536 + 512 * g + 512))
            plan(f"v{g}", (t_slots if g == 2 else n_slots)(w_in2, 3072 + 512 * g, 3072 + 512 * g + 512))
        plan("xr", t_slots(w_in2, 4608, 5632))
        plan("lru", [a[n][0].rearrange("h (i p) j -> p (h i) j", p=P) for n in ("lru_w_x_2", "lru_w_a_2")])
        plan("yr", t_slots(w_in2, 5632, 6656))
        for m in range(4):
            plan(f"gl{m}", t_slots(w_in2, 6656 + 256 * m, 6656 + 256 * m + 256)
                 + t_slots(w_in2, 7680 + 256 * m, 7680 + 256 * m + 256))
            plan(f"attn{m}", [a["w_attn_branch_2"][0][:, 256 * m:256 * m + 256].rearrange("(k p) n -> p k n", p=P)])
            plan(f"rec{m}", t_slots(a["w_rec_branch_2"][0], 256 * m, 256 * m + 256))
        plan("w_out2", d_slots(a["w_out_2"][0], D))
        ffn_slots("ffn2")

        loaded = [S(f"slot{i}_loaded") for i in range(RING)]

        def slot_view(i, n):
            return ring[:, i % RING, :].rearrange("p (k n) -> p k n", n=n)

        def load(sp, first, count):
            for i in range(first, first + count):
                if i >= RING:
                    sp.wait_ge(S("slots_used"), i - RING + 1)
                src = SLOTS[i]
                n = src.shape[-1]
                view = ring[:, i % RING, 0:src.shape[1] * n].rearrange("p (k n) -> p k n", n=n)
                sp.dma_start(view, src).then_inc(loaded[i % RING], 16)

        def need(pe, i):
            pe.wait_ge(loaded[i % RING], 16 * (i // RING + 1))

        vec1 = region(0, P)
        vec2 = region(P, P)
        VEC1 = [("b_ada", 48), ("norm_mix", 8), ("norm_ffn", 8), ("c", 8), ("conv_w", 48)]
        VEC2 = [("ffn1_norm_pre_2", 8), ("mix_norm_pre_2", 8), ("ffn2_norm_pre_2", 8), ("conv_w_2", 32),
                ("conv_b_2", 8), ("lru_b_x_2", 8), ("lru_b_a_2", 8), ("lru_a_param_2", 8)]
        wab = region(28752, KD * 16, "p (k n) -> p k n", n=16)

        def chunked(v, n):
            dims = " ".join("abcd"[:len(v.shape)])
            flat = v.rearrange(f"{dims} -> ({dims})")
            return flat.rearrange("(r p) -> r p", p=P)

        def col(c, table):
            at = 0
            for name, n in table:
                if name == c:
                    return at, n
                at += n

        def sp_small(sp):
            sp.dma_start(K[:, :], const_dram[:, 0:n_keep]).then_inc(S("const_loaded"), 16)
            for vec, table in ((vec1, VEC1), (vec2, VEC2)):
                at = 0
                for name, n in table:
                    sp.dma_start(vec[at:at + n, :], chunked(a[name], n)).then_inc(S("vectors_loaded"), 16)
                    at += n

        def sp_x(sp):
            for t in range(NT):
                sp.dma_start(X[:, t, :], a["x"][0, t * P:(t + 1) * P, :]).then_inc(S("x_loaded"), 16)

        def act_small(act):
            for name, (at, n) in ROWS.items():
                src = a[name][0:1, :].broadcast_to([P, n])
                act.dma_start(rows[:, at:at + n], src).then_inc(S("rows_loaded"), 16)
            act.dma_start(wab, w_in[:, 2048:2064].rearrange("(k p) n -> p k n", p=P)).then_inc(S("wab_loaded"), 16)

        def pe_small(pe):
            nxt(pe, "const_loaded", 16)
            nxt(pe, "vectors_loaded", 16 * (len(VEC1) + len(VEC2)))
            pe.transpose(bank[0][:, 0:120], vec1[0:120, :], ident[0:120, 0:120])
            pe.transpose(bank[1][:, 0:88], vec2[0:88, :], ident[0:88, 0:88]).then_inc(S("vectors_turned"), 1)

        def dve_small(dve):
            nxt(dve, "vectors_turned")
            dve.tensor_copy(cols1[:, :], bank[0][:, 0:120])
            dve.tensor_copy(cols2[:, :], bank[1][:, 0:88]).then_inc(S("columns_ready"), 1)

        def act_c(act):
            nxt(act, "columns_ready")
            at, n = col("c", VEC1)
            act.activation(cact[:, :], cols1[:, at:at + n], ACT.Silu).then_inc(S("cact_ready"), 1)

        def pe_ada(pe, name, m0, m1, b):
            if m0 == 0:
                nxt(pe, "cact_ready")
            for i in range(m0 // 2, m1 // 2):
                s = FIRST[name] + i - m0 // 2
                need(pe, s)
                w = slot_view(s, 256)
                for j in range(2):
                    m = 2 * i + j
                    for k in range(KD):
                        mm = pe.matmul(bank[b][:, m:m + 1], w[:, k, j * P:(j + 1) * P], cact[:, k:k + 1],
                                       start=(k == 0), stop=(k == KD - 1))
                mm.then_inc(S("slots_used"), 1)

        def dve_ada(dve, m0, m1, b):
            last = FIRST["ada1"] + 8 if m0 == 0 else FIRST["ada2"] + 16
            dve.wait_ge(S("slots_used"), last)
            dve.tensor_tensor(mod[:, m0:m1], bank[b][:, m0:m1], cols1[:, m0:m1], ALU.add)
            dve.drain()
            s0, gain = (8, "norm_mix") if m0 == 0 else (32, "norm_ffn")
            at, n = col(gain, VEC1)
            dve.scalar_tensor_tensor(mod[:, s0:s0 + 8], mod[:, s0:s0 + 8], 1.0, cols1[:, at:at + n],
                                     ALU.add, ALU.mult)
            dve.drain().then_inc(S("mod_ready"), 1)

        def act_norm(act, junk, scale, shift, high=None, x_new=False):
            for t in range(NT):
                if x_new:
                    nxt(act, "x_new")
                act.activation(junk, X[:, t, :], ACT.Square, accum_out=ss[:, t:t + 1])
                act.drain()
                act.activation(rstd[:, t:t + 1], ss[:, t:t + 1], ACT.Sqrt, bias=eps, scale=1.0 / D)\
                   .then_inc(S("rms_ready"), 1)
            for k in range(0, KD, 2):
                nxt(act, "x_turned", 2 if k else 1)
                if shift is None:
                    i = act.activation(hT[:, k, :], bank[k][:, :], ACT.Copy, scale=scale[:, k:k + 1])
                else:
                    i = act.activation(hT[:, k, :], bank[k][:, :], ACT.Identity, bias=shift[:, k:k + 1],
                                       scale=scale[:, k:k + 1])
                if high is not None:
                    act.drain()
                    i = act.activation(high[:, k, :], hT[:, k, :], ACT.Copy)
            tally[(str(act.engine), "x_turned")] += 1
            i.then_inc(S("hT_even"), 1)

        def dve_norm(dve, xn, scale, shift, high=None, high_number=0):
            for t in range(NT):
                nxt(dve, "rms_ready")
                dve.reciprocal(ss[:, t:t + 1], rstd[:, t:t + 1])
                dve.drain()
                dve.tensor_scalar(xn[:, t, :], X[:, t, :], ss[:, t:t + 1], None, ALU.mult).then_inc(S("xn_ready"), 1)
            for k in range(1, KD, 2):
                nxt(dve, "x_turned", 2)
                if shift is None:
                    i = dve.tensor_scalar(hT[:, k, :], bank[k][:, :], scale[:, k:k + 1], None, ALU.mult)
                else:
                    i = dve.tensor_scalar(hT[:, k, :], bank[k][:, :], scale[:, k:k + 1], shift[:, k:k + 1],
                                          ALU.mult, ALU.add)
                if high is not None:
                    dve.drain()
                    i = dve_split(dve, high[0][:, k, :], hT[:, k, :], high[1][:, k, :])
            if high is not None:
                dve.wait_ge(S("hT_even"), high_number)
                for k in range(0, KD, 2):
                    i = dve.tensor_tensor(high[1][:, k, :], hT[:, k, :], high[0][:, k, :].bitcast(F32), ALU.subtract)
            i.then_inc(S("hT_odd"), 1)

        def pe_turn(pe, src, ready):
            nxt(pe, *ready)
            for t in range(NT):
                if t and ready[0] == "xn_ready":
                    nxt(pe, *ready)
                for k in range(KD):
                    mm = pe.transpose(bank[k][:, t * P:(t + 1) * P], src[:, t, k * P:(k + 1) * P], ident)
                    if t == NT - 1:
                        mm.then_inc(S("x_turned"), 1)

        def pe_hT(pe):
            nxt(pe, "hT_even")
            nxt(pe, "hT_odd")

        convT = region(0, QKV // P * T, "p (m t) -> p m t", t=T)
        qkv = region(6144, NT * QKV, "p (t n) -> p t n", n=QKV)
        kbG = region(12288, 2048, "p (t n) -> p t n", n=512)
        z = region(14336, 2048, "p (t n) -> p t n", n=512)
        mixed = region(16384, 4096, "p (t n) -> p t n", n=D)
        ab = region(20480, 64, "p (t n) -> p t n", n=16)
        sq = region(20544, 2048, "p (t n) -> p t n", n=512)
        skv = region(22592, 1024, "p (t n) -> p t n", n=256)
        convin = region(23616, 1040, "p (b t) -> p b t", b=2)
        xn1 = region(24656, 4096, "p (t n) -> p t n", n=D)
        junk1 = region(1024, D)
        convacc = region(24656, 1024, "p (b t) -> p b t", b=2)
        NM = QKV // P

        def pe_gemm_t(pe, s, nk, rhs, banks, ready, free=None):
            need(pe, s)
            n = SLOTS[s].shape[-1]
            w = ring[:, s % RING, 0:nk * n].rearrange("p (k n) -> p k n", n=n)
            for j in range(n // P):
                if free is not None:
                    free(j)
                for k in range(nk):
                    mm = pe.matmul(banks[j][:, :], w[:, k, j * P:(j + 1) * P], rhs[:, k, :],
                                   start=(k == 0), stop=(k == nk - 1))
                if j < n // P - 1:
                    mm.then_inc(S(ready), 1)
            return mm

        def pe_gemm_n(pe, s, lhs, banks):
            for half in range(2):
                need(pe, s + half)
                w = slot_view(s + half, 512)
                for t in range(NT):
                    for k in range(4):
                        mm = pe.matmul(banks[t][:, :], lhs(4 * half + k, t), w[:, k, :],
                                       start=(half == 0 and k == 0), stop=(half == 1 and k == 3))
                mm.then_inc(S("slots_used"), 1)

        def tokens(k, t):
            return hT[:, k, t * P:(t + 1) * P]

        def pe_proj1(pe):
            for i in range(NM // 2):
                s = FIRST["qkv"] + i
                need(pe, s)
                w = slot_view(s, 256)
                for j in range(2):
                    if i > 0:
                        nxt(pe, "conv_in")
                    for k in range(KD):
                        mm = pe.matmul(bank[j][:, :], w[:, k, j * P:(j + 1) * P], hT[:, k, :],
                                       start=(k == 0), stop=(k == KD - 1))
                    if j == 0:
                        mm.then_inc(S("qkvT_ps"), 1)
                mm.then_inc(S("slots_used"), 1)
            nxt(pe, "conv_in", 2)
            pe_gemm_n(pe, FIRST["z"], tokens, bank[2:6])
            nxt(pe, "wab_loaded", 16)
            for t in range(NT):
                for k in range(KD):
                    mm = pe.matmul(bank[6][:, 16 * t:16 * t + 16], tokens(k, t), wab[:, k, :],
                                   start=(k == 0), stop=(k == KD - 1))
            mm.then_inc(S("ab_ps"), 1)
            nxt(pe, "z_taken")
            pe_gemm_n(pe, FIRST["sq"], tokens, bank[2:6])
            nxt(pe, "sq_taken")
            need(pe, FIRST["skv"])
            w = slot_view(FIRST["skv"], 256)
            for t in range(NT):
                for k in range(KD):
                    mm = pe.matmul(bank[2 + t][:, 0:256], tokens(k, t), w[:, k, :],
                                   start=(k == 0), stop=(k == KD - 1))
            mm.then_inc(S("slots_used"), 1)

        def act_proj1(act):
            for m in range(NM):
                i, j = m // 2, m % 2
                if j == 0:
                    nxt(act, "qkvT_ps")
                else:
                    act.wait_ge(S("slots_used"), FIRST["qkv"] + i + 1)
                if m >= 2:
                    nxt(act, "conv_done")
                act.activation(convin[:, j, 3:3 + T], bank[j][:, :], ACT.Copy).then_inc(S("conv_in"), 1)
                if m >= 2:
                    act.activation(convT[:, m - 2, :], convacc[:, j, :], ACT.Silu).then_inc(S("silu_done"), 1)
            for m in (NM - 2, NM - 1):
                nxt(act, "conv_done")
                act.activation(convT[:, m, :], convacc[:, m % 2, :], ACT.Silu).then_inc(S("silu_done"), 1)

        def dve_proj1(dve):
            dve.memset(convin[:, :, 0:3], 0.0)
            at, _ = col("conv_w", VEC1)
            for m in range(NM):
                j = m % 2
                nxt(dve, "conv_in")
                if m >= 2:
                    nxt(dve, "silu_done")
                dve.drain()
                dve.tensor_scalar(convacc[:, j, :], convin[:, j, 3:3 + T], cols1[:, at + 36 + m:at + 37 + m],
                                  None, ALU.mult)
                for tap in range(3):
                    dve.drain()
                    w = cols1[:, at + 12 * tap + m:at + 12 * tap + m + 1]
                    i = dve.scalar_tensor_tensor(convacc[:, j, :], convin[:, j, tap:tap + T], w,
                                                 convacc[:, j, :], ALU.mult, ALU.add)
                i.then_inc(S("conv_done"), 1)
            dve.wait_ge(S("slots_used"), FIRST["z"] + 2)
            for t in range(NT):
                i = dve.tensor_copy(z[:, t, :], bank[2 + t][:, :])
            i.then_inc(S("z_taken"), 1)
            nxt(dve, "ab_ps")
            dve.tensor_copy(ab, bank[6][:, 0:64].rearrange("p (t n) -> p t n", n=16))
            dve.wait_ge(S("slots_used"), FIRST["sq"] + 2)
            for t in range(NT):
                i = dve.tensor_copy(sq[:, t, :], bank[2 + t][:, :])
            i.then_inc(S("sq_taken"), 1)
            dve.wait_ge(S("slots_used"), FIRST["skv"] + 1)
            for t in range(NT):
                dve.tensor_copy(skv[:, t, :], bank[2 + t][:, 0:256])
            dve.drain().then_inc(S("proj1_done"), 1)

        def pe_qkv(pe):
            nxt(pe, "silu_done", NM)
            for t in range(NT):
                for g in range(3):
                    b = bank[(3 * t + g) % 2]
                    if 3 * t + g >= 2:
                        nxt(pe, "qkv_taken")
                    for m in range(4):
                        mm = pe.transpose(b[:, m * P:(m + 1) * P], convT[:, 4 * g + m, t * P:(t + 1) * P], ident)
                    mm.then_inc(S("qkv_turned"), 1)

        def act_qkv(act):
            for t in range(NT):
                for g in range(3):
                    nxt(act, "qkv_turned")
                    act.activation(qkv[:, t, 512 * g:512 * g + 512], bank[(3 * t + g) % 2][:, :], ACT.Copy)\
                       .then_inc(S("qkv_taken"), 1)

        small = region(28880, 1020)
        NW = H + 2

        def sm(at, width, pattern=None, **kw):
            r = small[:, at:at + width]
            return r.rearrange(pattern, **kw) if pattern else r

        pos_i = sm(0, NT).bitcast(I32)
        pos_f = sm(4, NT)
        cos = region(26960, 128, "p (t f) -> p t f", t=NT)
        sin = region(27088, 128, "p (t f) -> p t f", t=NT)
        ang = region(27216, 128, "p (t f) -> p t f", t=NT)
        turns = region(27344, 128, "p (t f) -> p t f", t=NT)
        w_ss = sm(8, 40, "p (t h) -> p t h", t=NT)
        w_r = sm(48, 40, "p (t h) -> p t h", t=NT)
        w_mx, w_nmx, w_den, w_es = (sm(88 + 32 * i, 32) for i in range(4))
        sq4 = sq.rearrange("p t (h e) -> p t h e", e=HD)
        sk3 = skv[:, :, 0:128]
        squares_q = region(0, 2048, "p (t n) -> p t n", t=NT)
        squares_k = region(2048, 512, "p (t n) -> p t n", t=NT)
        kk = region(4096, 1024, "p (t g i e) -> p t g i e", t=NT, g=2, i=2)
        q_T = region(0, 2048, "p (j t) -> p j t", base=hflat, t=T)
        k_T = region(2048, 1024, "p (g t) -> p g t", base=hflat, t=T)
        Pw = region(23616, 1024, "p (b i k) -> p b i k", b=2, i=2)
        PwT = region(24656, 1024, "p (b i k) -> p b i k", b=2, i=2)
        TWO_PI = 2 * np.pi
        C1 = 6.28125
        C2 = float(np.float32(TWO_PI - C1))
        C3 = TWO_PI - C1 - C2
        ROUND = 12582912.0
        NEAR_PI = 3.1415925

        def sp_positions(sp):
            sp.dma_start(pos_i, a["positions"][0].rearrange("(t p) -> p t", p=P),
                         allow_slow_non_contiguous=True).then_inc(S("positions_loaded"), 16)

        def act_swa_prep(act):
            nxt(act, "rows_loaded", 16 * len(ROWS))
            act.activation(squares_q, sq, ACT.Square)
            act.activation(squares_k, sk3, ACT.Square).then_inc(S("w_squares"), 1)
            nxt(act, "w_ss")
            act.activation(w_r, w_ss, ACT.Sqrt, bias=eps, scale=1.0 / HD).then_inc(S("w_roots"), 1)
            nxt(act, "angles")
            act.activation(sin, ang, ACT.Sin)
            act.activation(cos, turns, ACT.Sin).then_inc(S("rotation"), 1)

        def dve_swa_prep(dve):
            nxt(dve, "w_squares")
            dve.tensor_reduce(w_ss[:, :, 0:H], squares_q.rearrange("p t (h e) -> p t h e", e=HD), AX_X, ALU.add)
            dve.tensor_reduce(w_ss[:, :, H:NW], squares_k.rearrange("p t (h e) -> p t h e", e=HD), AX_X, ALU.add)\
               .then_inc(S("w_ss"), 1)
            nxt(dve, "positions_loaded", 16)
            dve.tensor_copy(pos_f, pos_i)
            dve.drain()
            shape = [P, NT, HD // 2]
            dve.tensor_tensor(ang, pos_f.unsqueeze(2).broadcast_to(shape),
                              con("inv_freq").unsqueeze(1).broadcast_to(shape), ALU.mult)
            dve.drain()
            dve.tensor_scalar(turns, ang, 1.0 / TWO_PI, ROUND, ALU.mult, ALU.add)
            dve.drain()
            dve.tensor_scalar(turns, turns, ROUND, None, ALU.subtract)
            for c in (C1, C2, C3):
                dve.drain()
                dve.scalar_tensor_tensor(ang, turns, -c, ang, ALU.mult, ALU.add)
            dve.drain()
            dve.tensor_scalar(ang, ang, NEAR_PI, -NEAR_PI, ALU.min, ALU.max)
            dve.drain()
            dve.scalar_tensor_tensor(turns, ang, -1.0, ang, ALU.mult, ALU.min)
            dve.drain()
            dve.tensor_scalar(turns, turns, float(np.pi / 2), None, ALU.add).then_inc(S("angles"), 1)
            nxt(dve, "w_roots")
            dve.reciprocal(w_ss, w_r)
            dve.drain()
            for t in range(NT):
                shape = [P, H, HD]
                dve.tensor_tensor(sq4[:, t], sq4[:, t], w_ss[:, t, 0:H].unsqueeze(2).broadcast_to(shape), ALU.mult)
                k4 = sk3[:, t, :].rearrange("p (h e) -> p h e", e=HD)
                dve.tensor_tensor(k4, k4, w_ss[:, t, H:NW].unsqueeze(2).broadcast_to([P, 2, HD]), ALU.mult)
            dve.drain()
            for t in range(NT):
                dve.tensor_tensor(sq4[:, t], sq4[:, t], row("q_norm").unsqueeze(1).broadcast_to([P, H, HD]), ALU.mult)
                k4 = sk3[:, t, :].rearrange("p (h e) -> p h e", e=HD)
                dve.tensor_tensor(k4, k4, row("k_norm").unsqueeze(1).broadcast_to([P, 2, HD]), ALU.mult)
            nxt(dve, "rotation")
            dve.drain()
            half = HD // 2
            for t in range(NT):
                for heads, src in ((H, sq4[:, t]), (2, sk3[:, t, :].rearrange("p (h e) -> p h e", e=HD))):
                    shape = [P, heads, half]
                    c = cos[:, t, :].unsqueeze(1).broadcast_to(shape)
                    s = sin[:, t, :].unsqueeze(1).broadcast_to(shape)
                    x1, x2 = src[:, :, 0:half], src[:, :, half:HD]
                    base = 1024 * (t % 2) + (0 if heads == H else 2048)
                    u = [region(base + 256 * i, heads * half, "p (h f) -> p h f", f=half) for i in range(4)]
                    dve.tensor_tensor(u[0], x1, c, ALU.mult)
                    dve.tensor_tensor(u[1], x2, s, ALU.mult)
                    dve.tensor_tensor(u[2], x1, s, ALU.mult)
                    dve.tensor_tensor(u[3], x2, c, ALU.mult)
                    dve.drain()
                    if heads == H:
                        dve.tensor_tensor(x1, u[0], u[1], ALU.subtract)
                        dve.tensor_tensor(x2, u[2], u[3], ALU.add)
                    else:
                        for i in range(2):
                            dve.tensor_tensor(kk[:, t, :, i, 0:half], u[0], u[1], ALU.subtract)
                            dve.tensor_tensor(kk[:, t, :, i, half:HD], u[2], u[3], ALU.add)
                    if t >= 1:
                        dve.drain()
            dve.drain().then_inc(S("w_qk"), 1)

        def pe_swa_turn(pe):
            nxt(pe, "w_qk")
            for j in range(NPAIR):
                for t in range(NT):
                    pe.transpose(bank[j][:, t * P:(t + 1) * P], sq[:, t, j * P:(j + 1) * P], ident)
            for g in range(2):
                for t in range(NT):
                    mm = pe.transpose(bank[4 + g][:, t * P:(t + 1) * P],
                                      kk[:, t, g].rearrange("p i e -> p (i e)"), ident)
            mm.then_inc(S("w_turned"), 1)

        def dve_swa_turn(dve):
            nxt(dve, "w_turned")
            for j in range(NPAIR):
                dve.tensor_copy(q_T[:, j, :], bank[j][:, :])
            dve.drain().then_inc(S("w_qT"), 1)

        def act_swa_turn(act):
            nxt(act, "w_turned")
            for g in range(2):
                act.activation(k_T[:, g, :], bank[4 + g][:, :], ACT.Copy)
            act.drain().then_inc(S("w_kT"), 1)

        UNITS = [(n, j) for n in range(NT) for j in range(NPAIR)]

        def span(n):
            return (n - 1, 2 * P) if n else (0, P)

        def pe_swa(pe):
            def scores(u):
                n, j = UNITS[u]
                n0, w = span(n)
                if u >= 2:
                    nxt(pe, "w_s_taken")
                for i in range(2):
                    r = slice(64 * i, 64 * i + 64)
                    mm = pe.matmul(bank[2 * (u % 2) + i][:, 0:w], q_T[r, j, n * P:(n + 1) * P],
                                   k_T[r, j // 2, n0 * P:n0 * P + w], start=True, stop=True)
                mm.then_inc(S("w_scores"), 1)

            def turn(u):
                n, j = UNITS[u]
                nxt(pe, "w_p")
                for i in range(2):
                    for b in range(span(n)[1] // P):
                        mm = pe.transpose(bank[4 + u % 2][:, (2 * i + b) * P:(2 * i + b + 1) * P],
                                          Pw[:, u % 2, i, b * P:(b + 1) * P], ident)
                mm.then_inc(S("w_p_turned"), 1)

            def values(u):
                n, j = UNITS[u]
                n0, w = span(n)
                nxt(pe, "w_pT_ready")
                if j == 0 and n >= 2:
                    nxt(pe, "w_o_taken")
                for i in range(2):
                    h = 2 * j + i
                    for b in range(w // P):
                        mm = pe.matmul(bank[6 + n % 2][:, h * HD:(h + 1) * HD], PwT[:, u % 2, i, b * P:(b + 1) * P],
                                       skv[:, n0 + b, 128 + HD * (h // 4):128 + HD * (h // 4) + HD],
                                       start=(b == 0), stop=(b == w // P - 1))
                mm.then_inc(S("w_values"), 1)

            nxt(pe, "w_qT")
            nxt(pe, "w_kT")
            scores(0)
            for u in range(len(UNITS)):
                if u + 1 < len(UNITS):
                    scores(u + 1)
                turn(u)
                if u:
                    values(u - 1)
            values(len(UNITS) - 1)

        def dve_swa(dve):
            mask = con("window")
            for u, (n, j) in enumerate(UNITS):
                _, w = span(n)
                c = slice(2 * u, 2 * u + 2)
                nxt(dve, "w_scores")
                if u >= 2:
                    nxt(dve, "w_p_turned")
                for i in range(2):
                    s = dve.scalar_tensor_tensor(Pw[:, u % 2, i, 0:w], bank[2 * (u % 2) + i][:, 0:w], HD ** -0.5,
                                                 mask[:, 2 * P - w:2 * P], ALU.mult, ALU.add)
                s.then_inc(S("w_s_taken"), 1)
                dve.drain()
                dve.tensor_reduce(w_mx[:, c], Pw[:, u % 2, :, 0:w], AX_X, ALU.max)
                dve.drain()
                dve.tensor_tensor(w_mx[:, c], w_mx[:, c], row("sinks")[:, 2 * j:2 * j + 2], ALU.max)
                dve.drain()
                dve.tensor_scalar(w_nmx[:, c], w_mx[:, c], -1.0, None, ALU.mult).then_inc(S("w_max"), 1)
                if u >= 1 and u % NPAIR == 0:
                    outputs(dve, n - 1)
            outputs(dve, NT - 1)

        def outputs(dve, n):
            c = slice(8 * n, 8 * n + 8)
            dve.wait_ge(S("w_values"), 4 * (n + 1))
            dve.wait_ge(S("w_p"), 4 * (n + 1))
            dve.tensor_tensor(w_den[:, c], w_den[:, c], w_es[:, c], ALU.add)
            dve.drain()
            dve.reciprocal(w_es[:, c], w_den[:, c])
            dve.drain()
            dve.tensor_tensor(mixed[:, n, 512:1024].rearrange("p (h e) -> p h e", e=HD),
                              bank[6 + n % 2][:, :].rearrange("p (h e) -> p h e", e=HD),
                              w_es[:, c].unsqueeze(2).broadcast_to([P, H, HD]), ALU.mult)\
               .then_inc(S("w_o_taken"), 1)

        def act_swa(act):
            def exps(u):
                n, j = UNITS[u]
                w = span(n)[1]
                nxt(act, "w_max")
                for i in range(2):
                    c = slice(2 * u + i, 2 * u + i + 1)
                    act.activation(w_es[:, c], row("sinks")[:, 2 * j + i:2 * j + i + 1], ACT.Exp, bias=w_nmx[:, c])
                    act.activation(Pw[:, u % 2, i, 0:w], Pw[:, u % 2, i, 0:w], ACT.Exp, bias=w_nmx[:, c],
                                   accum_out=w_den[:, c])
                act.drain().then_inc(S("w_p"), 1)

            def copy(u):
                w = span(UNITS[u][0])[1]
                nxt(act, "w_p_turned")
                if u >= 2:
                    nxt(act, "w_values")
                act.activation(PwT[:, u % 2, :, 0:w],
                               bank[4 + u % 2][:, :].rearrange("p (i k) -> p i k", i=2)[:, :, 0:w], ACT.Copy)
                act.drain().then_inc(S("w_pT_ready"), 1)

            exps(0)
            for u in range(len(UNITS)):
                if u + 1 < len(UNITS):
                    exps(u + 1)
                copy(u)

        a_in, b_in = ab[:, :, 0:H], ab[:, :, H:2 * H]

        def th(at):
            return sm(at, 32, "p (t h) -> p t h", t=NT)

        g_u, g_e, g_s, g_z, g_q, g_g, g_beta, g_G, g_expG, g_kdec, g_ea = (th(216 + 32 * i) for i in range(11))
        g_dec = sm(568, 32, "p (t c j) -> p t c j", t=NT, c=2)
        g_ss = sm(600, 64, "p (t h) -> p t h", t=NT)
        g_r = sm(664, 64, "p (t h) -> p t h", t=NT)
        g_os = th(728)
        g_or = th(760)
        squares = region(0, 4096, "p (t n) -> p t n", t=NT)
        qg = region(0, 2048, "p (t n) -> p t n", t=NT)
        kb = region(2048, 2048, "p (t n) -> p t n", t=NT)
        kdec = region(4096, 2048, "p (t n) -> p t n", t=NT)
        qn, kn, vb = (qkv[:, :, 512 * i:512 * i + 512] for i in range(3))
        TT, Tm, Xs, MT = (region(1024 * i, 1024, "p (h c) -> p h c", base=hflat, c=P) for i in range(4))
        MTl, DT, attnT, gU = (region(20544 + 1024 * i, 1024, "p (h c) -> p h c", c=P) for i in range(4))
        kT, kbT, qT, qgT, nwT = (region(24640 + 512 * i, 512, "p (j c) -> p j c", c=P) for i in range(5))
        vnew = region(27200, 1024, "p (c n) -> p c n", c=2)
        state = region(28224, 512, "p (j e) -> p j e", e=P)
        LEVELS = (2, 4, 8, 16, 32)

        def dve_log1p(dve, e, z_, q_, shape_out):
            dve.tensor_scalar(q_, e, 2.0, None, ALU.add)
            dve.drain()
            dve.reciprocal(q_, q_)
            dve.drain()
            dve.tensor_tensor(z_, e, q_, ALU.mult)
            dve.drain()
            dve.tensor_tensor(e, z_, z_, ALU.mult)
            dve.drain()
            dve.tensor_scalar(q_, e, 1.0 / 13, None, ALU.mult)
            for n in (11, 9, 7, 5, 3):
                dve.drain()
                dve.scalar_tensor_tensor(q_, q_, 1.0 / n, e, ALU.add, ALU.mult)
            dve.drain()
            dve.scalar_tensor_tensor(shape_out, q_, 1.0, z_, ALU.add, ALU.mult)
            dve.drain()
            dve.tensor_scalar(shape_out, shape_out, 2.0, None, ALU.mult)
            dve.drain()

        def dve_gdn_prep(dve):
            wide = [P, NT, H]
            dve.tensor_tensor(g_u, a_in, row("dt_bias").unsqueeze(1).broadcast_to(wide), ALU.add)
            dve.drain()
            dve.scalar_tensor_tensor(g_s, g_u, -1.0, g_u, ALU.mult, ALU.max).then_inc(S("g_abs"), 1)
            nxt(dve, "g_exp")
            dve_log1p(dve, g_e, g_z, g_q, g_s)
            dve.scalar_tensor_tensor(g_s, g_u, 0.0, g_s, ALU.max, ALU.add)
            dve.drain()
            dve.scalar_tensor_tensor(g_g, g_s, -1.0, g_ea, ALU.mult, ALU.mult).then_inc(S("g_ready"), 1)
            nxt(dve, "g_squares")
            dve.tensor_reduce(g_ss, squares.rearrange("p t (h e) -> p t h e", e=HD), AX_X, ALU.add)\
               .then_inc(S("g_ss"), 1)
            nxt(dve, "g_sums")
            dve.tensor_copy(g_G, bank[0][:, 0:32].rearrange("p (t h) -> p t h", t=NT))
            dve.drain()
            dve.tensor_tensor(g_kdec, bank[0][:, 32:64].rearrange("p (t h) -> p t h", t=NT), g_G, ALU.subtract)\
               .then_inc(S("g_G"), 1)
            nxt(dve, "g_roots")
            dve.reciprocal(g_ss, g_r)
            dve.drain()
            dve.tensor_scalar(g_ss[:, :, 0:H], g_ss[:, :, 0:H], HD ** -0.5, None, ALU.mult)
            dve.drain()
            nxt(dve, "g_exps")

            def scaled(dst, src, by):
                for t in range(NT):
                    dve.tensor_tensor(dst[:, t, :].rearrange("p (h e) -> p h e", e=HD),
                                      src[:, t, :].rearrange("p (h e) -> p h e", e=HD),
                                      by[:, t, :].unsqueeze(2).broadcast_to([P, H, HD]), ALU.mult)

            scaled(qn, qn, g_ss[:, :, 0:H])
            scaled(kn, kn, g_ss[:, :, H:2 * H])
            scaled(vb, vb, g_beta)
            dve.drain()
            scaled(qg, qn, g_expG)
            scaled(kb, kn, g_beta)
            scaled(kdec, kn, g_kdec)
            dve.drain()
            scaled(kbG, kb, g_expG)
            dve.memset(state, 0.0)
            dve.memset(vnew, 0.0)
            dve.drain().then_inc(S("g_scaled"), 1)

        def act_gdn_prep(act):
            act.activation(squares, qkv[:, :, 0:1024], ACT.Square).then_inc(S("g_squares"), 1)
            nxt(act, "g_abs")
            act.activation(g_e, g_s, ACT.Exp, scale=-1.0)
            act.activation(g_ea, row("a_log").unsqueeze(1).broadcast_to([P, NT, H]), ACT.Exp)
            act.activation(g_beta, b_in, ACT.Sigmoid)
            act.drain().then_inc(S("g_exp"), 1)
            nxt(act, "g_ss")
            act.activation(g_r, g_ss, ACT.Sqrt, bias=eps).then_inc(S("g_roots"), 1)
            nxt(act, "g_G")
            act.activation(g_expG, g_G, ACT.Exp)
            act.activation(g_kdec, g_kdec, ACT.Exp)
            for c in range(2):
                for i in range(2):
                    r = slice(64 * i, 64 * i + 64)
                    src = bank[0][r, 64 + 32 * c:96 + 32 * c].rearrange("p (t j i) -> p t j i", t=NT, i=2)
                    act.activation(g_dec[r, :, c, :], src[:, :, :, i], ACT.Exp)
            act.drain().then_inc(S("g_exps"), 1)

        def pe_gdn_prep(pe):
            nxt(pe, "g_ready")
            g = g_g.rearrange("p t h -> p (t h)")
            for i, name in enumerate(("cumsum", "chunk_all", "chunk0", "chunk1")):
                mm = pe.matmul(bank[0][:, 32 * i:32 * i + 32], con(name), g, start=True, stop=True)
            mm.then_inc(S("g_sums"), 1)
            nxt(pe, "g_scaled")

        def place(h):
            return 4 * (h % 2) + h // 2

        def by_parity(x):
            return x.rearrange("p (j i) -> p i j", i=2)

        def heads(x, g):
            return x[:, 4 * g:4 * g + 4, :].rearrange("p h c -> p (h c)")

        def pe_gdn(pe, t):
            if t:
                nxt(pe, "g_state")
            for i, x in enumerate((kn, kb, qn, qg)):
                for j in range(NPAIR):
                    mm = pe.transpose(bank[i][:, j * P:(j + 1) * P], x[:, t, j * P:(j + 1) * P], ident)
                mm.then_inc(S("g_turned"), 1)
            nxt(pe, "g_U")
            for g in range(2):
                mm = pe.matmul(bank[4 + g][:, :], ones, heads(gU, g), start=True, stop=True)
            mm.then_inc(S("g_Grow"), 1)
            nxt(pe, "g_T_even", 2)
            nxt(pe, "g_T_odd", 2)
            for h in range(H):
                j, r = h // 2, slice(64 * (h % 2), 64 * (h % 2) + 64)
                mm = pe.matmul(bank[6 + h % 2][:, j * P:(j + 1) * P], kT[r, j, :], kbT[r, j, :],
                               start=True, stop=True)
            mm.then_inc(S("g_kk"), 1)
            for h in range(H):
                j, r = h // 2, slice(64 * (h % 2), 64 * (h % 2) + 64)
                mm = pe.matmul(bank[h % 2][:, j * P:(j + 1) * P], kT[r, j, :], qT[r, j, :],
                               start=True, stop=True)
            mm.then_inc(S("g_kq"), 1)
            for g in range(2):
                nxt(pe, "g_T1")
                for h in range(4 * g, 4 * g + 4):
                    mm = pe.matmul(bank[2 + g][:, (h % 4) * P:(h % 4 + 1) * P], MTl[:, h, :], ident,
                                   start=True, stop=True)
                mm.then_inc(S("g_X1"), 1)
            for lv in LEVELS:
                last = lv == LEVELS[-1]
                for g in range(2):
                    nxt(pe, "g_Ml")
                    nxt(pe, "g_T")
                    for h in range(4 * g, 4 * g + 4):
                        mm = pe.matmul(bank[g][:, (h % 4) * P:(h % 4 + 1) * P], MTl[:, h, :], Tm[:, h, :],
                                       start=True, stop=True)
                    mm.then_inc(S("g_X"), 1)
                for g in range(2):
                    nxt(pe, "g_Xs")
                    for h in range(4 * g, 4 * g + 4):
                        mm = pe.matmul(bank[4 + g][:, (h % 4) * P:(h % 4 + 1) * P], Xs[:, h, :], TT[:, h, :],
                                       start=True, stop=True)
                    if not last:
                        for h in range(4 * g, 4 * g + 4):
                            mm = pe.matmul(bank[2 + g][:, (h % 4) * P:(h % 4 + 1) * P], TT[:, h, :], Xs[:, h, :],
                                           start=True, stop=True)
                    mm.then_inc(S("g_Y"), 1)
            nxt(pe, "g_T", 2)
            for h in range(H):
                j, r = h // 2, slice(64 * (h % 2), 64 * (h % 2) + 64)
                mm = pe.matmul(bank[1][r, j * P:(j + 1) * P], kbG[:, t, h * HD:(h + 1) * HD], TT[:, place(h), :],
                               start=True, stop=True)
            mm.then_inc(S("g_w"), 1)
            nxt(pe, "g_nw")
            for c in range(2):
                rc = slice(64 * c, 64 * c + 64)
                if c:
                    nxt(pe, "g_state")
                for j in range(NPAIR):
                    dst = bank[6][rc, j * P:(j + 1) * P]
                    pe.matmul(dst, nwT[:, j, rc], state[:, j, :], start=True, stop=False)
                    for i in range(2):
                        h = 2 * j + i
                        mm = pe.matmul(bank[6][rc, h * HD:(h + 1) * HD], TT[:, place(h), rc],
                                       vb[:, t, h * HD:(h + 1) * HD], start=False, stop=(i == 1))
                mm.then_inc(S("g_v"), 1)
                nxt(pe, "g_vnew")
                for j in range(NPAIR):
                    pe.matmul(bank[7][rc, j * P:(j + 1) * P], qgT[:, j, rc], state[:, j, :], start=True, stop=False)
                    for i in range(2):
                        h = 2 * j + i
                        pe.matmul(bank[7][rc, h * HD:(h + 1) * HD], attnT[:, place(h), rc],
                                  vnew[:, c, h * HD:(h + 1) * HD], start=False, stop=(i == 1))
                for j in range(NPAIR):
                    mm = pe.matmul(bank[0][:, j * P:(j + 1) * P], kdec[:, t, j * P:(j + 1) * P],
                                   vnew[:, c, j * P:(j + 1) * P], start=True, stop=True)
                mm.then_inc(S("g_out"), 1)
            nxt(pe, "g_o_taken")

        def act_gdn(act, t):
            for i, dst in enumerate((kT, kbT, qT, qgT)):
                nxt(act, "g_turned")
                if i % 2 == 0:
                    act.activation(dst.rearrange("p j c -> p (j c)"), bank[i][:, :], ACT.Copy)\
                       .then_inc(S("g_T_even"), 1)
            nxt(act, "g_diff")
            act.activation(DT, DT, ACT.Exp).then_inc(S("g_decay"), 1)
            for lv in LEVELS:
                for g in range(2):
                    nxt(act, "g_X")
                    act.activation(heads(Xs, g), bank[g][:, :], ACT.Copy).then_inc(S("g_Xs"), 1)
            nxt(act, "g_w")
            act.activation(nwT.rearrange("p j c -> p (j c)"), bank[1][:, :], ACT.Copy, scale=-1.0)\
               .then_inc(S("g_nw"), 1)
            for c in range(2):
                rc = slice(64 * c, 64 * c + 64)
                nxt(act, "g_v")
                act.activation(vnew[rc, c, :], bank[6][rc, :], ACT.Copy).then_inc(S("g_vnew"), 1)
            nxt(act, "g_out", 2)
            act.activation(mixed[:, t, 0:512], bank[7][:, :], ACT.Copy).then_inc(S("g_o_taken"), 1)

        def pool_gdn(pool, t):
            if t:
                pool.wait_ge(S("g_out"), 2 * t)
            else:
                nxt(pool, "g_ready")
            for g in range(2):
                four = [P, NPAIR, P]
                i = pool.tensor_tensor(gU[:, 4 * g:4 * g + 4, :], con("cumsum").unsqueeze(1).broadcast_to(four),
                                       by_parity(g_g[:, t, :])[:, g, :].unsqueeze(2).broadcast_to(four), ALU.mult)
            i.then_inc(S("g_U"), 1)
            nxt(pool, "g_MT")
            nxt(pool, "g_X1", 2)
            for n, lv in enumerate(LEVELS):
                for g in range(2):
                    if n:
                        nxt(pool, "g_X")
                    pool.tensor_tensor(MTl[:, 4 * g:4 * g + 4, :], MT[:, 4 * g:4 * g + 4, :],
                                       con(f"level{lv}").unsqueeze(1).broadcast_to([P, 4, P]), ALU.mult)\
                        .then_inc(S("g_Ml"), 1)
            nxt(pool, "g_X", 2)

        def dve_gdn(dve, t):
            for i, dst in enumerate((kT, kbT, qT, qgT)):
                nxt(dve, "g_turned")
                if i % 2 == 1:
                    dve.tensor_copy(dst.rearrange("p j c -> p (j c)"), bank[i][:, :]).then_inc(S("g_T_odd"), 1)
            nxt(dve, "g_Grow")
            for g in range(2):
                dve.tensor_tensor(DT[:, 4 * g:4 * g + 4, :], bank[4 + g][:, :].rearrange("p (h c) -> p h c", c=P),
                                  by_parity(g_G[:, t, :])[:, g, :].unsqueeze(2).broadcast_to([P, 4, P]), ALU.subtract)
            dve.drain()
            dve.tensor_scalar(DT, DT, 0.0, None, ALU.min).then_inc(S("g_diff"), 1)
            nxt(dve, "g_decay")
            dve.tensor_tensor(DT, DT, con("cumsum").unsqueeze(1).broadcast_to([P, H, P]), ALU.mult)
            dve.drain()
            nxt(dve, "g_kk")
            for g in range(2):
                dve.tensor_tensor(heads(MT, g), bank[6 + g][:, :], heads(DT, g), ALU.mult)
            dve.drain().then_inc(S("g_MT"), 1)
            nxt(dve, "g_kq")
            for g in range(2):
                four = [P, 4, P]
                hs = slice(4 * g, 4 * g + 4)
                dve.tensor_tensor(MTl[:, hs, :], MT[:, hs, :], con("level1").unsqueeze(1).broadcast_to(four), ALU.mult)
                dve.drain()
                dve.tensor_tensor(TT[:, hs, :], ident.unsqueeze(1).broadcast_to(four), MTl[:, hs, :],
                                  ALU.subtract).then_inc(S("g_T1"), 1)
            for g in range(2):
                dve.tensor_tensor(heads(attnT, g), bank[g][:, :], heads(DT, g), ALU.mult)
            for g in range(2):
                nxt(dve, "g_X1")
                dve.drain()
                dve.tensor_tensor(Tm[:, 4 * g:4 * g + 4, :], ident.unsqueeze(1).broadcast_to([P, 4, P]),
                                  bank[2 + g][:, :].rearrange("p (h c) -> p h c", c=P), ALU.subtract)\
                   .then_inc(S("g_T"), 1)
            for lv in LEVELS:
                for g in range(2):
                    nxt(dve, "g_Y")
                    dve.drain()
                    i = dve.tensor_tensor(heads(TT, g), heads(TT, g), bank[4 + g][:, :], ALU.subtract)
                    if lv != LEVELS[-1]:
                        i = dve.tensor_tensor(heads(Tm, g), heads(Tm, g), bank[2 + g][:, :], ALU.subtract)
                    i.then_inc(S("g_T"), 1)
            for c in range(2):
                nxt(dve, "g_out")
                for i in range(2):
                    r = slice(64 * i, 64 * i + 64)
                    dve.tensor_tensor(state[r, :, r], state[r, :, r],
                                      g_dec[r, t, c, :].unsqueeze(2).broadcast_to([64, NPAIR, HD]), ALU.mult)
                dve.drain()
                for i in range(2):
                    r = slice(64 * i, 64 * i + 64)
                    dve.tensor_tensor(state[r, :, r], state[r, :, r],
                                      bank[0][r, :].rearrange("p (j e) -> p j e", e=P)[:, :, r], ALU.add)
                dve.drain().then_inc(S("g_state"), 1)

        def act_gdn_end(act):
            act.drain()
            act.activation(squares[:, :, 0:512], mixed[:, :, 0:512], ACT.Square).then_inc(S("g_osq"), 1)
            act.activation(z, z, ACT.Silu)
            nxt(act, "g_oss")
            act.activation(g_or, g_os, ACT.Sqrt, bias=eps, scale=1.0 / HD)
            act.drain().then_inc(S("g_oroot"), 1)

        def dve_gdn_end(dve):
            nxt(dve, "g_osq")
            dve.tensor_reduce(g_os, squares[:, :, 0:512].rearrange("p t (h e) -> p t h e", e=HD), AX_X, ALU.add)\
               .then_inc(S("g_oss"), 1)
            nxt(dve, "g_oroot")
            dve.reciprocal(g_os, g_or)
            dve.drain()
            for by in (0, 1):
                for t in range(NT):
                    o = mixed[:, t, 0:512].rearrange("p (h e) -> p h e", e=HD)
                    r = g_os[:, t, :].unsqueeze(2) if by == 0 else row("gdn_out_norm").unsqueeze(1)
                    dve.tensor_tensor(o, o, r.broadcast_to([P, H, HD]), ALU.mult)
                dve.drain()
            for t in range(NT):
                dve.tensor_tensor(mixed[:, t, 0:512], mixed[:, t, 0:512], z[:, t, :], ALU.mult)
            dve.drain().then_inc(S("mixed_ready"), 1)

        def dve_gate(dve, dg, m0):
            for k in range(KD):
                i = dve.tensor_scalar(dg[:, k * P:(k + 1) * P], ident, mod[:, m0 + k:m0 + k + 1], None, ALU.mult)
            i.then_inc(S("gate_diag"), 1)

        def pe_gate(pe, dg, b0):
            nxt(pe, "gate_diag")
            for half in range(2):
                mm = pe.matmul(bank[b0 + half][:, :], ones, dg[:, 512 * half:512 * half + 512], start=True, stop=True)
            mm.then_inc(S("gate_row"), 1)

        def dve_gate_row(dve, gate, b0):
            nxt(dve, "gate_row")
            dve.tensor_copy(gate[:, 0:512], bank[b0][:, :])
            dve.tensor_copy(gate[:, 512:D], bank[b0 + 1][:, :])
            dve.drain().then_inc(S("gate_taken"), 1)

        gate1 = region(24656, D)
        diag1 = region(25680, D)

        def act_turned(act):
            for k in range(0, KD, 2):
                nxt(act, "x_turned", 2 if k else 1)
                i = act.activation(hT[:, k, :], bank[k][:, :], ACT.Copy)
            tally[(str(act.engine), "x_turned")] += 1
            i.then_inc(S("hT_even"), 1)

        def dve_turned(dve):
            for k in range(1, KD, 2):
                nxt(dve, "x_turned", 2)
                i = dve.tensor_copy(hT[:, k, :], bank[k][:, :])
            i.then_inc(S("hT_odd"), 1)

        def pe_down(pe, name, n_slots_, lhs):
            for i in range(n_slots_):
                s = FIRST[name] + i
                need(pe, s)
                w = slot_view(s, D)
                for kk_ in range(2):
                    k = 2 * i + kk_
                    for t in range(NT):
                        for half in range(2):
                            mm = pe.matmul(bank[2 * t + half][:, :], lhs(k, t), w[:, kk_, 512 * half:512 * half + 512],
                                           start=(k == 0), stop=(k == 2 * n_slots_ - 1))
                mm.then_inc(S("slots_used"), 1)

        def dve_out1(dve):
            dve.wait_ge(S("slots_used"), FIRST["w_out"] + 4)
            tmp = region(26704, 1024, "p (b n) -> p b n", b=2)
            for t in range(NT):
                for half in range(2):
                    c = slice(512 * half, 512 * half + 512)
                    dve.tensor_tensor(tmp[:, half, :], bank[2 * t + half][:, :], gate1[:, c], ALU.mult)
                dve.drain()
                dve.tensor_tensor(X[:, t, :], X[:, t, :], tmp.rearrange("p b n -> p (b n)"), ALU.add)
                dve.drain()

        NR = N_GRP + N_EXP
        SLOTS_ = 2 * T
        xn2 = region(4096, 4096, "p (t n) -> p t n", t=NT)
        h2tok = region(0, 4096, "p (t n) -> p t n", t=NT)
        m_G = region(4096, 4096, "p (t s) -> p t s", t=NT)
        m_xT = region(8192, KD * (SLOTS_ + CAP), "p (k s) -> p k s", k=KD)
        m_yT = region(19000, KD * (SLOTS_ + CAP), "p (k s) -> p k s", k=KD)
        m_C = region(19000, 4096, "p (t s) -> p t s", t=NT)
        m_eq = region(23096, 4096, "p (t s) -> p t s", t=NT)
        m_CT = region(0, 4096, "p (s t) -> p s t", t=T)
        m_sg = region(28216, 4 * CAP, "p (b f) -> p b f", b=2)
        m_hid = region(28728, 4 * CAP, "p (b f s) -> p b f s", b=2, f=2)
        m_y = region(8192, 8192, "p (s n) -> p s n", n=D)
        m_rw = region(17152, KD * NR, "p (k n) -> p k n", n=NR)
        junk2 = region(10240, D)

        def mr(at, width, pattern=None, **kw):
            r = region(17440 + at, width)
            return r.rearrange(pattern, **kw) if pattern else r

        r_lg = mr(0, NT * NR, "p (t n) -> p t n", t=NT)
        r_a = mr(144, 16, "p (t g) -> p t g", t=NT)
        r_b = mr(160, 16, "p (t g) -> p t g", t=NT)
        r_goh = mr(176, 16, "p (t g) -> p t g", t=NT)
        r_m = mr(192, 4)
        r_v = mr(196, 4)
        r_pg = mr(200, 4)
        r_m1 = mr(204, 4)
        r_m2 = mr(208, 4)
        r_w1 = mr(212, 4)
        r_w2 = mr(216, 4)
        r_ig = mr(224, 32, "p (t e) -> p t e", t=NT)
        r_o1 = mr(256, 32, "p (t e) -> p t e", t=NT)
        r_o2 = mr(288, 32, "p (t e) -> p t e", t=NT)
        r_c = mr(320, 32, "p (t e) -> p t e", t=NT)
        r_sel = mr(384, 128, "p (t e g) -> p t e g", t=NT, g=N_GRP)
        r_E = mr(512, 256, "p (c t e) -> p c t e", c=2, t=NT)
        r_M = mr(768, 128, "p (t e) -> p t e", t=NT)
        r_rank = mr(896, 128, "p (t e) -> p t e", t=NT)
        r_prod = mr(1024, 256, "p (c t e) -> p c t e", c=2, t=NT)
        r_place = mr(1280, 8, "p (c t) -> p c t", c=2)
        r_cnt = mr(1288, 32)
        r_ends = mr(1320, 32)
        r_off = mr(1352, 32)
        r_pm = mr(1384, 64, "p (c t s) -> p c t s", c=2, t=NT)
        r_offi = mr(1448, 32).bitcast(I32)
        o_expert = mr(1480, 16).bitcast(I32)
        o_place = mr(1496, 16).bitcast(I32)
        o_count = mr(1512, 2).bitcast(I32)

        gate2 = region(7168, D)
        diag2 = region(6144, D)

        def act_router_weights(act):
            for n0, name in ((0, "w_group"), (N_GRP, "w_router")):
                act.dma_start(m_rw[:, :, n0:n0 + a[name].shape[-1]],
                              a[name][0].rearrange("(k p) n -> p k n", p=P)).then_inc(S("rw_loaded"), 16)

        def pe_route(pe):
            pe_hT(pe)
            nxt(pe, "rw_loaded", 32)
            for t in range(NT):
                for k in range(KD):
                    mm = pe.matmul(bank[0][:, NR * t:NR * t + NR], tokens(k, t), m_rw[:, k, :],
                                   start=(k == 0), stop=(k == KD - 1))
            mm.then_inc(S("r_logits"), 1)
            for t in range(1, NT):
                pe_h2(pe, t)
            pe.wait_ge(S("r_taken"), 1)
            pe_h2(pe, 0)
            nxt(pe, "h2_ready", NT)
            nxt(pe, "r_M")
            for t in range(NT):
                for s in range(t):
                    pe.matmul(bank[2][:, 32 * t:32 * t + 32], ones, r_M[:, s, :], start=(s == 0), stop=False)
                pe.matmul(bank[2][:, 32 * t:32 * t + 32], con("before"), r_M[:, t, :], start=(t == 0), stop=True)
            for t in range(NT):
                mm = pe.matmul(bank[2][:, 128:160], ones, r_M[:, t, :], start=(t == 0), stop=(t == NT - 1))
            mm.then_inc(S("r_ranks"), 1)
            nxt(pe, "r_G", NT)
            for k in range(KD):
                for half in range(2):
                    n = 2 * k + half
                    if n >= 8:
                        nxt(pe, ("m_x_even", "m_x_odd")[half])
                    for t in range(NT):
                        mm = pe.matmul(bank[n % 8][:, :], h2tok[:, t, k * P:(k + 1) * P],
                                       m_G[:, t, 512 * half:512 * half + 512], start=(t == 0), stop=(t == NT - 1))
                    mm.then_inc(S("m_x_ps"), 1)
            nxt(pe, "m_x_even", 4)
            nxt(pe, "m_x_odd", 4)
            nxt(pe, "r_C", NT)
            for s in range(8):
                for t in range(NT):
                    mm = pe.transpose(bank[s][:, t * P:(t + 1) * P], m_C[:, t, s * P:(s + 1) * P], ident)
                mm.then_inc(S("r_C_turned"), 1)
            nxt(pe, "r_CT_even", 4)
            nxt(pe, "r_CT_odd", 4)

        def pe_h2(pe, t):
            for k in range(KD):
                mm = pe.transpose(bank[2 * t + k // 4][:, (k % 4) * P:(k % 4 + 1) * P],
                                  hT[:, k, t * P:(t + 1) * P], ident)
            mm.then_inc(S("h2_turned"), 1)

        def act_h2(act):
            for t in (1, 2, 3, 0):
                nxt(act, "h2_turned")
                for half in range(2):
                    act.activation(h2tok[:, t, 512 * half:512 * half + 512], bank[2 * t + half][:, :], ACT.Copy)
                act.drain().then_inc(S("h2_ready"), 1)

        def act_route(act):
            nxt(act, "r_gmax")
            act.activation(r_a, r_a, ACT.Exp)
            act.drain().then_inc(S("r_gexp"), 1)
            nxt(act, "r_diff")
            act.activation(r_w2, r_m2, ACT.Exp).then_inc(S("r_wexp"), 1)
            for k in range(KD):
                nxt(act, "m_x_ps", 2 if k else 1)
                act.activation(m_xT[:, k, 0:512], bank[2 * k % 8][:, :], ACT.Copy).then_inc(S("m_x_even"), 1)
            nxt(act, "m_x_ps")
            for s in range(0, 8, 2):
                nxt(act, "r_C_turned", 2 if s else 1)
                act.activation(m_CT[:, s, :], bank[s][:, :], ACT.Copy).then_inc(S("r_CT_even"), 1)

        def dve_first_of(dve, dst, values, best, tie, n, tmp):
            shape = [P, NT, n]
            dve.tensor_tensor(tmp, values, best.unsqueeze(2).broadcast_to(shape), ALU.is_equal)
            dve.drain()
            dve.tensor_tensor(tmp, tmp, con(tie).unsqueeze(1).broadcast_to(shape), ALU.mult)
            dve.drain()
            dve.tensor_reduce(r_v, tmp, AX_X, ALU.max)
            dve.drain()
            dve.tensor_tensor(dst, tmp, r_v.unsqueeze(2).broadcast_to(shape), ALU.is_equal)
            dve.drain()

        def dve_route(dve):
            nxt(dve, "r_logits")
            at = ROWS["b_group"][0]
            dve.tensor_tensor(r_lg, bank[0][:, 0:NT * NR].rearrange("p (t n) -> p t n", t=NT),
                              rows[:, at:at + NR].unsqueeze(1).broadcast_to([P, NT, NR]), ALU.add)
            dve.drain().then_inc(S("r_taken"), 1)
            groups = r_lg[:, :, 0:N_GRP]
            dve.tensor_reduce(r_m, groups, AX_X, ALU.max)
            dve.drain()
            dve.tensor_tensor(r_a, groups, r_m.unsqueeze(2).broadcast_to([P, NT, N_GRP]), ALU.subtract)\
               .then_inc(S("r_gmax"), 1)
            dve_first_of(dve, r_goh, groups, r_m, "tie4", N_GRP, r_b)
            for t in range(NT):
                dve.tensor_tensor(r_sel[:, t], r_lg[:, t, N_GRP:NR].rearrange("p (g e) -> p e g", g=N_GRP),
                                  r_goh[:, t, :].unsqueeze(1).broadcast_to([P, EPG, N_GRP]), ALU.mult)
            dve.drain()
            dve.tensor_reduce(r_ig, r_sel, AX_X, ALU.add)
            dve.drain()
            dve.tensor_reduce(r_m1, r_ig, AX_X, ALU.max)
            dve.drain()
            dve_first_of(dve, r_o1, r_ig, r_m1, "tie8", EPG, r_c)
            dve.scalar_tensor_tensor(r_ig, r_o1, -BIG, r_ig, ALU.mult, ALU.add)
            dve.drain()
            dve.tensor_reduce(r_m2, r_ig, AX_X, ALU.max)
            dve.drain()
            dve_first_of(dve, r_o2, r_ig, r_m2, "tie8", EPG, r_c)
            dve.tensor_tensor(r_m2, r_m2, r_m1, ALU.subtract).then_inc(S("r_diff"), 1)
            nxt(dve, "r_gexp")
            dve.tensor_reduce(r_pg, r_a, AX_X, ALU.add)
            nxt(dve, "r_wexp")
            dve.drain()
            dve.tensor_scalar(r_w1, r_w2, 1.0, None, ALU.add)
            dve.drain()
            dve.tensor_tensor(r_w1, r_w1, r_pg, ALU.mult)
            dve.drain()
            dve.reciprocal(r_w1, r_w1)
            dve.drain()
            dve.tensor_tensor(r_w2, r_w2, r_w1, ALU.mult)
            for c, o in enumerate((r_o1, r_o2)):
                for t in range(NT):
                    shape = [P, N_GRP, EPG]
                    dve.tensor_tensor(r_E[:, c, t, :].rearrange("p (g e) -> p g e", g=N_GRP),
                                      r_goh[:, t, :].unsqueeze(2).broadcast_to(shape),
                                      o[:, t, :].unsqueeze(1).broadcast_to(shape), ALU.mult)
            dve.drain()
            dve.tensor_tensor(r_M, r_E[:, 0], r_E[:, 1], ALU.add)
            dve.drain().then_inc(S("r_M"), 1)
            nxt(dve, "r_ranks")
            dve.tensor_copy(r_cnt, bank[2][:, 128:160])
            dve.drain()
            dve.tensor_tensor_scan(r_ends, r_cnt, r_cnt, 0.0, ALU.add, ALU.bypass)
            dve.drain()
            dve.tensor_tensor(r_off, r_ends, r_cnt, ALU.subtract)
            dve.drain()
            dve.tensor_copy(r_offi, r_off)
            dve.tensor_tensor(r_rank, bank[2][:, 0:128].rearrange("p (t e) -> p t e", t=NT),
                              r_off.unsqueeze(1).broadcast_to([P, NT, N_EXP]), ALU.add)
            dve.drain()
            for c in range(2):
                dve.tensor_tensor(r_prod[:, c], r_E[:, c], r_rank, ALU.mult)
            dve.drain()
            dve.tensor_reduce(r_place, r_prod, AX_X, ALU.add)
            dve.drain()
            for s in range(8):
                dve.tensor_scalar(r_pm[:, :, :, s], r_place, float(P * s), None, ALU.subtract)
            dve.drain()
            for t in range(NT):
                first, second = m_C[:, t, :], m_eq[:, t, :]
                for c, eq in enumerate((first, second)):
                    shape = [P, 8, P]
                    dve.tensor_tensor(eq.rearrange("p (s i) -> p s i", i=P), con("iota").unsqueeze(1).broadcast_to(shape),
                                      r_pm[:, c, t, :].unsqueeze(2).broadcast_to(shape), ALU.is_equal)
                dve.drain().then_inc(S("m_eq"), 1)
            for t in range(NT):
                nxt(dve, "r_G")
                dve.tensor_scalar(m_C[:, t, :], m_C[:, t, :], r_w1[:, t:t + 1], None, ALU.mult)
                dve.drain()
                dve.scalar_tensor_tensor(m_C[:, t, :], m_eq[:, t, :], r_w2[:, t:t + 1], m_C[:, t, :],
                                         ALU.mult, ALU.add).then_inc(S("r_C"), 1)
            for k in range(KD):
                nxt(dve, "m_x_ps", 2)
                dve.tensor_copy(m_xT[:, k, 512:1024], bank[(2 * k + 1) % 8][:, :]).then_inc(S("m_x_odd"), 1)
            for s in range(1, 8, 2):
                nxt(dve, "r_C_turned", 2)
                dve.tensor_copy(m_CT[:, s, :], bank[s][:, :]).then_inc(S("r_CT_odd"), 1)

        def pool_route(pool):
            for t in range(NT):
                nxt(pool, "m_eq")
                pool.tensor_tensor(m_G[:, t, :], m_C[:, t, :], m_eq[:, t, :], ALU.add).then_inc(S("r_G"), 1)

        w_gate, w_up, w_down = a["w_gate"][0], a["w_up"][0], a["w_down"][0]
        gu = [ring[:, 2 * b:2 * b + 2, :].rearrange("p u (k n) -> p u k n", n=F_EXP) for b in range(2)]
        dn = [ring[:, 4 + b, :].rearrange("p (f n) -> p f n", n=D) for b in range(2)]

        def flat_rows(w, e, n):
            rows_ = w.shape[1]
            return w.rearrange("e k n -> (e k) n")[bass.ds(e * rows_, rows_), :].rearrange("(k p) n -> p k n", p=P)

        def sp_gate_up(sp, e, b):
            if not (isinstance(e, int) and e < 2):
                sp.wait_ge(S("gu_used"), e - 1)
            sp.dma_start(gu[b][:, 0], flat_rows(w_gate, e, F_EXP)).then_inc(S(f"gu_loaded{b}"), 16)
            sp.dma_start(gu[b][:, 1], flat_rows(w_up, e, F_EXP)).then_inc(S(f"gu_loaded{b}"), 16)

        def sp_down(sp, e, b):
            if not (isinstance(e, int) and e < 2):
                sp.wait_ge(S("dn_used"), e - 1)
            sp.dma_start(dn[b], flat_rows(w_down, e, D)).then_inc(S(f"dn_loaded{b}"), 16)

        def sp_moe_first(sp):
            sp.wait_ge(S("slots_used"), MOE_AT)
            for e in range(2):
                sp_gate_up(sp, e, e)
                sp_down(sp, e, e)

        def sp_moe(sp):
            sp_gate_up(sp, 2, 0)
            with sp.Fori(1, N_EXP // 2 - 1) as i:
                sp_gate_up(sp, 2 * i + 1, 1)
                sp_down(sp, 2 * i, 0)
                sp_gate_up(sp, 2 * i + 2, 0)
                sp_down(sp, 2 * i + 1, 1)
            sp_gate_up(sp, N_EXP - 1, 1)
            sp_down(sp, N_EXP - 2, 0)
            sp_down(sp, N_EXP - 1, 1)

        def first_place(e, expert):
            return e.value_load(r_offi[0:1, bass.ds(expert, 1)], min_val=0, max_val=SLOTS_)

        def places(x, at):
            return x[:, :, bass.ds(at, CAP)]

        def pe_gate_up(pe, dst, w, at):
            for u in range(2):
                for f in range(2):
                    c = (2 * u + f) * CAP
                    for k in range(KD):
                        mm = pe.matmul(dst[:, c:c + CAP], w[:, u, k, f * P:(f + 1) * P], m_xT[:, k, bass.ds(at, CAP)],
                                       start=(k == 0), stop=(k == KD - 1))
            return mm

        def pe_down_t(pe, dst, w, hid):
            for k in range(KD):
                for f in range(2):
                    mm = pe.matmul(dst[k // 4][:, (k % 4) * CAP:(k % 4 + 1) * CAP], w[:, f, k * P:(k + 1) * P],
                                   hid[:, f, :], start=(f == 0), stop=(f == 1))
            return mm

        def chunks(b):
            return b[:, 0:4 * CAP].rearrange("p (k s) -> p k s", s=CAP)

        def pe_moe(pe):
            def gate_up(i, b):
                at = first_place(pe, 2 * i + b)
                pe.wait_ge(S(f"gu_loaded{b}"), 32 * (i + 1))
                pe_gate_up(pe, bank[b], gu[b], at).then_inc(S("gu_used"), 1)

            def down(i, b):
                pe.wait_ge(S(f"dn_loaded{b}"), 16 * (i + 1))
                pe.wait_ge(S("m_hid"), 2 * i + b + 1)
                if not (isinstance(i, int) and i <= 0):
                    pe.wait_ge(S("m_y_act"), 2 * i + b - 1)
                    pe.wait_ge(S("m_y_dve"), 2 * i + b - 1)
                pe_down_t(pe, bank[2 + 2 * b:4 + 2 * b], dn[b], m_hid[:, b]).then_inc(S("dn_used"), 1)

            gate_up(0, 0)
            gate_up(0, 1)
            down(0, 0)
            gate_up(1, 0)
            down(0, 1)
            gate_up(1, 1)
            down(1, 0)
            with pe.Fori(2, N_EXP // 2) as i:
                gate_up(i, 0)
                down(i - 1, 1)
                gate_up(i, 1)
                down(i, 0)
            down(N_EXP // 2 - 1, 1)

        def act_moe(act):
            def silu(i, b):
                act.wait_ge(S("gu_used"), 2 * i + b + 1)
                if not (isinstance(i, int) and i == 0):
                    act.wait_ge(S("m_hid"), 2 * i + b - 1)
                act.activation(m_sg[:, b, :], bank[b][:, 0:2 * CAP], ACT.Silu).then_inc(S("m_sg"), 1)

            def results(i, b):
                at = first_place(act, 2 * i + b)
                act.wait_ge(S("dn_used"), 2 * i + b + 1)
                act.activation(places(m_yT[:, 0:4, :], at), chunks(bank[2 + 2 * b]), ACT.Copy)
                act.drain().then_inc(S("m_y_act"), 1)

            silu(0, 0)
            silu(0, 1)
            results(0, 0)
            with act.Fori(1, N_EXP // 2) as i:
                silu(i, 0)
                results(i - 1, 1)
                silu(i, 1)
                results(i, 0)
            results(N_EXP // 2 - 1, 1)

        def dve_moe(dve):
            def hidden(i, b):
                dve.wait_ge(S("m_sg"), 2 * i + b + 1)
                dve.tensor_tensor(m_hid[:, b].rearrange("p f s -> p (f s)"), m_sg[:, b, :], bank[b][:, 2 * CAP:4 * CAP],
                                  ALU.mult)
                dve.drain().then_inc(S("m_hid"), 1)

            def results(i, b):
                at = first_place(dve, 2 * i + b)
                dve.wait_ge(S("dn_used"), 2 * i + b + 1)
                dve.tensor_copy(places(m_yT[:, 4:8, :], at), chunks(bank[3 + 2 * b]))
                dve.drain().then_inc(S("m_y_dve"), 1)

            hidden(0, 0)
            hidden(0, 1)
            results(0, 0)
            with dve.Fori(1, N_EXP // 2) as i:
                hidden(i, 0)
                results(i - 1, 1)
                hidden(i, 1)
                results(i, 0)
            results(N_EXP // 2 - 1, 1)

        MORE = -(-T // CAP) - 1
        ITEMS = (2 * T - 1) // CAP
        o_gu = region(0, 4096, "p (u k n) -> p u k n", base=hflat, u=2, n=F_EXP)
        o_dn = region(4096, 2048, "p (f n) -> p f n", n=D)

        def dve_more_list(dve):
            n = MORE * N_EXP
            flag, prefix, expert, place = (region(23096 + n * i, n, "p (e q) -> p e q", q=MORE) for i in range(4))
            sel, val = (region(23096 + 4 * n + ITEMS * n * i, ITEMS * n, "p (i j) -> p i j", j=n) for i in range(2))
            shape = [P, ITEMS, n]

            def flat(x):
                return x.rearrange("p e q -> p (e q)")

            for q in range(MORE):
                dve.tensor_scalar(flag[:, :, q], r_cnt, float(CAP * (q + 1)), None, ALU.is_gt)
                dve.tensor_scalar(place[:, :, q], r_off, float(CAP * (q + 1)), None, ALU.add)
                dve.tensor_copy(expert[:, :, q], con("iota")[:, 0:N_EXP])
            dve.drain()
            dve.tensor_tensor_scan(flat(prefix), flat(flag), flat(flag), 0.0, ALU.add, ALU.bypass)
            dve.drain()
            dve.tensor_copy(o_count[:, 0:1], prefix[:, N_EXP - 1, MORE - 1:MORE])
            dve.tensor_tensor(sel, flat(prefix).unsqueeze(1).broadcast_to(shape),
                              con("iota")[:, 1:ITEMS + 1].unsqueeze(2).broadcast_to(shape), ALU.is_equal)
            dve.drain()
            dve.tensor_tensor(sel, sel, flat(flag).unsqueeze(1).broadcast_to(shape), ALU.mult)
            dve.drain()
            for table, dst in ((expert, o_expert), (place, o_place)):
                dve.tensor_tensor(val, sel, flat(table).unsqueeze(1).broadcast_to(shape), ALU.mult)
                dve.drain()
                dve.tensor_reduce(flat(prefix)[:, 0:ITEMS], val, AX_X, ALU.add)
                dve.drain()
                dve.tensor_copy(dst[:, 0:ITEMS], flat(prefix)[:, 0:ITEMS])
                dve.drain()
            dve.memset(m_xT[:, :, SLOTS_:SLOTS_ + CAP], 0.0)
            dve.drain().then_inc(S("r_count"), 1)

        def more(e, body):
            e.wait_ge(S("r_count"), 1)
            count = e.value_load(o_count[0:1, 0:1], min_val=0, max_val=ITEMS)
            with e.Fori(0, ITEMS) as i:
                with e.If(count > i):
                    body(i)

        def further_place(e, i):
            return e.value_load(o_place[0:1, bass.ds(i, 1)], min_val=0, max_val=SLOTS_)

        def sp_more(sp):
            nxt(sp, "h2_ready", NT)
            nxt(sp, "m_x_ps", 2 * KD)

            def body(n):
                ex = sp.value_load(o_expert[0:1, bass.ds(n, 1)], min_val=0, max_val=N_EXP - 1)
                sp.wait_ge(S("o_free"), n + 1)
                sp.dma_start(o_gu[:, 0], flat_rows(w_gate, ex, F_EXP)).then_inc(S("o_loaded"), 16)
                sp.dma_start(o_gu[:, 1], flat_rows(w_up, ex, F_EXP)).then_inc(S("o_loaded"), 16)
                sp.dma_start(o_dn, flat_rows(w_down, ex, D)).then_inc(S("o_loaded"), 16)
            more(sp, body)

        def pe_more(pe):
            pe.drain().then_inc(S("o_free"), 1)

            def body(n):
                at = further_place(pe, n)
                pe.wait_ge(S("o_loaded"), 48 * n + 48)
                pe_gate_up(pe, bank[0], o_gu, at).then_inc(S("o_gate_up"), 1)
                pe.wait_ge(S("o_hid"), n + 1)
                pe_down_t(pe, bank[2:4], o_dn, m_hid[:, 0]).then_inc(S("o_y"), 1)
                pe.wait_ge(S("o_out"), n + 1)
                pe.transpose(bank[1][:, 0:P], ident, ident).then_inc(S("o_free"), 1)
            more(pe, body)

        def act_more(act):
            def body(n):
                act.wait_ge(S("o_gate_up"), n + 1)
                act.activation(m_sg[:, 0, :], bank[0][:, 0:2 * CAP], ACT.Silu).then_inc(S("o_sg"), 1)
            more(act, body)

        def dve_more(dve):
            def body(n):
                at = further_place(dve, n)
                dve.wait_ge(S("o_sg"), n + 1)
                dve.tensor_tensor(m_hid[:, 0].rearrange("p f s -> p (f s)"), m_sg[:, 0, :], bank[0][:, 2 * CAP:4 * CAP],
                                  ALU.mult)
                dve.drain().then_inc(S("o_hid"), 1)
                dve.wait_ge(S("o_y"), n + 1)
                for half in range(2):
                    dve.tensor_copy(places(m_yT[:, 4 * half:4 * half + 4, :], at), chunks(bank[2 + half]))
                dve.drain().then_inc(S("o_out"), 1)
            more(dve, body)

        def pe_moe_end(pe):
            nxt(pe, "m_y_act", N_EXP)
            nxt(pe, "m_y_dve", N_EXP)
            for s in range(8):
                for half in range(2):
                    b = (2 * s + half) % 6
                    if 2 * s + half >= 6:
                        nxt(pe, f"m_rows{b % 2}")
                    for k in range(4):
                        mm = pe.transpose(bank[b][:, k * P:(k + 1) * P], m_yT[:, 4 * half + k, s * P:(s + 1) * P], ident)
                    mm.then_inc(S("m_y_turned"), 1)
            nxt(pe, "m_rows0", 3)
            nxt(pe, "m_rows1", 3)
            nxt(pe, "gate_taken")
            for t in range(NT):
                for half in range(2):
                    for s in range(8):
                        mm = pe.matmul(bank[2 * t + half][:, :], m_CT[:, s, t * P:(t + 1) * P],
                                       m_y[:, s, 512 * half:512 * half + 512], start=(s == 0), stop=(s == 7))
                mm.then_inc(S("m_sum_ps"), 1)

        def act_moe_end(act):
            for s in range(8):
                nxt(act, "m_y_turned", 2 if s else 1)
                act.activation(m_y[:, s, 0:512], bank[2 * s % 6][:, :], ACT.Copy).then_inc(S("m_rows0"), 1)

        def dve_moe_end(dve):
            for s in range(8):
                nxt(dve, "m_y_turned", 2)
                dve.tensor_copy(m_y[:, s, 512:D], bank[(2 * s + 1) % 6][:, :]).then_inc(S("m_rows1"), 1)
            tmp = region(19000, 2048, "p (b n) -> p b n", b=2)
            for t in range(NT):
                nxt(dve, "m_sum_ps")
                for half in range(2):
                    c = slice(512 * half, 512 * half + 512)
                    dve.tensor_tensor(tmp[:, t % 2, c], bank[2 * t + half][:, :], gate2[:, c], ALU.mult)
                dve.drain()
                dve.tensor_tensor(X[:, t, :], X[:, t, :], tmp[:, t % 2, :], ALU.add)
            dve.drain()

        NPAIRS = NFF // 2
        ROUNDS = NPAIRS // 3
        F_SLOTS = 3 * NPAIRS
        hid_hi = region(0, HID, "p (f t) -> p f t", base=split["hid_high"], t=T)
        hid_lo = region(0, HID, "p (f t) -> p f t", base=split["hid_low"], t=T)
        f_sg = region(2 * HID, 1024, "p (b t) -> p b t", b=2)
        hT_hi = region(0, KD * T, "p (k t) -> p k t", base=split["hT_high"], t=T)
        hT_lo = split["hT"]
        f_hid = region(23552, 1024, "p (b t) -> p b t", b=2)
        post = region(HI_AT, D)
        f_tmp = region(HI_AT + 1024, 2048, "p (b n) -> p b n", b=2)
        f_sq = region(HI_AT + 3072, 1024, "p (b n) -> p b n", b=2)
        f_ss = region(HI_AT + 4096, 8, "p (t h) -> p t h", t=NT)
        f_r = region(HI_AT + 4104, 8, "p (c t) -> p c t", c=2)
        xnf = region(0, 4096, "p (t n) -> p t n", n=D)
        junkf = region(4096, D)
        xn3 = region(20480, 4096, "p (t n) -> p t n", n=D)

        def raw(n):
            return ring[:, n % 3, :]

        def high(n):
            return split["ring"][:, 3 + n % 3, :]

        def low(n):
            return split["ring"][:, n % 3, :]

        def dve_split(dve, hi, x, lo):
            dve.tensor_copy(hi, x)
            dve.drain()
            return dve.tensor_tensor(lo, x, hi.bitcast(F32), ALU.subtract)

        def sp_ffn(sp, tag):
            f = FIRST[tag]
            wg, wu = a[f"{tag}_w_gate_2"][0], a[f"{tag}_w_up_2"][0]

            def load_slot(n, it, src):
                sp.dma_start(raw(n).rearrange("p (k n) -> p k n", n=src.shape[-1]),
                             src.rearrange("(k p) n -> p k n", p=P)).then_inc(S(f"{tag}_raw{n % 3}"), 16)

            sp.wait_ge(S("slots_used"), f)
            for jj in range(3):
                load_slot(jj, 0, (wg, wu)[jj % 2][:, 256 * (jj // 2):256 * (jj // 2) + 256])
            for jj in range(3, 6):
                sp.wait_ge(S("slots_used"), f + jj - 2)
                load_slot(jj, 0, (wg, wu)[jj % 2][:, 256 * (jj // 2):256 * (jj // 2) + 256])
            with sp.Fori(1, ROUNDS) as it:
                for jj in range(6):
                    sp.wait_ge(S("slots_used"), 6 * it + (f + jj - 2))
                    load_slot(jj, it, (wg, wu)[jj % 2][:, bass.ds(768 * it + 256 * (jj // 2), 256)])
            for n in range(6 * ROUNDS, F_SLOTS):
                sp.wait_ge(S("slots_used"), f + n - 2)
                if n < 2 * NPAIRS:
                    load_slot(n, 0, (wg, wu)[n % 2][:, 256 * (n // 2):256 * (n // 2) + 256])
                else:
                    r = 256 * (n - 2 * NPAIRS)
                    load_slot(n, 0, a[f"{tag}_w_down_2"][0][r:r + 256, :])

        def act_high(act, tag, n, it=0):
            act.wait_ge(S(f"{tag}_raw{n % 3}"), 32 * it + (16 * (n // 3 + 1) + before(f"{tag}_raw{n % 3}")))
            act.activation(high(n), raw(n), ACT.Copy).then_inc(S(f"{tag}_high"), 1)

        def pool_ffn(pool, tag):
            def one(n, it=0):
                pool.wait_ge(S(f"{tag}_high"), 6 * it + n + 1)
                pool.tensor_tensor(low(n), raw(n), high(n).bitcast(F32), ALU.subtract)\
                    .then_inc(S(f"{tag}_low"), 1)

            with pool.Fori(0, ROUNDS) as it:
                for n in range(6):
                    one(n, it)
            for n in range(6 * ROUNDS, F_SLOTS):
                one(n)

        def pool_low(pool, tag, n):
            pool.wait_ge(S(f"{tag}_high"), n + 1 + before(f"{tag}_high"))
            pool.tensor_tensor(low(n), raw(n), high(n).bitcast(F32), ALU.subtract).then_inc(S(f"{tag}_low"), 1)

        def three(pe, dst, left, right, start, stop):
            for n, (l, r) in enumerate(((0, 0), (0, 1), (1, 0))):
                mm = pe.matmul(dst, left[l], right[r], start=start and n == 0, stop=stop and n == 2)
            return mm

        def pe_ffn(pe, tag):
            f = FIRST[tag]

            def parts(n, cols):
                return [x.rearrange("p (k n) -> p k n", n=cols) for x in (high(n), low(n))]

            def pair(pp, it):
                for which in range(2):
                    n = 2 * pp + which
                    pe.wait_ge(S(f"{tag}_low"), 6 * it + (n + 1))
                    w = parts(n, 256)
                    for j in range(2):
                        if which == 0:
                            pe.wait_ge(S(f"{tag}_free"), 6 * it + (2 * pp + j + 1) + before(f"{tag}_free"))
                        b = bank[2 * ((2 * pp + j) % 3) + which]
                        for k in range(KD):
                            mm = three(pe, b[:, :], [x[:, k, j * P:(j + 1) * P] for x in w],
                                       (hT_hi[:, k, :], hT_lo[:, k, :]), k == 0, k == KD - 1)
                        if j == 1:
                            mm.then_inc(S("slots_used"), 1)
                        elif which == 1:
                            mm.then_inc(S(f"{tag}_gu"), 1)

            with pe.Fori(0, ROUNDS) as it:
                for pp in range(3):
                    pair(pp, it)
            for pp in range(NPAIRS - 3 * ROUNDS):
                pair(pp, ROUNDS)
            pe.wait_ge(S(f"{tag}_free"), NFF + 3 + before(f"{tag}_free"))
            for i in range(NPAIRS):
                n = 2 * NPAIRS + i
                pe.wait_ge(S(f"{tag}_low"), n + 1)
                w = parts(n, D)
                for kk_ in range(2):
                    k = 2 * i + kk_
                    for t in range(NT):
                        for half in range(2):
                            c, r = slice(t * P, (t + 1) * P), slice(512 * half, 512 * half + 512)
                            mm = three(pe, bank[2 * t + half][:, :], (hid_hi[:, k, c], hid_lo[:, k, c]),
                                       [x[:, kk_, r] for x in w], k == 0, k == NFF - 1)
                mm.then_inc(S("slots_used"), 1)

        def act_ffn(act, tag):
            f = FIRST[tag]

            def unit(u, it):
                if u % 2 == 0:
                    act.wait_ge(S(f"{tag}_gu"), 3 * it + (u // 2 + 1) + before(f"{tag}_gu"))
                else:
                    act.wait_ge(S("slots_used"), 6 * it + (f + u + 1))
                act.wait_ge(S(f"{tag}_free"), 6 * it + (u + 2) + before(f"{tag}_free"))
                act.activation(f_sg[:, u % 2, :], bank[2 * (u % 3)][:, :], ACT.Silu).then_inc(S(f"{tag}_sg"), 1)

            def pair(pp, it):
                for n in (2 * pp + 2, 2 * pp + 3):
                    act_high(act, tag, n, it)
                for u in (2 * pp, 2 * pp + 1):
                    unit(u, it)

            act_high(act, tag, 0)
            act_high(act, tag, 1)
            with act.Fori(0, ROUNDS) as it:
                for pp in range(3):
                    pair(pp, it)
            for pp in range(NPAIRS - 3 * ROUNDS):
                pair(pp, ROUNDS)
            for n in range(2 * NPAIRS + 2, F_SLOTS):
                act_high(act, tag, n)

        def dve_ffn(dve, tag):
            dve.drain().then_inc(S(f"{tag}_free"), 3)

            def unit(u, it):
                dve.wait_ge(S(f"{tag}_sg"), 6 * it + (u + 1) + before(f"{tag}_sg"))
                hid = f_hid[:, u % 2, :]
                dve.tensor_tensor(hid, f_sg[:, u % 2, :], bank[2 * (u % 3) + 1][:, :], ALU.mult)
                dve.drain()
                at = [x[:, bass.ds(6 * it + u, 1), :].rearrange("p f t -> p (f t)") for x in (hid_hi, hid_lo)]
                dve.tensor_copy(at[0], hid)
                dve.drain()
                dve.tensor_tensor(at[1], hid, at[0].bitcast(F32), ALU.subtract).then_inc(S(f"{tag}_free"), 1)
                dve.drain()

            with dve.Fori(0, ROUNDS) as it:
                for u in range(6):
                    unit(u, it)
            for u in range(NFF - 6 * ROUNDS):
                unit(u, ROUNDS)

        def act_gain(act, name, after=None):
            if after is not None:
                act.wait_ge(S("slots_used"), after)
            act.dma_start(post, a[name][0:1, :].broadcast_to([P, D])).then_inc(S("post_loaded"), 16)

        def act_post(act, last):
            def root(t):
                nxt(act, "f_ss")
                act.activation(f_r[:, 1, t:t + 1], f_r[:, 0, t:t + 1], ACT.Sqrt, bias=eps, scale=1.0 / D)\
                   .then_inc(S("f_root"), 1)

            act.wait_ge(S("slots_used"), last)
            for t in range(NT):
                for half in range(2):
                    act.activation(f_sq[:, half, :], bank[2 * t + half][:, :], ACT.Square,
                                   accum_out=f_ss[:, t, half:half + 1])
                act.drain().then_inc(S("f_squares"), 1)
                if t:
                    root(t - 1)
            root(NT - 1)

        def dve_post(dve, factor):
            def total(t):
                nxt(dve, "f_squares")
                dve.tensor_tensor(f_r[:, 0, t:t + 1], f_ss[:, t, 0:1], f_ss[:, t, 1:2], ALU.add).then_inc(S("f_ss"), 1)

            nxt(dve, "post_loaded", 16)
            if factor != 1.0:
                dve.tensor_scalar(post, post, factor, None, ALU.mult)
            total(0)
            for t in range(NT):
                if t < NT - 1:
                    total(t + 1)
                nxt(dve, "f_root")
                dve.reciprocal(f_r[:, 0, t:t + 1], f_r[:, 1, t:t + 1])
                dve.drain()
                for half in range(2):
                    c = slice(512 * half, 512 * half + 512)
                    dve.scalar_tensor_tensor(f_tmp[:, t % 2, c], bank[2 * t + half][:, :], f_r[:, 0, t:t + 1],
                                             post[:, c], ALU.mult, ALU.mult)
                dve.drain()
                dve.tensor_tensor(X[:, t, :], X[:, t, :], f_tmp[:, t % 2, :], ALU.add).then_inc(S("x_new"), 1)
            dve.drain()

        d_q, d_k, d_v = ([region(6144 * g + 2048 * i, 2048, "p (h t) -> p h t", t=512) for g in range(3)]
                         for i in range(3))
        REC = 4 * HD2 + 8
        comb = [region(18432 + 2080 * g, 2080, "p (t n) -> p t n", t=NT) for g in range(3)]
        tables = [region(24672, 1024, "p (h k) -> p h k", h=4), region(25696, 512, "p (h k) -> p h k", h=4),
                  region(26208, 512, "p (h k) -> p h k", h=4)]
        Pd = region(26720, 1024, "p (b n) -> p b n", b=2)
        PdT = region(27744, 1024, "p (b n) -> p b n", b=2)
        rec = region(28768, 2 * REC, "p (b n) -> p b n", b=2)
        d_nmx = region(29808, 64)
        phase16 = Pd[:, 0, 0:P]
        BIAS = ((2 * P, 0, 3 * P), (P, P, 2 * P), (P, P, 2 * P))
        brow_dram = [nc.dram_tensor(f"bias_rows{g}", (4, P, BIAS[g][2]), F32, kind="Internal").ap() for g in range(3)]
        rec_dram = nc.dram_tensor("attention_rows", (2, T, REC), F32, kind="Internal").ap()
        buckets = region(2048, 1536)
        btab = region(3584, 12)
        brow = region(4096, 1536, "p (g j) -> p g j", g=3)

        def sp_bias(sp):
            at, _ = WHERE["bucket0"]
            sp.dma_start(buckets[0:33, :], const_dram[0:33, at:at + 1536]).then_inc(S("buckets_loaded"), 16)
            sp.dma_start(btab[0:32, :], a["rel_bias_table_2"]).then_inc(S("buckets_loaded"), 16)

        def dve_bias(dve):
            dve.memset(btab[32:33, :], 1.0).then_inc(S("btab_ones"), 1)
            nxt(dve, "brow_ps")
            for g in range(3):
                dve.tensor_copy(brow[0:12, g, :], bank[2 + g][0:12, :])
            dve.drain().then_inc(S("brow_ready"), 1)

        def pe_bias(pe):
            nxt(pe, "buckets_loaded", 32)
            nxt(pe, "btab_ones")
            for g in range(3):
                mm = pe.matmul(bank[2 + g][0:12, :], btab[0:33, :], buckets[0:33, 512 * g:512 * g + 512],
                               start=True, stop=True)
            mm.then_inc(S("brow_ps"), 1)

        def sp_bias_store(sp):
            nxt(sp, "brow_ready")
            for g, (w, lo, n) in enumerate(BIAS):
                sp.dma_start(brow_dram[g], brow[4 * g:4 * g + 4, g, lo:lo + n].unsqueeze(1).broadcast_to([4, P, n]))\
                  .then_inc(S("brow_stored"), 16)

        def act_tables(act):
            nxt(act, "brow_stored", 48)
            for g, (w, lo, n) in enumerate(BIAS):
                src = bass.AP(brow_dram[g].tensor, P - 1, [[n - 1, P], [P * n, 4], [1, w]])
                act.dma_start(tables[g], src).then_inc(S("tables_loaded"), 16)
            at, n = WHERE["phase16"]
            act.dma_start(phase16, const_dram[:, at:at + n]).then_inc(S("tables_loaded"), 16)

        def dve_tables(dve):
            nxt(dve, "tables_loaded", 64)
            dve.tensor_tensor(tables[2], tables[2], phase16.unsqueeze(1).broadcast_to([P, 4, P]), ALU.add)
            dve.drain()

        mix_hi = hT_hi
        mix_lo = region(18432 - HID, KD * T, "p (k t) -> p k t", base=split["hid_low"], t=T)
        d_vT = region(22528, 2048, "p (h t) -> p h t", t=T)
        MIX_SLOTS = FIRST["xr"] - FIRST["q0"]
        MIX_T = [(FIRST[f"{name}{g}"] + i - FIRST["q0"], g, dst[g], i)
                 for g in range(3) for name, dst in (("q", d_q), ("k", d_k), ("v", (None, None, d_vT)))
                 if dst[g] is not None for i in range(2)]

        def sp_proj2(sp):
            f = FIRST["q0"]
            for n in range(MIX_SLOTS):
                sp.wait_ge(S("slots_used"), f + max(n - 2, 0))
                src = SLOTS[f + n]
                sp.dma_start(raw(n).rearrange("p (k n) -> p k n", n=src.shape[-1]), src).then_inc(S(f"mix_raw{n % 3}"), 16)

        def pool_proj2(pool):
            for n in range(MIX_SLOTS):
                pool_low(pool, "mix", n)

        def mix_parts(n, cols):
            return [x.rearrange("p (k n) -> p k n", n=cols) for x in (high(n), low(n))]

        def pe_proj2(pe):
            pe_hT(pe)
            where = {n: g for n, g, dst, i in MIX_T}
            for n in range(MIX_SLOTS):
                pe.wait_ge(S("mix_low"), n + 1 + before("mix_low"))
                if n in where:
                    w = mix_parts(n, 256)
                    for j in range(2):
                        if n:
                            nxt(pe, f"d_taken{j}")
                        for k in range(KD):
                            mm = three(pe, bank[j][:, :], [x[:, k, j * P:(j + 1) * P] for x in w],
                                       (mix_hi[:, k, :], mix_lo[:, k, :]), k == 0, k == KD - 1)
                        if j == 0:
                            mm.then_inc(S("d_ps0"), 1)
                    mm.then_inc(S("slots_used"), 1)
                else:
                    g = 0 if n < FIRST["q1"] - FIRST["q0"] else 1
                    half = n - FIRST[f"v{g}"] + FIRST["q0"]
                    if g and half == 0:
                        nxt(pe, "d_v_taken")
                    w = mix_parts(n, 512)
                    for t in range(NT):
                        for kk_ in range(4):
                            k = 4 * half + kk_
                            at = slice(t * P, (t + 1) * P) if g == 0 else slice(t, T, DILATIONS[1])
                            mm = three(pe, bank[2 + t][:, :], (mix_hi[:, k, at], mix_lo[:, k, at]),
                                       [x[:, kk_, :] for x in w], k == 0, k == KD - 1)
                    mm.then_inc(S("slots_used"), 1)
            nxt(pe, "d_v_taken")
            for j in range(2):
                nxt(pe, f"d_taken{j}")
            for t in range(NT):
                for h in range(4):
                    mm = pe.transpose(bank[2 + t][:, h * P:(h + 1) * P], d_vT[:, h, t * P:(t + 1) * P], ident)
            mm.then_inc(S("d_vT_turned"), 1)

        def unphased(x, dil):
            return x.rearrange("p (d l) -> p l d", d=dil)

        def act_proj2(act):
            for n in range(2):
                act_high(act, "mix", n)
            where = {n: (g, dst, i) for n, g, dst, i in MIX_T}
            for n in range(MIX_SLOTS):
                if n + 2 < MIX_SLOTS:
                    act_high(act, "mix", n + 2)
                if n in where:
                    g, dst, i = where[n]
                    nxt(act, "d_ps0")
                    act.activation(unphased(dst[:, 2 * i, :], DILATIONS[g]),
                                   bank[0][:, :].rearrange("p (l d) -> p l d", d=DILATIONS[g]), ACT.Copy)\
                       .then_inc(S("d_taken0"), 1)
            act.wait_ge(S("slots_used"), FIRST["xr"])

        def dve_proj2(dve):
            def values(g):
                for t in range(NT):
                    i = dve.tensor_copy(d_v[g][:, t, :], bank[2 + t][:, :])
                i.then_inc(S("d_v_taken"), 1)

            for n, g, dst, i in MIX_T:
                if g and n == FIRST[f"q{g}"] - FIRST["q0"]:
                    dve.wait_ge(S("slots_used"), FIRST[f"v{g - 1}"] + 2)
                    values(g - 1)
                dve.wait_ge(S("slots_used"), FIRST["q0"] + n + 1)
                dve.tensor_copy(unphased(dst[:, 2 * i + 1, :], DILATIONS[g]),
                                bank[1][:, :].rearrange("p (l d) -> p l d", d=DILATIONS[g]))\
                   .then_inc(S("d_taken1"), 1)
            nxt(dve, "d_vT_turned")
            values(2)

        DUNITS = [(0, n, hs, max(n - 1, 0), P if n == 0 else 2 * P) for n in range(NT) for hs in ((0, 1), (2, 3))]
        DUNITS += [(g, i, (0, 1, 2, 3), i, P) for g in (1, 2) for i in range(NT)]

        def record(u):
            g, i, hs, k0, w = DUNITS[u]
            return comb[0][:, i, :] if g == 0 else rec[:, u % 2, :]

        def pe_dil(pe):
            def scores(u):
                g, i, hs, k0, w = DUNITS[u]
                if u >= 2:
                    nxt(pe, "d_s_taken")
                for n, h in enumerate(hs):
                    mm = pe.matmul(bank[u % 2][:, n * w:(n + 1) * w], d_q[g][:, h, i * P:(i + 1) * P],
                                   d_k[g][:, h, k0 * P:k0 * P + w], start=True, stop=True)
                mm.then_inc(S("d_scores"), 1)

            def turn(u):
                g, i, hs, k0, w = DUNITS[u]
                nxt(pe, "d_p")
                for n in range(len(hs) * w // P):
                    mm = pe.transpose(bank[2 + u % 2][:, n * P:(n + 1) * P], Pd[:, u % 2, n * P:(n + 1) * P], ident)
                mm.then_inc(S("d_p_turned"), 1)

            def values(u):
                g, i, hs, k0, w = DUNITS[u]
                nxt(pe, "d_pT")
                if u >= 2:
                    nxt(pe, "d_o_taken")
                nb = w // P
                for n, h in enumerate(hs):
                    for b in range(nb):
                        c = (n * nb + b) * P
                        mm = pe.matmul(bank[4 + u % 2][:, n * HD2:(n + 1) * HD2], PdT[:, u % 2, c:c + P],
                                       d_v[g][:, k0 + b, h * HD2:(h + 1) * HD2], start=(b == 0), stop=(b == nb - 1))
                mm.then_inc(S("d_values"), 1)

            scores(0)
            for u in range(len(DUNITS)):
                if u + 1 < len(DUNITS):
                    scores(u + 1)
                turn(u)
                if u:
                    values(u - 1)
            values(len(DUNITS) - 1)

        def dve_dil(dve):
            def outputs(u):
                g, i, hs, k0, w = DUNITS[u]
                nxt(dve, "d_values")
                dve.tensor_copy(record(u)[:, hs[0] * HD2:(hs[-1] + 1) * HD2], bank[4 + u % 2][:, 0:len(hs) * HD2])
                dve.drain().then_inc(S("d_o_taken"), 1)

            for u, (g, i, hs, k0, w) in enumerate(DUNITS):
                nh = len(hs)
                nxt(dve, "d_scores")
                if u >= 2:
                    nxt(dve, "d_p_turned")
                p3 = Pd[:, u % 2, 0:nh * w].rearrange("p (h k) -> p h k", h=nh)
                tab = tables[g][:, hs[0]:hs[-1] + 1, :]
                tab = tab[:, :, 2 * P - w:2 * P] if g == 0 else tab
                dve.scalar_tensor_tensor(p3, bank[u % 2][:, 0:nh * w].rearrange("p (h k) -> p h k", h=nh),
                                         HD2 ** -0.5, tab, ALU.mult, ALU.add).then_inc(S("d_s_taken"), 1)
                dve.drain()
                if g and u >= 10:
                    n_st = 1 if DUNITS[u - 2][0] == 1 else 4
                    nxt(dve, f"rec_stored{u % 2}", 16 * n_st)
                mx = record(u)[:, 512 + hs[0]:512 + hs[-1] + 1]
                dve.tensor_reduce(mx, p3, AX_X, ALU.max)
                dve.drain()
                dve.tensor_scalar(d_nmx[:, 4 * u:4 * u + nh], mx, -1.0, None, ALU.mult).then_inc(S("d_max"), 1)
                if u:
                    outputs(u - 1)
            outputs(len(DUNITS) - 1)

        def act_dil(act):
            def exps(u):
                g, i, hs, k0, w = DUNITS[u]
                nxt(act, "d_max")
                for n, h in enumerate(hs):
                    p = Pd[:, u % 2, n * w:(n + 1) * w]
                    act.activation(p, p, ACT.Exp, bias=d_nmx[:, 4 * u + n:4 * u + n + 1],
                                   accum_out=record(u)[:, 516 + h:517 + h])
                act.drain().then_inc(S("d_p"), 1)

            def copy(u):
                g, i, hs, k0, w = DUNITS[u]
                n = len(hs) * w
                nxt(act, "d_p_turned")
                if u >= 2:
                    nxt(act, "d_values")
                act.activation(PdT[:, u % 2, 0:n], bank[2 + u % 2][:, 0:n], ACT.Copy)
                act.drain().then_inc(S("d_pT"), 1)

            exps(0)
            for u in range(len(DUNITS)):
                if u + 1 < len(DUNITS):
                    exps(u + 1)
                copy(u)

        def pool_dil(pool):
            for u, (g, i, hs, k0, w) in enumerate(DUNITS):
                if g == 0:
                    continue
                pool.wait_ge(S("d_o_taken"), u + 1 + before("d_o_taken"))
                pool.wait_ge(S("d_p"), u + 1 + before("d_p"))
                rows_ = rec_dram[g - 1].rearrange("(l d) c -> d l c", d=DILATIONS[g])
                if g == 1:
                    pool.dma_start(rows_[i], rec[:, u % 2, :]).then_inc(S(f"rec_stored{u % 2}"), 16)
                else:
                    for q in range(4):
                        pool.dma_start(rows_[4 * i + q], rec[32 * q:32 * q + 32, u % 2, :])\
                            .then_inc(S(f"rec_stored{u % 2}"), 16)

        def sp_records(sp):
            for g in (1, 2):
                for b in range(2):
                    sp.wait_ge(S(f"rec_stored{b}"), 16 * (2 if g == 1 else 2 + 8))
                sp.dma_start(comb[g], rec_dram[g - 1].rearrange("(t p) c -> p t c", p=P))\
                  .then_inc(S("rec_loaded"), 16)

        c_m = region(4096, 16, "p (t h) -> p t h", t=NT)
        c_e = [region(4112 + 16 * g, 16, "p (t h) -> p t h", t=NT) for g in range(3)]
        c_x = [region(4160 + 16 * g, 16, "p (t h) -> p t h", t=NT) for g in range(3)]
        c_s = region(4208, 16, "p (t h) -> p t h", t=NT)
        attn = region(0, 2048, "p (t n) -> p t n", t=NT)
        attnT2 = region(2048, 2048, "p (k t) -> p k t", t=T)

        def dve_combine(dve):
            nxt(dve, "rec_loaded", 32)
            mx = [comb[g][:, :, 512:516] for g in range(3)]
            den = [comb[g][:, :, 516:520] for g in range(3)]
            dve.tensor_tensor(c_m, mx[0], mx[1], ALU.max)
            dve.drain()
            dve.tensor_tensor(c_m, c_m, mx[2], ALU.max)
            dve.drain()
            for g in range(3):
                dve.tensor_tensor(c_e[g], mx[g], c_m, ALU.subtract)
            dve.drain().then_inc(S("c_diff"), 1)
            nxt(dve, "c_exp")
            for g in range(3):
                dve.tensor_tensor(c_x[g], c_e[g], den[g], ALU.mult)
            dve.drain()
            dve.tensor_tensor(c_s, c_x[0], c_x[1], ALU.add)
            dve.drain()
            dve.tensor_tensor(c_s, c_s, c_x[2], ALU.add)
            dve.drain()
            dve.reciprocal(c_m, c_s)
            dve.drain()
            for g in range(3):
                dve.tensor_tensor(c_e[g], c_e[g], c_m, ALU.mult)
            dve.drain()
            for g in range(3):
                for t in range(NT):
                    o = comb[g][:, t, 0:512].rearrange("p (h e) -> p h e", h=4)
                    dve.tensor_tensor(o, o, c_e[g][:, t, :].unsqueeze(2).broadcast_to([P, 4, HD2]), ALU.mult)
            dve.drain()
            dve.tensor_tensor(attn, comb[0][:, :, 0:512], comb[1][:, :, 0:512], ALU.add)
            dve.drain()
            dve.tensor_tensor(attn, attn, comb[2][:, :, 0:512], ALU.add)
            dve.drain().then_inc(S("attn_ready"), 1)

        def act_combine(act):
            nxt(act, "c_diff")
            for g in range(3):
                act.activation(c_e[g], c_e[g], ACT.Exp)
            act.drain().then_inc(S("c_exp"), 1)

        def act_attn(act):
            nxt(act, "attn_turned")
            for k in range(4):
                act.activation(attnT2[:, k, :], bank[4 + k][:, :], ACT.Copy)
            act.drain().then_inc(S("attnT_ready"), 1)

        def pe_combine(pe):
            nxt(pe, "attn_ready")
            for k in range(4):
                for t in range(NT):
                    mm = pe.transpose(bank[4 + k][:, t * P:(t + 1) * P], attn[:, t, k * P:(k + 1) * P], ident)
            mm.then_inc(S("attn_turned"), 1)

        l_in = region(28768, 1040, "p (b t) -> p b t", b=2)
        l_gx, l_xc, l_t, l_q, l_r = (region(4096 * (i + 1), 4096, "p (m t) -> p m t", t=T) for i in range(5))
        l_gy = l_xc
        rec_hi = region(3 * 4096 - HID, 4096, "p (m t) -> p m t", base=split["hid_low"], t=T)
        rec_lo = region(4096, 4096, "p (m t) -> p m t", base=split["hid_high"], t=T)
        l_c = region(29808, 8)
        l_e, l_z, l_p, l_s = (region(29816 + 8 * i, 8) for i in range(4))
        merged = l_q
        s_gate = l_xc[:, 0:4, :]
        s_val = l_xc[:, 4:8, :]

        def col2(name, i):
            at, _ = col(name, VEC2)
            return cols2[:, at + i:at + i + 1]

        REST = FIRST["xr"]
        N_REST = FIRST["ffn2"] - REST
        SPLIT = [FIRST[name] + i - REST for name, c in
                 [("xr", 4), ("yr", 4)] + [x for q in range(4) for x in ((f"gl{q}", 2), (f"rec{q}", 1))]
                 for i in range(c)]

        def sp_rest(sp):
            for n in range(N_REST):
                sp.wait_ge(S("slots_used"), REST + max(n - 2, 0))
                src = SLOTS[REST + n]
                cols = src.shape[-1]
                sp.dma_start(raw(n)[:, 0:src.shape[1] * cols].rearrange("p (k n) -> p k n", n=cols), src)\
                  .then_inc(S(f"rest_raw{n % 3}"), 16)
                if n == 2:
                    sp_records(sp)

        def act_rest(act, n):
            if n in SPLIT:
                act_high(act, "rest", n)

        def pool_rest(pool, i0, i1):
            for i, n in list(enumerate(SPLIT))[i0:i1]:
                pool.wait_ge(S("rest_high"), i + 1 + before("rest_high"))
                pool.tensor_tensor(low(n), raw(n), high(n).bitcast(F32), ALU.subtract).then_inc(S("rest_low"), 1)

        def need_rest(pe, n):
            if n in SPLIT:
                pe.wait_ge(S("rest_low"), SPLIT.index(n) + 1 + before("rest_low"))
                return mix_parts(n, 256)
            pe.wait_ge(S(f"rest_raw{n % 3}"), 16 * (n // 3 + 1) + before(f"rest_raw{n % 3}"))
            cols = SLOTS[REST + n].shape[-1]
            return raw(n)[:, 0:SLOTS[REST + n].shape[1] * cols].rearrange("p (k n) -> p k n", n=cols)

        def act_hT_parts(act):
            for k in range(KD):
                act.activation(hT_hi[:, k, :], hT[:, k, :], ACT.Copy)
            act.drain().then_inc(S("l_hT_high"), 1)

        def dve_hT_parts(dve):
            nxt(dve, "l_hT_high")
            for k in range(KD):
                dve.tensor_tensor(hT_lo[:, k, :], hT[:, k, :], hT_hi[:, k, :].bitcast(F32), ALU.subtract)
            dve.drain().then_inc(S("l_hT_low"), 1)

        def pe_split_t(pe, dst, w, j, hi, lo):
            for k in range(KD):
                mm = three(pe, dst[:, :], [x[:, k, j * P:(j + 1) * P] for x in w], (hi[:, k, :], lo[:, k, :]),
                           k == 0, k == KD - 1)
            return mm

        def pe_lru(pe):
            nxt(pe, "l_hT_low")
            for m in range(KD):
                i, j = m // 2, m % 2
                if j == 0:
                    w = need_rest(pe, i)
                if m >= 2:
                    nxt(pe, "l_in")
                mm = pe_split_t(pe, bank[j], w, j, hT_hi, hT_lo)
                if j == 0:
                    mm.then_inc(S("l_ps"), 1)
                else:
                    mm.then_inc(S("slots_used"), 1)
            nxt(pe, "l_in", 2)
            pe_combine(pe)
            nxt(pe, "attnT_ready")
            w_lru = [need_rest(pe, FIRST["lru"] - REST + which) for which in range(2)]
            for m in range(KD):
                h, j = m // 2, m % 2
                pe.wait_ge(S("l_conv"), 2 * h + 2 + before("l_conv"))
                if m >= 2:
                    nxt(pe, "l_gates")
                for which in range(2):
                    w = w_lru[which]
                    for i in range(2):
                        mm = pe.matmul(bank[2 + 2 * j + which][:, :], w[:, 2 * h + i, j * P:(j + 1) * P],
                                       l_xc[:, 2 * h + i, :], start=(i == 0), stop=(i == 1))
                    if which == 0 and m == KD - 1:
                        mm.then_inc(S("slots_used"), 1)
                if m < KD - 1:
                    mm.then_inc(S("l_gate_ps"), 1)
                else:
                    mm.then_inc(S("slots_used"), 1)
            for m in range(KD):
                i, j = m // 2, m % 2
                if j == 0:
                    w = need_rest(pe, FIRST["yr"] - REST + i)
                if m >= 4:
                    nxt(pe, "l_gelu")
                mm = pe_split_t(pe, bank[Y_BANKS[m % 4]], w, j, hT_hi, hT_lo)
                if j == 0:
                    mm.then_inc(S("l_y_ps"), 1)
                else:
                    mm.then_inc(S("slots_used"), 1)

        Y_BANKS = (6, 7, 0, 1)

        def act_lru(act):
            act_hT_parts(act)
            nxt(act, "l_abs")
            act.activation(l_e, l_z, ACT.Exp, scale=-1.0).then_inc(S("l_exp"), 1)
            act_combine(act)
            for m in range(KD):
                j = m % 2
                if j == 0:
                    act_rest(act, m // 2 + 2)
                    nxt(act, "l_ps")
                else:
                    act.wait_ge(S("slots_used"), FIRST["xr"] + m // 2 + 1)
                if m >= 2:
                    act.wait_ge(S("l_conv"), m - 1 + before("l_conv"))
                act.activation(l_in[:, j, 3:3 + T], bank[j][:, :], ACT.Copy).then_inc(S("l_in"), 1)
            act_attn(act)
            nxt(act, "l_c")
            act_rest(act, FIRST["yr"] - REST)
            for m in range(KD):
                j = m % 2
                if m < KD - 1:
                    nxt(act, "l_gate_ps")
                else:
                    act.wait_ge(S("slots_used"), FIRST["lru"] + 2)
                act.activation(l_gx[:, m, :], bank[2 + 2 * j][:, :], ACT.Sigmoid, bias=col2("lru_b_x_2", m))
                act.activation(l_t[:, m, :], bank[3 + 2 * j][:, :], ACT.Sigmoid, bias=col2("lru_b_a_2", m))
                act.drain().then_inc(S("l_gates"), 1)
                act.activation(l_t[:, m, :], l_t[:, m, :], ACT.Tanh, scale=l_c[:, m:m + 1])
            act.drain().then_inc(S("l_tanh"), 1)
            act_rest(act, FIRST["yr"] - REST + 1)
            nxt(act, "l_floor")
            for m in range(KD):
                act.activation(l_q[:, m, :], l_t[:, m, :], ACT.Sqrt).then_inc(S("l_sqrt"), 1)
            for m in range(KD):
                j = m % 2
                if j == 0:
                    act_rest(act, FIRST["yr"] - REST + m // 2 + 2)
                    nxt(act, "l_y_ps")
                else:
                    act.wait_ge(S("slots_used"), FIRST["yr"] + m // 2 + 1)
                nxt(act, "l_mixed")
                act.activation(l_gy[:, m, :], bank[Y_BANKS[m % 4]][:, :], ACT.Gelu_apprx_tanh)\
                   .then_inc(S("l_gelu"), 1)
            for m in range(KD):
                nxt(act, "l_rec")
                act.activation(rec_hi[:, m, :], l_r[:, m, :], ACT.Copy).then_inc(S("rec_high"), 1)

        def dve_lru(dve):
            dve_hT_parts(dve)
            at, _ = col("lru_a_param_2", VEC2)
            ap_ = cols2[:, at:at + 8]
            dve.scalar_tensor_tensor(l_z, ap_, -1.0, ap_, ALU.mult, ALU.max).then_inc(S("l_abs"), 1)
            nxt(dve, "l_exp")
            dve_log1p(dve, l_e, l_z, l_p, l_s)
            dve.tensor_scalar(l_z, ap_, -1.0, 0.0, ALU.mult, ALU.max)
            dve.drain()
            dve.tensor_tensor(l_s, l_z, l_s, ALU.add)
            dve.drain()
            dve.tensor_scalar(l_c, l_s, 4.0, None, ALU.mult)
            dve.drain().then_inc(S("l_c"), 1)
            dve_combine(dve)
            dve.memset(l_in[:, :, 0:3], 0.0)
            dve.drain()
            for m in range(KD):
                j = m % 2
                dve.wait_ge(S("l_in"), m + 1 + before("l_in"))
                dve.tensor_scalar(l_xc[:, m, :], l_in[:, j, 3:3 + T], col2("conv_w_2", 24 + m),
                                  col2("conv_b_2", m), ALU.mult, ALU.add)
                for tap in range(3):
                    dve.drain()
                    dve.scalar_tensor_tensor(l_xc[:, m, :], l_in[:, j, tap:tap + T], col2("conv_w_2", 8 * tap + m),
                                             l_xc[:, m, :], ALU.mult, ALU.add)
                dve.drain().then_inc(S("l_conv"), 1)
            nxt(dve, "l_tanh")
            dve.tensor_scalar(l_t, l_t, 1.0e-30, None, ALU.max)
            dve.drain().then_inc(S("l_floor"), 1)
            dve.tensor_scalar(l_r, l_t, -1.0, -1.0, ALU.mult, ALU.add)
            dve.drain()
            for m in range(KD):
                dve.reciprocal(l_r[:, m, :], l_r[:, m, :])
                dve.tensor_tensor(l_gx[:, m, :], l_gx[:, m, :], l_xc[:, m, :], ALU.mult)
                dve.drain().then_inc(S("l_mixed"), 1)
                nxt(dve, "l_sqrt")
                dve.scalar_tensor_tensor(l_t[:, m, :], l_t[:, m, :], -1.0, l_r[:, m, :], ALU.add, ALU.mult)
                dve.scalar_tensor_tensor(l_q[:, m, :], l_r[:, m, :], -2.0, l_q[:, m, :], ALU.mult, ALU.mult)
                dve.drain()
                dve.tensor_tensor(l_q[:, m, :], l_q[:, m, :], l_gx[:, m, :], ALU.mult)
                dve.drain()
                dve.tensor_tensor_scan(l_r[:, m, :], l_t[:, m, :], l_q[:, m, :], 0.0, ALU.mult, ALU.add)
                dve.drain()
            for m in range(KD):
                nxt(dve, "l_gelu")
                dve.tensor_tensor(l_r[:, m, :], l_r[:, m, :], l_gy[:, m, :], ALU.mult).then_inc(S("l_rec"), 1)
            for m in range(KD):
                nxt(dve, "rec_high")
                dve.tensor_tensor(rec_lo[:, m, :], l_r[:, m, :], rec_hi[:, m, :].bitcast(F32), ALU.subtract)
            dve.drain().then_inc(S("rec_ready"), 1)

        def pe_merge(pe):
            for q in range(4):
                first = FIRST[f"gl{q}"] - REST
                for b in range(2):
                    w = need_rest(pe, first + b)
                    if b == 0 and q:
                        nxt(pe, "m_sigmoids")
                    elif b == 0:
                        nxt(pe, "l_gelu", 4)
                    for j in range(2):
                        mm = pe_split_t(pe, bank[4 * j + b], w, j, hT_hi, hT_lo)
                    mm.then_inc(S("slots_used"), 1)
                w = need_rest(pe, first + 2)
                if q:
                    nxt(pe, "m_merged")
                for j in range(2):
                    for k in range(4):
                        mm = pe.matmul(bank[4 * j + 2][:, :], w[:, k, j * P:(j + 1) * P], attnT2[:, k, :],
                                       start=(k == 0), stop=(k == 3))
                mm.then_inc(S("slots_used"), 1)
                w = need_rest(pe, first + 3)
                if q == 0:
                    nxt(pe, "rec_ready")
                for j in range(2):
                    mm = pe_split_t(pe, bank[4 * j + 3], w, j, rec_hi, rec_lo)
                mm.then_inc(S("slots_used"), 1)

        def act_merge(act):
            for q in range(4):
                first = FIRST[f"gl{q}"] - REST
                act_rest(act, first + 3)
                act.wait_ge(S("slots_used"), REST + first + 2)
                if q:
                    nxt(act, "m_merged")
                for j in range(2):
                    for b in range(2):
                        act.activation(s_gate[:, 2 * j + b, :], bank[4 * j + b][:, :], ACT.Sigmoid)
                act.drain().then_inc(S("m_sigmoids"), 1)
                if q < 3:
                    act_rest(act, first + 4)
                    act_rest(act, first + 5)

        def dve_merge(dve):
            for q in range(4):
                nxt(dve, "m_sigmoids")
                dve.wait_ge(S("slots_used"), FIRST[f"rec{q}"] + 1)
                for j in range(2):
                    for b in range(2):
                        dve.tensor_tensor(s_val[:, 2 * j + b, :], s_gate[:, 2 * j + b, :],
                                          bank[4 * j + 2 + b][:, :], ALU.mult)
                dve.drain()
                for j in range(2):
                    dve.tensor_tensor(merged[:, 2 * q + j, :], s_val[:, 2 * j, :], s_val[:, 2 * j + 1, :], ALU.add)
                dve.drain().then_inc(S("m_merged"), 1)

        def pe_out2(pe):
            for i in range(4):
                w = need_rest(pe, FIRST["w_out2"] - REST + i)
                for kk_ in range(2):
                    k = 2 * i + kk_
                    for t in range(NT):
                        for half in range(2):
                            mm = pe.matmul(bank[2 * t + half][:, :], merged[:, k, t * P:(t + 1) * P],
                                           w[:, kk_, 512 * half:512 * half + 512], start=(k == 0), stop=(k == KD - 1))
                mm.then_inc(S("slots_used"), 1)

        def sp_out(sp):
            nxt(sp, "x_new", 2 * NT)
            for t in range(NT):
                nxt(sp, "x_new")
                sp.dma_start(out[t * P:(t + 1) * P, :], X[:, t, :]).then_inc(S("out_stored"), 16)
            sp.wait_ge(S("out_stored"), 16 * NT)

        block = ctx.enter_context(nc.Block())

        def c1(i):
            return mod[:, i:i + 8]

        def gain2(name):
            at, n = col(name, VEC2)
            return cols2[:, at:at + n]

        @block.sync
        def _(sp):
            sp_small(sp)
            load(sp, 0, 4)
            sp_x(sp)
            sp_bias(sp)
            load(sp, 4, 4)
            sp_bias_store(sp)
            load(sp, 8, FIRST["ada2"] - 8)
            sp_positions(sp)
            load(sp, FIRST["ada2"], MOE_AT - FIRST["ada2"])
            sp_moe_first(sp)
            sp_more(sp)
            sp_moe(sp)
            sp.wait_ge(S("gu_used"), N_EXP)
            sp.wait_ge(S("dn_used"), N_EXP)
            sp_ffn(sp, "ffn1")
            sp_proj2(sp)
            sp_rest(sp)
            sp_ffn(sp, "ffn2")
            sp_out(sp)

        @block.scalar
        def _(act):
            act_small(act)
            act_c(act)
            nxt(act, "x_loaded", 16 * NT)
            nxt(act, "mod_ready")
            act_norm(act, junk1, c1(8), c1(0))
            act_proj1(act)
            act_qkv(act)
            meet(act)
            act_swa_prep(act)
            act_swa_turn(act)
            act_swa(act)
            meet(act)
            act_gdn_prep(act)
            for t in range(NT):
                act_gdn(act, t)
            act_gdn_end(act)
            act_turned(act)
            meet(act)
            act_router_weights(act)
            nxt(act, "mod_ready")
            act_norm(act, junk2, c1(32), c1(24))
            act_h2(act)
            act_route(act)
            act_more(act)
            act_moe(act)
            act_moe_end(act)
            meet(act)
            act_norm(act, junkf, gain2("ffn1_norm_pre_2"), None, hT_hi)
            act_ffn(act, "ffn1")
            act_gain(act, "ffn1_norm_post_2", FIRST["ffn1"] + 2 * NPAIRS)
            act_post(act, FIRST["ffn1_down"] + NPAIRS)
            act_norm(act, region(0, D), gain2("mix_norm_pre_2"), None, mix_hi, x_new=True)
            act_proj2(act)
            act_tables(act)
            meet(act)
            act_rest(act, 0)
            act_rest(act, 1)
            act_dil(act)
            meet(act)
            act_lru(act)
            act_merge(act)
            meet(act)
            act_gain(act, "mix_norm_post_2")
            act_post(act, FIRST["w_out2"] + 4)
            act_norm(act, junkf, gain2("ffn2_norm_pre_2"), None, hT_hi, x_new=True)
            act_ffn(act, "ffn2")
            act_gain(act, "ffn2_norm_post_2", FIRST["ffn2"] + 2 * NPAIRS)
            act_post(act, FIRST["ffn2_down"] + NPAIRS)

        @block.tensor
        def _(pe):
            pe_small(pe)
            pe_ada(pe, "ada1", 0, 16, 7)
            pe_bias(pe)
            pe_turn(pe, xn1, ("xn_ready",))
            pe_hT(pe)
            pe_proj1(pe)
            pe_qkv(pe)
            meet(pe)
            pe_ada(pe, "ada2", 16, 48, 7)
            pe_swa_turn(pe)
            pe_swa(pe)
            meet(pe)
            pe_gdn_prep(pe)
            for t in range(NT):
                pe_gdn(pe, t)
            pe_gate(pe, diag1, 0)
            nxt(pe, "gate_taken")
            pe_turn(pe, mixed, ("mixed_ready",))
            pe_hT(pe)
            pe_down(pe, "w_out", 4, tokens)
            meet(pe)
            pe_turn(pe, xn2, ("xn_ready",))
            pe_route(pe)
            pe_gate(pe, diag2, 6)
            pe_more(pe)
            pe_moe(pe)
            pe_moe_end(pe)
            meet(pe)
            pe_turn(pe, xnf, ("xn_ready",))
            pe_hT(pe)
            pe_ffn(pe, "ffn1")
            pe_turn(pe, xn3, ("xn_ready",))
            pe_proj2(pe)
            meet(pe)
            pe_dil(pe)
            meet(pe)
            pe_lru(pe)
            pe_merge(pe)
            nxt(pe, "m_merged")
            meet(pe)
            pe_out2(pe)
            pe_turn(pe, xnf, ("xn_ready",))
            pe_hT(pe)
            pe_ffn(pe, "ffn2")

        @block.vector
        def _(dve):
            dve_small(dve)
            nxt(dve, "x_loaded", 16 * NT)
            dve_ada(dve, 0, 16, 7)
            dve_bias(dve)
            dve_norm(dve, xn1, c1(8), c1(0))
            dve_proj1(dve)
            meet(dve)
            dve_swa_prep(dve)
            dve_ada(dve, 16, 48, 7)
            dve_swa_turn(dve)
            dve_swa(dve)
            meet(dve)
            dve_gdn_prep(dve)
            for t in range(NT):
                dve_gdn(dve, t)
            dve_gate(dve, diag1, 16)
            dve_gate_row(dve, gate1, 0)
            dve_gdn_end(dve)
            dve_turned(dve)
            dve_out1(dve)
            meet(dve)
            dve_norm(dve, xn2, c1(32), c1(24))
            dve_route(dve)
            dve_gate(dve, diag2, 40)
            dve_more_list(dve)
            dve_gate_row(dve, gate2, 6)
            dve_more(dve)
            dve_moe(dve)
            dve_moe_end(dve)
            meet(dve)
            dve_norm(dve, xnf, gain2("ffn1_norm_pre_2"), None, (hT_hi, hT_lo), 4)
            dve_ffn(dve, "ffn1")
            dve_post(dve, 0.5)
            dve_norm(dve, xn3, gain2("mix_norm_pre_2"), None, (mix_hi, mix_lo), 5)
            dve_proj2(dve)
            dve_tables(dve)
            meet(dve)
            dve_dil(dve)
            meet(dve)
            dve_lru(dve)
            dve_merge(dve)
            meet(dve)
            dve_post(dve, 1.0)
            dve_norm(dve, xnf, gain2("ffn2_norm_pre_2"), None, (hT_hi, hT_lo), 6)
            dve_ffn(dve, "ffn2")
            dve_post(dve, 0.5)

        @block.gpsimd
        def _(pool):
            meet(pool)
            meet(pool)
            for t in range(NT):
                pool_gdn(pool, t)
            meet(pool)
            pool_route(pool)
            meet(pool)
            pool_ffn(pool, "ffn1")
            pool_proj2(pool)
            meet(pool)
            pool_rest(pool, 0, 2)
            pool_dil(pool)
            meet(pool)
            pool_rest(pool, 2, len(SPLIT))
            meet(pool)
            pool_ffn(pool, "ffn2")


def kernel(**inputs):
    import concourse.bacc as bacc
    from concourse.bass_utils import run_bass_kernel_spmd

    nc = bacc.Bacc("TRN2", target_bir_lowering=False, num_devices=1)
    arrays, args = {}, {}
    for name in NAMES:
        v = np.ascontiguousarray(inputs[name])
        arrays[f"in_{name}"] = v
        args[name] = nc.dram_tensor(f"in_{name}", v.shape, mybir.dt.from_np(v.dtype), kind="ExternalInput").ap()
    arrays["constants_dram"] = POSITION_CONSTANTS
    const_dram = nc.dram_tensor("constants_dram", POSITION_CONSTANTS.shape, F32, kind="ExternalInput").ap()
    out = nc.dram_tensor("out", (T, D), F32, kind="ExternalOutput").ap()
    build(nc, args, const_dram, out)
    r = run_bass_kernel_spmd(nc, [arrays], core_ids=[0])
    return r.results[0]["out"].reshape(1, T, D)
```
